# Optimizing a Trainium2 kernel written in Bass

```python
import math
import jax
import jax.numpy as jnp
from jax import lax
import numpy as np

D_MODEL = 1024
BATCH = 1
SEQ = 512
DEPTH = 2
DEC_BATCH = 8
DEC_SEQ = 1
PAST_LEN = 1024
PAGE_SIZE = 128

N_EVEN = (DEPTH + 1) // 2
N_ODD = DEPTH // 2
EPS = 1e-6
BLOCK = 128
NEG = -1e30

SW_HEADS = 8
SW_KV_HEADS = 2
SW_GROUP = SW_HEADS // SW_KV_HEADS
SW_HEAD_DIM = 64
SW_WINDOW = 128
SW_ROT_DIM = SW_HEAD_DIM // 4
ROPE_THETA = 500000.0

ML_HEADS = 4
ML_QK_DIM = 64
ML_V_DIM = 128

SSD_HEADS = 16
SSD_HEAD_DIM = 64
SSD_INNER = SSD_HEADS * SSD_HEAD_DIM
SSD_GROUPS = 2
SSD_STATE = 128
SSD_CONV = 4
SSD_CONV_DIM = SSD_INNER + 2 * SSD_GROUPS * SSD_STATE

RET_HEADS = 4
RET_QK_DIM = 128
RET_V_DIM = 128
RET_ROPE_THETA = 10000.0

MEM_LEN = 256
MEM_HEADS = 4
MEM_HEAD_DIM = 128
MEM_WIDTH = MEM_HEADS * MEM_HEAD_DIM

FFN_DIM = 4 * D_MODEL

EVEN_SIZES = (SW_HEADS * SW_HEAD_DIM, SW_KV_HEADS * SW_HEAD_DIM, SW_KV_HEADS * SW_HEAD_DIM,
              ML_HEADS * ML_QK_DIM, ML_HEADS * ML_QK_DIM, ML_HEADS * ML_V_DIM, ML_HEADS * ML_V_DIM,
              ML_HEADS, ML_HEADS)
EVEN_IN = sum(EVEN_SIZES)
EVEN_OUT = SW_HEADS * SW_HEAD_DIM + ML_HEADS * ML_V_DIM
ODD_SIZES = (SSD_INNER, SSD_CONV_DIM, SSD_HEADS,
             RET_HEADS * RET_QK_DIM, RET_HEADS * RET_QK_DIM, RET_HEADS * RET_V_DIM, RET_HEADS * RET_V_DIM)
ODD_IN = sum(ODD_SIZES)
ODD_OUT = SSD_INNER + RET_HEADS * RET_V_DIM

kernel_name = 'hybrid_swa_mlstm_ssd_retention_decode_step'

def split_cols(a, sizes):
    idx = [int(i) for i in np.cumsum(sizes)[:-1]]
    return jnp.split(a, idx, axis=-1)

def rmsnorm(x, g):
    xf = x.astype(jnp.float32)
    y = xf * lax.rsqrt(jnp.mean(xf * xf, axis=-1, keepdims=True) + EPS)
    return (y * g.astype(jnp.float32)).astype(x.dtype)

def group_norm(x, g):
    xf = x.astype(jnp.float32)
    mu = jnp.mean(xf, axis=-1, keepdims=True)
    xc = xf - mu
    var = jnp.mean(xc * xc, axis=-1, keepdims=True)
    return xc * lax.rsqrt(var + EPS) * g.astype(jnp.float32)

def rope(x, pos, rot_dim, theta):
    half = rot_dim // 2
    inv = jnp.power(jnp.float32(theta), -jnp.arange(half, dtype=jnp.float32) * (2.0 / rot_dim))
    ang = pos.astype(jnp.float32)[:, None] * inv[None, :]
    cos = jnp.cos(ang)[:, None, :]
    sin = jnp.sin(ang)[:, None, :]
    xr = x[..., :rot_dim].astype(jnp.float32)
    x1, x2 = xr[..., :half], xr[..., half:]
    rot = jnp.concatenate([x1 * cos - x2 * sin, x2 * cos + x1 * sin], axis=-1).astype(x.dtype)
    return jnp.concatenate([rot, x[..., rot_dim:]], axis=-1)

def to_chunks(a, L):
    a = a.reshape((a.shape[0], a.shape[1] // L, L) + a.shape[2:])
    return a.transpose((1, 0, 3, 2) + tuple(range(4, a.ndim)))

def from_chunks(a):
    a = a.transpose((1, 0, 3, 2) + tuple(range(4, a.ndim)))
    return a.reshape((a.shape[0], a.shape[1] * a.shape[2]) + a.shape[3:])

def sink_probs(scores, valid, sink):
    s = jnp.where(valid, scores, NEG)
    m = jnp.maximum(jnp.max(s, axis=-1, keepdims=True), sink)
    p = jnp.exp(s - m)
    return p / (jnp.sum(p, axis=-1, keepdims=True) + jnp.exp(sink - m))

def swa_prompt(q, k, v, sinks):
    bsz, seq = q.shape[0], q.shape[1]
    nb = seq // BLOCK
    qb = q.astype(jnp.float32).reshape(bsz, nb, BLOCK, SW_KV_HEADS, SW_GROUP, SW_HEAD_DIM)
    kb = k.astype(jnp.float32).reshape(bsz, nb, BLOCK, SW_KV_HEADS, SW_HEAD_DIM)
    vb = v.astype(jnp.float32).reshape(bsz, nb, BLOCK, SW_KV_HEADS, SW_HEAD_DIM)
    kk = jnp.concatenate([jnp.concatenate([jnp.zeros_like(kb[:, :1]), kb[:, :-1]], axis=1), kb], axis=2)
    vv = jnp.concatenate([jnp.concatenate([jnp.zeros_like(vb[:, :1]), vb[:, :-1]], axis=1), vb], axis=2)
    scores = jnp.einsum('bnqkgd,bnskd->bnkgqs', qb, kk) * (SW_HEAD_DIM ** -0.5)
    qpos = BLOCK + jnp.arange(BLOCK)
    kpos = jnp.arange(2 * BLOCK)
    diff = qpos[:, None] - kpos[None, :]
    band = (diff >= 0) & (diff <= SW_WINDOW)
    has_prev = (jnp.arange(nb) > 0)[:, None, None] | (kpos >= BLOCK)[None, None, :]
    valid = (band[None] & has_prev)[None, :, None, None]
    sink = sinks.astype(jnp.float32).reshape(SW_KV_HEADS, SW_GROUP)[None, None, :, :, None, None]
    p = sink_probs(scores, valid, sink)
    o = jnp.einsum('bnkgqs,bnskd->bnqkgd', p, vv)
    return o.reshape(bsz, seq, SW_HEADS * SW_HEAD_DIM)

def swa_step(q, k, v, buf_k, buf_v, sinks):
    bsz, t = q.shape[0], q.shape[1]
    wb = buf_k.shape[1]
    kk = jnp.concatenate([buf_k.astype(jnp.float32), k.astype(jnp.float32)], axis=1)
    vv = jnp.concatenate([buf_v.astype(jnp.float32), v.astype(jnp.float32)], axis=1)
    qg = q.astype(jnp.float32).reshape(bsz, t, SW_KV_HEADS, SW_GROUP, SW_HEAD_DIM)
    scores = jnp.einsum('btkgd,bskd->bkgts', qg, kk) * (SW_HEAD_DIM ** -0.5)
    kpos = jnp.arange(wb + t) - wb
    diff = jnp.arange(t)[:, None] - kpos[None, :]
    valid = ((diff >= 0) & (diff <= SW_WINDOW))[None, None, None]
    sink = sinks.astype(jnp.float32).reshape(SW_KV_HEADS, SW_GROUP)[None, :, :, None, None]
    p = sink_probs(scores, valid, sink)
    o = jnp.einsum('bkgts,bskd->btkgd', p, vv).reshape(bsz, t, SW_HEADS * SW_HEAD_DIM)
    return o, kk[:, -SW_WINDOW:].astype(buf_k.dtype), vv[:, -SW_WINDOW:].astype(buf_v.dtype)

def mlstm_chunked(q, k, v, ig, fg_log, c0, n0, m0):
    seq = q.shape[1]
    L = math.gcd(seq, BLOCK)
    causal = jnp.tril(jnp.ones((L, L), dtype=bool))

    def step(carry, inp):
        c, n, m = carry
        qc, kc, vc, ic, fc = inp
        fcum = jnp.cumsum(fc, axis=-1)
        m_t = fcum + jnp.maximum(m[..., None], lax.cummax(ic - fcum, axis=2))
        logw = fcum[..., :, None] - fcum[..., None, :] + ic[..., None, :] - m_t[..., :, None]
        w = jnp.exp(jnp.where(causal, logw, -jnp.inf))
        carry_scale = jnp.exp(fcum + m[..., None] - m_t)
        sqk = jnp.einsum('bhtd,bhsd->bhts', qc, kc) * w
        num = carry_scale[..., None] * jnp.einsum('bhtd,bhde->bhte', qc, c) + jnp.einsum('bhts,bhse->bhte', sqk, vc)
        den = carry_scale * jnp.einsum('bhtd,bhd->bht', qc, n) + jnp.sum(sqk, axis=-1)
        h = num / jnp.maximum(jnp.abs(den), jnp.exp(-m_t))[..., None]
        m_end = m_t[..., -1]
        f_end = fcum[..., -1]
        w_end = jnp.exp(f_end[..., None] - fcum + ic - m_end[..., None])
        decay = jnp.exp(f_end + m - m_end)
        c = decay[..., None, None] * c + jnp.einsum('bhs,bhsd,bhse->bhde', w_end, kc, vc)
        n = decay[..., None] * n + jnp.einsum('bhs,bhsd->bhd', w_end, kc)
        return (c, n, m_end), h

    f32 = jnp.float32
    inputs = (to_chunks(q.astype(f32), L), to_chunks(k.astype(f32), L), to_chunks(v.astype(f32), L),
              to_chunks(ig.astype(f32), L), to_chunks(fg_log.astype(f32), L))
    (c, n, m), h = lax.scan(step, (c0, n0, m0), inputs)
    return from_chunks(h), c, n, m

def ssd_chunked(x, dt, a, bm, cm, s0):
    bsz, seq = x.shape[0], x.shape[1]
    L = math.gcd(seq, BLOCK)
    hg = SSD_HEADS // SSD_GROUPS
    causal = jnp.tril(jnp.ones((L, L), dtype=bool))
    da = dt * a

    def step(s, inp):
        xc, dtc, dac, bc, cc = inp
        xc = xc.reshape(bsz, SSD_GROUPS, hg, L, SSD_HEAD_DIM)
        dtc = dtc.reshape(bsz, SSD_GROUPS, hg, L)
        dac = dac.reshape(bsz, SSD_GROUPS, hg, L)
        cum = jnp.cumsum(dac, axis=-1)
        seg = cum[..., :, None] - cum[..., None, :]
        lmat = jnp.exp(jnp.where(causal, seg, -jnp.inf))
        cb = jnp.einsum('bgtn,bgsn->bgts', cc, bc)
        wmat = cb[:, :, None] * lmat * dtc[..., None, :]
        y = jnp.einsum('bghts,bghsp->bghtp', wmat, xc) + jnp.exp(cum)[..., None] * jnp.einsum('bgtn,bghpn->bghtp', cc, s)
        w_end = jnp.exp(cum[..., -1:] - cum) * dtc
        s = jnp.exp(cum[..., -1])[..., None, None] * s + jnp.einsum('bghs,bgsn,bghsp->bghpn', w_end, bc, xc)
        return s, y.reshape(bsz, SSD_HEADS, L, SSD_HEAD_DIM)

    inputs = (to_chunks(x, L), to_chunks(dt, L), to_chunks(da, L), to_chunks(bm, L), to_chunks(cm, L))
    s0 = s0.reshape(bsz, SSD_GROUPS, hg, SSD_HEAD_DIM, SSD_STATE)
    s, y = lax.scan(step, s0, inputs)
    return from_chunks(y), s.reshape(bsz, SSD_HEADS, SSD_HEAD_DIM, SSD_STATE)

def retention_chunked(q, k, v, r0):
    seq = q.shape[1]
    L = math.gcd(seq, BLOCK)
    lg = jnp.log(1.0 - jnp.exp2(-5.0 - jnp.arange(RET_HEADS, dtype=jnp.float32)))
    idx = jnp.arange(L, dtype=jnp.float32)
    diff = idx[:, None] - idx[None, :]
    dmat = jnp.exp(jnp.where(diff >= 0, diff[None] * lg[:, None, None], -jnp.inf))
    q_scale = jnp.exp((idx[None] + 1.0) * lg[:, None])
    k_scale = jnp.exp((L - 1.0 - idx[None]) * lg[:, None])
    chunk_decay = jnp.exp(L * lg)

    def step(r, inp):
        qc, kc, vc = inp
        att = jnp.einsum('bhtd,bhsd->bhts', qc, kc) * dmat
        o = jnp.einsum('bhts,bhse->bhte', att, vc) + q_scale[..., None] * jnp.einsum('bhtd,bhde->bhte', qc, r)
        r = chunk_decay[:, None, None] * r + jnp.einsum('bhsd,bhse->bhde', kc * k_scale[..., None], vc)
        return r, o

    f32 = jnp.float32
    inputs = (to_chunks(q.astype(f32), L), to_chunks(k.astype(f32), L), to_chunks(v.astype(f32), L))
    r, o = lax.scan(step, r0, inputs)
    return from_chunks(o), r

def even_mixer(h, pos, w_in, gate_bias, q_norm, k_norm, sinks, out_norm, w_out, swa_cache, ml_state):
    bsz, t, _ = h.shape
    f32 = jnp.float32
    sq, sk, sv, mq, mk, mv, mo, mi, mf = split_cols(h @ w_in, EVEN_SIZES)
    sq = rope(rmsnorm(sq.reshape(bsz, t, SW_HEADS, SW_HEAD_DIM), q_norm), pos, SW_ROT_DIM, ROPE_THETA)
    sk = rope(rmsnorm(sk.reshape(bsz, t, SW_KV_HEADS, SW_HEAD_DIM), k_norm), pos, SW_ROT_DIM, ROPE_THETA)
    sv = sv.reshape(bsz, t, SW_KV_HEADS, SW_HEAD_DIM)
    if swa_cache is None:
        ya = swa_prompt(sq, sk, sv, sinks)
        new_k, new_v = sk[:, -SW_WINDOW:], sv[:, -SW_WINDOW:]
    else:
        ya, new_k, new_v = swa_step(sq, sk, sv, swa_cache[0], swa_cache[1], sinks)
    gb = gate_bias.astype(f32)
    ig = mi.astype(f32) + gb[:ML_HEADS]
    fg_log = jax.nn.log_sigmoid(mf.astype(f32) + gb[ML_HEADS:])
    if ml_state is None:
        c0 = jnp.zeros((bsz, ML_HEADS, ML_QK_DIM, ML_V_DIM), f32)
        n0 = jnp.zeros((bsz, ML_HEADS, ML_QK_DIM), f32)
        m0 = jnp.zeros((bsz, ML_HEADS), f32)
    else:
        c0, n0, m0 = ml_state[0].astype(f32), ml_state[1].astype(f32), ml_state[2].astype(f32)
    hb, c, n, m = mlstm_chunked(mq.reshape(bsz, t, ML_HEADS, ML_QK_DIM),
                                mk.reshape(bsz, t, ML_HEADS, ML_QK_DIM).astype(f32) * (ML_QK_DIM ** -0.5),
                                mv.reshape(bsz, t, ML_HEADS, ML_V_DIM), ig, fg_log, c0, n0, m0)
    hb = rmsnorm(hb, out_norm.reshape(ML_HEADS, ML_V_DIM)).reshape(bsz, t, ML_HEADS * ML_V_DIM) * jax.nn.sigmoid(mo.astype(f32))
    y = jnp.concatenate([ya.astype(h.dtype), hb.astype(h.dtype)], axis=-1) @ w_out
    return y, (new_k, new_v, c, n, m)

def odd_mixer(h, pos, w_in, conv_w, conv_b, dt_bias, a_log, d_skip, ssd_norm, ret_norm, w_out, conv_buf, ssd_state, ret_state):
    bsz, t, _ = h.shape
    f32 = jnp.float32
    z, xbc, dt, rq, rk, rv, rg = split_cols(h @ w_in, ODD_SIZES)
    if conv_buf is None:
        conv_buf = jnp.zeros((bsz, SSD_CONV - 1, SSD_CONV_DIM), xbc.dtype)
    full = jnp.concatenate([conv_buf.astype(xbc.dtype), xbc], axis=1)
    acc = full[:, 0:t].astype(f32) * conv_w[0].astype(f32)
    for j in range(1, SSD_CONV):
        acc = acc + full[:, j:j + t].astype(f32) * conv_w[j].astype(f32)
    xbc_act = jax.nn.silu(acc + conv_b.astype(f32))
    new_buf = full[:, -(SSD_CONV - 1):]
    xs, bm, cm = split_cols(xbc_act, (SSD_INNER, SSD_GROUPS * SSD_STATE, SSD_GROUPS * SSD_STATE))
    dt = jax.nn.softplus(dt.astype(f32) + dt_bias.astype(f32))
    a = -jnp.exp(a_log.astype(f32))
    xs = xs.reshape(bsz, t, SSD_HEADS, SSD_HEAD_DIM)
    s0 = jnp.zeros((bsz, SSD_HEADS, SSD_HEAD_DIM, SSD_STATE), f32) if ssd_state is None else ssd_state.astype(f32)
    yc, s_new = ssd_chunked(xs, dt, a, bm.reshape(bsz, t, SSD_GROUPS, SSD_STATE), cm.reshape(bsz, t, SSD_GROUPS, SSD_STATE), s0)
    yc = yc + d_skip.astype(f32)[:, None] * xs
    yc = (yc.reshape(bsz, t, SSD_INNER) * jax.nn.silu(z.astype(f32))).reshape(bsz, t, SSD_GROUPS, SSD_INNER // SSD_GROUPS)
    yc = rmsnorm(yc, ssd_norm.reshape(SSD_GROUPS, SSD_INNER // SSD_GROUPS)).reshape(bsz, t, SSD_INNER)
    rq = rope(rq.reshape(bsz, t, RET_HEADS, RET_QK_DIM), pos, RET_QK_DIM, RET_ROPE_THETA)
    rk = rope(rk.reshape(bsz, t, RET_HEADS, RET_QK_DIM), pos, RET_QK_DIM, RET_ROPE_THETA).astype(f32) * (RET_QK_DIM ** -0.5)
    rv = rv.reshape(bsz, t, RET_HEADS, RET_V_DIM)
    r0 = jnp.zeros((bsz, RET_HEADS, RET_QK_DIM, RET_V_DIM), f32) if ret_state is None else ret_state.astype(f32)
    yr, r_new = retention_chunked(rq, rk, rv, r0)
    yr = group_norm(yr, ret_norm.reshape(RET_HEADS, RET_V_DIM)).reshape(bsz, t, RET_HEADS * RET_V_DIM) * jax.nn.silu(rg.astype(f32))
    y = jnp.concatenate([yc, yr], axis=-1).astype(h.dtype) @ w_out
    return y, (new_buf, s_new, r_new)

def memory_kv(mem, g, wk, wv, k_norm):
    bsz, mlen, _ = mem.shape
    hm = rmsnorm(mem, g)
    k = rmsnorm((hm @ wk).reshape(bsz, mlen, MEM_HEADS, MEM_HEAD_DIM), k_norm)
    v = (hm @ wv).reshape(bsz, mlen, MEM_HEADS, MEM_HEAD_DIM)
    return k, v

def cross_attn(h, mk, mv, wq, q_norm, wo):
    bsz, t, _ = h.shape
    q = rmsnorm((h @ wq).reshape(bsz, t, MEM_HEADS, MEM_HEAD_DIM), q_norm)
    s = jnp.einsum('bthd,bmhd->bhtm', q.astype(jnp.float32), mk.astype(jnp.float32)) * (MEM_HEAD_DIM ** -0.5)
    p = jax.nn.softmax(s, axis=-1)
    o = jnp.einsum('bhtm,bmhd->bthd', p, mv.astype(jnp.float32)).reshape(bsz, t, MEM_WIDTH)
    return o.astype(h.dtype) @ wo

def ffn(h, w1, w2):
    return jnp.square(jax.nn.relu(h @ w1)) @ w2

def setup_inputs(seed: int = 0) -> dict:
    key = jax.random.key(seed)
    ks = iter(jax.random.split(key, 64))
    f32 = jnp.float32

    def nrm(shape, scale=1.0):
        return scale * jax.random.normal(next(ks), shape, f32)

    def gain(shape):
        return 1.0 + nrm(shape, 0.02)

    win = min(SW_WINDOW, PAST_LEN)
    x_prompt = nrm((BATCH, SEQ, D_MODEL))
    x_sample = nrm((DEC_BATCH, DEC_SEQ, D_MODEL))
    cache_mem_k = nrm((DEPTH, DEC_BATCH, MEM_LEN, MEM_HEADS, MEM_HEAD_DIM))
    cache_mem_v = nrm((DEPTH, DEC_BATCH, MEM_LEN, MEM_HEADS, MEM_HEAD_DIM))
    cache_swa_k = nrm((N_EVEN, DEC_BATCH, win, SW_KV_HEADS, SW_HEAD_DIM))
    cache_swa_v = nrm((N_EVEN, DEC_BATCH, win, SW_KV_HEADS, SW_HEAD_DIM))
    state_mlstm_C = nrm((N_EVEN, DEC_BATCH, ML_HEADS, ML_QK_DIM, ML_V_DIM), 0.5)
    state_mlstm_n = nrm((N_EVEN, DEC_BATCH, ML_HEADS, ML_QK_DIM), 0.5)
    state_mlstm_m = nrm((N_EVEN, DEC_BATCH, ML_HEADS))
    state_ssd_conv = nrm((N_ODD, DEC_BATCH, SSD_CONV - 1, SSD_CONV_DIM))
    state_ssd = nrm((N_ODD, DEC_BATCH, SSD_HEADS, SSD_HEAD_DIM, SSD_STATE), 0.1)
    state_ret = nrm((N_ODD, DEC_BATCH, RET_HEADS, RET_QK_DIM, RET_V_DIM))
    mem_prompt = nrm((BATCH, MEM_LEN, D_MODEL))
    ml_i_bias = -1.0 + nrm((N_EVEN, ML_HEADS), 0.1)
    ml_f_bias = jnp.linspace(3.0, 6.0, ML_HEADS, dtype=f32)[None] + nrm((N_EVEN, ML_HEADS), 0.1)
    dt0 = jnp.exp(jax.random.uniform(next(ks), (N_ODD, SSD_HEADS), f32, math.log(1e-3), math.log(1e-1)))
    dt_bias = dt0 + jnp.log(-jnp.expm1(-dt0))
    a_log = jnp.log(jax.random.uniform(next(ks), (N_ODD, SSD_HEADS), f32, 1.0, 16.0))
    return {
        'x_prompt': x_prompt,
        'x_sample': x_sample,
        'cache_mem_k': cache_mem_k,
        'cache_mem_v': cache_mem_v,
        'cache_swa_k': cache_swa_k,
        'cache_swa_v': cache_swa_v,
        'state_mlstm_C': state_mlstm_C,
        'state_mlstm_n': state_mlstm_n,
        'state_mlstm_m': state_mlstm_m,
        'state_ssd_conv': state_ssd_conv,
        'state_ssd': state_ssd,
        'state_ret': state_ret,
        'mem_prompt': mem_prompt,
        'norm_mix': gain((DEPTH, D_MODEL)),
        'norm_xattn': gain((DEPTH, D_MODEL)),
        'norm_mem': gain((DEPTH, D_MODEL)),
        'norm_ffn': gain((DEPTH, D_MODEL)),
        'even_w_in': nrm((N_EVEN, D_MODEL, EVEN_IN), D_MODEL ** -0.5),
        'mlstm_gate_bias': jnp.concatenate([ml_i_bias, ml_f_bias], axis=-1),
        'swa_q_norm': gain((N_EVEN, SW_HEAD_DIM)),
        'swa_k_norm': gain((N_EVEN, SW_HEAD_DIM)),
        'swa_sinks': nrm((N_EVEN, SW_HEADS), 0.5),
        'mlstm_out_norm': gain((N_EVEN, ML_HEADS * ML_V_DIM)),
        'even_w_out': nrm((N_EVEN, EVEN_OUT, D_MODEL), EVEN_OUT ** -0.5),
        'odd_w_in': nrm((N_ODD, D_MODEL, ODD_IN), D_MODEL ** -0.5),
        'ssd_conv_w': nrm((N_ODD, SSD_CONV, SSD_CONV_DIM), SSD_CONV ** -0.5),
        'ssd_conv_b': nrm((N_ODD, SSD_CONV_DIM), 0.01),
        'ssd_dt_bias': dt_bias,
        'ssd_a_log': a_log,
        'ssd_d': 1.0 + nrm((N_ODD, SSD_HEADS), 0.1),
        'ssd_norm': gain((N_ODD, SSD_INNER)),
        'ret_norm': gain((N_ODD, RET_HEADS * RET_V_DIM)),
        'odd_w_out': nrm((N_ODD, ODD_OUT, D_MODEL), ODD_OUT ** -0.5),
        'mem_wq': nrm((DEPTH, D_MODEL, MEM_WIDTH), D_MODEL ** -0.5),
        'mem_wk': nrm((DEPTH, D_MODEL, MEM_WIDTH), D_MODEL ** -0.5),
        'mem_wv': nrm((DEPTH, D_MODEL, MEM_WIDTH), D_MODEL ** -0.5),
        'mem_q_norm': gain((DEPTH, MEM_HEAD_DIM)),
        'mem_k_norm': gain((DEPTH, MEM_HEAD_DIM)),
        'mem_wo': nrm((DEPTH, MEM_WIDTH, D_MODEL), MEM_WIDTH ** -0.5),
        'ffn_w1': nrm((DEPTH, D_MODEL, FFN_DIM), D_MODEL ** -0.5),
        'ffn_w2': nrm((DEPTH, FFN_DIM, D_MODEL), FFN_DIM ** -0.5),
    }

def reference(x_prompt, x_sample, cache_mem_k, cache_mem_v, cache_swa_k, cache_swa_v, state_mlstm_C, state_mlstm_n,
              state_mlstm_m, state_ssd_conv, state_ssd, state_ret, mem_prompt, norm_mix, norm_xattn, norm_mem, norm_ffn,
              even_w_in, mlstm_gate_bias, swa_q_norm, swa_k_norm, swa_sinks, mlstm_out_norm, even_w_out, odd_w_in,
              ssd_conv_w, ssd_conv_b, ssd_dt_bias, ssd_a_log, ssd_d, ssd_norm, ret_norm, odd_w_out, mem_wq, mem_wk,
              mem_wv, mem_q_norm, mem_k_norm, mem_wo, ffn_w1, ffn_w2):
    pos_p = jnp.arange(x_prompt.shape[1], dtype=jnp.int32)
    pos_s = PAST_LEN + jnp.arange(x_sample.shape[1], dtype=jnp.int32)
    yp, ys = x_prompt, x_sample
    p_mk, p_mv = [], []
    p_swk, p_swv, p_c, p_n, p_m = [], [], [], [], []
    s_swk, s_swv, s_c, s_n, s_m = [], [], [], [], []
    p_conv, p_ssd, p_ret = [], [], []
    s_conv, s_ssd, s_ret = [], [], []
    for l in range(DEPTH):
        hp = rmsnorm(yp, norm_mix[l])
        hs = rmsnorm(ys, norm_mix[l])
        if l % 2 == 0:
            e = l // 2
            w = (even_w_in[e], mlstm_gate_bias[e], swa_q_norm[e], swa_k_norm[e], swa_sinks[e], mlstm_out_norm[e], even_w_out[e])
            op, stp = even_mixer(hp, pos_p, *w, None, None)
            osm, sts = even_mixer(hs, pos_s, *w, (cache_swa_k[e], cache_swa_v[e]),
                                  (state_mlstm_C[e], state_mlstm_n[e], state_mlstm_m[e]))
            for lst, val in zip((p_swk, p_swv, p_c, p_n, p_m), stp):
                lst.append(val)
            for lst, val in zip((s_swk, s_swv, s_c, s_n, s_m), sts):
                lst.append(val)
        else:
            o = l // 2
            w = (odd_w_in[o], ssd_conv_w[o], ssd_conv_b[o], ssd_dt_bias[o], ssd_a_log[o], ssd_d[o], ssd_norm[o], ret_norm[o], odd_w_out[o])
            op, stp = odd_mixer(hp, pos_p, *w, None, None, None)
            osm, sts = odd_mixer(hs, pos_s, *w, state_ssd_conv[o], state_ssd[o], state_ret[o])
            for lst, val in zip((p_conv, p_ssd, p_ret), stp):
                lst.append(val)
            for lst, val in zip((s_conv, s_ssd, s_ret), sts):
                lst.append(val)
        yp = yp + op
        ys = ys + osm
        mk, mv = memory_kv(mem_prompt, norm_mem[l], mem_wk[l], mem_wv[l], mem_k_norm[l])
        p_mk.append(mk)
        p_mv.append(mv)
        yp = yp + cross_attn(rmsnorm(yp, norm_xattn[l]), mk, mv, mem_wq[l], mem_q_norm[l], mem_wo[l])
        ys = ys + cross_attn(rmsnorm(ys, norm_xattn[l]), cache_mem_k[l], cache_mem_v[l], mem_wq[l], mem_q_norm[l], mem_wo[l])
        yp = yp + ffn(rmsnorm(yp, norm_ffn[l]), ffn_w1[l], ffn_w2[l])
        ys = ys + ffn(rmsnorm(ys, norm_ffn[l]), ffn_w1[l], ffn_w2[l])
    return (yp, ys,
            jnp.stack(p_mk), jnp.stack(p_mv), jnp.stack(p_swk), jnp.stack(p_swv),
            jnp.stack(p_c), jnp.stack(p_n), jnp.stack(p_m),
            jnp.stack(p_conv), jnp.stack(p_ssd), jnp.stack(p_ret),
            jnp.stack(s_swk), jnp.stack(s_swv), jnp.stack(s_c), jnp.stack(s_n), jnp.stack(s_m),
            jnp.stack(s_conv), jnp.stack(s_ssd), jnp.stack(s_ret))


_drawn_inputs = setup_inputs


def setup_inputs(seed=0):
    import zlib

    import numpy as np

    out = dict(_drawn_inputs(seed))
    spreads = {}
    factors = {'norm_xattn': 8.0,
     'norm_mem': 2.905,
     'swa_q_norm': 8.0,
     'swa_k_norm': 3.037,
     'swa_sinks': 8.0,
     'mlstm_out_norm': 5.144,
     'ssd_conv_b': 3.205,
     'ssd_norm': 6.313,
     'ret_norm': 8.0,
     'mem_q_norm': 8.0,
     'mem_k_norm': 2.758}
    for name, (base, spread) in spreads.items():
        noise = np.random.default_rng([zlib.crc32(name.encode()), seed]).standard_normal(out[name].shape)
        drawn = base * np.exp(spread * noise) if base else spread * noise
        out[name] = jnp.asarray(drawn.astype(out[name].dtype))
    for name, factor in factors.items():
        out[name] = (out[name] * factor).astype(out[name].dtype)
    return out
```

```python
import math
from contextlib import ExitStack

import numpy as np

import concourse.bass as bass
from concourse import mybir

F32 = mybir.dt.float32
F32R = mybir.dt.float32r
ALU = mybir.AluOpType
ACT = mybir.ActivationFunctionType
AX = mybir.AxisListType

P = 128
D_MODEL, SEQ, NSAMPLE, PAST = 1024, 512, 8, 1024
TOK = SEQ + NSAMPLE
HALF = TOK // 2
DC = D_MODEL // P
NBLK = SEQ // P
MEM = 256
FFN = 4 * D_MODEL
EPS = 1e-6
NEG = -1e30
RING = 2

E_SQ, E_SK, E_SV, E_MQ, E_MK, E_MV, E_MO, E_GI, E_GF = 0, 4, 5, 6, 8, 10, 14, 18, 19
O_Z, O_X, O_B, O_C, O_DT, O_RQ, O_RK, O_RV, O_RG = 0, 8, 16, 18, 20, 21, 25, 29, 33
NPROJ = 37

V_MIX, V_XATT, V_MEM, V_FFN, V_MLN, V_SSDN, V_RETN, V_CB = 0, 16, 32, 48, 64, 68, 76, 80
V_CW, V_QN, V_KN, V_SQ, V_SK = 92, 140, 142, 144, 145


def layout(parts):
    at, out = 0, {}
    for name, n in parts:
        out[name] = (at, n)
        at += n
    return out, at


COMMON, NCOMMON = layout([("ident", P), ("ones", P), ("blk64", P), ("causal", P), ("own_head", 4), ("eps", 1)])
EVEN, NEVEN = layout([("rot", P), ("mask_first", 2 * P), ("mask_later", 2 * P), ("cos", TOK), ("sin", TOK)])
ODD, NODD = layout([("rot", P), ("cos", TOK), ("sin", TOK), ("decay", 4 * P), ("qscale", 4 * P), ("kscale", 4)])
NLAYER = max(NEVEN, NODD)


def shape_constants():
    p = np.arange(P)
    pos = np.concatenate([np.arange(SEQ), PAST + np.zeros(NSAMPLE)]).astype(np.float32)

    def rope(rot_dim, head, theta):
        half = rot_dim // 2
        inv = np.power(np.float32(theta), -np.arange(half, dtype=np.float32) * np.float32(2.0 / rot_dim))
        ang = (pos[None, :] * inv[:, None]).astype(np.float32)
        cos, sin, rot = np.ones((P, TOK)), np.zeros((P, TOK)), np.zeros((P, P))
        for at in range(0, P, head):
            for part in range(2):
                rows = at + part * half + np.arange(half)
                cos[rows], sin[rows] = np.cos(ang), np.sin(ang)
            for i in range(half):
                rot[at + i + half, at + i] = -1.0
                rot[at + i, at + i + half] = 1.0
        return cos, sin, rot

    c = {"ident": np.eye(P), "ones": np.ones((P, P)), "blk64": np.kron(np.eye(2), np.ones((64, 64))),
         "causal": np.where(p[:, None] <= p[None, :], 0.0, NEG),
         "own_head": np.tile(np.eye(4), (P // 4, 1)), "eps": np.full((P, 1), EPS)}
    e, o = {}, {}
    e["cos"], e["sin"], e["rot"] = rope(16, 64, 500000.0)
    k = np.arange(2 * P)
    e["mask_first"] = np.where(p[:, None] >= k[None, :], 0.0, NEG)
    diff = P + p[:, None] - k[None, :]
    e["mask_later"] = np.where((diff >= 0) & (diff <= P), 0.0, NEG)
    o["cos"], o["sin"], o["rot"] = rope(128, 128, 10000.0)
    lg = np.log(1.0 - np.exp2(-5.0 - np.arange(4)))
    d = p[None, :] - p[:, None]
    o["decay"] = np.concatenate([np.where(d >= 0, np.exp(np.maximum(d, 0) * g), 0.0) for g in lg], axis=1)
    o["qscale"] = np.concatenate([np.tile(np.exp((p + 1.0) * g), (P, 1)) for g in lg], axis=1)
    o["kscale"] = np.exp((P - 1.0 - p)[:, None] * lg[None, :])
    out = np.zeros((P, NCOMMON + NEVEN + NODD), np.float32)
    for table, at, vals in ((COMMON, 0, c), (EVEN, NCOMMON, e), (ODD, NCOMMON + NEVEN, o)):
        for name, (a, n) in table.items():
            out[:, at + a:at + a + n] = vals[name]
    return out


RET_DECAY = [float(1.0 - 2.0 ** (-5.0 - h)) for h in range(4)]
RET_CHUNK_DECAY = [float(np.exp(P * np.log(1.0 - 2.0 ** (-5.0 - h)))) for h in range(4)]


class Signal:

    def __init__(self, s):
        self.s, self.seen = s, {}

    def next(self, reader, n=1):
        self.seen[reader] = self.seen.get(reader, 0) + n
        return self.seen[reader]


class Region:

    def __init__(self, nc, base, size):
        self.nc, self.base, self.size, self.at = nc, base, size, 0

    def reset(self, at=0):
        self.at = at

    def __call__(self, name, shape, dt=F32):
        n = 4 * int(np.prod(shape[1:]))
        n = -(-n // 32) * 32
        assert self.at + n <= self.size, (name, self.at, n, self.size)
        t = self.nc.alloc_sbuf_tensor_at(name, shape, dt, offset=self.base + self.at)
        self.at += n
        return t


class Core:

    def __init__(self, nc, ctx, A, C, O):
        self.nc, self.ctx, self.A, self.C, self.O = nc, ctx, A, C, O
        self.n_semaphores = 0
        size = 212800
        arena = ctx.enter_context(nc.sbuf_tensor("arena", [P, size // 4], F32))
        base = size_of_base(nc, arena, size)
        whole = Region(nc, base, size)
        self.x = whole("x", [P, DC, TOK])
        self.w_raw = [whole(f"w_raw{i}", [P, DC, P]) for i in range(RING)]
        self.w_hi = [whole(f"w_hi{i}", [P, DC, P], F32R) for i in range(RING)]
        self.w_lo = [whole(f"w_lo{i}", [P, DC, P], F32R) for i in range(RING)]
        self.const = whole("const", [P, NCOMMON])
        self.lconst = whole("lconst", [P, NLAYER])
        self.vcol = whole("vcol", [P, V_SK + 1])
        self.params = Region(nc, base + whole.at, 256 + 64)
        whole.at += 320
        at = whole.at
        self.big = Region(nc, base + at, NPROJ * TOK * 4)
        whole.at += NPROJ * TOK * 4
        at = whole.at
        self.mid = Region(nc, base + at, 24 * TOK * 4)
        whole.at += 24 * TOK * 4
        self.small = Region(nc, base + whole.at, size - whole.at)
        self.proj = self.big("proj", [P, NPROJ, TOK])
        self.big.reset()
        self.hid_hi = [self.big(f"hid_hi{i}", [P, DC, TOK], F32R) for i in range(2)]
        self.hid_lo = [self.big(f"hid_lo{i}", [P, DC, TOK], F32R) for i in range(2)]
        self.xn_hi = self.mid("xn_hi", [P, DC, TOK], F32R)
        self.xn_lo = self.mid("xn_lo", [P, DC, TOK], F32R)
        self.mid.reset()
        self.y_hi = self.mid("y_hi", [P, 12, TOK], F32R)
        self.y_lo = self.mid("y_lo", [P, 12, TOK], F32R)
        self.ps = ctx.enter_context(nc.psum_tensor("banks", [P, 8, 512], F32))
        self.w_here = [self.counter(f"weight_arrived{i}") for i in range(RING)]
        self.w_hi_ready = self.counter("weight_high_ready")
        self.w_lo_ready = self.counter("weight_low_ready")
        self.tile_done = self.counter("gemm_tile_done")
        self.tile_out = self.counter("gemm_bank_free")
        self.end = {e: self.counter(f"stage_end_{e}") for e in ("pe", "dve", "act")}
        self.dve_step, self.act_step = self.counter("dve_step"), self.counter("act_step")
        self.stored = self.counter("stored")
        self.n_stored = 0
        self.n_tiles = 0
        self.tiles = []

    def counter(self, name):
        self.n_semaphores += 1
        return Signal(self.ctx.enter_context(self.nc.semaphore(name)))

    def c(self, name, rows=P):
        a, n = COMMON[name]
        return self.const[0:rows, a:a + n]

    def lc(self, table, name):
        a, n = table[name]
        return self.lconst[:, a:a + n]

    def col(self, v):
        return self.vcol[:, v:v + 1]

    def pair(self, j, rows, cols, rhs):
        return [(cols, self.const[0:rows, 2 * j + t:2 * j + t + 1].to_broadcast([rows, 64]), rhs, 64 * t)
                for t in range(2)]

    def onehot(self, h, rows):
        return self.const[0:rows, h:h + 1].to_broadcast([rows, P])

    def dve_link(self, ins):
        ins.then_inc(self.dve_step.s, 1)
        self.nc.vector.wait_ge(self.dve_step.s, self.dve_step.next("dve"))

    def act_link(self, ins):
        ins.then_inc(self.act_step.s, 1)
        self.nc.scalar.wait_ge(self.act_step.s, self.act_step.next("act"))

    def fence(self, eng, me):
        eng.drain().then_inc(self.end[me].s, 1)
        for other in ("pe", "dve", "act"):
            eng.wait_ge(self.end[other].s, self.end[other].next(me))

    def store(self, out, in_, few=False):
        self.nc.scalar.dma_start(out, in_, allow_slow_non_contiguous=few).then_inc(self.stored.s, 16)
        self.n_stored += 1

    def stores_done(self):
        self.nc.scalar.wait_ge(self.stored.s, 16 * self.n_stored)


def size_of_base(nc, arena, size):
    lo = nc.sbuf_usable_end - nc.sbuf_base
    base = -(-(nc.sbuf_base - size) // 32) * 32
    assert base >= 0 and lo >= 0
    return base


class Stage:
    def __init__(self, k):
        self.k = k

    def pe(self, pe): pass
    def dve(self, dve): pass
    def act(self, act): pass


class Gemm(Stage):

    def __init__(self, k, tiles, rhs_wait=None):
        super().__init__(k)
        self.base = len(k.tiles)
        self.mine = tiles
        k.tiles += tiles

    def pe(self, pe):
        k, ps = self.k, self.k.ps
        for i, t in enumerate(self.mine):
            n = self.base + i
            pe.wait_ge(k.w_hi_ready.s, n + 1)
            pe.wait_ge(k.w_lo_ready.s, n + 1)
            if n >= 3:
                pe.wait_ge(k.tile_out.s, n - 2)
            if "rhs_ready" in t:
                sig, count = t["rhs_ready"]
                pe.wait_ge(sig.s, count)
            hi, lo = k.w_hi[n % RING], k.w_lo[n % RING]
            rh, rl = t["rhs"]
            m, nk = t["m"], t["nk"]
            last = None
            for kk in range(nk):
                for b, (c0, c1) in enumerate(t["halves"]):
                    out = ps[0:m, 2 * (n % 3) + b, 0:c1 - c0]
                    r, q = rh[:, t["k0"] + kk, c0:c1], rl[:, t["k0"] + kk, c0:c1]
                    pe.matmul(out, hi[:, kk, 0:m], r, start=kk == 0, stop=False)
                    pe.matmul(out, hi[:, kk, 0:m], q, start=False, stop=False)
                    last = pe.matmul(out, lo[:, kk, 0:m], r, start=False, stop=kk == nk - 1)
            last.then_inc(k.tile_done.s, 1)

    def dve(self, dve):
        k, ps = self.k, self.k.ps
        for i, t in enumerate(self.mine):
            n = self.base + i
            dve.wait_ge(k.tile_done.s, n + 1)
            w = t["halves"][0][1] - t["halves"][0][0]
            nb = len(t["halves"])
            src = ps[0:t["m"], 2 * (n % 3):2 * (n % 3) + nb, 0:w]
            t["out"](dve, src, nb)
            dve.wait_ge(k.tile_out.s, n + 1)

    def act(self, act):
        k = self.k
        for i, t in enumerate(self.mine):
            n = self.base + i
            if "act" in t:
                t["act"](act)
            if n + RING < len(k.tiles):
                act.wait_ge(k.tile_done.s, n + 1)
                split_high(k, act, n + RING)


def split_high(k, act, n):
    t = k.tiles[n]
    act.wait_ge(k.w_here[n % RING].s, 16 * k.arrivals[n])
    act.activation(k.w_hi[n % RING][:, 0:t["nk"], 0:t["m"]], k.w_raw[n % RING][:, 0:t["nk"], 0:t["m"]],
                   ACT.Copy).then_inc(k.w_hi_ready.s, 1)


def split_low(k, pool):
    for n, t in enumerate(k.tiles):
        pool.wait_ge(k.w_hi_ready.s, n + 1)
        if n >= RING:
            pool.wait_ge(k.tile_done.s, n - RING + 1)
        view = slice(0, t["nk"]), slice(0, t["m"])
        pool.tensor_tensor(k.w_lo[n % RING][:, view[0], view[1]], k.w_raw[n % RING][:, view[0], view[1]],
                           k.w_hi[n % RING][:, view[0], view[1]].bitcast(F32),
                           ALU.subtract).then_inc(k.w_lo_ready.s, 1)


def stream_weights(k, sp):
    for n, t in enumerate(k.tiles):
        if n >= RING:
            sp.wait_ge(k.w_lo_ready.s, n - RING + 1)
        for (p0, p1), (k0, k1), (c0, c1), src in t["parts"]:
            sp.dma_start(k.w_raw[n % RING][p0:p1, k0:k1, c0:c1], src).then_inc(k.w_here[n % RING].s, 16)


def weight_parts(w, k0, nk, pieces):
    v = w.rearrange("(k p) n -> p k n", p=P)
    out, at = [], 0
    for c, n in pieces:
        out.append(((0, P), (0, nk), (at, at + n), v[:, k0:k0 + nk, c:c + n]))
        at += n
    return out, at


HALVES = [(0, HALF), (HALF, TOK)]


def two(ap):
    return ap.rearrange("p (a b) -> p a b", a=2)


def gemm_tile(w, pieces, rhs, out, k0=0, nk=DC, halves=HALVES, row0=None, **more):
    parts, m = weight_parts(w, k0 if row0 is None else row0, nk, pieces)
    return dict(parts=parts, m=m, nk=nk, k0=k0, rhs=rhs, halves=halves, out=out, **more)


def out_copy(k, dst, scale=None):
    def emit(dve, src, nb):
        d = two(dst) if nb == 2 else dst.unsqueeze(1)
        if scale is None:
            dve.tensor_copy(d, src).then_inc(k.tile_out.s, 1)
        else:
            dve.tensor_scalar(d, src, scale, None, ALU.mult).then_inc(k.tile_out.s, 1)
    return emit


def out_residual(k, m):
    def emit(dve, src, nb):
        d = two(k.x[:, m, :])
        dve.tensor_tensor(d, src, d, ALU.add).then_inc(k.tile_out.s, 1)
    return emit


class HeadNorm(Stage):

    def __init__(self, k, name, units, mask, features, apply, width=TOK, region=None, extra=None):
        super().__init__(k)
        self.units, self.mask, self.features, self.apply, self.width = units, mask, features, apply, width
        region = region or k.small
        self.sq = [region(f"{name}_sq{i}", [P, width]) for i in range(2)]
        self.rstd = [region(f"{name}_rstd{i}", [P, width]) for i in range(2)]
        s = k.norm_signals
        self.sq_ready, self.summed, self.rstd_ready, self.rstd_used = s
        self.halves = HALVES if width == TOK else [(0, width)]
        self.first, self.first_unit = k.norm_count
        k.norm_count = (self.first + sum(len(c) for c in units), self.first_unit + len(units))

    def banks(self, u, rows=P):
        w = self.halves[0][1]
        return self.k.ps[:, 2 * (u % 2):2 * (u % 2) + len(self.halves), 0:w]

    def pe(self, pe):
        n = 0
        for u, chunks in enumerate(self.units):
            if u >= 2:
                pe.wait_ge(self.rstd_used.s, self.first_unit + u - 1)
            for i, _ in enumerate(chunks):
                pe.wait_ge(self.sq_ready.s, self.first + n + 1)
                for b, (c0, c1) in enumerate(self.halves):
                    last = pe.matmul(self.k.ps[:, 2 * (u % 2) + b, 0:c1 - c0], self.mask,
                                     self.sq[n % 2][:, c0:c1],
                                     start=i == 0, stop=i == len(chunks) - 1)
                last.then_inc(self.summed.s, 1)
                n += 1

    def squares(self, act, u):
        for src in self.units[u]:
            n = self.sent
            if n >= 2:
                act.wait_ge(self.summed.s, self.first + n - 1)
            act.activation(self.sq[n % 2][:, 0:self.width], src, ACT.Square).then_inc(self.sq_ready.s, 1)
            self.sent += 1

    def act(self, act):
        k = self.k
        self.sent = 0
        nb, w = len(self.halves), self.halves[0][1]
        self.squares(act, 0)
        for u, chunks in enumerate(self.units):
            if u + 1 < len(self.units):
                self.squares(act, u + 1)
            act.wait_ge(self.summed.s, self.first + sum(len(c) for c in self.units[:u + 1]))
            if u >= 2:
                act.wait_ge(self.rstd_used.s, self.first_unit + u - 1)
            rstd = self.rstd[u % 2][:, 0:self.width]
            ln = rstd.rearrange("p (a b) -> p a b", a=nb)
            k.act_link(act.activation(ln, self.banks(u), ACT.Ln, scale=1.0 / self.features, bias=k.c("eps")))
            act.activation(rstd, rstd, ACT.Exp, scale=-0.5).then_inc(self.rstd_ready.s, 1)

    def dve(self, dve):
        for u in range(len(self.units)):
            dve.wait_ge(self.rstd_ready.s, self.first_unit + u + 1)
            last = self.apply(dve, u, self.rstd[u % 2][:, 0:self.width])
            last.then_inc(self.rstd_used.s, 1)


class Load(Stage):

    def __init__(self, k):
        super().__init__(k)
        r = k.big
        r.reset()
        self.xtok = r("xtok", [P, NBLK, D_MODEL])
        self.xs = r("xs", [NSAMPLE, D_MODEL])
        self.rows = [r("param_rows0", [P, P]), r("param_rows1", [P, P])]
        self.here, self.done, self.out = k.counter("inputs_here"), k.counter("in_transposed"), k.counter("in_free")
        A = k.A
        self.loads = [(k.const[:, :], k.C[:, 0:NCOMMON]), (k.lconst[:, 0:NEVEN], k.C[:, NCOMMON:NCOMMON + NEVEN]),
                      (self.xtok[:, :, :], A["x_prompt"].rearrange("b (n p) d -> p (b n) d", p=P)),
                      (self.xs[:, :], A["x_sample"].rearrange("b t d -> (b t) d"))]
        at = 0
        for name, n in (("norm_mix", 16), ("norm_xattn", 16), ("norm_mem", 16), ("norm_ffn", 16),
                        ("mlstm_out_norm", 4), ("ssd_norm", 8), ("ret_norm", 4), ("ssd_conv_b", 12)):
            self.loads.append((self.rows[0][at:at + n, :], A[name].rearrange("l (c p) -> (l c) p", p=P)))
            at += n
        self.n0 = at
        self.loads.append((self.rows[1][0:48, :], A["ssd_conv_w"].rearrange("l j (c p) -> (l j c) p", p=P)))
        self.loads.append((self.rows[1][48:50, :], A["mem_q_norm"]))
        self.loads.append((self.rows[1][50:52, :], A["mem_k_norm"]))
        for i, name in ((52, "swa_q_norm"), (53, "swa_k_norm")):
            for half in range(2):
                self.loads.append((self.rows[1][i:i + 1, 64 * half:64 * half + 64], A[name]))
        colv = lambda ap, n: ap.rearrange("l (h a) -> (l h) a", a=1)[0:n]
        gb = A["mlstm_gate_bias"]
        self.loads += [(k.gate_i[:, :], gb[:, 0:4].rearrange("l (h a) -> (l h) a", a=1)),
                       (k.gate_f[:, :], gb[:, 4:8].rearrange("l (h a) -> (l h) a", a=1)),
                       (k.dt_bias[:, :], A["ssd_dt_bias"].rearrange("l (h a) -> (l h) a", a=1)),
                       (k.a_log[:, :], A["ssd_a_log"].rearrange("l (h a) -> (l h) a", a=1)),
                       (k.d_skip[:, :], A["ssd_d"].rearrange("l (h a) -> (l h) a", a=1)),
                       (k.sink_row[:, :], A["swa_sinks"].to_broadcast([P, 8]))]
        for b in range(NSAMPLE):
            self.loads.append((k.sink_col[8 * b:8 * b + 8, :], A["swa_sinks"].rearrange("l (h a) -> (l h) a", a=1)))

    def pe(self, pe):
        k, ps = self.k, self.k.ps
        pe.wait_ge(self.here.s, 16 * len(self.loads))
        ident = k.c("ident")
        for c in range(DC):
            if c >= 2:
                pe.wait_ge(self.out.s, c - 1)
            b = 2 * (c % 2)
            for n in range(NBLK):
                pe.transpose(ps[:, b, n * P:n * P + P], self.xtok[:, n, c * P:c * P + P], ident)
            pe.transpose(ps[:, b + 1, 0:8], self.xs[:, c * P:c * P + P], k.c("ident", 8)[:, 0:8])\
              .then_inc(self.done.s, 1)
        pe.transpose(ps[:, 4, 0:self.n0], self.rows[0][0:self.n0, :], k.c("ident", self.n0)[:, 0:self.n0])
        pe.transpose(ps[:, 4, 128:182], self.rows[1][0:54, :], k.c("ident", 54)[:, 0:54]).then_inc(self.done.s, 1)

    def dve(self, dve):
        k, ps = self.k, self.k.ps
        for c in range(DC):
            dve.wait_ge(self.done.s, c + 1)
            b = 2 * (c % 2)
            dve.tensor_copy(k.x[:, c, 0:SEQ], ps[:, b, :])
            dve.tensor_copy(k.x[:, c, SEQ:TOK], ps[:, b + 1, 0:8]).then_inc(self.out.s, 1)
        dve.wait_ge(self.done.s, DC + 1)
        dve.tensor_copy(k.vcol[:, 0:self.n0], ps[:, 4, 0:self.n0])
        dve.tensor_copy(k.vcol[:, self.n0:self.n0 + 54], ps[:, 4, 128:182])

    def act(self, act):
        for out, src in self.loads:
            act.dma_start(out, src).then_inc(self.here.s, 16)
        for n in range(RING):
            split_high(self.k, act, n)


def stream_norm(k, name, gain, width=TOK, src=None, dst=None):
    src = src if src is not None else k.x
    hi, lo = dst if dst is not None else (k.xn_hi, k.xn_lo)
    k.small.reset()
    tmp = [k.small(f"{name}_tmp{i}", [P, width]) for i in range(2)]

    def apply(dve, u, rstd):
        for c in range(DC):
            t = tmp[c % 2][:, :]
            k.dve_link(dve.scalar_tensor_tensor(t, src[:, c, :], k.col(gain + c), rstd, ALU.mult, ALU.mult))
            k.dve_link(dve.tensor_copy(hi[:, c, :], t))
            last = dve.tensor_tensor(lo[:, c, :], t, hi[:, c, :].bitcast(F32), ALU.subtract)
        return last

    return HeadNorm(k, name, [[src[:, c, :] for c in range(DC)]], k.c("ones"), D_MODEL, apply, width)


def gain_in_place(k, chunks, gains):
    def apply(dve, u, rstd):
        return dve.scalar_tensor_tensor(chunks[u], chunks[u], k.col(gains[u]), rstd, ALU.mult, ALU.mult)
    return apply


class Rope(Stage):

    def __init__(self, k, name, chunks, table, kept=0):
        super().__init__(k)
        self.chunks, self.table = chunks, table
        k.small.reset(kept)
        self.t = [k.small(f"{name}_sin{i}", [P, TOK]) for i in range(2)]
        self.rot, self.free = k.counter(f"{name}_rotated"), k.counter(f"{name}_free")

    def pe(self, pe):
        for i, x in enumerate(self.chunks):
            if i >= 2:
                pe.wait_ge(self.free.s, i - 1)
            for b, (c0, c1) in enumerate(HALVES):
                last = pe.matmul(self.k.ps[:, 2 * (i % 2) + b, 0:HALF], self.k.lc(self.table, "rot"), x[:, c0:c1],
                                 start=True, stop=True)
            last.then_inc(self.rot.s, 1)

    def dve(self, dve):
        k = self.k
        for i, x in enumerate(self.chunks):
            dve.wait_ge(self.rot.s, i + 1)
            t = self.t[i % 2][:, :]
            dve.tensor_tensor(two(t), k.ps[:, 2 * (i % 2):2 * (i % 2) + 2, 0:HALF], two(k.lc(self.table, "sin")),
                              ALU.mult).then_inc(self.free.s, 1)
            k.dve_link(dve.tensor_tensor(x, x, k.lc(self.table, "cos"), ALU.mult))
            dve.tensor_tensor(x, x, t, ALU.add)


class Turn(Stage):

    def __init__(self, k, name, items):
        super().__init__(k)
        self.items = items
        self.done, self.free = k.turn_signals
        self.base = k.turn_count
        k.turn_count += len(items)

    def pe(self, pe):
        k = self.k
        for i, (pieces, _, _) in enumerate(self.items):
            if i >= 4:
                pe.wait_ge(self.free.s, self.base + i - 3)
            for src, c0 in pieces:
                rows, n = src.shape
                last = pe.transpose(k.ps[0:n, 4 + i % 4, c0:c0 + rows], src, self.ident(src, rows))
            last.then_inc(self.done.s, 1)

    def ident(self, src, rows):
        at = src.base_partition() if callable(src.base_partition) else src.base_partition
        return self.k.const[at:at + rows, at:at + rows]

    def copy(self, eng, me):
        k = self.k
        for i, (_, view, dst) in enumerate(self.items):
            if (i % 2 == 0) == (me == "dve"):
                eng.wait_ge(self.done.s, self.base + i + 1)
                src = view(k.ps[:, 4 + i % 4, :])
                if i:
                    eng.wait_ge(self.free.s, self.base + i)
                if me == "dve":
                    eng.tensor_copy(dst, src).then_inc(self.free.s, 1)
                else:
                    eng.activation(dst, src, ACT.Copy).then_inc(self.free.s, 1)

    def dve(self, dve):
        self.copy(dve, "dve")

    def act(self, act):
        self.copy(act, "act")


def split_out(k, dve, dst_hi, dst_lo, src):
    k.dve_link(dve.tensor_copy(dst_hi, src))
    return dve.tensor_tensor(dst_lo, src, dst_hi.bitcast(F32), ALU.subtract)


class Ffn(Gemm):

    def __init__(self, k, layer):
        w1, w2 = k.A["ffn_w1"][layer], k.A["ffn_w2"][layer]
        k.small.reset()
        self.relu = [k.small(f"relu{layer}_{i}", [P, TOK]) for i in range(2)]
        self.sqr = [k.small(f"sqr{layer}_{i}", [P, TOK]) for i in range(2)]
        self.relu_ready, self.sq_ready, self.hid_ready = k.ffn_signals
        self.hid0 = layer * FFN // P
        tiles = []
        for what, q in (("up", 0), ("up", 1), ("down", 0), ("up", 2), ("down", 1), ("up", 3), ("down", 2), ("down", 3)):
            for m in range(DC):
                if what == "up":
                    h = q * DC + m
                    tiles.append(gemm_tile(w1, [(h * P, P)], (k.xn_hi, k.xn_lo), None, hidden=h))
                else:
                    tiles.append(gemm_tile(w2, [(m * P, P)], (k.hid_hi[q % 2], k.hid_lo[q % 2]),
                                           out_residual(k, m), row0=q * DC,
                                           rhs_ready=(self.hid_ready, self.hid0 + (q + 1) * DC)))
        super().__init__(k, tiles)

    def low(self, dve, h):
        k = self.k
        dve.wait_ge(self.sq_ready.s, self.hid0 + h + 1)
        hi, lo = k.hid_hi[h // DC % 2][:, h % DC, :], k.hid_lo[h // DC % 2][:, h % DC, :]
        dve.tensor_tensor(lo, self.sqr[h % 2][:, :], hi.bitcast(F32), ALU.subtract).then_inc(self.hid_ready.s, 1)

    def dve(self, dve):
        k, ps = self.k, self.k.ps
        pending = None
        for i, t in enumerate(self.mine):
            n = self.base + i
            dve.wait_ge(k.tile_done.s, n + 1)
            src = ps[:, 2 * (n % 3):2 * (n % 3) + 2, 0:HALF]
            if "hidden" in t:
                h = t["hidden"]
                dve.tensor_scalar(two(self.relu[h % 2][:, :]), src, 0.0, None, ALU.max).then_inc(k.tile_out.s, 1)
            else:
                t["out"](dve, src, 2)
            dve.wait_ge(k.tile_out.s, n + 1)
            if pending is not None:
                self.low(dve, pending)
            pending = t.get("hidden")

    def act(self, act):
        k = self.k
        for i, t in enumerate(self.mine):
            n = self.base + i
            if "hidden" in t:
                h = t["hidden"]
                act.wait_ge(k.tile_out.s, n + 1)
                hi = k.hid_hi[h // DC % 2][:, h % DC, :]
                act.activation(self.sqr[h % 2][:, :], self.relu[h % 2][:, :], ACT.Square)
                act.activation(hi, self.relu[h % 2][:, :], ACT.Square).then_inc(self.sq_ready.s, 1)
            if n + RING < len(k.tiles):
                act.wait_ge(k.tile_done.s, n + 1)
                split_high(k, act, n + RING)


class Spread(Stage):

    def __init__(self, k, name, items):
        super().__init__(k)
        self.items = items
        self.full, self.free = k.spread_signals
        self.base = k.spread_count
        k.spread_count += len(items)

    def pe(self, pe):
        for i, (products, _) in enumerate(self.items):
            if i >= 8:
                pe.wait_ge(self.free.s, self.base + i - 7)
            for (c0, c1), lhsT, rhs, row in products:
                last = pe.matmul(self.k.ps[row:row + lhsT.shape[1], i % 8, c0:c1], lhsT, rhs, start=True, stop=True)
            last.then_inc(self.full.s, 1)

    def dve(self, dve):
        for i, (_, take) in enumerate(self.items):
            dve.wait_ge(self.full.s, self.base + i + 1)
            take(dve, self.k.ps[:, i % 8, :]).then_inc(self.free.s, 1)


def blocks(ap):
    return ap.rearrange("p (n t) -> p n t", t=P)


def even_projection(k):
    w, xn = k.A["even_w_in"][0], (k.xn_hi, k.xn_lo)
    tiles = []
    for g in range(4):
        tiles.append(gemm_tile(w, [(64 * g, 64), (256 + 64 * g, 64)], xn, out_copy(k, k.proj[:, g, :])))
    for c in range(4, 18):
        scale = 64 ** -0.5 if E_MK <= c < E_MV else None
        tiles.append(gemm_tile(w, [(c * P, P)], xn, out_copy(k, k.proj[:, c, :], scale)))
    for c, at in ((E_GI, 18 * P), (E_GF, 18 * P + 4)):
        tiles.append(gemm_tile(w, [(at, 4)], xn, out_copy(k, k.proj[0:4, c, :])))
    return Gemm(k, tiles)


class EvenTurn(Turn):

    def __init__(self, k):
        p = k.proj
        k.big.reset(20 * TOK * 4)
        k.sv_tok = k.big("sv_tok", [P, NBLK, P])
        k.mk_tok = k.big("mk_tok", [P, NBLK, 2 * P])
        k.mv_tok = k.big("mv_tok", [P, NBLK, 4, P + 1])
        k.small.reset()
        k.kout = k.small("k_last_block", [P, P])
        k.kv_s = k.small("kv_sample", [NSAMPLE, 2, P])
        k.mv_s = k.small("mv_sample", [NSAMPLE, 512])
        k.even_kept = k.small.at
        four = lambda b: blocks(b[:, 0:512])
        turn4 = lambda c: [(p[:, c, n * P:n * P + P], n * P) for n in range(NBLK)]
        items = [(turn4(E_SV), four, k.sv_tok[:, :, :])]
        items += [(turn4(E_MK + j), four, k.mk_tok[:, :, j * P:j * P + P]) for j in range(2)]
        items += [(turn4(E_MV + h), four, k.mv_tok[:, :, h, 0:P]) for h in range(4)]
        items.append(([(p[:, E_SK, 3 * P:SEQ], 0)], lambda b: b[:, 0:P], k.kout[:, :]))
        items.append(([(p[:, E_SK + i, SEQ:TOK], i * P) for i in range(2)],
                      lambda b: b[0:8, 0:2 * P].rearrange("p (i f) -> p i f", i=2), k.kv_s[:, :, :]))
        items.append(([(p[:, E_MV + h, SEQ:TOK], h * P) for h in range(4)], lambda b: b[0:8, 0:512], k.mv_s[:, :]))
        super().__init__(k, "even_turn", items)

    def dve(self, dve):
        dve.memset(self.k.mv_tok[:, :, :, P:P + 1], 1.0)
        super().dve(dve)

    def act(self, act):
        k = self.k
        mo = k.proj[:, E_MO:E_MO + 4, :]
        act.activation(mo, mo, ACT.Sigmoid)
        super().act(act)
        act.wait_ge(self.free.s, self.base + len(self.items))
        k.store(k.O["p_swa_k"].rearrange("l b p h d -> (l b p) (h d)"), k.kout[:, :])
        k.store(k.O["p_swa_v"].rearrange("l b p h d -> (l b p) (h d)"), k.sv_tok[:, 3, :])
        for i, name in enumerate(("k", "v")):
            new = k.O[f"s_swa_{name}"][0].rearrange("b s h d -> b s (h d)")
            old = k.A[f"cache_swa_{name}"][0].rearrange("b s h d -> b s (h d)")
            k.store(new[:, 0:P - 1, :], old[:, 1:P, :])
            k.store(new[:, P - 1, :], k.kv_s[:, i, :])


class SwaPrompt(Stage):

    def __init__(self, k):
        super().__init__(k)
        k.small.reset(k.even_kept)
        self.s = k.small("swa_s", [P, 8, 2 * P])
        self.pt = k.small("swa_pt", [P, 4, 4, P])
        self.mx, self.m, self.nm, self.d, self.den, self.es, self.r = (
            k.small(f"swa_{n}", [P, 8]) for n in ("mx", "m", "nm", "d", "den", "es", "r"))
        (self.scores, self.max_ready, self.exps, self.probs, self.turned, self.pt_ready, self.pv, self.pv_free) = (
            k.counter(f"swa_{n}") for n in ("scores", "max", "exps", "probs", "turned", "pt", "pv", "pv_free"))

    def pe(self, pe):
        k, ps, p = self.k, self.k.ps, self.k.proj
        for n in range(NBLK):
            kb = max(n - 1, 0)
            if n:
                pe.wait_ge(self.pv_free.s, n)
            for g in range(4):
                for v in range(2):
                    rows, at = slice(64 * v, 64 * v + 64), 256 * (g % 2)
                    last = pe.matmul(ps[:, 2 * v + g // 2, at:at + 256], p[rows, g, n * P:n * P + P],
                                     p[rows, E_SK, kb * P:kb * P + 2 * P], start=True, stop=True)
            last.then_inc(self.scores.s, 1)
            pe.wait_ge(self.probs.s, n + 1)
            for g in range(4):
                for v in range(2):
                    for s in range(2):
                        at = (2 * v + s) * P
                        last = pe.transpose(ps[:, 4 + g, at:at + P], self.s[:, 4 * v + g, s * P:s * P + P], k.c("ident"))
            last.then_inc(self.turned.s, 1)
            pe.wait_ge(self.pt_ready.s, n + 1)
            for g in range(4):
                for v in range(2):
                    for s in range(2):
                        last = pe.matmul(ps[64 * v:64 * v + 64, 0, g * P:g * P + P],
                                         k.sv_tok[:, kb + s, 64 * v:64 * v + 64], self.pt[:, g, 2 * v + s, :],
                                         start=s == 0, stop=s == 1)
            last.then_inc(self.pv.s, 1)

    def dve(self, dve):
        k, ps = self.k, self.k.ps
        sink = k.sink_row[:, :]
        for n in range(NBLK):
            mask = k.lc(EVEN, "mask_later" if n else "mask_first").unsqueeze(1).to_broadcast([P, 2, 2 * P])
            dve.wait_ge(self.scores.s, n + 1)
            for g in range(4):
                ins = dve.tensor_tensor(self.s[:, 2 * g:2 * g + 2, :],
                                        ps[:, g, :].rearrange("p (v s) -> p v s", v=2), mask, ALU.add)
            k.dve_link(ins)
            k.dve_link(dve.tensor_reduce(self.mx[:, :], self.s[:, :, :], AX.X, ALU.max))
            k.dve_link(dve.scalar_tensor_tensor(self.m[:, :], self.mx[:, :], 0.125, sink, ALU.mult, ALU.max))
            dve.tensor_tensor(self.d[:, :], sink, self.m[:, :], ALU.subtract)
            dve.tensor_scalar(self.nm[:, :], self.m[:, :], -1.0, None, ALU.mult).then_inc(self.max_ready.s, 1)
            dve.wait_ge(self.exps.s, n + 1)
            k.dve_link(dve.tensor_tensor(self.r[:, :], self.den[:, :], self.es[:, :], ALU.add))
            k.dve_link(dve.reciprocal(self.r[:, :], self.r[:, :]))
            dve.tensor_tensor(self.s[:, :, :], self.s[:, :, :], self.r[:, :].unsqueeze(2).to_broadcast([P, 8, 2 * P]),
                              ALU.mult).then_inc(self.probs.s, 1)
            dve.wait_ge(self.pv.s, n + 1)
            cols = slice(n * P, n * P + P)
            split_out(k, dve, k.y_hi[:, 0:4, cols], k.y_lo[:, 0:4, cols], blocks(ps[:, 0, :]))\
                .then_inc(self.pv_free.s, 1)

    def act(self, act):
        k, ps = self.k, self.k.ps
        for n in range(NBLK):
            act.wait_ge(self.max_ready.s, n + 1)
            for i in range(8):
                act.activation(self.s[:, i, :], self.s[:, i, :], ACT.Exp, scale=0.125, bias=self.nm[:, i:i + 1],
                               accum_out=self.den[:, i:i + 1])
            act.activation(self.es[:, :], self.d[:, :], ACT.Exp).then_inc(self.exps.s, 1)
            act.wait_ge(self.turned.s, n + 1)
            for g in range(4):
                ins = act.activation(self.pt[:, g, :, :], blocks(ps[:, 4 + g, :]), ACT.Copy)
            ins.then_inc(self.pt_ready.s, 1)


class SwaSample(Stage):

    def __init__(self, k):
        super().__init__(k)
        k.small.reset(k.even_kept)
        self.kc, self.vc, self.kt = (k.small(f"swas_{n}", [P, 8, P]) for n in ("kc", "vc", "kt"))
        self.qz = k.small("swas_q", [P, 8, 2, 4])
        self.prod, self.st, self.pt, self.o, self.t = (
            k.small(f"swas_{n}", [P, 64]) for n in ("prod", "st", "pt", "o", "t"))
        self.s = k.small("swas_s", [64, P])
        self.own, self.mx, self.m, self.nm, self.d, self.den, self.eo, self.es, self.r = (
            k.small(f"swas_{n}", [64, 1]) for n in ("own", "mx", "m", "nm", "d", "den", "eo", "es", "r"))
        (self.here, self.kturn, self.kt_ready, self.q_ready, self.scores, self.st_ready, self.rows, self.max_ready,
         self.exps, self.probs, self.pturn, self.pt_ready, self.pv) = (
            k.counter(f"swas_{n}") for n in ("here", "kturn", "kt", "q", "scores", "st", "rows", "max", "exps",
                                            "probs", "pturn", "pt", "pv"))

    def act(self, act):
        k, ps = self.k, self.k.ps
        for t, name in ((self.kc, "k"), (self.vc, "v")):
            act.dma_start(t[:, :, :], k.A[f"cache_swa_{name}"][0].rearrange("b s h d -> s b (h d)"))\
               .then_inc(self.here.s, 16)
        act.wait_ge(self.kturn.s, 1)
        for i in range(2):
            ins = act.activation(self.kt[:, 4 * i:4 * i + 4, :], blocks(ps[:, i, :]), ACT.Copy)
        ins.then_inc(self.kt_ready.s, 1)
        act.wait_ge(self.max_ready.s, 1)
        act.activation(self.s[:, :], self.s[:, :], ACT.Exp, scale=0.125, bias=self.nm[:, :], accum_out=self.den[:, :])
        act.activation(self.eo[:, :], self.own[:, :], ACT.Exp, scale=0.125, bias=self.nm[:, :])
        act.activation(self.es[:, :], self.d[:, :], ACT.Exp).then_inc(self.exps.s, 1)

    def pe(self, pe):
        k, ps = self.k, self.k.ps
        pe.wait_ge(self.here.s, 32)
        for b in range(8):
            last = pe.transpose(ps[:, b // 4, (b % 4) * P:(b % 4) * P + P], self.kc[:, b, :], k.c("ident"))
        last.then_inc(self.kturn.s, 1)
        pe.wait_ge(self.kt_ready.s, 1)
        pe.wait_ge(self.q_ready.s, 1)
        for b in range(8):
            pe.matmul(ps[:, 2, 8 * b:8 * b + 8], self.kt[:, b, :], self.qz[:, b, :, :], start=True, stop=True)
        pe.matmul(ps[0:64, 3, 0:1], self.prod[:, :], k.c("ones")[:, 0:1], start=True, stop=True)\
          .then_inc(self.scores.s, 1)
        pe.wait_ge(self.st_ready.s, 1)
        pe.transpose(ps[0:64, 4, 0:P], self.st[:, :], k.c("ident")).then_inc(self.rows.s, 1)
        pe.wait_ge(self.probs.s, 1)
        pe.transpose(ps[:, 5, 0:64], self.s[:, :], k.c("ident", 64)[:, 0:64])
        pe.matmul(ps[:, 6, 0:64], self.eo[:, :].to_broadcast([64, P]), k.c("ident", 64)[:, 0:64], start=True, stop=True)\
          .then_inc(self.pturn.s, 1)
        pe.wait_ge(self.pt_ready.s, 1)
        for b in range(8):
            last = pe.matmul(ps[:, 7, 8 * b:8 * b + 8], self.vc[:, b, :], self.pt[:, 8 * b:8 * b + 8], start=True, stop=True)
        last.then_inc(self.pv.s, 1)

    def dve(self, dve):
        k, ps, p = self.k, self.k.ps, self.k.proj
        k.dve_link(dve.memset(self.qz[:, :, :, :], 0.0))
        for v in range(2):
            rows = slice(64 * v, 64 * v + 64)
            ins = dve.tensor_copy(self.qz[rows, :, v, :], p[rows, 0:4, SEQ:TOK].rearrange("p g b -> p b g"))
        k.dve_link(ins)
        spread = lambda t: t[:, :].rearrange("p (b h) -> p b h", b=8)
        new = lambda c: p[:, c, SEQ:TOK].unsqueeze(2).to_broadcast([P, 8, 8])
        dve.tensor_tensor(spread(self.prod), self.qz[:, :, :, :].rearrange("p b v g -> p b (v g)"), new(E_SK), ALU.mult)\
           .then_inc(self.q_ready.s, 1)
        dve.wait_ge(self.scores.s, 1)
        dve.tensor_copy(self.own[:, :], ps[0:64, 3, 0:1])
        dve.tensor_copy(self.st[:, :], ps[:, 2, 0:64]).then_inc(self.st_ready.s, 1)
        dve.wait_ge(self.rows.s, 1)
        k.dve_link(dve.tensor_copy(self.s[:, :], ps[0:64, 4, 0:P]))
        k.dve_link(dve.tensor_reduce(self.mx[:, :], self.s[:, :], AX.X, ALU.max))
        k.dve_link(dve.tensor_tensor(self.mx[:, :], self.mx[:, :], self.own[:, :], ALU.max))
        k.dve_link(dve.scalar_tensor_tensor(self.m[:, :], self.mx[:, :], 0.125, k.sink_col[:, :], ALU.mult, ALU.max))
        dve.tensor_tensor(self.d[:, :], k.sink_col[:, :], self.m[:, :], ALU.subtract)
        dve.tensor_scalar(self.nm[:, :], self.m[:, :], -1.0, None, ALU.mult).then_inc(self.max_ready.s, 1)
        dve.wait_ge(self.exps.s, 1)
        k.dve_link(dve.tensor_tensor(self.r[:, :], self.den[:, :], self.es[:, :], ALU.add))
        k.dve_link(dve.tensor_tensor(self.r[:, :], self.r[:, :], self.eo[:, :], ALU.add))
        k.dve_link(dve.reciprocal(self.r[:, :], self.r[:, :]))
        dve.tensor_tensor(self.eo[:, :], self.eo[:, :], self.r[:, :], ALU.mult)
        dve.tensor_scalar(self.s[:, :], self.s[:, :], self.r[:, :], None, ALU.mult).then_inc(self.probs.s, 1)
        dve.wait_ge(self.pturn.s, 1)
        dve.tensor_copy(self.pt[:, :], ps[:, 5, 0:64]).then_inc(self.pt_ready.s, 1)
        k.dve_link(dve.tensor_tensor(spread(self.t), ps[:, 6, 0:64].rearrange("p (b h) -> p b h", b=8), new(E_SV), ALU.mult))
        dve.wait_ge(self.pv.s, 1)
        k.dve_link(dve.tensor_tensor(self.o[:, :], self.t[:, :], ps[:, 7, 0:64], ALU.add))
        for v in range(2):
            rows = slice(64 * v, 64 * v + 64)
            src = self.o[rows, :].rearrange("p (b v g) -> p v g b", b=8, v=2)[:, v]
            split_out(k, dve, k.y_hi[rows, 0:4, SEQ:TOK], k.y_lo[rows, 0:4, SEQ:TOK], src)


def log1p_exp(k, dve, act, me, name, x, e, u, l, w):
    here, ready = k.log_signals
    if me == "dve":
        dve.scalar_tensor_tensor(e, x, -1.0, x, ALU.mult, ALU.min).then_inc(here.s, 1)
        dve.wait_ge(ready.s, ready.next("dve"))
        dve.tensor_scalar(u, e, 1.0, None, ALU.add).then_inc(here.s, 1)
        dve.wait_ge(ready.s, ready.next("dve"))
        k.dve_link(dve.tensor_scalar(w, u, -1.0, None, ALU.add))
        k.dve_link(dve.tensor_tensor(w, e, w, ALU.subtract))
        k.dve_link(dve.reciprocal(u, u))
        k.dve_link(dve.tensor_tensor(w, w, u, ALU.mult))
        k.dve_link(dve.tensor_tensor(l, l, w, ALU.add))
    else:
        act.wait_ge(here.s, here.next("act"))
        act.activation(e, e, ACT.Exp).then_inc(ready.s, 1)
        act.wait_ge(here.s, here.next("act"))
        act.activation(l, u, ACT.Ln).then_inc(ready.s, 1)


class EvenGates(Stage):

    def __init__(self, k):
        super().__init__(k)
        k.small.reset(k.even_kept)
        (k.g_m, k.g_a, k.g_c, k.g_em, k.g_cs) = (k.small(f"gate_{n}", [4, TOK]) for n in ("m", "a", "c", "em", "cs"))
        kept = k.big.at
        (k.g_i, k.g_f, self.x, self.e, self.u, self.l, self.w, k.g_cum) = (
            k.big(f"gate_{n}", [4, TOK]) for n in ("i_", "f_", "x", "e", "u", "l", "w", "cum"))
        k.big.reset(kept)
        k.g_m0, k.g_ws = k.small("gate_m0", [4, 8]), k.small("gate_ws", [4, 8])
        self.here, self.exponents, self.ready = (k.counter(f"gates_{n}") for n in ("m0_here", "exponents", "ready"))

    def act(self, act):
        k = self.k
        act.dma_start(k.g_m0[:, :], k.A["state_mlstm_m"][0].rearrange("b h -> h b"),
                      allow_slow_non_contiguous=True).then_inc(self.here.s, 16)
        log1p_exp(k, None, act, "act", "even", self.x[:, :], self.e[:, :], self.u[:, :], self.l[:, :], self.w[:, :])
        act.wait_ge(self.exponents.s, 1)
        act.activation(k.g_em[:, :], k.g_m[:, :], ACT.Exp, scale=-1.0)
        act.activation(k.g_cs[:, :], k.g_cs[:, :], ACT.Exp)
        act.activation(k.g_ws[:, :], k.g_ws[:, :], ACT.Exp).then_inc(self.ready.s, 1)

    def dve(self, dve):
        k, p = self.k, self.k.proj
        dve.tensor_scalar(k.g_i[:, :], p[0:4, E_GI, :], k.gate_i[:, :], None, ALU.add)
        k.dve_link(dve.memset(self.w[:, :], 0.0))
        k.dve_link(dve.tensor_scalar(self.x[:, :], p[0:4, E_GF, :], k.gate_f[:, :], None, ALU.add))
        log1p_exp(k, dve, None, "dve", "even", self.x[:, :], self.e[:, :], self.u[:, :], self.l[:, :], self.w[:, :])
        k.dve_link(dve.scalar_tensor_tensor(k.g_f[:, :], self.x[:, :], 0.0, self.l[:, :], ALU.min, ALU.subtract))
        k.dve_link(dve.memset(self.w[:, :], 0.0))
        for n in range(NBLK):
            c = slice(n * P, n * P + P)
            dve.tensor_tensor_scan(k.g_cum[:, c], k.g_f[:, c], self.w[:, c], 0.0, ALU.add, ALU.add)
        dve.tensor_tensor_scan(k.g_m[:, 0:SEQ], k.g_f[:, 0:SEQ], k.g_i[:, 0:SEQ], 0.0, ALU.add, ALU.max)
        dve.wait_ge(self.here.s, 16)
        k.dve_link(dve.tensor_tensor(k.g_cs[:, SEQ:TOK], k.g_f[:, SEQ:TOK], k.g_m0[:, :], ALU.add))
        k.dve_link(dve.tensor_tensor(k.g_m[:, SEQ:TOK], k.g_cs[:, SEQ:TOK], k.g_i[:, SEQ:TOK], ALU.max))
        dve.tensor_tensor(k.g_cs[:, SEQ:TOK], k.g_cs[:, SEQ:TOK], k.g_m[:, SEQ:TOK], ALU.subtract)
        dve.tensor_tensor(k.g_ws[:, :], k.g_i[:, SEQ:TOK], k.g_m[:, SEQ:TOK], ALU.subtract)
        dve.tensor_tensor(k.g_c[:, 0:SEQ], k.g_i[:, 0:SEQ], k.g_cum[:, 0:SEQ], ALU.subtract)
        k.dve_link(dve.tensor_tensor(k.g_a[:, 0:SEQ], k.g_cum[:, 0:SEQ], k.g_m[:, 0:SEQ], ALU.subtract))
        ins = dve.tensor_copy(k.g_cs[:, 0:P], k.g_a[:, 0:P])
        for n in range(1, NBLK):
            c = slice(n * P, n * P + P)
            ins = dve.tensor_scalar(k.g_cs[:, c], k.g_a[:, c], k.g_m[:, n * P - 1:n * P], None, ALU.add)
        ins.then_inc(self.exponents.s, 1)
        dve.wait_ge(self.ready.s, 1)


def even_spread(k):
    k.w_ml = k.big("ml_weight", [P, 4, SEQ])
    k.em = k.big("ml_em", [P, 4, TOK])
    k.cs = k.big("ml_cs", [P, 2, TOK])
    k.c_col = k.small("ml_c_col", [P, NBLK, 4])
    k.ws = k.small("ml_ws", [P, 2, 8])
    k.even_kept2 = k.small.at
    items = []
    for h in range(4):
        def mask(dve, bank, h=h):
            return dve.tensor_tensor(blocks(k.w_ml[:, h, :]), blocks(bank[:, 0:512]),
                                     k.c("causal").unsqueeze(1).to_broadcast([P, NBLK, P]), ALU.add)
        items.append(([((0, SEQ), k.onehot(h, 4), k.g_a[:, 0:SEQ], 0)], mask))
        items.append(([((0, SEQ), k.onehot(h, 4), k.g_em[:, 0:SEQ], 0)],
                      lambda dve, bank, h=h: dve.tensor_copy(k.em[:, h, 0:SEQ], bank[:, 0:SEQ])))
    items.append(([((8 * h, 8 * h + 8), k.onehot(h, 4), k.g_em[:, SEQ:TOK], 0) for h in range(4)],
                  lambda dve, bank: dve.tensor_copy(k.em[:, :, SEQ:TOK], bank[:, 0:32].rearrange("p (h b) -> p h b", h=4))))
    for j in range(2):
        items.append((k.pair(j, 4, (0, SEQ), k.g_cs[:, 0:SEQ]),
                      lambda dve, bank, j=j: dve.tensor_copy(k.cs[:, j, 0:SEQ], bank[:, 0:SEQ])))
    pairs = lambda src: k.pair(0, 4, (0, 8), src) + k.pair(1, 4, (8, 16), src)
    take = lambda dst: lambda dve, bank: dve.tensor_copy(dst, bank[:, 0:16].rearrange("p (j b) -> p j b", j=2))
    items.append((pairs(k.g_cs[:, SEQ:TOK]), take(k.cs[:, :, SEQ:TOK])))
    items.append((pairs(k.g_ws[:, :]), take(k.ws[:, :, :])))
    items.append(([((4 * n, 4 * n + 4), k.g_c[:, n * P:n * P + P], k.c("ident", 4)[:, 0:4], 0) for n in range(NBLK)],
                  lambda dve, bank: dve.tensor_copy(k.c_col[:, :, :], bank[:, 0:16].rearrange("p (n h) -> p n h", n=4))))
    return Spread(k, "even_spread", items)


class MlstmPrompt(Stage):

    def __init__(self, k):
        super().__init__(k)
        k.small.reset(k.even_kept2)
        k.ml_state = k.small("ml_state", [P, 2, P + 1])
        self.a = k.small("ml_a", [P, 4, P])
        self.kw = k.small("ml_kw", [P, 4, 64])
        self.den = k.small("ml_den", [P, 4, P])
        self.weights, self.st, self.a_ready, self.num, self.state = (
            k.counter(f"ml_{n}") for n in ("weights", "scores", "weighted", "num", "state"))

    def act(self, act):
        k = self.k
        for n in range(NBLK):
            c = slice(n * P, n * P + P)
            for h in range(4):
                ins = act.activation(k.w_ml[:, h, c], k.w_ml[:, h, c], ACT.Exp, bias=k.c_col[:, n, h:h + 1])
            ins.then_inc(self.weights.s, 1)
        act.wait_ge(self.state.s, NBLK)
        k.store(k.O["p_C"][0, 0].rearrange("(j t) d e -> (t d) j e", t=2), k.ml_state[:, :, 0:P])
        k.store(k.O["p_n"][0, 0].rearrange("(j t) d -> (t d) j", t=2), k.ml_state[:, :, P], few=True)
        k.store(k.O["p_m"].rearrange("l b h -> h (l b)"), k.g_m[:, SEQ - 1:SEQ])
        k.store(k.O["s_m"][0].rearrange("b h -> h b"), k.g_m[:, SEQ:TOK], few=True)

    def pe(self, pe):
        k, ps, p = self.k, self.k.ps, self.k.proj
        for n in range(NBLK):
            c = slice(n * P, n * P + P)
            for h in range(4):
                rows = slice(64 * (h % 2), 64 * (h % 2) + 64)
                at = (h // 2) * P
                last = pe.matmul(ps[:, 4 * (h % 2), at:at + P], p[rows, E_MK + h // 2, c], p[rows, E_MQ + h // 2, c],
                                 start=True, stop=True)
            last.then_inc(self.st.s, 1)
            pe.wait_ge(self.a_ready.s, n + 1)
            if n:
                pe.wait_ge(self.state.s, n)
            for h in range(4):
                rows, j = slice(64 * (h % 2), 64 * (h % 2) + 64), h // 2
                out = ps[:, 1 + 4 * (h % 2), j * P:j * P + P]
                pe.matmul(out, k.mv_tok[:, n, h, 0:P], self.a[:, h, :], start=True, stop=n == 0)
                if n:
                    pe.matmul(out, k.ml_state[rows, j, 0:P], self.qs[rows, j, c], start=False, stop=True)
                out = ps[:, 2 + 4 * (h % 2), j * P:j * P + P]
                pe.matmul(out, k.c("ones"), self.a[:, h, :], start=True, stop=n == 0)
                if n:
                    pe.matmul(out, k.ml_state[rows, j, P:P + 1].to_broadcast([64, P]), self.qs[rows, j, c],
                              start=False, stop=True)
            for h in range(4):
                last = pe.matmul(ps[64 * (h % 2):64 * (h % 2) + 64, 3, (h // 2) * (P + 1):(h // 2 + 1) * (P + 1)],
                                 self.kw[:, h, :], k.mv_tok[:, n, h, :], start=True, stop=True)
            last.then_inc(self.num.s, 1)

    @property
    def qs(self):
        return self.k.qs_view

    def dve(self, dve):
        k, ps, p = self.k, self.k.ps, self.k.proj
        for j in range(2):
            dve.tensor_tensor(k.qs_view[:, j, :], p[:, E_MQ + j, 0:SEQ], k.cs[:, j, 0:SEQ], ALU.mult)
        for n in range(NBLK):
            c = slice(n * P, n * P + P)
            dve.wait_ge(self.weights.s, n + 1)
            k.dve_link(dve.tensor_tensor(self.kw[:, :, :], k.mk_tok[:, n, :].rearrange("p (h d) -> p h d", h=4),
                                         k.w_ml[:, :, n * P + P - 1:n * P + P].to_broadcast([P, 4, 64]), ALU.mult))
            dve.wait_ge(self.st.s, n + 1)
            for t in range(2):
                ins = dve.tensor_tensor(self.a[:, t::2, :], blocks(ps[:, 4 * t, 0:2 * P]), k.w_ml[:, t::2, c], ALU.mult)
            ins.then_inc(self.a_ready.s, 1)
            dve.wait_ge(self.num.s, n + 1)
            for t in range(2):
                ins = dve.scalar_tensor_tensor(self.den[:, t::2, :], blocks(ps[:, 2 + 4 * t, 0:2 * P]), -1.0,
                                               k.em[:, t::2, c], ALU.mult, ALU.max)
            k.dve_link(ins)
            for t in range(2):
                ins = dve.tensor_tensor(self.den[:, t::2, :], self.den[:, t::2, :], blocks(ps[:, 2 + 4 * t, 0:2 * P]),
                                        ALU.max)
            k.dve_link(ins)
            k.dve_link(dve.reciprocal(self.den[:, :, :], self.den[:, :, :]))
            for t in range(2):
                dve.tensor_tensor(p[:, E_MV + t:E_MV + 4:2, c], blocks(ps[:, 1 + 4 * t, 0:2 * P]), self.den[:, t::2, :],
                                  ALU.mult)
            if n == 0:
                ins = dve.tensor_copy(k.ml_state[:, :, :], ps[:, 3, 0:2 * (P + 1)].rearrange("p (j e) -> p j e", j=2))
            else:
                for j in range(2):
                    ins = dve.scalar_tensor_tensor(k.ml_state[:, j, :], k.ml_state[:, j, :],
                                                   k.cs[:, j, n * P + P - 1:n * P + P],
                                                   ps[:, 3, j * (P + 1):(j + 1) * (P + 1)], ALU.mult, ALU.add)
            ins.then_inc(self.state.s, 1)
            dve.wait_ge(self.state.s, n + 1)


class MlstmSample(Stage):

    def __init__(self, k):
        super().__init__(k)
        k.small.reset(k.even_kept2)
        self.c = k.small("mls_c", [P, 8, 2, P])
        self.t = k.small("mls_t", [P, 2, 2, P])
        self.ntok, self.nout = k.small("mls_n_tok", [8, 2 * P]), k.small("mls_n_out", [8, 2 * P])
        self.n, self.kw, self.prod = (k.small(f"mls_{n}", [P, 2, 8]) for n in ("n", "kw", "prod"))
        self.qz = k.small("mls_q", [P, 8, 2, 2])
        self.den = k.small("mls_den", [P, 2, 2, 8])
        (self.here, self.nturn, self.prep, self.vb, self.c_new, self.num) = (
            k.counter(f"mls_{n}") for n in ("here", "n_turned", "prepared", "v_spread", "c_new", "num"))
        self.n_out, self.n_back = k.counter("mls_n_out"), k.counter("mls_n_back")

    def act(self, act):
        k = self.k
        act.dma_start(self.ntok[:, :], k.A["state_mlstm_n"][0].rearrange("b h d -> b (h d)")).then_inc(self.here.s, 16)
        act.dma_start(self.c[:, :, :, :], k.A["state_mlstm_C"][0].rearrange("b (j t) d e -> (t d) b j e", t=2))\
           .then_inc(self.here.s, 16)
        act.wait_ge(self.c_new.s, 8)
        k.store(k.O["s_C"][0].rearrange("b (j t) d e -> (t d) b j e", t=2), self.c[:, :, :, :])
        act.wait_ge(self.n_out.s, 1)
        k.store(k.O["s_n"][0].rearrange("b h d -> b (h d)"), self.nout[:, :])
        k.stores_done()

    def pe(self, pe):
        k, ps = self.k, self.k.ps
        pe.wait_ge(self.here.s, 32)
        for j in range(2):
            last = pe.transpose(ps[:, 0, 8 * j:8 * j + 8], self.ntok[:, j * P:j * P + P], k.c("ident", 8)[:, 0:8])
        last.then_inc(self.nturn.s, 1)
        for b in range(8):
            if b >= 4:
                pe.wait_ge(self.c_new.s, b - 3)
            pe.matmul(ps[:, 4 + b % 4, :], k.onehot(b, 8), k.mv_s[:, :], start=True, stop=True).then_inc(self.vb.s, 1)
        pe.wait_ge(self.prep.s, 1)
        for t in range(2):
            pe.matmul(ps[:, 1, 16 * t:16 * t + 16], k.c("blk64")[:, 64 * t:64 * t + 1].to_broadcast([P, P]),
                      self.prod[:, :, :], start=True, stop=True)
        for j in range(2):
            last = pe.transpose(ps[0:8, 3, j * P:j * P + P], self.n[:, j, :], k.c("ident"))
        last.then_inc(self.n_back.s, 1)
        for b in range(8):
            pe.wait_ge(self.c_new.s, b + 1)
            for j in range(2):
                last = pe.matmul(ps[:, 2, 4 * b + 2 * j:4 * b + 2 * j + 2], self.c[:, b, j, :], self.qz[:, b, j, :],
                                 start=True, stop=True)
        last.then_inc(self.num.s, 1)

    def dve(self, dve):
        k, ps, p = self.k, self.k.ps, self.k.proj
        s = slice(SEQ, TOK)
        k.dve_link(dve.memset(self.qz[:, :, :, :], 0.0))
        for t in range(2):
            rows = slice(64 * t, 64 * t + 64)
            dve.tensor_copy(self.qz[rows, :, :, t], p[rows, E_MQ:E_MQ + 2, s].rearrange("p j b -> p b j"))
        k.dve_link(dve.tensor_tensor(self.kw[:, :, :], p[:, E_MK:E_MK + 2, s], k.ws[:, :, :], ALU.mult))
        dve.wait_ge(self.nturn.s, 1)
        k.dve_link(dve.tensor_tensor(self.n[:, :, :], ps[:, 0, 0:16].rearrange("p (j b) -> p j b", j=2), k.cs[:, :, s], ALU.mult))
        k.dve_link(dve.tensor_tensor(self.n[:, :, :], self.n[:, :, :], self.kw[:, :, :], ALU.add))
        dve.tensor_tensor(self.prod[:, :, :], self.n[:, :, :], p[:, E_MQ:E_MQ + 2, s], ALU.mult).then_inc(self.prep.s, 1)
        dve.wait_ge(self.here.s, 32)
        for b in range(8):
            dve.wait_ge(self.vb.s, b + 1)
            t = self.t[:, b % 2, :, :]
            for half in range(2):
                rows = slice(64 * half, 64 * half + 64)
                v = ps[rows, 4 + b % 4, :].rearrange("p (j t e) -> p t j e", j=2, t=2)[:, half]
                dve.tensor_tensor(t[rows], v, self.kw[rows, :, b:b + 1].to_broadcast([64, 2, P]), ALU.mult)
            k.dve_link(dve.tensor_tensor(self.c[:, b, :, :], self.c[:, b, :, :],
                                         k.cs[:, :, SEQ + b:SEQ + b + 1].to_broadcast([P, 2, P]), ALU.mult))
            dve.tensor_tensor(self.c[:, b, :, :], self.c[:, b, :, :], t, ALU.add).then_inc(self.c_new.s, 1)
        dve.wait_ge(self.n_back.s, 1)
        dve.tensor_copy(self.nout[:, :], ps[0:8, 3, 0:2 * P]).then_inc(self.n_out.s, 1)
        em = k.em[:, :, s].rearrange("p (j t) b -> p t j b", t=2)
        den = ps[:, 1, 0:32].rearrange("p (t j b) -> p t j b", t=2, j=2)
        for t in range(2):
            ins = dve.scalar_tensor_tensor(self.den[:, t], den[:, t], -1.0, em[:, t], ALU.mult, ALU.max)
        k.dve_link(ins)
        for t in range(2):
            ins = dve.tensor_tensor(self.den[:, t], self.den[:, t], den[:, t], ALU.max)
        k.dve_link(ins)
        k.dve_link(dve.reciprocal(self.den[:, :, :, :], self.den[:, :, :, :]))
        dve.wait_ge(self.num.s, 1)
        num = ps[:, 2, 0:32].rearrange("p (b j t) -> p t j b", b=8, j=2)
        hb = p[:, E_MV:E_MV + 4, s].rearrange("p (j t) b -> p t j b", t=2)
        for t in range(2):
            dve.tensor_tensor(hb[:, t], num[:, t], self.den[:, t], ALU.mult)


def mlstm_norm(k):
    k.small.reset()
    def apply(dve, u, rstd):
        x = k.proj[:, E_MV + u, :]
        k.dve_link(dve.scalar_tensor_tensor(x, x, k.col(V_MLN + u), rstd, ALU.mult, ALU.mult))
        k.dve_link(dve.tensor_tensor(x, x, k.proj[:, E_MO + u, :], ALU.mult))
        return split_out(k, dve, k.y_hi[:, 4 + u, :], k.y_lo[:, 4 + u, :], x)
    return HeadNorm(k, "ml_norm", [[k.proj[:, E_MV + u, :]] for u in range(4)], k.c("ones"), P, apply)


def even_layer(k):
    s = [stream_norm(k, "mix0", V_MIX), even_projection(k)]
    k.small.reset()
    qk = [k.proj[:, c, :] for c in range(5)]
    s.append(HeadNorm(k, "qk_norm", [[c] for c in qk], k.c("blk64"), 64, gain_in_place(k, qk, [V_SQ] * 4 + [V_SK])))
    s.append(Rope(k, "even_rope", qk, EVEN))
    s += [EvenTurn(k), SwaPrompt(k), SwaSample(k), EvenGates(k), even_spread(k)]
    k.mid.reset(8 * TOK * 4)
    k.qs_view = k.mid("ml_scaled_q", [P, 2, SEQ])
    s += [MlstmPrompt(k), MlstmSample(k), mlstm_norm(k)]
    w = k.A["even_w_out"][0]
    tiles = []
    for m in range(DC):
        t, cols = gemm_tile(w, [(m * P, P)], (k.y_hi, k.y_lo), out_residual(k, m)), slice(m * P, m * P + P)
        t["parts"] = [((64 * v, 64 * v + 64), (0, 4), (0, P),
                       w[256 * v:256 * v + 256, cols].rearrange("(k p) n -> p k n", p=64)) for v in range(2)]
        t["parts"].append(((0, P), (4, 8), (0, P), w[512:1024, cols].rearrange("(k p) n -> p k n", p=P)))
        tiles.append(t)
    s.append(Gemm(k, tiles))
    return s


class Buffers:
    pass


class MemTurn(Turn):

    def __init__(self, k, m, layer):
        k.big.reset(k.cross_kept)
        self.mtok = k.big(f"mem_tok{layer}", [P, 2, D_MODEL])
        m.mem_t = k.big(f"mem_t{layer}", [P, DC, MEM])
        m.hm_hi, m.hm_lo = (k.big(f"hm_{n}{layer}", [P, DC, MEM], F32R) for n in ("hi", "lo"))
        items = []
        for c in range(0, DC, 2):
            items.append(([(self.mtok[:, s, (c + i) * P:(c + i + 1) * P], i * MEM + s * P) for i in range(2)
                           for s in range(2)],
                          lambda b: b[:, 0:512].rearrange("p (i t) -> p i t", i=2), m.mem_t[:, c:c + 2, :]))
        super().__init__(k, f"mem_turn{layer}", items)
        self.layer, self.m = layer, m

    def act(self, act):
        k = self.k
        act.dma_start(self.mtok[:, :, :], k.A["mem_prompt"].rearrange("b (s p) d -> p (b s) d", p=P))\
           .then_inc(k.mem_here.s, 16)
        super().act(act)

    def pe(self, pe):
        pe.wait_ge(self.k.mem_here.s, 16 * (self.layer + 1))
        super().pe(pe)


class KvTurn(Turn):

    def __init__(self, k, m, layer):
        four = lambda b: b[:, 0:512]
        items = []
        for src, dst in ((m.k_t, m.k_tok), (m.v_t, m.v_tok)):
            for s in range(2):
                items.append(([(src[:, h, s * P:s * P + P], h * P) for h in range(4)], four, dst[:, s, :]))
        super().__init__(k, f"kv_turn{layer}", items)
        self.layer, self.m = layer, m

    def act(self, act):
        k, m = self.k, self.m
        super().act(act)
        act.wait_ge(self.free.s, self.base + len(self.items))
        for name, t in (("mem_k", m.k_tok), ("mem_v", m.v_tok)):
            k.store(k.O[name][self.layer, 0].rearrange("(s p) h d -> p s (h d)", p=P), t[:, :, :])


class CrossPrompt(Stage):

    def __init__(self, k, m, layer):
        super().__init__(k)
        k.small.reset()
        self.s = [k.small(f"xa_s{layer}{i}", [P, 4, MEM]) for i in range(2)]
        self.pt = k.small(f"xa_pt{layer}", [P, 4, 2, P])
        self.mx, self.nm, self.den, self.r = (
            [k.small(f"xa_{n}{layer}{i}", [P, 4]) for i in range(2)] for n in ("mx", "nm", "den", "r"))
        (self.scores, self.max_ready, self.exps, self.probs, self.turned, self.pt_ready, self.pv, self.out) = k.xa_signals
        self.n0 = layer * NBLK
        k.mid.reset(4 * TOK * 4)
        m.kc = [k.mid(f"kc{layer}{b}", [P, 2, 512]) for b in range(4)]
        k.mid.reset(16 * TOK * 4)
        m.kc += [k.mid(f"kc{layer}{b + 4}", [P, 2, 512]) for b in range(4)]
        k.big.reset(k.cross_kept)
        m.vc = [k.big(f"vc{layer}{b}", [P, 2, 512]) for b in range(8)]
        self.layer, self.m = layer, m

    def pe_scores(self, pe, n):
        k, m, ps = self.k, self.m, self.k.ps
        if n >= 2:
            pe.wait_ge(self.exps.s, self.n0 + n - 1)
        for h in range(4):
            last = pe.matmul(ps[:, 2 * (n % 2) + h // 2, MEM * (h % 2):MEM * (h % 2) + MEM],
                             m.q[:, h, n * P:n * P + P], m.k_t[:, h, :], start=True, stop=True)
        last.then_inc(self.scores.s, 1)

    def pe(self, pe):
        k, m, ps = self.k, self.m, self.k.ps
        self.pe_scores(pe, 0)
        for n in range(NBLK):
            if n + 1 < NBLK:
                self.pe_scores(pe, n + 1)
            pe.wait_ge(self.probs.s, self.n0 + n + 1)
            for h in range(4):
                for s in range(2):
                    last = pe.transpose(ps[:, 4 + h // 2, 256 * (h % 2) + s * P:256 * (h % 2) + s * P + P],
                                        self.s[n % 2][:, h, s * P:s * P + P], k.c("ident"))
            last.then_inc(self.turned.s, 1)
            pe.wait_ge(self.pt_ready.s, self.n0 + n + 1)
            if n >= 2:
                pe.wait_ge(self.out.s, self.n0 + n - 1)
            for h in range(4):
                for s in range(2):
                    last = pe.matmul(ps[:, 6 + n % 2, h * P:h * P + P], m.v_tok[:, s, h * P:h * P + P],
                                     self.pt[:, h, s, :], start=s == 0, stop=s == 1)
            last.then_inc(self.pv.s, 1)

    def dve_max(self, dve, n):
        k, m, ps = self.k, self.m, self.k.ps
        dve.wait_ge(self.scores.s, self.n0 + n + 1)
        src = ps[:, 2 * (n % 2):2 * (n % 2) + 2, :].rearrange("p a (b m) -> p (a b) m", b=2)
        k.dve_link(dve.tensor_reduce(self.mx[n % 2][:, :], src, AX.X, ALU.max))
        dve.tensor_scalar(self.nm[n % 2][:, :], self.mx[n % 2][:, :], -(P ** -0.5), None, ALU.mult)\
           .then_inc(self.max_ready.s, 1)

    def dve(self, dve):
        k, m, ps = self.k, self.m, self.k.ps
        self.dve_max(dve, 0)
        for n in range(NBLK):
            if n + 1 < NBLK:
                self.dve_max(dve, n + 1)
            dve.wait_ge(self.exps.s, self.n0 + n + 1)
            r, s = self.r[n % 2], self.s[n % 2]
            k.dve_link(dve.reciprocal(r[:, :], self.den[n % 2][:, :]))
            dve.tensor_tensor(s[:, :, :], s[:, :, :], r[:, :].unsqueeze(2).to_broadcast([P, 4, MEM]), ALU.mult)\
               .then_inc(self.probs.s, 1)
            dve.wait_ge(self.pv.s, self.n0 + n + 1)
            cols = slice(n * P, n * P + P)
            split_out(k, dve, k.y_hi[:, 0:4, cols], k.y_lo[:, 0:4, cols], blocks(ps[:, 6 + n % 2, :]))\
                .then_inc(self.out.s, 1)

    def act_exps(self, act, n):
        k, m, ps = self.k, self.m, self.k.ps
        act.wait_ge(self.max_ready.s, self.n0 + n + 1)
        if n >= 2:
            act.wait_ge(self.turned.s, self.n0 + n - 1)
        for h in range(4):
            ins = act.activation(self.s[n % 2][:, h, :], ps[:, 2 * (n % 2) + h // 2, MEM * (h % 2):MEM * (h % 2) + MEM],
                                 ACT.Exp, scale=P ** -0.5, bias=self.nm[n % 2][:, h:h + 1],
                                 accum_out=self.den[n % 2][:, h:h + 1])
        ins.then_inc(self.exps.s, 1)

    def act(self, act):
        k, m, ps = self.k, self.m, self.k.ps
        for cache, tiles in (("cache_mem_k", m.kc), ("cache_mem_v", m.vc)):
            for b in range(8):
                act.dma_start(tiles[b][:, :, :], k.A[cache][self.layer, b].rearrange("(s p) h d -> p s (h d)", p=P))\
                   .then_inc(k.cache_here.s, 16)
        self.act_exps(act, 0)
        for n in range(NBLK):
            if n + 1 < NBLK:
                self.act_exps(act, n + 1)
            act.wait_ge(self.turned.s, self.n0 + n + 1)
            for a in range(2):
                ins = act.activation(self.pt[:, 2 * a:2 * a + 2, :, :],
                                     ps[:, 4 + a, :].rearrange("p (h s q) -> p h s q", h=2, s=2), ACT.Copy)
            ins.then_inc(self.pt_ready.s, 1)


class CrossSample(Stage):

    def __init__(self, k, m, layer):
        super().__init__(k)
        k.small.reset()
        self.kt = [k.small(f"xs_kt{layer}{i}", [P, 4, 2, P]) for i in range(2)]
        self.qz = k.small(f"xs_q{layer}", [P, 32 * 32])
        self.pz = k.small(f"xs_p{layer}", [P, 2, 8, 60])
        self.s = k.small(f"xs_s{layer}", [32, MEM])
        self.t = k.small(f"xs_t{layer}", [32, 4, P])
        self.o = k.small(f"xs_o{layer}", [32, P])
        self.mx, self.nm, self.den, self.r = (k.small(f"xs_{n}{layer}", [32, 1]) for n in ("mx", "nm", "den", "r"))
        (self.kturn, self.kt_ready, self.q_ready, self.scored, self.scores, self.max_ready, self.exps, self.probs,
         self.pturn, self.pt_ready, self.pv, self.o_ready, self.oturn) = k.xs_signals
        self.layer, self.m = layer, m

    def pe(self, pe):
        k, m, ps, l = self.k, self.m, self.k.ps, self.layer
        pe.wait_ge(k.cache_here.s, 256 * (l + 1))
        def turn(b):
            if b >= 2:
                pe.wait_ge(self.kt_ready.s, 8 * l + b - 1)
            for h in range(4):
                for s in range(2):
                    last = pe.transpose(ps[:, 2 * (b % 2) + h // 2, 256 * (h % 2) + s * P:256 * (h % 2) + s * P + P],
                                        m.kc[b][:, s, h * P:h * P + P], k.c("ident"))
            last.then_inc(self.kturn.s, 1)
        turn(0)
        pe.wait_ge(self.q_ready.s, l + 1)
        for b in range(8):
            if b < 7:
                turn(b + 1)
            pe.wait_ge(self.kt_ready.s, 8 * l + b + 1)
            for h in range(4):
                r = 4 * b + h
                last = pe.matmul(ps[0:32, 4, 0:MEM], self.qz[:, 32 * r:32 * r + 32], self.kt[b % 2][:, h, :, :],
                                 start=r == 0, stop=r == 31)
            last.then_inc(self.scored.s, 1)
        last = None
        pe.wait_ge(self.probs.s, l + 1)
        for s in range(2):
            last = pe.transpose(ps[:, 5, 32 * s:32 * s + 32], self.s[:, s * P:s * P + P], k.c("ident", 32)[:, 0:32])
        last.then_inc(self.pturn.s, 1)
        pe.wait_ge(self.pt_ready.s, l + 1)
        for b in range(8):
            for s in range(2):
                last = pe.matmul(ps[0:32, 6, :], self.pz[:, s, b, 28 - 4 * b:60 - 4 * b], m.vc[b][:, s, :],
                                 start=b + s == 0, stop=b == 7 and s == 1)
        last.then_inc(self.pv.s, 1)
        pe.wait_ge(self.o_ready.s, l + 1)
        pe.transpose(ps[:, 7, 0:32], self.o[:, :], k.c("ident", 32)[:, 0:32]).then_inc(self.oturn.s, 1)

    def act(self, act):
        k, m, ps, l = self.k, self.m, self.k.ps, self.layer
        for b in range(8):
            act.wait_ge(self.kturn.s, 8 * l + b + 1)
            if b >= 2:
                act.wait_ge(self.scored.s, 8 * l + b - 1)
            for a in range(2):
                ins = act.activation(self.kt[b % 2][:, 2 * a:2 * a + 2, :, :],
                                     ps[:, 2 * (b % 2) + a, :].rearrange("p (h s q) -> p h s q", h=2, s=2), ACT.Copy)
            ins.then_inc(self.kt_ready.s, 1)
        act.wait_ge(self.max_ready.s, l + 1)
        act.activation(self.s[:, :], ps[0:32, 4, 0:MEM], ACT.Exp, scale=P ** -0.5, bias=self.nm[:, :],
                       accum_out=self.den[:, :]).then_inc(self.exps.s, 1)

    def dve(self, dve):
        k, m, ps, l = self.k, self.m, self.k.ps, self.layer
        dve.memset(self.pz[:, :, :, :], 0.0)
        k.dve_link(dve.memset(self.qz[:, :], 0.0))
        dve.tensor_copy(self.qz[:, 0:1024:33].rearrange("p (b h) -> p b h", b=8),
                        m.q[:, :, SEQ:TOK].rearrange("p h b -> p b h")).then_inc(self.q_ready.s, 1)
        dve.wait_ge(self.scored.s, 8 * (l + 1))
        k.dve_link(dve.tensor_reduce(self.mx[:, :], ps[0:32, 4, 0:MEM], AX.X, ALU.max))
        dve.tensor_scalar(self.nm[:, :], self.mx[:, :], -(P ** -0.5), None, ALU.mult).then_inc(self.max_ready.s, 1)
        dve.wait_ge(self.exps.s, l + 1)
        k.dve_link(dve.reciprocal(self.r[:, :], self.den[:, :]))
        dve.tensor_scalar(self.s[:, :], self.s[:, :], self.r[:, :], None, ALU.mult).then_inc(self.probs.s, 1)
        dve.wait_ge(self.pturn.s, l + 1)
        for s in range(2):
            ins = dve.tensor_copy(self.pz[:, s, :, 28:32], ps[:, 5, 32 * s:32 * s + 32].rearrange("p (b h) -> p b h", b=8))
        ins.then_inc(self.pt_ready.s, 1)
        dve.wait_ge(self.pv.s, l + 1)
        k.dve_link(dve.tensor_tensor(self.t[:, :, :], blocks(ps[0:32, 6, :]),
                                     k.c("own_head", 32).unsqueeze(2).to_broadcast([32, 4, P]), ALU.mult))
        dve.tensor_reduce(self.o[:, :], self.t[:, :, :].rearrange("p h d -> p d h"), AX.X, ALU.add)\
           .then_inc(self.o_ready.s, 1)
        dve.wait_ge(self.oturn.s, l + 1)
        split_out(k, dve, k.y_hi[:, 0:4, SEQ:TOK], k.y_lo[:, 0:4, SEQ:TOK],
                  ps[:, 7, 0:32].rearrange("p (b h) -> p h b", b=8))


def cross_layer(k, l):
    m = Buffers()
    k.big.reset()
    m.k_t, m.v_t = (k.big(f"mem_{n}_t{l}", [P, 4, MEM]) for n in "kv")
    m.k_tok, m.v_tok = (k.big(f"mem_{n}_tok{l}", [P, 2, 512]) for n in "kv")
    m.q = k.big(f"xq{l}", [P, 4, TOK])
    k.cross_kept = k.big.at
    s = [MemTurn(k, m, l)]
    s.append(stream_norm(k, f"mem_norm{l}", V_MEM + DC * l, MEM, m.mem_t, (m.hm_hi, m.hm_lo)))
    s.append(stream_norm(k, f"xattn_norm{l}", V_XATT + DC * l))
    tiles = []
    for w, dst in (("mem_wk", m.k_t), ("mem_wv", m.v_t)):
        tiles += [gemm_tile(k.A[w][l], [(h * P, P)], (m.hm_hi, m.hm_lo), out_copy(k, dst[:, h, :]), halves=[(0, MEM)])
                  for h in range(4)]
    tiles += [gemm_tile(k.A["mem_wq"][l], [(h * P, P)], (k.xn_hi, k.xn_lo), out_copy(k, m.q[:, h, :])) for h in range(4)]
    s.append(Gemm(k, tiles))
    k.small.reset()
    kt = [m.k_t[:, h, :] for h in range(4)]
    s.append(HeadNorm(k, f"mk_norm{l}", [[c] for c in kt], k.c("ones"), P, gain_in_place(k, kt, [V_KN + l] * 4), MEM))
    k.small.reset()
    q = [m.q[:, h, :] for h in range(4)]
    s.append(HeadNorm(k, f"q_norm{l}", [[c] for c in q], k.c("ones"), P, gain_in_place(k, q, [V_QN + l] * 4)))
    s += [KvTurn(k, m, l), CrossPrompt(k, m, l), CrossSample(k, m, l)]
    w = k.A["mem_wo"][l]
    s.append(Gemm(k, [gemm_tile(w, [(c * P, P)], (k.y_hi, k.y_lo), out_residual(k, c), nk=4) for c in range(DC)]))
    return s


def ffn_layer(k, l):
    return [stream_norm(k, f"ffn_norm{l}", V_FFN + DC * l), Ffn(k, l)]


def odd_projection(k):
    w, xn = k.A["odd_w_in"][0], (k.xn_hi, k.xn_lo)
    tiles = [gemm_tile(w, [(c * P, P)], xn, out_copy(k, k.proj[:, c, :])) for c in range(20)]
    tiles.append(gemm_tile(w, [(20 * P, 16)], xn, out_copy(k, k.proj[0:16, O_DT, :])))
    for c in range(O_RQ, NPROJ):
        scale = P ** -0.5 if O_RK <= c < O_RV else None
        tiles.append(gemm_tile(w, [(20 * P + 16 + (c - O_RQ) * P, P)], xn, out_copy(k, k.proj[:, c, :], scale)))
    return Gemm(k, tiles)


class ConvTurn(Turn):

    def __init__(self, k):
        k.small.reset()
        self.p_new, self.s_new = k.small("conv_p", [3, 1536]), k.small("conv_s", [8, 1536])
        self.old = k.small("conv_old", [24, 1536])
        k.small.reset(k.small.size - 12 * 24 * 4 - 12 * 8 * 4 - 64)
        k.hist = k.small("conv_hist", [P, 12, 24])
        self.here = k.counter("conv_state_here")
        items = [([(self.old[:, c * P:c * P + P], 24 * c) for c in range(12)],
                  lambda b: b[:, 0:288].rearrange("p (c r) -> p c r", c=12), k.hist[:, :, :])]
        for g in range(3):
            for dst, c0, c1 in ((self.p_new, SEQ - 3, SEQ), (self.s_new, SEQ, TOK)):
                n = c1 - c0
                items.append(([(k.proj[:, O_X + 4 * g + i, c0:c1], i * P) for i in range(4)],
                              lambda b, n=n: b[0:n, 0:512], dst[:, 512 * g:512 * g + 512]))
        super().__init__(k, "conv_turn", items)

    def pe(self, pe):
        pe.wait_ge(self.here.s, 16)
        super().pe(pe)

    def act(self, act):
        k, p = self.k, self.k.proj
        act.dma_start(self.old[:, :], k.A["state_ssd_conv"][0].rearrange("b j c -> (b j) c")).then_inc(self.here.s, 16)
        act.activation(p[:, O_Z:O_Z + 8, :], p[:, O_Z:O_Z + 8, :], ACT.Silu)
        act.activation(p[:, O_RG:O_RG + 4, :], p[:, O_RG:O_RG + 4, :], ACT.Silu)
        super().act(act)
        act.wait_ge(self.free.s, self.base + len(self.items))
        k.store(k.O["p_conv"][0, 0], self.p_new[:, :])
        k.store(k.O["s_conv"][0][:, 2, :], self.s_new[:, :])
        k.store(k.O["s_conv"][0][:, 0:2, :], k.A["state_ssd_conv"][0][:, 1:3, :])
        k.stores_done()


class Conv(Stage):

    def __init__(self, k):
        super().__init__(k)
        k.small.reset()
        self.acc = [k.small(f"conv_acc{i}", [P, TOK]) for i in range(3)]
        self.prod = k.small("conv_prod", [P, 3, 12, 8])
        self.started, self.acc_ready, self.silu = (k.counter(f"conv_{n}") for n in ("last_tap", "taps", "silu"))

    def act(self, act):
        k, p = self.k, self.k.proj
        def start(c):
            if c >= 3:
                act.wait_ge(self.silu.s, c - 2)
            act.activation(self.acc[c % 3][:, :], p[:, O_X + c, :], ACT.Copy, scale=k.col(V_CW + 36 + c))\
               .then_inc(self.started.s, 1)
        start(0)
        start(1)
        for c in range(12):
            if c + 2 < 12:
                start(c + 2)
            act.wait_ge(self.acc_ready.s, c + 1)
            act.activation(p[:, O_X + c, :], self.acc[c % 3][:, :], ACT.Silu, bias=k.col(V_CB + c))\
               .then_inc(self.silu.s, 1)

    def dve(self, dve):
        k, p = self.k, self.k.proj
        for j in range(3):
            old = k.hist[:, :, j::3]
            w = k.vcol[:, V_CW + 12 * j:V_CW + 12 * j + 12].unsqueeze(2).to_broadcast([P, 12, 8])
            ins = dve.tensor_tensor(self.prod[:, j], old, w, ALU.mult)
        k.dve_link(ins)
        k.dve_link(dve.tensor_tensor(self.prod[:, 0], self.prod[:, 0], self.prod[:, 1], ALU.add))
        k.dve_link(dve.tensor_tensor(self.prod[:, 0], self.prod[:, 0], self.prod[:, 2], ALU.add))
        for c in range(12):
            acc, x = self.acc[c % 3], p[:, O_X + c, :]
            dve.wait_ge(self.started.s, c + 1)
            dve.tensor_tensor(acc[:, SEQ:TOK], acc[:, SEQ:TOK], self.prod[:, 0, c, :], ALU.add)
            for j in range(3):
                back = 3 - j
                ins = dve.scalar_tensor_tensor(acc[:, back:SEQ], x[:, 0:SEQ - back], k.col(V_CW + 12 * j + c),
                                               acc[:, back:SEQ], ALU.mult, ALU.add)
                if j < 2:
                    k.dve_link(ins)
            ins.then_inc(self.acc_ready.s, 1)


class OddGates(Stage):

    def __init__(self, k):
        super().__init__(k)
        k.small.reset()
        k.dt, k.cum, k.ncum, k.ecum = (k.small(f"ssd_{n}", [16, TOK]) for n in ("dt", "cum", "ncum", "ecum"))
        k.dg, self.a = k.small("ssd_dg", [16, NBLK, 16]), k.small("ssd_a", [16, 1])
        kept = k.small.at
        self.x, self.e, self.u, self.l, self.w = (k.small(f"dt_{n}", [16, TOK]) for n in "xeulw")
        k.small.reset(kept)
        self.cum_ready, self.e_ready, self.a_ready = (k.counter(f"ssd_{n}_ready") for n in ("cum", "ecum", "a"))

    def act(self, act):
        k = self.k
        act.activation(self.a[:, :], k.a_log[:, :], ACT.Exp).then_inc(self.a_ready.s, 1)
        log1p_exp(k, None, act, "act", "odd", self.x[:, :], self.e[:, :], self.u[:, :], self.l[:, :], self.w[:, :])
        act.wait_ge(self.cum_ready.s, 1)
        act.activation(k.ecum[:, :], k.cum[:, :], ACT.Exp).then_inc(self.e_ready.s, 1)

    def dve(self, dve):
        k, p = self.k, self.k.proj
        x, w = self.x[:, :], self.w[:, :]
        k.dve_link(dve.tensor_scalar(x, p[0:16, O_DT, :], k.dt_bias[:, :], None, ALU.add))
        log1p_exp(k, dve, None, "dve", "odd", x, self.e[:, :], self.u[:, :], self.l[:, :], w)
        k.dve_link(dve.scalar_tensor_tensor(k.dt[:, :], x, 0.0, self.l[:, :], ALU.max, ALU.add))
        k.dve_link(dve.memset(w, 0.0))
        dve.wait_ge(self.a_ready.s, 1)
        k.dve_link(dve.tensor_scalar(x, k.dt[:, :], self.a[:, :], -1.0, ALU.mult, ALU.mult))
        for n in range(NBLK):
            c = slice(n * P, n * P + P)
            dve.tensor_tensor_scan(k.cum[:, c], x[:, c], w[:, c], 0.0, ALU.add, ALU.add)
        dve.tensor_copy(k.cum[:, SEQ:TOK], x[:, SEQ:TOK]).then_inc(self.cum_ready.s, 1)
        dve.wait_ge(self.cum_ready.s, 1)
        dve.tensor_scalar(k.ncum[:, :], k.cum[:, :], -1.0, None, ALU.mult)
        dve.wait_ge(self.e_ready.s, 1)
        for n in range(NBLK):
            dve.tensor_scalar(k.dg[:, n, :], k.c("ident", 16)[:, 0:16], k.ecum[:, n * P + P - 1:n * P + P], None, ALU.mult)


def odd_spread(k):
    k.dt_col = k.small("dt_col", [P, NBLK, 16])
    k.dec = k.small("ssd_dec", [P, NBLK, 16])
    k.dt_pair, k.d_pair = k.small("dt_pair", [P, 8, 8]), k.small("d_pair", [P, 8])
    k.odd_kept = k.small.at
    k.mid.reset()
    k.ec = k.mid("ecum_pair", [P, 8, TOK])
    items = [([((16 * n, 16 * n + 16), k.dt[:, n * P:n * P + P], k.c("ident", 16)[:, 0:16], 0) for n in range(NBLK)],
              lambda dve, b: dve.tensor_copy(k.dt_col[:, :, :], b[:, 0:64].rearrange("p (n h) -> p n h", n=NBLK))),
             ([((0, 64), k.c("ones", 16), k.dg[:, :, :], 0)],
              lambda dve, b: dve.tensor_copy(k.dec[:, :, :], b[:, 0:64].rearrange("p (n h) -> p n h", n=NBLK)))]
    eight = lambda src: sum((k.pair(j, 16, (8 * j, 8 * j + 8), src) for j in range(8)), [])
    take = lambda dst: lambda dve, b: dve.tensor_copy(dst, b[:, 0:64].rearrange("p (j b) -> p j b", j=8))
    items.append((eight(k.dt[:, SEQ:TOK]), take(k.dt_pair[:, :, :])))
    items.append((eight(k.ecum[:, SEQ:TOK]), take(k.ec[:, :, SEQ:TOK])))
    items.append((sum((k.pair(j, 16, (j, j + 1), k.d_skip[:, :]) for j in range(8)), []),
                  lambda dve, b: dve.tensor_copy(k.d_pair[:, :], b[:, 0:8])))
    for j in range(8):
        items.append((k.pair(j, 16, (0, SEQ), k.ecum[:, 0:SEQ]),
                      lambda dve, b, j=j: dve.tensor_copy(k.ec[:, j, 0:SEQ], b[:, :])))
    return Spread(k, "odd_spread", items)


def ret_turn(k):
    p = k.proj
    k.small.reset(k.odd_kept)
    k.rk_tok, k.rv_tok = k.small("rk_tok", [P, NBLK, 512]), None
    k.rv_s = k.small("rv_s", [8, 512])
    k.ret_kept = k.small.at
    k.mid.reset(12 * TOK * 4)
    k.rv_tok = k.mid("rv_tok", [P, NBLK, 512])
    items = []
    for base, dst in ((O_RK, k.rk_tok), (O_RV, k.rv_tok)):
        for h in range(4):
            items.append(([(p[:, base + h, n * P:n * P + P], n * P) for n in range(NBLK)],
                          lambda b: blocks(b[:, 0:512]), dst[:, :, h * P:h * P + P]))
    items.append(([(p[:, O_RV + h, SEQ:TOK], h * P) for h in range(4)], lambda b: b[0:8, 0:512], k.rv_s[:, :]))
    return Turn(k, "ret_turn", items)


class RetPrompt(Stage):

    def __init__(self, k):
        super().__init__(k)
        k.small.reset(k.ret_kept)
        self.a, self.ks, self.qs = ([k.small(f"ret_{n}{i}", [P, 4, P]) for i in range(2)] for n in ("a", "ks", "qs"))
        self.r = k.mid("ret_state", [P, 4, P])
        self.scores, self.a_ready, self.o, self.state = (k.counter(f"ret_{n}") for n in ("scores", "a", "o", "state"))

    def pe_scores(self, pe, n):
        k, ps, p, c = self.k, self.k.ps, self.k.proj, slice(n * P, n * P + P)
        if n >= 2:
            pe.wait_ge(self.a_ready.s, n - 1)
        for h in range(4):
            last = pe.matmul(ps[:, n % 2, h * P:h * P + P], p[:, O_RK + h, c], p[:, O_RQ + h, c], start=True, stop=True)
        last.then_inc(self.scores.s, 1)

    def pe(self, pe):
        k, ps = self.k, self.k.ps
        self.pe_scores(pe, 0)
        for n in range(NBLK):
            if n + 1 < NBLK:
                self.pe_scores(pe, n + 1)
            pe.wait_ge(self.a_ready.s, n + 1)
            if n:
                pe.wait_ge(self.state.s, n)
            for h in range(4):
                out = ps[:, 2, h * P:h * P + P]
                pe.matmul(out, k.rv_tok[:, n, h * P:h * P + P], self.a[n % 2][:, h, :], start=True, stop=n == 0)
                if n:
                    pe.matmul(out, self.r[:, h, :], self.qs[n % 2][:, h, :], start=False, stop=True)
            for h in range(4):
                last = pe.matmul(ps[:, 3, h * P:h * P + P], self.ks[n % 2][:, h, :], k.rv_tok[:, n, h * P:h * P + P],
                                 start=True, stop=True)
            last.then_inc(self.o.s, 1)

    def dve(self, dve):
        k, ps, p = self.k, self.k.ps, self.k.proj
        def prepare(n):
            c = slice(n * P, n * P + P)
            dve.tensor_tensor(self.ks[n % 2][:, :, :], blocks(k.rk_tok[:, n, :]),
                              k.lc(ODD, "kscale").unsqueeze(2).to_broadcast([P, 4, P]), ALU.mult)
            dve.tensor_tensor(self.qs[n % 2][:, :, :], p[:, O_RQ:O_RQ + 4, c], blocks(k.lc(ODD, "qscale")), ALU.mult)
            dve.wait_ge(self.scores.s, n + 1)
            dve.tensor_tensor(self.a[n % 2][:, :, :], blocks(ps[:, n % 2, :]), blocks(k.lc(ODD, "decay")), ALU.mult)\
               .then_inc(self.a_ready.s, 1)
        prepare(0)
        for n in range(NBLK):
            if n + 1 < NBLK:
                prepare(n + 1)
            c = slice(n * P, n * P + P)
            dve.wait_ge(self.o.s, n + 1)
            dve.tensor_copy(p[:, O_RQ:O_RQ + 4, c], blocks(ps[:, 2, :]))
            if n == 0:
                ins = dve.tensor_copy(self.r[:, :, :], blocks(ps[:, 3, :]))
            else:
                for h in range(4):
                    ins = dve.scalar_tensor_tensor(self.r[:, h, :], self.r[:, h, :], RET_CHUNK_DECAY[h],
                                                   ps[:, 3, h * P:h * P + P], ALU.mult, ALU.add)
            ins.then_inc(self.state.s, 1)
            dve.wait_ge(self.state.s, n + 1)

    def act(self, act):
        k = self.k
        act.wait_ge(self.state.s, NBLK)
        k.store(k.O["p_ret"][0, 0].rearrange("h d e -> d h e"), self.r[:, :, :])
        k.stores_done()


class RetSample(Stage):

    def __init__(self, k):
        super().__init__(k)
        k.small.reset(k.ret_kept)
        self.t = [k.small(f"rets_t{i}", [P, 4, P]) for i in range(2)]
        k.mid.reset(12 * TOK * 4)
        self.r = k.mid("rets_r", [P, 8, 4, P])
        self.here, self.vb, self.r_new, self.o = (k.counter(f"rets_{n}") for n in ("here", "v_spread", "r_new", "o"))

    def act(self, act):
        k = self.k
        act.dma_start(self.r[:, :, :, :], k.A["state_ret"][0].rearrange("b h d e -> d b h e")).then_inc(self.here.s, 16)
        act.wait_ge(self.r_new.s, 8)
        k.store(k.O["s_ret"][0].rearrange("b h d e -> d b h e"), self.r[:, :, :, :])
        k.stores_done()

    def pe(self, pe):
        k, ps, p = self.k, self.k.ps, self.k.proj
        for b in range(8):
            if b >= 4:
                pe.wait_ge(self.r_new.s, b - 3)
            pe.matmul(ps[:, 4 + b % 4, :], k.onehot(b, 8), k.rv_s[:, :], start=True, stop=True).then_inc(self.vb.s, 1)
        for b in range(8):
            pe.wait_ge(self.r_new.s, b + 1)
            for h in range(4):
                last = pe.matmul(ps[:, 0, 8 * h + b:8 * h + b + 1], self.r[:, b, h, :], p[:, O_RQ + h, SEQ + b:SEQ + b + 1],
                                 start=True, stop=True)
        last.then_inc(self.o.s, 1)

    def dve(self, dve):
        k, ps, p = self.k, self.k.ps, self.k.proj
        dve.wait_ge(self.here.s, 16)
        for b in range(8):
            dve.wait_ge(self.vb.s, b + 1)
            t = self.t[b % 2]
            k.dve_link(dve.tensor_tensor(t[:, :, :], blocks(ps[:, 4 + b % 4, :]),
                                         p[:, O_RK:O_RK + 4, SEQ + b:SEQ + b + 1].to_broadcast([P, 4, P]), ALU.mult))
            for h in range(4):
                ins = dve.scalar_tensor_tensor(self.r[:, b, h, :], self.r[:, b, h, :], RET_DECAY[h], t[:, h, :],
                                               ALU.mult, ALU.add)
            ins.then_inc(self.r_new.s, 1)
        dve.wait_ge(self.o.s, 1)
        dve.tensor_copy(p[:, O_RQ:O_RQ + 4, SEQ:TOK], ps[:, 0, 0:32].rearrange("p (h b) -> p h b", h=4))


class Center(Stage):

    def __init__(self, k, name, chunks):
        super().__init__(k)
        self.chunks = chunks
        self.mean, self.free = k.counter(f"{name}_mean"), k.counter(f"{name}_free")

    def pe(self, pe):
        for i, x in enumerate(self.chunks):
            for b, (c0, c1) in enumerate(HALVES):
                last = pe.matmul(self.k.ps[:, 2 * i + b, 0:HALF], self.k.c("ones"), x[:, c0:c1], start=True, stop=True)
            last.then_inc(self.mean.s, 1)

    def dve(self, dve):
        for i, x in enumerate(self.chunks):
            dve.wait_ge(self.mean.s, i + 1)
            dve.scalar_tensor_tensor(two(x), self.k.ps[:, 2 * i:2 * i + 2, 0:HALF], -1.0 / P, two(x), ALU.mult, ALU.add)


def ret_norm(k):
    k.small.reset(k.odd_kept)
    def apply(dve, u, rstd):
        x = k.proj[:, O_RQ + u, :]
        k.dve_link(dve.scalar_tensor_tensor(x, x, k.col(V_RETN + u), rstd, ALU.mult, ALU.mult))
        k.dve_link(dve.tensor_tensor(x, x, k.proj[:, O_RG + u, :], ALU.mult))
        return split_out(k, dve, k.y_hi[:, 8 + u, :], k.y_lo[:, 8 + u, :], x)
    return HeadNorm(k, "ret_norm", [[k.proj[:, O_RQ + u, :]] for u in range(4)], k.c("ones"), P, apply)


class SsdPrompt(Stage):

    def __init__(self, k):
        super().__init__(k)
        k.small.reset(k.odd_kept)
        k.mid.reset(12 * TOK * 4)
        self.l = k.small("ssd_l", [P, 16, P])
        self.t = k.small("ssd_t", [P, 8, P])
        self.bt = k.small("ssd_bt", [P, 2 * P])
        self.xdt = k.mid("ssd_xdt", [P, 16, 64])
        self.xw = k.mid("ssd_xw", [P, 16, 64])
        k.ssd_state = k.mid("ssd_state", [P, 16, 64])
        (self.xturn, self.xdt_ready, self.bt_ready, self.seg, self.masked, self.l_ready, self.w_ready, self.y,
         self.state) = (k.counter(f"ssd_{n}") for n in ("x_turned", "xdt", "bt", "seg", "masked", "l", "w", "y", "state"))
        k.big.reset(O_RQ * TOK * 4)
        k.ssd_s = [k.big(f"ssd_s{b}", [P, 8, P]) for b in range(8)]

    def pe(self, pe):
        k, ps, p = self.k, self.k.ps, self.k.proj
        for n in range(NBLK):
            c = slice(n * P, n * P + P)
            if n:
                pe.wait_ge(self.state.s, n)
            for j in range(8):
                pe.transpose(ps[:, 5 + j // 4, (j % 4) * P:(j % 4) * P + P], p[:, O_X + j, c], k.c("ident"))
            for g in range(2):
                last = pe.transpose(ps[:, 7, g * P:g * P + P], p[:, O_B + g, c], k.c("ident"))
            last.then_inc(self.xturn.s, 1)
            for g in range(2):
                pe.matmul(ps[:, 4, g * P:g * P + P], p[:, O_B + g, c], p[:, O_C + g, c], start=True, stop=True)
            for h in range(16):
                out = ps[:, h // 4, (h % 4) * P:(h % 4) * P + P]
                pe.matmul(out, k.onehot(h, 16), k.cum[:, c], start=True, stop=False)
                last = pe.matmul(out, k.ncum[:, c], k.onehot(h, 16), start=False, stop=True)
            last.then_inc(self.seg.s, 1)
            pe.wait_ge(self.w_ready.s, n + 1)
            pe.wait_ge(self.bt_ready.s, n + 1)
            for h in range(16):
                j = h // 2
                pe.matmul(ps[64 * (h % 2):64 * (h % 2) + 64, j // 4, (j % 4) * P:(j % 4) * P + P], self.xdt[:, h, :],
                          self.l[:, h, :], start=True, stop=True)
            if n:
                for j in range(8):
                    pe.matmul(ps[:, 2 + j // 4, (j % 4) * P:(j % 4) * P + P], k.ssd_state[:, 2 * j:2 * j + 2, :],
                              p[:, O_C + j // 4, c], start=True, stop=True)
            for g in range(2):
                last = pe.matmul(ps[:, 5 + g, :], self.bt[:, g * P:g * P + P], self.xw[:, 8 * g:8 * g + 8, :],
                                 start=True, stop=True)
            last.then_inc(self.y.s, 1)

    def act(self, act):
        k, ps = self.k, self.k.ps
        for b in range(8):
            act.dma_start(k.ssd_s[b][:, :, :], k.A["state_ssd"][0, b].rearrange("(j t) p n -> (t p) j n", t=2))\
               .then_inc(k.ssd_here.s, 16)
        for n in range(NBLK):
            act.wait_ge(self.xturn.s, n + 1)
            if n:
                act.wait_ge(self.y.s, n)
            act.activation(self.bt[:, :], ps[:, 7, 0:2 * P], ACT.Copy).then_inc(self.bt_ready.s, 1)
            for q in range(4):
                act.wait_ge(self.masked.s, 4 * n + q + 1)
                act.activation(self.l[:, 4 * q:4 * q + 4, :], self.l[:, 4 * q:4 * q + 4, :], ACT.Exp)\
                   .then_inc(self.l_ready.s, 1)

    def dve(self, dve):
        k, ps, p = self.k, self.k.ps, self.k.proj
        for n in range(NBLK):
            c = slice(n * P, n * P + P)
            dve.wait_ge(self.xturn.s, n + 1)
            for g in range(2):
                dve.tensor_tensor(self.xdt[:, 8 * g:8 * g + 8, :], ps[:, 5 + g, :].rearrange("p (h d) -> p h d", h=8),
                                  k.dt_col[:, n, 8 * g:8 * g + 8].unsqueeze(2).to_broadcast([P, 8, 64]), ALU.mult)
            dve.wait_ge(self.seg.s, n + 1)
            for q in range(4):
                dve.tensor_tensor(self.l[:, 4 * q:4 * q + 4, :], blocks(ps[:, q, :]),
                                  k.c("causal").unsqueeze(1).to_broadcast([P, 4, P]), ALU.add).then_inc(self.masked.s, 1)
            dve.wait_ge(self.l_ready.s, 4 * n + 4)
            k.dve_link(dve.tensor_tensor(self.xw[:, :, :], self.xdt[:, :, :],
                                         self.l[:, :, P - 1:P].to_broadcast([P, 16, 64]), ALU.mult))
            for g in range(2):
                ins = dve.tensor_tensor(self.l[:, 8 * g:8 * g + 8, :], self.l[:, 8 * g:8 * g + 8, :],
                                        ps[:, 4, g * P:g * P + P].unsqueeze(1).to_broadcast([P, 8, P]), ALU.mult)
            ins.then_inc(self.w_ready.s, 1)
            dve.wait_ge(self.y.s, n + 1)
            for a in range(2):
                t = self.t[:, 4 * a:4 * a + 4, :]
                if n:
                    k.dve_link(dve.tensor_tensor(t, blocks(ps[:, 2 + a, :]), k.ec[:, 4 * a:4 * a + 4, c], ALU.mult))
                    k.dve_link(dve.tensor_tensor(t, t, blocks(ps[:, a, :]), ALU.add))
                else:
                    k.dve_link(dve.tensor_copy(t, blocks(ps[:, a, :])))
            for j in range(8):
                x = p[:, O_X + j, c]
                dve.scalar_tensor_tensor(x, x, k.d_pair[:, j:j + 1], self.t[:, j, :], ALU.mult, ALU.add)
            if n:
                k.dve_link(dve.tensor_tensor(k.ssd_state[:, :, :], k.ssd_state[:, :, :],
                                             k.dec[:, n, :].unsqueeze(2).to_broadcast([P, 16, 64]), ALU.mult))
            for g in range(2):
                s, q = k.ssd_state[:, 8 * g:8 * g + 8, :], ps[:, 5 + g, :].rearrange("p (h d) -> p h d", h=8)
                ins = dve.tensor_tensor(s, s, q, ALU.add) if n else dve.tensor_copy(s, q)
            ins.then_inc(self.state.s, 1)
            dve.wait_ge(self.state.s, n + 1)


class SsdTurn(Turn):

    def __init__(self, k):
        k.small.reset(k.odd_kept)
        self.out = k.small("ssd_out", [P, 8, P])
        k.bc_s = k.small("ssd_bc_s", [8, 512])
        k.ssd_kept = k.small.at
        items = [([(k.ssd_state[:, 2 * j:2 * j + 2, :].rearrange("p a b -> p (a b)"), (j - 4 * a) * P)
                   for j in range(4 * a, 4 * a + 4)], lambda b: blocks(b[:, 0:512]), self.out[:, 4 * a:4 * a + 4, :])
                 for a in range(2)]
        items.append(([(k.proj[:, O_B + i, SEQ:TOK], i * P) for i in range(4)], lambda b: b[0:8, 0:512], k.bc_s[:, :]))
        super().__init__(k, "ssd_turn", items)

    def act(self, act):
        k = self.k
        super().act(act)
        act.wait_ge(self.free.s, self.base + len(self.items))
        k.store(k.O["p_ssd"][0, 0].rearrange("(j t) p n -> (t p) j n", t=2), self.out[:, :, :])


class SsdSample(Stage):

    def __init__(self, k):
        super().__init__(k)
        k.small.reset(k.ssd_kept)
        self.xdt, self.y = k.small("ssds_xdt", [P, 8, 8]), k.small("ssds_y", [P, 8, 8])
        self.t = [k.small(f"ssds_t{i}", [P, 8, P]) for i in range(2)]
        self.u = [k.small(f"ssds_u{i}", [P, 8, P]) for i in range(2)]
        self.bc, self.scaled, self.s_new, self.free = (k.counter(f"ssds_{n}") for n in ("bc", "scaled", "s_new", "bc_free"))

    def act(self, act):
        k = self.k
        act.wait_ge(k.ssd_here.s, 128)
        for b in range(8):
            for j in range(8):
                ins = act.activation(k.ssd_s[b][:, j, :], k.ssd_s[b][:, j, :], ACT.Copy,
                                     scale=k.ec[:, j, SEQ + b:SEQ + b + 1])
            ins.then_inc(self.scaled.s, 1)
        for b in range(8):
            act.wait_ge(self.s_new.s, b + 1)
            k.store(k.O["s_ssd"][0, b].rearrange("(j t) p n -> (t p) j n", t=2), k.ssd_s[b][:, :, :])

    def pe(self, pe):
        k, ps = self.k, self.k.ps
        for b in range(8):
            if b >= 4:
                pe.wait_ge(self.free.s, b - 3)
            pe.matmul(ps[:, b % 4, :], k.onehot(b, 8), k.bc_s[:, :], start=True, stop=True).then_inc(self.bc.s, 1)

    def dve(self, dve):
        k, ps, p = self.k, self.k.ps, self.k.proj
        s = slice(SEQ, TOK)
        x = p[:, O_X:O_X + 8, s]
        k.dve_link(dve.tensor_tensor(self.xdt[:, :, :], x, k.dt_pair[:, :, :], ALU.mult))
        four = lambda t: t.rearrange("p (g j) n -> p g j n", g=2)
        for b in range(8):
            row = lambda i: ps[:, b % 4, 256 * i:256 * i + 256].rearrange("p (g n) -> p g n", g=2).unsqueeze(2)\
                .to_broadcast([P, 2, 4, P])
            t, u, st = self.t[b % 2][:, :, :], self.u[b % 2][:, :, :], k.ssd_s[b][:, :, :]
            dve.wait_ge(self.bc.s, b + 1)
            k.dve_link(dve.tensor_tensor(four(t), row(0),
                                         four(self.xdt[:, :, b:b + 1].to_broadcast([P, 8, P])), ALU.mult))
            dve.wait_ge(self.scaled.s, b + 1)
            dve.tensor_tensor(st, st, t, ALU.add).then_inc(self.s_new.s, 1)
            dve.wait_ge(self.s_new.s, b + 1)
            dve.tensor_tensor(four(u), four(st), row(1), ALU.mult).then_inc(self.free.s, 1)
            dve.wait_ge(self.free.s, b + 1)
            ins = dve.tensor_reduce(self.y[:, :, b:b + 1], u, AX.X, ALU.add)
        k.dve_link(ins)
        k.dve_link(dve.tensor_tensor(self.xdt[:, :, :], x, k.d_pair[:, :].unsqueeze(2).to_broadcast([P, 8, 8]), ALU.mult))
        dve.tensor_tensor(x, self.xdt[:, :, :], self.y[:, :, :], ALU.add)


class SsdGate(Stage):

    def dve(self, dve):
        p = self.k.proj
        dve.tensor_tensor(p[:, O_X:O_X + 8, :], p[:, O_X:O_X + 8, :], p[:, O_Z:O_Z + 8, :], ALU.mult)


def ssd_norm(k):
    k.small.reset()
    def apply(dve, u, rstd):
        for j in range(4 * u, 4 * u + 4):
            x = k.proj[:, O_X + j, :]
            k.dve_link(dve.scalar_tensor_tensor(x, x, k.col(V_SSDN + j), rstd, ALU.mult, ALU.mult))
            last = split_out(k, dve, k.y_hi[:, j, :], k.y_lo[:, j, :], x)
        return last
    return HeadNorm(k, "ssd_norm", [[k.proj[:, O_X + 4 * u + j, :] for j in range(4)] for u in range(2)], k.c("ones"),
                    512, apply)


class OddConstants(Stage):
    def act(self, act):
        k = self.k
        act.dma_start(k.lconst[:, 0:NODD], k.C[:, NCOMMON + NEVEN:NCOMMON + NEVEN + NODD]).then_inc(k.odd_here.s, 16)
        act.wait_ge(k.odd_here.s, 16)


def odd_layer(k):
    s = [OddConstants(k), stream_norm(k, "mix1", V_MIX + DC), odd_projection(k), ConvTurn(k), Conv(k), OddGates(k),
         odd_spread(k)]
    k.small.reset(k.odd_kept)
    kept = k.odd_kept
    rope = Rope(k, "odd_rope", [k.proj[:, c, :] for c in range(O_RQ, O_RV)], ODD, kept)
    s += [rope, ret_turn(k), RetPrompt(k), RetSample(k), Center(k, "ret", [k.proj[:, O_RQ + h, :] for h in range(4)]),
          ret_norm(k), SsdPrompt(k), SsdTurn(k), SsdSample(k), SsdGate(k), ssd_norm(k)]
    w = k.A["odd_w_out"][0]
    s.append(Gemm(k, [gemm_tile(w, [(m * P, P)], (k.y_hi, k.y_lo), out_residual(k, m), nk=6, k0=6 * i)
                      for i in range(2) for m in range(DC)]))
    return s


def plan(k):
    stages = [Load(k)]
    for layer, mixer in enumerate((even_layer, odd_layer)):
        stages += mixer(k) + cross_layer(k, layer) + ffn_layer(k, layer)
    return stages + [Emit(k)]


class Emit(Stage):

    def __init__(self, k):
        super().__init__(k)
        k.big.reset()
        self.y = k.big("y_tok", [P, NBLK, D_MODEL])
        self.ys = k.big("ys_tok", [NSAMPLE, D_MODEL])
        items = []
        for n in range(NBLK):
            for g in range(2):
                items.append(([(k.x[:, 4 * g + c, n * P:n * P + P], c * P) for c in range(4)],
                              lambda b: b[:, 0:512], self.y[:, n, 512 * g:512 * g + 512]))
        for g in range(2):
            items.append(([(k.x[:, 4 * g + c, SEQ:TOK], c * P) for c in range(4)],
                          lambda b: b[0:8, 0:512], self.ys[:, 512 * g:512 * g + 512]))
        self.turn = Turn(k, "emit", items)

    def pe(self, pe): self.turn.pe(pe)
    def dve(self, dve): self.turn.dve(dve)

    def act(self, act):
        k = self.k
        self.turn.act(act)
        act.wait_ge(self.turn.free.s, self.turn.base + len(self.turn.items))
        k.store(k.O["y_prompt"].rearrange("b (n p) d -> p (b n) d", p=P), self.y[:, :, :])
        k.store(k.O["y_sample"].rearrange("b t d -> (b t) d"), self.ys[:, :])


def program(nc, A, C, O):
    with ExitStack() as ctx:
        k = Core(nc, ctx, A, C, O)
        k.gate_i, k.gate_f = k.params("gate_i", [4, 1]), k.params("gate_f", [4, 1])
        k.dt_bias, k.a_log, k.d_skip = (k.params(n, [16, 1]) for n in ("dt_bias", "a_log", "d_skip"))
        k.sink_row, k.sink_col = k.params("sink_row", [P, 8]), k.params("sink_col", [64, 1])
        k.norm_signals = [k.counter(n) for n in ("squares_ready", "squares_summed", "rstd_ready", "rstd_used")]
        k.norm_count = (0, 0)
        k.turn_signals, k.turn_count = (k.counter("turned"), k.counter("turn_copied")), 0
        k.spread_signals, k.spread_count = (k.counter("spread"), k.counter("spread_free")), 0
        k.log_signals = (k.counter("log_input"), k.counter("log_ready"))
        k.ssd_here, k.odd_here = k.counter("ssd_states_here"), k.counter("odd_constants_here")
        k.mem_here, k.cache_here = k.counter("memory_here"), k.counter("memory_cache_here")
        k.xa_signals = [k.counter(f"xa_{n}") for n in ("scores", "max", "exps", "probs", "turned", "pt", "pv", "out")]
        k.xs_signals = [k.counter(f"xs_{n}") for n in ("k_turned", "kt", "q", "scored", "scores", "max", "exps", "probs",
                                                      "p_turned", "pt", "pv", "o", "o_turned")]
        k.ffn_signals = [k.counter(n) for n in ("relu_ready", "squared", "hidden_ready")]
        stages = plan(k)
        count = [0] * RING
        k.arrivals = []
        for n, t in enumerate(k.tiles):
            count[n % RING] += len(t["parts"])
            k.arrivals.append(count[n % RING])
        block = ctx.enter_context(nc.Block())

        @block.sync
        def _(sp):
            stream_weights(k, sp)

        @block.gpsimd
        def _(pool):
            split_low(k, pool)

        @block.tensor
        def _(pe):
            for s in stages:
                s.pe(pe)
                k.fence(pe, "pe")

        @block.vector
        def _(dve):
            for s in stages:
                s.dve(dve)
                k.fence(dve, "dve")

        @block.scalar
        def _(act):
            for s in stages:
                s.act(act)
                k.fence(act, "act")
            k.stores_done()


OUTPUTS = [
    ("y_prompt", (1, SEQ, D_MODEL)), ("y_sample", (8, 1, D_MODEL)),
    ("mem_k", (2, 1, MEM, 4, P)), ("mem_v", (2, 1, MEM, 4, P)),
    ("p_swa_k", (1, 1, P, 2, 64)), ("p_swa_v", (1, 1, P, 2, 64)),
    ("p_C", (1, 1, 4, 64, P)), ("p_n", (1, 1, 4, 64)), ("p_m", (1, 1, 4)),
    ("p_conv", (1, 1, 3, 1536)), ("p_ssd", (1, 1, 16, 64, P)), ("p_ret", (1, 1, 4, P, P)),
    ("s_swa_k", (1, 8, P, 2, 64)), ("s_swa_v", (1, 8, P, 2, 64)),
    ("s_C", (1, 8, 4, 64, P)), ("s_n", (1, 8, 4, 64)), ("s_m", (1, 8, 4)),
    ("s_conv", (1, 8, 3, 1536)), ("s_ssd", (1, 8, 16, 64, P)), ("s_ret", (1, 8, 4, P, P)),
]


def kernel(**inputs):
    import concourse.bacc as bacc
    from concourse.bass_utils import run_bass_kernel_spmd

    nc = bacc.Bacc("TRN2", target_bir_lowering=False, num_devices=1)
    arrays, A, O = {}, {}, {}
    for name, a in inputs.items():
        a = np.ascontiguousarray(a)
        arrays[f"in_{name}"] = a
        A[name] = nc.dram_tensor(f"in_{name}", a.shape, mybir.dt.from_np(a.dtype), kind="ExternalInput").ap()
    arrays["shape_constants"] = shape_constants()
    C = nc.dram_tensor("shape_constants", arrays["shape_constants"].shape, F32, kind="ExternalInput").ap()
    for name, shape in OUTPUTS:
        O[name] = nc.dram_tensor(f"out_{name}", shape, F32, kind="ExternalOutput").ap()
    program(nc, A, C, O)
    r = run_bass_kernel_spmd(nc, [arrays], core_ids=[0])
    return tuple(r.results[0][f"out_{name}"] for name, _ in OUTPUTS)
```

```python
import math
from contextlib import ExitStack

import numpy as np

import concourse.bass as bass
from concourse import mybir

F32 = mybir.dt.float32
F32R = mybir.dt.float32r
ALU = mybir.AluOpType
ACT = mybir.ActivationFunctionType
AX = mybir.AxisListType

P = 128
D_MODEL, SEQ, NSAMPLE, PAST = 1024, 512, 8, 1024
TOK = SEQ + NSAMPLE
HALF = TOK // 2
DC = D_MODEL // P
NBLK = SEQ // P
MEM = 256
FFN = 4 * D_MODEL
EPS = 1e-6
NEG = -1e30
RING = 2

E_SQ, E_SK, E_SV, E_MQ, E_MK, E_MV, E_MO, E_GI, E_GF = 0, 4, 5, 6, 8, 10, 14, 18, 19
O_Z, O_X, O_B, O_C, O_DT, O_RQ, O_RK, O_RV, O_RG = 0, 8, 16, 18, 20, 21, 25, 29, 33
NPROJ = 37

V_MIX, V_XATT, V_MEM, V_FFN, V_MLN, V_SSDN, V_RETN, V_CB = 0, 16, 32, 48, 64, 68, 76, 80
V_CW, V_QN, V_KN, V_SQ, V_SK = 92, 140, 142, 144, 145


def layout(parts):
    at, out = 0, {}
    for name, n in parts:
        out[name] = (at, n)
        at += n
    return out, at


COMMON, NCOMMON = layout([("ident", P), ("ones", P), ("blk64", P), ("causal", P), ("own_head", 4), ("eps", 1)])
EVEN, NEVEN = layout([("rot", P), ("mask_first", 2 * P), ("mask_later", 2 * P), ("cos", TOK), ("sin", TOK)])
ODD, NODD = layout([("rot", P), ("cos", TOK), ("sin", TOK), ("decay", 4 * P), ("qscale", 4 * P), ("kscale", 4)])
NLAYER = max(NEVEN, NODD)


def shape_constants():
    p = np.arange(P)
    pos = np.concatenate([np.arange(SEQ), PAST + np.zeros(NSAMPLE)]).astype(np.float32)

    def rope(rot_dim, head, theta):
        half = rot_dim // 2
        inv = np.power(np.float32(theta), -np.arange(half, dtype=np.float32) * np.float32(2.0 / rot_dim))
        ang = (pos[None, :] * inv[:, None]).astype(np.float32)
        cos, sin, rot = np.ones((P, TOK)), np.zeros((P, TOK)), np.zeros((P, P))
        for at in range(0, P, head):
            for part in range(2):
                rows = at + part * half + np.arange(half)
                cos[rows], sin[rows] = np.cos(ang), np.sin(ang)
            for i in range(half):
                rot[at + i + half, at + i] = -1.0
                rot[at + i, at + i + half] = 1.0
        return cos, sin, rot

    c = {"ident": np.eye(P), "ones": np.ones((P, P)), "blk64": np.kron(np.eye(2), np.ones((64, 64))),
         "causal": np.where(p[:, None] <= p[None, :], 0.0, NEG),
         "own_head": np.tile(np.eye(4), (P // 4, 1)), "eps": np.full((P, 1), EPS)}
    e, o = {}, {}
    e["cos"], e["sin"], e["rot"] = rope(16, 64, 500000.0)
    k = np.arange(2 * P)
    e["mask_first"] = np.where(p[:, None] >= k[None, :], 0.0, NEG)
    diff = P + p[:, None] - k[None, :]
    e["mask_later"] = np.where((diff >= 0) & (diff <= P), 0.0, NEG)
    o["cos"], o["sin"], o["rot"] = rope(128, 128, 10000.0)
    lg = np.log(1.0 - np.exp2(-5.0 - np.arange(4)))
    d = p[None, :] - p[:, None]
    o["decay"] = np.concatenate([np.where(d >= 0, np.exp(np.maximum(d, 0) * g), 0.0) for g in lg], axis=1)
    o["qscale"] = np.concatenate([np.tile(np.exp((p + 1.0) * g), (P, 1)) for g in lg], axis=1)
    o["kscale"] = np.exp((P - 1.0 - p)[:, None] * lg[None, :])
    out = np.zeros((P, NCOMMON + NEVEN + NODD), np.float32)
    for table, at, vals in ((COMMON, 0, c), (EVEN, NCOMMON, e), (ODD, NCOMMON + NEVEN, o)):
        for name, (a, n) in table.items():
            out[:, at + a:at + a + n] = vals[name]
    return out


RET_DECAY = [float(1.0 - 2.0 ** (-5.0 - h)) for h in range(4)]
RET_CHUNK_DECAY = [float(np.exp(P * np.log(1.0 - 2.0 ** (-5.0 - h)))) for h in range(4)]


class Signal:

    def __init__(self, s):
        self.s, self.seen = s, {}

    def next(self, reader, n=1):
        self.seen[reader] = self.seen.get(reader, 0) + n
        return self.seen[reader]


class Region:

    def __init__(self, nc, base, size):
        self.nc, self.base, self.size, self.at = nc, base, size, 0

    def reset(self, at=0):
        self.at = at

    def __call__(self, name, shape, dt=F32):
        n = 4 * int(np.prod(shape[1:]))
        n = -(-n // 32) * 32
        assert self.at + n <= self.size, (name, self.at, n, self.size)
        t = self.nc.alloc_sbuf_tensor_at(name, shape, dt, offset=self.base + self.at)
        self.at += n
        return t


class Core:

    def __init__(self, nc, ctx, A, C, O):
        self.nc, self.ctx, self.A, self.C, self.O = nc, ctx, A, C, O
        self.n_semaphores = 0
        size = 212800
        arena = ctx.enter_context(nc.sbuf_tensor("arena", [P, size // 4], F32))
        base = size_of_base(nc, arena, size)
        whole = Region(nc, base, size)
        self.x = whole("x", [P, DC, TOK])
        self.w_raw = [whole(f"w_raw{i}", [P, DC, P]) for i in range(RING)]
        self.w_hi = [whole(f"w_hi{i}", [P, DC, P], F32R) for i in range(RING)]
        self.w_lo = [whole(f"w_lo{i}", [P, DC, P], F32R) for i in range(RING)]
        self.const = whole("const", [P, NCOMMON])
        self.lconst = whole("lconst", [P, NLAYER])
        self.vcol = whole("vcol", [P, V_SK + 1])
        self.params = Region(nc, base + whole.at, 256 + 64)
        whole.at += 320
        self.rstd = whole("rstd", [P, TOK])
        self.mem_rstd = whole("mem_rstd", [P, MEM])
        at = whole.at
        self.big = Region(nc, base + at, NPROJ * TOK * 4)
        whole.at += NPROJ * TOK * 4
        at = whole.at
        self.mid = Region(nc, base + at, 24 * TOK * 4)
        whole.at += 24 * TOK * 4
        self.small = Region(nc, base + whole.at, size - whole.at)
        self.proj = self.big("proj", [P, NPROJ, TOK])
        self.big.reset()
        self.hid_hi = [self.big(f"hid_hi{i}", [P, DC, TOK], F32R) for i in range(2)]
        self.hid_lo = [self.big(f"hid_lo{i}", [P, DC, TOK], F32R) for i in range(2)]
        self.big.reset(self.big.size - 2 * DC * TOK * 4)
        self.xn = tuple(self.mid(f"xn_{n}", [P, DC, TOK], F32R) for n in ("hi", "lo"))
        self.xc = tuple(self.big(f"xc_{n}", [P, DC, TOK], F32R) for n in ("hi", "lo"))
        self.xa_hi, self.xa_lo = (self.mid(f"xa_{n}", [P, 4, TOK], F32R) for n in ("hi", "lo"))
        self.mid.reset()
        self.y_hi = self.mid("y_hi", [P, 12, TOK], F32R)
        self.y_lo = self.mid("y_lo", [P, 12, TOK], F32R)
        self.ps = ctx.enter_context(nc.psum_tensor("banks", [P, 8, 512], F32))
        self.w_here = [self.counter(f"weight_arrived{i}") for i in range(RING)]
        self.w_hi_ready = self.counter("weight_high_ready")
        self.w_lo_ready = self.counter("weight_low_ready")
        self.tile_done = self.counter("gemm_tile_done")
        self.tile_out = self.counter("gemm_bank_free")
        self.square_ready, self.square_summed = self.counter("square_ready"), self.counter("square_summed")
        self.rstd_done, self.n_squares = self.counter("rstd_done"), 0
        self.end = {e: self.counter(f"stage_end_{e}") for e in ("pe", "dve", "act")}
        self.dve_step, self.act_step = self.counter("dve_step"), self.counter("act_step")
        self.stored = self.counter("stored")
        self.n_stored = 0
        self.n_tiles = 0
        self.tiles = []

    def counter(self, name):
        self.n_semaphores += 1
        return Signal(self.ctx.enter_context(self.nc.semaphore(name)))

    def c(self, name, rows=P):
        a, n = COMMON[name]
        return self.const[0:rows, a:a + n]

    def lc(self, table, name):
        a, n = table[name]
        return self.lconst[:, a:a + n]

    def col(self, v):
        return self.vcol[:, v:v + 1]

    def pair(self, j, rows, cols, rhs):
        return [(cols, self.const[0:rows, 2 * j + t:2 * j + t + 1].to_broadcast([rows, 64]), rhs, 64 * t)
                for t in range(2)]

    def onehot(self, h, rows):
        return self.const[0:rows, h:h + 1].to_broadcast([rows, P])

    def dve_link(self, ins):
        ins.then_inc(self.dve_step.s, 1)
        self.nc.vector.wait_ge(self.dve_step.s, self.dve_step.next("dve"))

    def act_link(self, ins):
        ins.then_inc(self.act_step.s, 1)
        self.nc.scalar.wait_ge(self.act_step.s, self.act_step.next("act"))

    def fence(self, eng, me):
        eng.drain().then_inc(self.end[me].s, 1)
        for other in ("pe", "dve", "act"):
            eng.wait_ge(self.end[other].s, self.end[other].next(me))

    def store(self, out, in_, few=False):
        self.nc.scalar.dma_start(out, in_, allow_slow_non_contiguous=few).then_inc(self.stored.s, 16)
        self.n_stored += 1

    def stores_done(self):
        self.nc.scalar.wait_ge(self.stored.s, 16 * self.n_stored)


def size_of_base(nc, arena, size):
    lo = nc.sbuf_usable_end - nc.sbuf_base
    base = -(-(nc.sbuf_base - size) // 32) * 32
    assert base >= 0 and lo >= 0
    return base


class Stage:
    def __init__(self, k):
        self.k = k

    def pe(self, pe): pass
    def dve(self, dve): pass
    def act(self, act): pass


class NextNorm:

    def __init__(self, k, gain, dst, sq):
        self.k, self.gain, self.dst, self.sq = k, gain, dst, sq
        self.first = k.n_squares
        k.n_squares += DC

    def dve(self, dve, c):
        k, x, g = self.k, self.k.x[:, c, :], self.k.col(self.gain + c)
        hi, lo = self.dst[0][:, c, :], self.dst[1][:, c, :]
        k.dve_link(dve.tensor_scalar(hi, x, g, None, ALU.mult))
        dve.scalar_tensor_tensor(lo, x, g, hi.bitcast(F32), ALU.mult, ALU.subtract)

    def act(self, act, c):
        k = self.k
        if c >= 2:
            act.wait_ge(k.square_summed.s, self.first + c - 1)
        act.activation(self.sq[c % 2][:, :], k.x[:, c, :], ACT.Square).then_inc(k.square_ready.s, 1)

    def pe(self, pe, c):
        k = self.k
        pe.wait_ge(k.square_ready.s, self.first + c + 1)
        for b, (c0, c1) in enumerate(HALVES):
            last = pe.matmul(k.ps[:, 6 + b, 0:HALF], k.c("ones"), self.sq[c % 2][:, c0:c1],
                             start=c == 0, stop=c == DC - 1)
        last.then_inc(k.square_summed.s, 1)

    def act_rstd(self, act):
        k = self.k
        act.wait_ge(k.square_summed.s, self.first + DC)
        k.act_link(act.activation(two(k.rstd[:, :]), k.ps[:, 6:8, 0:HALF], ACT.Ln, scale=1.0 / D_MODEL,
                                  bias=k.c("eps")))
        act.activation(k.rstd[:, :], k.rstd[:, :], ACT.Exp, scale=-0.5)


def next_norm(k, name, gain, dst):
    return NextNorm(k, gain, dst, [k.small(f"{name}_sq{i}", [P, TOK]) for i in range(2)])


class Gemm(Stage):

    def __init__(self, k, tiles, norm=None):
        super().__init__(k)
        self.norm = norm
        self.base = len(k.tiles)
        self.mine = tiles
        k.tiles += tiles

    def pe(self, pe):
        k, ps = self.k, self.k.ps
        for i, t in enumerate(self.mine):
            n = self.base + i
            pe.wait_ge(k.w_hi_ready.s, n + 1)
            pe.wait_ge(k.w_lo_ready.s, n + 1)
            if n >= 3:
                pe.wait_ge(k.tile_out.s, n - 2)
            if "rhs_ready" in t:
                sig, count = t["rhs_ready"]
                pe.wait_ge(sig.s, count)
            hi, lo = k.w_hi[n % RING], k.w_lo[n % RING]
            rh, rl = t["rhs"]
            m, nk = t["m"], t["nk"]
            last = None
            for kk in range(nk):
                for b, (c0, c1) in enumerate(t["halves"]):
                    out = ps[0:m, 2 * (n % 3) + b, 0:c1 - c0]
                    r, q = rh[:, t["k0"] + kk, c0:c1], rl[:, t["k0"] + kk, c0:c1]
                    pe.matmul(out, hi[:, kk, 0:m], r, start=kk == 0, stop=False)
                    pe.matmul(out, hi[:, kk, 0:m], q, start=False, stop=False)
                    last = pe.matmul(out, lo[:, kk, 0:m], r, start=False, stop=kk == nk - 1)
            last.then_inc(k.tile_done.s, 1)
            if i and "finish" in self.mine[i - 1]:
                self.norm.pe(pe, self.mine[i - 1]["finish"])
        if "finish" in t:
            self.norm.pe(pe, t["finish"])

    def dve(self, dve):
        k, ps = self.k, self.k.ps
        for i, t in enumerate(self.mine):
            n = self.base + i
            dve.wait_ge(k.tile_done.s, n + 1)
            w = t["halves"][0][1] - t["halves"][0][0]
            nb = len(t["halves"])
            src = ps[0:t["m"], 2 * (n % 3):2 * (n % 3) + nb, 0:w]
            t["out"](dve, src, nb)
            dve.wait_ge(k.tile_out.s, n + 1)
            for step in t.get("dve_after", ()):
                step(dve, n)
            if "finish" in t:
                self.norm.dve(dve, t["finish"])

    def act(self, act):
        k = self.k
        for i, t in enumerate(self.mine):
            n = self.base + i
            if "finish" in t:
                act.wait_ge(k.tile_out.s, n + 1)
                self.norm.act(act, t["finish"])
            if n + RING < len(k.tiles):
                act.wait_ge(k.tile_done.s, n + 1)
                split_high(k, act, n + RING)
            for step in t.get("act_after", ()):
                step(act, n)
        if "finish" in t:
            self.norm.act_rstd(act)


def split_high(k, act, n):
    t = k.tiles[n]
    act.wait_ge(k.w_here[n % RING].s, 16 * k.arrivals[n])
    act.activation(k.w_hi[n % RING][:, 0:t["nk"], 0:t["m"]], k.w_raw[n % RING][:, 0:t["nk"], 0:t["m"]],
                   ACT.Copy).then_inc(k.w_hi_ready.s, 1)


def split_low(k, pool):
    for n, t in enumerate(k.tiles):
        pool.wait_ge(k.w_hi_ready.s, n + 1)
        if n >= RING:
            pool.wait_ge(k.tile_done.s, n - RING + 1)
        view = slice(0, t["nk"]), slice(0, t["m"])
        pool.tensor_tensor(k.w_lo[n % RING][:, view[0], view[1]], k.w_raw[n % RING][:, view[0], view[1]],
                           k.w_hi[n % RING][:, view[0], view[1]].bitcast(F32),
                           ALU.subtract).then_inc(k.w_lo_ready.s, 1)


def stream_weights(k, sp):
    for n, t in enumerate(k.tiles):
        if n >= RING:
            sp.wait_ge(k.w_lo_ready.s, n - RING + 1)
        for (p0, p1), (k0, k1), (c0, c1), src in t["parts"]:
            sp.dma_start(k.w_raw[n % RING][p0:p1, k0:k1, c0:c1], src).then_inc(k.w_here[n % RING].s, 16)


def weight_parts(w, k0, nk, pieces):
    v = w.rearrange("(k p) n -> p k n", p=P)
    out, at = [], 0
    for c, n in pieces:
        out.append(((0, P), (0, nk), (at, at + n), v[:, k0:k0 + nk, c:c + n]))
        at += n
    return out, at


HALVES = [(0, HALF), (HALF, TOK)]


def two(ap):
    return ap.rearrange("p (a b) -> p a b", a=2)


def gemm_tile(w, pieces, rhs, out, k0=0, nk=DC, halves=HALVES, row0=None, **more):
    parts, m = weight_parts(w, k0 if row0 is None else row0, nk, pieces)
    return dict(parts=parts, m=m, nk=nk, k0=k0, rhs=rhs, halves=halves, out=out, **more)


def out_copy(k, dst, scale=None):
    def emit(dve, src, nb):
        d = two(dst) if nb == 2 else dst.unsqueeze(1)
        m = dst.shape[0]
        r = two(k.rstd[0:m, :]) if nb == 2 else k.mem_rstd[0:m, :].unsqueeze(1)
        if scale is None:
            dve.tensor_tensor(d, src, r, ALU.mult).then_inc(k.tile_out.s, 1)
        else:
            dve.scalar_tensor_tensor(d, src, scale, r, ALU.mult, ALU.mult).then_inc(k.tile_out.s, 1)
    return emit


def out_residual(k, m):
    def emit(dve, src, nb):
        d = two(k.x[:, m, :])
        dve.tensor_tensor(d, src, d, ALU.add).then_inc(k.tile_out.s, 1)
    return emit


def follow(tiles, i, dve=None, act=None):
    for key, step in (("dve_after", dve), ("act_after", act)):
        if step:
            tiles[i].setdefault(key, []).append(step)


class HeadNorm(Stage):

    def __init__(self, k, name, units, mask, features, apply, width=TOK, region=None, extra=None):
        super().__init__(k)
        self.units, self.mask, self.features, self.apply, self.width = units, mask, features, apply, width
        region = region or k.small
        self.sq = [region(f"{name}_sq{i}", [P, width]) for i in range(2)]
        self.rstd = [region(f"{name}_rstd{i}", [P, width]) for i in range(2)]
        s = k.norm_signals
        self.sq_ready, self.summed, self.rstd_ready, self.rstd_used = s
        self.halves = HALVES if width == TOK else [(0, width)]
        self.first, self.first_unit = k.norm_count
        k.norm_count = (self.first + sum(len(c) for c in units), self.first_unit + len(units))

    def banks(self, u, rows=P):
        w = self.halves[0][1]
        return self.k.ps[:, 2 * (u % 2):2 * (u % 2) + len(self.halves), 0:w]

    def pe(self, pe):
        n = 0
        for u, chunks in enumerate(self.units):
            if u >= 2:
                pe.wait_ge(self.rstd_used.s, self.first_unit + u - 1)
            for i, _ in enumerate(chunks):
                pe.wait_ge(self.sq_ready.s, self.first + n + 1)
                for b, (c0, c1) in enumerate(self.halves):
                    last = pe.matmul(self.k.ps[:, 2 * (u % 2) + b, 0:c1 - c0], self.mask,
                                     self.sq[n % 2][:, c0:c1],
                                     start=i == 0, stop=i == len(chunks) - 1)
                last.then_inc(self.summed.s, 1)
                n += 1

    def squares(self, act, u):
        for src in self.units[u]:
            n = self.sent
            if n >= 2:
                act.wait_ge(self.summed.s, self.first + n - 1)
            act.activation(self.sq[n % 2][:, 0:self.width], src, ACT.Square).then_inc(self.sq_ready.s, 1)
            self.sent += 1

    def act(self, act):
        k = self.k
        self.sent = 0
        nb, w = len(self.halves), self.halves[0][1]
        self.squares(act, 0)
        for u, chunks in enumerate(self.units):
            if u + 1 < len(self.units):
                self.squares(act, u + 1)
            act.wait_ge(self.summed.s, self.first + sum(len(c) for c in self.units[:u + 1]))
            if u >= 2:
                act.wait_ge(self.rstd_used.s, self.first_unit + u - 1)
            rstd = self.rstd[u % 2][:, 0:self.width]
            ln = rstd.rearrange("p (a b) -> p a b", a=nb)
            k.act_link(act.activation(ln, self.banks(u), ACT.Ln, scale=1.0 / self.features, bias=k.c("eps")))
            act.activation(rstd, rstd, ACT.Exp, scale=-0.5).then_inc(self.rstd_ready.s, 1)

    def dve(self, dve):
        for u in range(len(self.units)):
            dve.wait_ge(self.rstd_ready.s, self.first_unit + u + 1)
            last = self.apply(dve, u, self.rstd[u % 2][:, 0:self.width])
            last.then_inc(self.rstd_used.s, 1)


class Load(Stage):

    def __init__(self, k):
        super().__init__(k)
        r = k.big
        r.reset()
        self.xtok = r("xtok", [P, NBLK, D_MODEL])
        self.xs = r("xs", [NSAMPLE, D_MODEL])
        self.rows = [r("param_rows0", [P, P]), r("param_rows1", [P, P])]
        k.small.reset()
        self.norm = next_norm(k, "load", V_MIX, k.xn)
        self.here, self.done, self.out = k.counter("inputs_here"), k.counter("in_transposed"), k.counter("in_free")
        A = k.A
        self.loads = [(k.const[:, :], k.C[:, 0:NCOMMON]), (k.lconst[:, 0:NEVEN], k.C[:, NCOMMON:NCOMMON + NEVEN]),
                      (self.xtok[:, :, :], A["x_prompt"].rearrange("b (n p) d -> p (b n) d", p=P)),
                      (self.xs[:, :], A["x_sample"].rearrange("b t d -> (b t) d"))]
        at = 0
        for name, n in (("norm_mix", 16), ("norm_xattn", 16), ("norm_mem", 16), ("norm_ffn", 16),
                        ("mlstm_out_norm", 4), ("ssd_norm", 8), ("ret_norm", 4), ("ssd_conv_b", 12)):
            self.loads.append((self.rows[0][at:at + n, :], A[name].rearrange("l (c p) -> (l c) p", p=P)))
            at += n
        self.n0 = at
        self.loads.append((self.rows[1][0:48, :], A["ssd_conv_w"].rearrange("l j (c p) -> (l j c) p", p=P)))
        self.loads.append((self.rows[1][48:50, :], A["mem_q_norm"]))
        self.loads.append((self.rows[1][50:52, :], A["mem_k_norm"]))
        for i, name in ((52, "swa_q_norm"), (53, "swa_k_norm")):
            for half in range(2):
                self.loads.append((self.rows[1][i:i + 1, 64 * half:64 * half + 64], A[name]))
        colv = lambda ap, n: ap.rearrange("l (h a) -> (l h) a", a=1)[0:n]
        gb = A["mlstm_gate_bias"]
        self.loads += [(k.gate_i[:, :], gb[:, 0:4].rearrange("l (h a) -> (l h) a", a=1)),
                       (k.gate_f[:, :], gb[:, 4:8].rearrange("l (h a) -> (l h) a", a=1)),
                       (k.dt_bias[:, :], A["ssd_dt_bias"].rearrange("l (h a) -> (l h) a", a=1)),
                       (k.a_log[:, :], A["ssd_a_log"].rearrange("l (h a) -> (l h) a", a=1)),
                       (k.d_skip[:, :], A["ssd_d"].rearrange("l (h a) -> (l h) a", a=1)),
                       (k.sink_row[:, :], A["swa_sinks"].to_broadcast([P, 8]))]
        for b in range(NSAMPLE):
            self.loads.append((k.sink_col[8 * b:8 * b + 8, :], A["swa_sinks"].rearrange("l (h a) -> (l h) a", a=1)))

    def pe(self, pe):
        k, ps = self.k, self.k.ps
        pe.wait_ge(self.here.s, 16 * len(self.loads))
        ident = k.c("ident")
        pe.transpose(ps[:, 4, 0:self.n0], self.rows[0][0:self.n0, :], k.c("ident", self.n0)[:, 0:self.n0])
        pe.transpose(ps[:, 4, 128:182], self.rows[1][0:54, :], k.c("ident", 54)[:, 0:54]).then_inc(self.done.s, 1)
        for c in range(DC):
            if c >= 2:
                pe.wait_ge(self.out.s, c - 1)
            b = 2 * (c % 2)
            for n in range(NBLK):
                pe.transpose(ps[:, b, n * P:n * P + P], self.xtok[:, n, c * P:c * P + P], ident)
            pe.transpose(ps[:, b + 1, 0:8], self.xs[:, c * P:c * P + P], k.c("ident", 8)[:, 0:8])\
              .then_inc(self.done.s, 1)
            if c:
                self.norm.pe(pe, c - 1)
        self.norm.pe(pe, DC - 1)

    def dve(self, dve):
        k, ps = self.k, self.k.ps
        dve.wait_ge(self.done.s, 1)
        dve.tensor_copy(k.vcol[:, 0:self.n0], ps[:, 4, 0:self.n0])
        k.dve_link(dve.tensor_copy(k.vcol[:, self.n0:self.n0 + 54], ps[:, 4, 128:182]))
        for c in range(DC):
            dve.wait_ge(self.done.s, c + 2)
            b = 2 * (c % 2)
            dve.tensor_copy(k.x[:, c, 0:SEQ], ps[:, b, :])
            dve.tensor_copy(k.x[:, c, SEQ:TOK], ps[:, b + 1, 0:8]).then_inc(self.out.s, 1)
            dve.wait_ge(self.out.s, c + 1)
            self.norm.dve(dve, c)

    def act(self, act):
        for out, src in self.loads:
            act.dma_start(out, src).then_inc(self.here.s, 16)
        self.k.nc.scalar.preload_act_table_set("natural_log_exp_and_others")
        for n in range(RING):
            split_high(self.k, act, n)
        for c in range(DC):
            act.wait_ge(self.out.s, c + 1)
            self.norm.act(act, c)
        self.norm.act_rstd(act)


def gain_in_place(k, chunks, gains):
    def apply(dve, u, rstd):
        return dve.scalar_tensor_tensor(chunks[u], chunks[u], k.col(gains[u]), rstd, ALU.mult, ALU.mult)
    return apply


class Rope(Stage):

    def __init__(self, k, name, chunks, table, kept=0):
        super().__init__(k)
        self.chunks, self.table = chunks, table
        k.small.reset(kept)
        self.t = [k.small(f"{name}_sin{i}", [P, TOK]) for i in range(2)]
        self.rot, self.free = k.counter(f"{name}_rotated"), k.counter(f"{name}_free")

    def pe(self, pe):
        for i, x in enumerate(self.chunks):
            if i >= 2:
                pe.wait_ge(self.free.s, i - 1)
            for b, (c0, c1) in enumerate(HALVES):
                last = pe.matmul(self.k.ps[:, 2 * (i % 2) + b, 0:HALF], self.k.lc(self.table, "rot"), x[:, c0:c1],
                                 start=True, stop=True)
            last.then_inc(self.rot.s, 1)

    def dve(self, dve):
        k = self.k
        for i, x in enumerate(self.chunks):
            dve.wait_ge(self.rot.s, i + 1)
            t = self.t[i % 2][:, :]
            dve.tensor_tensor(two(t), k.ps[:, 2 * (i % 2):2 * (i % 2) + 2, 0:HALF], two(k.lc(self.table, "sin")),
                              ALU.mult).then_inc(self.free.s, 1)
            k.dve_link(dve.tensor_tensor(x, x, k.lc(self.table, "cos"), ALU.mult))
            dve.tensor_tensor(x, x, t, ALU.add)


class Turn(Stage):

    def __init__(self, k, name, items):
        super().__init__(k)
        self.items = items
        self.done, self.free = k.turn_signals
        self.base = k.turn_count
        k.turn_count += len(items)

    def pe(self, pe):
        k = self.k
        for i, (pieces, _, _) in enumerate(self.items):
            if i >= 4:
                pe.wait_ge(self.free.s, self.base + i - 3)
            for src, c0 in pieces:
                rows, n = src.shape
                last = pe.transpose(k.ps[0:n, 4 + i % 4, c0:c0 + rows], src, self.ident(src, rows))
            last.then_inc(self.done.s, 1)

    def ident(self, src, rows):
        at = src.base_partition() if callable(src.base_partition) else src.base_partition
        return self.k.const[at:at + rows, at:at + rows]

    def copy(self, eng, me):
        k = self.k
        for i, (_, view, dst) in enumerate(self.items):
            if (i % 2 == 0) == (me == "dve"):
                eng.wait_ge(self.done.s, self.base + i + 1)
                src = view(k.ps[:, 4 + i % 4, :])
                if i:
                    eng.wait_ge(self.free.s, self.base + i)
                if me == "dve":
                    eng.tensor_copy(dst, src).then_inc(self.free.s, 1)
                else:
                    eng.activation(dst, src, ACT.Copy).then_inc(self.free.s, 1)

    def dve(self, dve):
        self.copy(dve, "dve")

    def act(self, act):
        self.copy(act, "act")


def split_out(k, dve, dst_hi, dst_lo, src):
    k.dve_link(dve.tensor_copy(dst_hi, src))
    return dve.tensor_tensor(dst_lo, src, dst_hi.bitcast(F32), ALU.subtract)


class Ffn(Gemm):

    def __init__(self, k, layer):
        w1, w2 = k.A["ffn_w1"][layer], k.A["ffn_w2"][layer]
        k.small.reset()
        self.relu = [k.small(f"relu{layer}_{i}", [P, TOK]) for i in range(2)]
        self.sqr = [k.small(f"sqr{layer}_{i}", [P, TOK]) for i in range(2)]
        self.relu_ready, self.sq_ready, self.hid_ready = k.ffn_signals
        self.hid0 = layer * FFN // P
        tiles = []
        for what, q in (("up", 0), ("up", 1), ("down", 0), ("up", 2), ("down", 1), ("up", 3), ("down", 2), ("down", 3)):
            for m in range(DC):
                if what == "up":
                    h = q * DC + m
                    tiles.append(gemm_tile(w1, [(h * P, P)], k.xn, None, hidden=h))
                else:
                    tiles.append(gemm_tile(w2, [(m * P, P)], (k.hid_hi[q % 2], k.hid_lo[q % 2]),
                                           out_residual(k, m), row0=q * DC,
                                           **({"finish": m} if q == 3 and layer == 0 else {}),
                                           rhs_ready=(self.hid_ready, self.hid0 + (q + 1) * DC)))
        super().__init__(k, tiles, next_norm(k, f"ffn{layer}", V_MIX + DC, k.xn) if layer == 0 else None)

    def low(self, dve, h):
        k = self.k
        dve.wait_ge(self.sq_ready.s, self.hid0 + h + 1)
        hi, lo = k.hid_hi[h // DC % 2][:, h % DC, :], k.hid_lo[h // DC % 2][:, h % DC, :]
        dve.tensor_tensor(lo, self.sqr[h % 2][:, :], hi.bitcast(F32), ALU.subtract).then_inc(self.hid_ready.s, 1)

    def dve(self, dve):
        k, ps = self.k, self.k.ps
        pending = None
        for i, t in enumerate(self.mine):
            n = self.base + i
            dve.wait_ge(k.tile_done.s, n + 1)
            src = ps[:, 2 * (n % 3):2 * (n % 3) + 2, 0:HALF]
            if "hidden" in t:
                h = t["hidden"]
                dve.scalar_tensor_tensor(two(self.relu[h % 2][:, :]), src, 0.0, two(k.rstd[:, :]), ALU.max,
                                         ALU.mult).then_inc(k.tile_out.s, 1)
            else:
                t["out"](dve, src, 2)
            dve.wait_ge(k.tile_out.s, n + 1)
            if "finish" in t:
                self.norm.dve(dve, t["finish"])
            if pending is not None:
                self.low(dve, pending)
            pending = t.get("hidden")

    def act(self, act):
        k = self.k
        for i, t in enumerate(self.mine):
            n = self.base + i
            if "hidden" in t:
                h = t["hidden"]
                act.wait_ge(k.tile_out.s, n + 1)
                hi = k.hid_hi[h // DC % 2][:, h % DC, :]
                act.activation(self.sqr[h % 2][:, :], self.relu[h % 2][:, :], ACT.Square)
                act.activation(hi, self.relu[h % 2][:, :], ACT.Square).then_inc(self.sq_ready.s, 1)
            if "finish" in t:
                act.wait_ge(k.tile_out.s, n + 1)
                self.norm.act(act, t["finish"])
            if n + RING < len(k.tiles):
                act.wait_ge(k.tile_done.s, n + 1)
                split_high(k, act, n + RING)
        if self.norm:
            self.norm.act_rstd(act)


class Spread(Stage):

    def __init__(self, k, name, items):
        super().__init__(k)
        self.items = items
        self.full, self.free = k.spread_signals
        self.base = k.spread_count
        k.spread_count += len(items)

    def pe(self, pe):
        for i, (products, _) in enumerate(self.items):
            if i >= 8:
                pe.wait_ge(self.free.s, self.base + i - 7)
            for (c0, c1), lhsT, rhs, row in products:
                last = pe.matmul(self.k.ps[row:row + lhsT.shape[1], i % 8, c0:c1], lhsT, rhs, start=True, stop=True)
            last.then_inc(self.full.s, 1)

    def dve(self, dve):
        for i, (_, take) in enumerate(self.items):
            dve.wait_ge(self.full.s, self.base + i + 1)
            take(dve, self.k.ps[:, i % 8, :]).then_inc(self.free.s, 1)


def blocks(ap):
    return ap.rearrange("p (n t) -> p n t", t=P)


def even_small(k):
    k.small.reset()
    (k.g_m, k.g_a, k.g_c, k.g_em, k.g_cs) = (k.small(f"gate_{n}", [4, TOK]) for n in ("m", "a", "c", "em", "cs"))
    k.g_m0, k.g_ws = k.small("gate_m0", [4, 8]), k.small("gate_ws", [4, 8])
    k.kout = k.small("k_last_block", [P, P])
    k.kv_s = k.small("kv_sample", [NSAMPLE, 2, P])
    k.mv_s = k.small("mv_sample", [NSAMPLE, 512])
    k.even_kept = k.small.at


def even_projection(k):
    w, xn = k.A["even_w_in"][0], k.xn
    tiles = []
    for c, at in ((E_GI, 18 * P), (E_GF, 18 * P + 4)):
        tiles.append(gemm_tile(w, [(at, 4)], xn, out_copy(k, k.proj[0:4, c, :])))
    for g in range(4):
        tiles.append(gemm_tile(w, [(64 * g, 64), (256 + 64 * g, 64)], xn, out_copy(k, k.proj[:, g, :])))
    for c in range(4, 18):
        scale = 64 ** -0.5 if E_MK <= c < E_MV else None
        tiles.append(gemm_tile(w, [(c * P, P)], xn, out_copy(k, k.proj[:, c, :], scale)))
    gates = EvenGates(k)
    follow(tiles, 0, None, gates.act_load)
    follow(tiles, 1, gates.dve_input, gates.act_exp)
    follow(tiles, 2, gates.dve_one_plus, gates.act_log)
    follow(tiles, 3, gates.dve_running)
    follow(tiles, 4, gates.dve_exponents, gates.act_exponents)
    for c in range(E_MO, E_MO + 4):
        def sigmoid(act, n, c=c):
            act.wait_ge(k.tile_out.s, n + 1)
            act.activation(k.proj[:, c, :], k.proj[:, c, :], ACT.Sigmoid)
        follow(tiles, c + 2, None, sigmoid)
    follow(tiles, len(tiles) - 1, None,
           lambda act, n: k.nc.scalar.preload_act_table_set("natural_log_exp_and_others"))
    return Gemm(k, tiles)


class EvenTurn(Turn):

    def __init__(self, k):
        p = k.proj
        k.big.reset(20 * TOK * 4)
        k.sv_tok = k.big("sv_tok", [P, NBLK, P])
        k.mk_tok = k.big("mk_tok", [P, NBLK, 2 * P])
        k.mv_tok = k.big("mv_tok", [P, NBLK, 4, P + 1])
        four = lambda b: blocks(b[:, 0:512])
        turn4 = lambda c: [(p[:, c, n * P:n * P + P], n * P) for n in range(NBLK)]
        items = [(turn4(E_SV), four, k.sv_tok[:, :, :])]
        items += [(turn4(E_MK + j), four, k.mk_tok[:, :, j * P:j * P + P]) for j in range(2)]
        items += [(turn4(E_MV + h), four, k.mv_tok[:, :, h, 0:P]) for h in range(4)]
        items.append(([(p[:, E_SK, 3 * P:SEQ], 0)], lambda b: b[:, 0:P], k.kout[:, :]))
        items.append(([(p[:, E_SK + i, SEQ:TOK], i * P) for i in range(2)],
                      lambda b: b[0:8, 0:2 * P].rearrange("p (i f) -> p i f", i=2), k.kv_s[:, :, :]))
        items.append(([(p[:, E_MV + h, SEQ:TOK], h * P) for h in range(4)], lambda b: b[0:8, 0:512], k.mv_s[:, :]))
        super().__init__(k, "even_turn", items)

    def dve(self, dve):
        dve.memset(self.k.mv_tok[:, :, :, P:P + 1], 1.0)
        super().dve(dve)

    def act(self, act):
        k = self.k
        super().act(act)
        act.wait_ge(self.free.s, self.base + len(self.items))
        k.store(k.O["p_swa_k"].rearrange("l b p h d -> (l b p) (h d)"), k.kout[:, :])
        k.store(k.O["p_swa_v"].rearrange("l b p h d -> (l b p) (h d)"), k.sv_tok[:, 3, :])
        for i, name in enumerate(("k", "v")):
            new = k.O[f"s_swa_{name}"][0].rearrange("b s h d -> b s (h d)")
            old = k.A[f"cache_swa_{name}"][0].rearrange("b s h d -> b s (h d)")
            k.store(new[:, 0:P - 1, :], old[:, 1:P, :])
            k.store(new[:, P - 1, :], k.kv_s[:, i, :])


class SwaPrompt(Stage):

    def __init__(self, k):
        super().__init__(k)
        k.small.reset(k.even_kept)
        kept = k.big.at
        self.s = [k.big(f"swa_s{i}", [P, 8, 2 * P]) for i in range(2)]
        k.big.reset(kept)
        self.pt = k.small("swa_pt", [P, 4, 4, P])
        self.mx, self.m, self.nm, self.d, self.den, self.es, self.r = (
            [k.small(f"swa_{n}{i}", [P, 8]) for i in range(2)] for n in ("mx", "m", "nm", "d", "den", "es", "r"))
        (self.scores, self.masked, self.max_ready, self.exps, self.probs, self.turned, self.pt_ready, self.pv,
         self.pv_free) = (k.counter(f"swa_{n}") for n in ("scores", "masked", "max", "exps", "probs", "turned", "pt",
                                                         "pv", "pv_free"))

    def pe_scores(self, pe, n):
        k, ps, p = self.k, self.k.ps, self.k.proj
        kb = max(n - 1, 0)
        if n:
            pe.wait_ge(self.masked.s, n)
        for g in range(4):
            for v in range(2):
                rows, at = slice(64 * v, 64 * v + 64), 256 * (g % 2)
                last = pe.matmul(ps[:, 2 * v + g // 2, at:at + 256], p[rows, g, n * P:n * P + P],
                                 p[rows, E_SK, kb * P:kb * P + 2 * P], start=True, stop=True)
        last.then_inc(self.scores.s, 1)

    def pe(self, pe):
        k, ps, p = self.k, self.k.ps, self.k.proj
        self.pe_scores(pe, 0)
        self.pe_scores(pe, 1)
        for n in range(NBLK):
            kb = max(n - 1, 0)
            pe.wait_ge(self.probs.s, n + 1)
            if n:
                pe.wait_ge(self.pv_free.s, n)
            for g in range(4):
                for v in range(2):
                    for s in range(2):
                        at = (2 * v + s) * P
                        last = pe.transpose(ps[:, 4 + g, at:at + P], self.s[n % 2][:, 4 * v + g, s * P:s * P + P],
                                            k.c("ident"))
            last.then_inc(self.turned.s, 1)
            if n + 2 < NBLK:
                self.pe_scores(pe, n + 2)
            pe.wait_ge(self.pt_ready.s, n + 1)
            for g in range(4):
                for v in range(2):
                    for s in range(2):
                        last = pe.matmul(ps[64 * v:64 * v + 64, 4, g * P:g * P + P],
                                         k.sv_tok[:, kb + s, 64 * v:64 * v + 64], self.pt[:, g, 2 * v + s, :],
                                         start=s == 0, stop=s == 1)
            last.then_inc(self.pv.s, 1)

    def dve_max(self, dve, n):
        k, ps, i, sink = self.k, self.k.ps, n % 2, self.k.sink_row[:, :]
        mask = k.lc(EVEN, "mask_later" if n else "mask_first").unsqueeze(1).to_broadcast([P, 2, 2 * P])
        dve.wait_ge(self.scores.s, n + 1)
        if n >= 2:
            dve.wait_ge(self.turned.s, n - 1)
        for g in range(4):
            ins = dve.tensor_tensor(self.s[i][:, 2 * g:2 * g + 2, :],
                                    ps[:, g, :].rearrange("p (v s) -> p v s", v=2), mask, ALU.add)
        ins.then_inc(self.masked.s, 1)
        dve.wait_ge(self.masked.s, n + 1)
        k.dve_link(dve.tensor_reduce(self.mx[i][:, :], self.s[i][:, :, :], AX.X, ALU.max))
        k.dve_link(dve.scalar_tensor_tensor(self.m[i][:, :], self.mx[i][:, :], 0.125, sink, ALU.mult, ALU.max))
        dve.tensor_tensor(self.d[i][:, :], sink, self.m[i][:, :], ALU.subtract)
        dve.tensor_scalar(self.nm[i][:, :], self.m[i][:, :], -1.0, None, ALU.mult).then_inc(self.max_ready.s, 1)

    def dve_probs(self, dve, n):
        k, s, r = self.k, self.s[n % 2][:, :, :], self.r[n % 2][:, :]
        dve.wait_ge(self.exps.s, n + 1)
        k.dve_link(dve.tensor_tensor(r, self.den[n % 2][:, :], self.es[n % 2][:, :], ALU.add))
        k.dve_link(dve.reciprocal(r, r))
        dve.tensor_tensor(s, s, r.unsqueeze(2).to_broadcast([P, 8, 2 * P]), ALU.mult).then_inc(self.probs.s, 1)

    def dve(self, dve):
        k, ps = self.k, self.k.ps
        self.dve_max(dve, 0)
        self.dve_max(dve, 1)
        self.dve_probs(dve, 0)
        for n in range(NBLK):
            if n + 1 < NBLK:
                self.dve_probs(dve, n + 1)
            if n + 2 < NBLK:
                self.dve_max(dve, n + 2)
            dve.wait_ge(self.pv.s, n + 1)
            cols = slice(n * P, n * P + P)
            split_out(k, dve, k.y_hi[:, 0:4, cols], k.y_lo[:, 0:4, cols], blocks(ps[:, 4, :]))\
                .then_inc(self.pv_free.s, 1)

    def act_exps(self, act, n):
        i = n % 2
        act.wait_ge(self.max_ready.s, n + 1)
        for h in range(8):
            act.activation(self.s[i][:, h, :], self.s[i][:, h, :], ACT.Exp, scale=0.125, bias=self.nm[i][:, h:h + 1],
                           accum_out=self.den[i][:, h:h + 1])
        act.activation(self.es[i][:, :], self.d[i][:, :], ACT.Exp).then_inc(self.exps.s, 1)

    def act(self, act):
        k, ps = self.k, self.k.ps
        self.act_exps(act, 0)
        self.act_exps(act, 1)
        for n in range(NBLK):
            act.wait_ge(self.turned.s, n + 1)
            for g in range(4):
                ins = act.activation(self.pt[:, g, :, :], blocks(ps[:, 4 + g, :]), ACT.Copy)
            ins.then_inc(self.pt_ready.s, 1)
            if n + 2 < NBLK:
                self.act_exps(act, n + 2)


class SwaSample(Stage):

    def __init__(self, k):
        super().__init__(k)
        k.small.reset(k.even_kept)
        self.kc, self.vc, self.kt = (k.small(f"swas_{n}", [P, 8, P]) for n in ("kc", "vc", "kt"))
        self.qz = k.small("swas_q", [P, 8, 2, 4])
        self.prod, self.st, self.pt, self.o, self.t = (
            k.small(f"swas_{n}", [P, 64]) for n in ("prod", "st", "pt", "o", "t"))
        self.s = k.small("swas_s", [64, P])
        self.own, self.mx, self.m, self.nm, self.d, self.den, self.eo, self.es, self.r = (
            k.small(f"swas_{n}", [64, 1]) for n in ("own", "mx", "m", "nm", "d", "den", "eo", "es", "r"))
        (self.here, self.kturn, self.kt_ready, self.q_ready, self.scores, self.st_ready, self.rows, self.max_ready,
         self.exps, self.probs, self.pturn, self.pt_ready, self.pv) = (
            k.counter(f"swas_{n}") for n in ("here", "kturn", "kt", "q", "scores", "st", "rows", "max", "exps",
                                            "probs", "pturn", "pt", "pv"))

    def act(self, act):
        k, ps = self.k, self.k.ps
        for t, name in ((self.kc, "k"), (self.vc, "v")):
            act.dma_start(t[:, :, :], k.A[f"cache_swa_{name}"][0].rearrange("b s h d -> s b (h d)"))\
               .then_inc(self.here.s, 16)
        act.wait_ge(self.kturn.s, 1)
        for i in range(2):
            ins = act.activation(self.kt[:, 4 * i:4 * i + 4, :], blocks(ps[:, i, :]), ACT.Copy)
        ins.then_inc(self.kt_ready.s, 1)
        act.wait_ge(self.max_ready.s, 1)
        act.activation(self.s[:, :], self.s[:, :], ACT.Exp, scale=0.125, bias=self.nm[:, :], accum_out=self.den[:, :])
        act.activation(self.eo[:, :], self.own[:, :], ACT.Exp, scale=0.125, bias=self.nm[:, :])
        act.activation(self.es[:, :], self.d[:, :], ACT.Exp).then_inc(self.exps.s, 1)

    def pe(self, pe):
        k, ps = self.k, self.k.ps
        pe.wait_ge(self.here.s, 32)
        for b in range(8):
            last = pe.transpose(ps[:, b // 4, (b % 4) * P:(b % 4) * P + P], self.kc[:, b, :], k.c("ident"))
        last.then_inc(self.kturn.s, 1)
        pe.wait_ge(self.kt_ready.s, 1)
        pe.wait_ge(self.q_ready.s, 1)
        for b in range(8):
            pe.matmul(ps[:, 2, 8 * b:8 * b + 8], self.kt[:, b, :], self.qz[:, b, :, :], start=True, stop=True)
        pe.matmul(ps[0:64, 3, 0:1], self.prod[:, :], k.c("ones")[:, 0:1], start=True, stop=True)\
          .then_inc(self.scores.s, 1)
        pe.wait_ge(self.st_ready.s, 1)
        pe.transpose(ps[0:64, 4, 0:P], self.st[:, :], k.c("ident")).then_inc(self.rows.s, 1)
        pe.wait_ge(self.probs.s, 1)
        pe.transpose(ps[:, 5, 0:64], self.s[:, :], k.c("ident", 64)[:, 0:64])
        pe.matmul(ps[:, 6, 0:64], self.eo[:, :].to_broadcast([64, P]), k.c("ident", 64)[:, 0:64], start=True, stop=True)\
          .then_inc(self.pturn.s, 1)
        pe.wait_ge(self.pt_ready.s, 1)
        for b in range(8):
            last = pe.matmul(ps[:, 7, 8 * b:8 * b + 8], self.vc[:, b, :], self.pt[:, 8 * b:8 * b + 8], start=True, stop=True)
        last.then_inc(self.pv.s, 1)

    def dve(self, dve):
        k, ps, p = self.k, self.k.ps, self.k.proj
        k.dve_link(dve.memset(self.qz[:, :, :, :], 0.0))
        for v in range(2):
            rows = slice(64 * v, 64 * v + 64)
            ins = dve.tensor_copy(self.qz[rows, :, v, :], p[rows, 0:4, SEQ:TOK].rearrange("p g b -> p b g"))
        k.dve_link(ins)
        spread = lambda t: t[:, :].rearrange("p (b h) -> p b h", b=8)
        new = lambda c: p[:, c, SEQ:TOK].unsqueeze(2).to_broadcast([P, 8, 8])
        dve.tensor_tensor(spread(self.prod), self.qz[:, :, :, :].rearrange("p b v g -> p b (v g)"), new(E_SK), ALU.mult)\
           .then_inc(self.q_ready.s, 1)
        dve.wait_ge(self.scores.s, 1)
        dve.tensor_copy(self.own[:, :], ps[0:64, 3, 0:1])
        dve.tensor_copy(self.st[:, :], ps[:, 2, 0:64]).then_inc(self.st_ready.s, 1)
        dve.wait_ge(self.rows.s, 1)
        k.dve_link(dve.tensor_copy(self.s[:, :], ps[0:64, 4, 0:P]))
        k.dve_link(dve.tensor_reduce(self.mx[:, :], self.s[:, :], AX.X, ALU.max))
        k.dve_link(dve.tensor_tensor(self.mx[:, :], self.mx[:, :], self.own[:, :], ALU.max))
        k.dve_link(dve.scalar_tensor_tensor(self.m[:, :], self.mx[:, :], 0.125, k.sink_col[:, :], ALU.mult, ALU.max))
        dve.tensor_tensor(self.d[:, :], k.sink_col[:, :], self.m[:, :], ALU.subtract)
        dve.tensor_scalar(self.nm[:, :], self.m[:, :], -1.0, None, ALU.mult).then_inc(self.max_ready.s, 1)
        dve.wait_ge(self.exps.s, 1)
        k.dve_link(dve.tensor_tensor(self.r[:, :], self.den[:, :], self.es[:, :], ALU.add))
        k.dve_link(dve.tensor_tensor(self.r[:, :], self.r[:, :], self.eo[:, :], ALU.add))
        k.dve_link(dve.reciprocal(self.r[:, :], self.r[:, :]))
        dve.tensor_tensor(self.eo[:, :], self.eo[:, :], self.r[:, :], ALU.mult)
        dve.tensor_scalar(self.s[:, :], self.s[:, :], self.r[:, :], None, ALU.mult).then_inc(self.probs.s, 1)
        dve.wait_ge(self.pturn.s, 1)
        dve.tensor_copy(self.pt[:, :], ps[:, 5, 0:64]).then_inc(self.pt_ready.s, 1)
        k.dve_link(dve.tensor_tensor(spread(self.t), ps[:, 6, 0:64].rearrange("p (b h) -> p b h", b=8), new(E_SV), ALU.mult))
        dve.wait_ge(self.pv.s, 1)
        k.dve_link(dve.tensor_tensor(self.o[:, :], self.t[:, :], ps[:, 7, 0:64], ALU.add))
        for v in range(2):
            rows = slice(64 * v, 64 * v + 64)
            src = self.o[rows, :].rearrange("p (b v g) -> p v g b", b=8, v=2)[:, v]
            split_out(k, dve, k.y_hi[rows, 0:4, SEQ:TOK], k.y_lo[rows, 0:4, SEQ:TOK], src)


class Log1pExp:

    def __init__(self, k, name, x, e, u, l, w):
        self.k, self.x, self.e, self.u, self.l, self.w = k, x, e, u, l, w
        self.input, self.exp, self.one_plus, self.log = (k.counter(f"{name}_{n}") for n in (
            "minus_abs", "exp_ready", "one_plus_exp", "log_ready"))

    def dve_input(self, dve):
        dve.scalar_tensor_tensor(self.e, self.x, -1.0, self.x, ALU.mult, ALU.min).then_inc(self.input.s, 1)

    def act_exp(self, act):
        act.wait_ge(self.input.s, 1)
        act.activation(self.e, self.e, ACT.Exp).then_inc(self.exp.s, 1)

    def dve_one_plus(self, dve):
        dve.wait_ge(self.exp.s, 1)
        dve.tensor_scalar(self.u, self.e, 1.0, None, ALU.add).then_inc(self.one_plus.s, 1)

    def act_log(self, act):
        act.wait_ge(self.one_plus.s, 1)
        act.activation(self.l, self.u, ACT.Ln).then_inc(self.log.s, 1)

    def dve_result(self, dve):
        k, e, u, l, w = self.k, self.e, self.u, self.l, self.w
        dve.wait_ge(self.log.s, 1)
        k.dve_link(dve.tensor_scalar(w, u, -1.0, None, ALU.add))
        k.dve_link(dve.tensor_tensor(w, e, w, ALU.subtract))
        k.dve_link(dve.reciprocal(u, u))
        k.dve_link(dve.tensor_tensor(w, w, u, ALU.mult))
        k.dve_link(dve.tensor_tensor(l, l, w, ALU.add))


class EvenGates:

    def __init__(self, k):
        self.k = k
        even_small(k)
        k.big.reset(20 * TOK * 4)
        (k.g_i, k.g_f, self.x, self.e, self.u, self.l, self.w, k.g_cum) = (
            k.big(f"gate_{n}", [4, TOK]) for n in ("i_", "f_", "x", "e", "u", "l", "w", "cum"))
        self.log1p = Log1pExp(k, "even", self.x[:, :], self.e[:, :], self.u[:, :], self.l[:, :], self.w[:, :])
        self.here, self.exponents, self.ready = (k.counter(f"gates_{n}") for n in ("m0_here", "exponents", "ready"))

    def act_load(self, act, n):
        act.dma_start(self.k.g_m0[:, :], self.k.A["state_mlstm_m"][0].rearrange("b h -> h b"),
                      allow_slow_non_contiguous=True).then_inc(self.here.s, 16)

    def dve_input(self, dve, n):
        k, p = self.k, self.k.proj
        dve.tensor_scalar(k.g_i[:, :], p[0:4, E_GI, :], k.gate_i[:, :], None, ALU.add)
        k.dve_link(dve.tensor_scalar(self.x[:, :], p[0:4, E_GF, :], k.gate_f[:, :], None, ALU.add))
        self.log1p.dve_input(dve)

    def act_exp(self, act, n):
        self.log1p.act_exp(act)

    def dve_one_plus(self, dve, n):
        self.log1p.dve_one_plus(dve)

    def act_log(self, act, n):
        self.log1p.act_log(act)

    def dve_running(self, dve, n):
        k = self.k
        self.log1p.dve_result(dve)
        k.dve_link(dve.scalar_tensor_tensor(k.g_f[:, :], self.x[:, :], 0.0, self.l[:, :], ALU.min, ALU.subtract))
        k.dve_link(dve.memset(self.w[:, :], 0.0))
        for b in range(NBLK):
            c = slice(b * P, b * P + P)
            dve.tensor_tensor_scan(k.g_cum[:, c], k.g_f[:, c], self.w[:, c], 0.0, ALU.add, ALU.add)
        dve.tensor_tensor_scan(k.g_m[:, 0:SEQ], k.g_f[:, 0:SEQ], k.g_i[:, 0:SEQ], 0.0, ALU.add, ALU.max)

    def dve_exponents(self, dve, n):
        k = self.k
        dve.wait_ge(self.here.s, 16)
        k.dve_link(dve.tensor_tensor(k.g_cs[:, SEQ:TOK], k.g_f[:, SEQ:TOK], k.g_m0[:, :], ALU.add))
        k.dve_link(dve.tensor_tensor(k.g_m[:, SEQ:TOK], k.g_cs[:, SEQ:TOK], k.g_i[:, SEQ:TOK], ALU.max))
        dve.tensor_tensor(k.g_cs[:, SEQ:TOK], k.g_cs[:, SEQ:TOK], k.g_m[:, SEQ:TOK], ALU.subtract)
        dve.tensor_tensor(k.g_ws[:, :], k.g_i[:, SEQ:TOK], k.g_m[:, SEQ:TOK], ALU.subtract)
        dve.tensor_tensor(k.g_c[:, 0:SEQ], k.g_i[:, 0:SEQ], k.g_cum[:, 0:SEQ], ALU.subtract)
        k.dve_link(dve.tensor_tensor(k.g_a[:, 0:SEQ], k.g_cum[:, 0:SEQ], k.g_m[:, 0:SEQ], ALU.subtract))
        ins = dve.tensor_copy(k.g_cs[:, 0:P], k.g_a[:, 0:P])
        for b in range(1, NBLK):
            c = slice(b * P, b * P + P)
            ins = dve.tensor_scalar(k.g_cs[:, c], k.g_a[:, c], k.g_m[:, b * P - 1:b * P], None, ALU.add)
        ins.then_inc(self.exponents.s, 1)

    def act_exponents(self, act, n):
        k = self.k
        act.wait_ge(self.exponents.s, 1)
        act.activation(k.g_em[:, :], k.g_m[:, :], ACT.Exp, scale=-1.0)
        act.activation(k.g_cs[:, :], k.g_cs[:, :], ACT.Exp)
        act.activation(k.g_ws[:, :], k.g_ws[:, :], ACT.Exp)


def even_spread(k):
    k.small.reset(k.even_kept)
    k.w_ml = k.big("ml_weight", [P, 4, SEQ])
    k.em = k.big("ml_em", [P, 4, TOK])
    k.cs = k.big("ml_cs", [P, 2, TOK])
    k.c_col = k.small("ml_c_col", [P, NBLK, 4])
    k.ws = k.small("ml_ws", [P, 2, 8])
    k.even_kept2 = k.small.at
    items = []
    for h in range(4):
        def mask(dve, bank, h=h):
            return dve.tensor_tensor(blocks(k.w_ml[:, h, :]), blocks(bank[:, 0:512]),
                                     k.c("causal").unsqueeze(1).to_broadcast([P, NBLK, P]), ALU.add)
        items.append(([((0, SEQ), k.onehot(h, 4), k.g_a[:, 0:SEQ], 0)], mask))
        items.append(([((0, SEQ), k.onehot(h, 4), k.g_em[:, 0:SEQ], 0)],
                      lambda dve, bank, h=h: dve.tensor_copy(k.em[:, h, 0:SEQ], bank[:, 0:SEQ])))
    items.append(([((8 * h, 8 * h + 8), k.onehot(h, 4), k.g_em[:, SEQ:TOK], 0) for h in range(4)],
                  lambda dve, bank: dve.tensor_copy(k.em[:, :, SEQ:TOK], bank[:, 0:32].rearrange("p (h b) -> p h b", h=4))))
    for j in range(2):
        items.append((k.pair(j, 4, (0, SEQ), k.g_cs[:, 0:SEQ]),
                      lambda dve, bank, j=j: dve.tensor_copy(k.cs[:, j, 0:SEQ], bank[:, 0:SEQ])))
    pairs = lambda src: k.pair(0, 4, (0, 8), src) + k.pair(1, 4, (8, 16), src)
    take = lambda dst: lambda dve, bank: dve.tensor_copy(dst, bank[:, 0:16].rearrange("p (j b) -> p j b", j=2))
    items.append((pairs(k.g_cs[:, SEQ:TOK]), take(k.cs[:, :, SEQ:TOK])))
    items.append((pairs(k.g_ws[:, :]), take(k.ws[:, :, :])))
    items.append(([((4 * n, 4 * n + 4), k.g_c[:, n * P:n * P + P], k.c("ident", 4)[:, 0:4], 0) for n in range(NBLK)],
                  lambda dve, bank: dve.tensor_copy(k.c_col[:, :, :], bank[:, 0:16].rearrange("p (n h) -> p n h", n=4))))
    return Spread(k, "even_spread", items)


class MlstmPrompt(Stage):

    def __init__(self, k):
        super().__init__(k)
        k.small.reset(k.even_kept2)
        k.ml_state = k.small("ml_state", [P, 2, P + 1])
        self.a = k.small("ml_a", [P, 4, P])
        self.kw = k.small("ml_kw", [P, 4, 64])
        self.den = k.small("ml_den", [P, 4, P])
        self.weights, self.st, self.a_ready, self.num, self.state = (
            k.counter(f"ml_{n}") for n in ("weights", "scores", "weighted", "num", "state"))

    def act(self, act):
        k = self.k
        for n in range(NBLK):
            c = slice(n * P, n * P + P)
            for h in range(4):
                ins = act.activation(k.w_ml[:, h, c], k.w_ml[:, h, c], ACT.Exp, bias=k.c_col[:, n, h:h + 1])
            ins.then_inc(self.weights.s, 1)
        act.wait_ge(self.state.s, NBLK)
        k.store(k.O["p_C"][0, 0].rearrange("(j t) d e -> (t d) j e", t=2), k.ml_state[:, :, 0:P])
        k.store(k.O["p_n"][0, 0].rearrange("(j t) d -> (t d) j", t=2), k.ml_state[:, :, P], few=True)
        k.store(k.O["p_m"].rearrange("l b h -> h (l b)"), k.g_m[:, SEQ - 1:SEQ])
        k.store(k.O["s_m"][0].rearrange("b h -> h b"), k.g_m[:, SEQ:TOK], few=True)

    def pe(self, pe):
        k, ps, p = self.k, self.k.ps, self.k.proj
        for n in range(NBLK):
            c = slice(n * P, n * P + P)
            for h in range(4):
                rows = slice(64 * (h % 2), 64 * (h % 2) + 64)
                at = (h // 2) * P
                last = pe.matmul(ps[:, 4 * (h % 2), at:at + P], p[rows, E_MK + h // 2, c], p[rows, E_MQ + h // 2, c],
                                 start=True, stop=True)
            last.then_inc(self.st.s, 1)
            pe.wait_ge(self.a_ready.s, n + 1)
            if n:
                pe.wait_ge(self.state.s, n)
            for h in range(4):
                rows, j = slice(64 * (h % 2), 64 * (h % 2) + 64), h // 2
                out = ps[:, 1 + 4 * (h % 2), j * P:j * P + P]
                pe.matmul(out, k.mv_tok[:, n, h, 0:P], self.a[:, h, :], start=True, stop=n == 0)
                if n:
                    pe.matmul(out, k.ml_state[rows, j, 0:P], self.qs[rows, j, c], start=False, stop=True)
                out = ps[:, 2 + 4 * (h % 2), j * P:j * P + P]
                pe.matmul(out, k.c("ones"), self.a[:, h, :], start=True, stop=n == 0)
                if n:
                    pe.matmul(out, k.ml_state[rows, j, P:P + 1].to_broadcast([64, P]), self.qs[rows, j, c],
                              start=False, stop=True)
            for h in range(4):
                last = pe.matmul(ps[64 * (h % 2):64 * (h % 2) + 64, 3, (h // 2) * (P + 1):(h // 2 + 1) * (P + 1)],
                                 self.kw[:, h, :], k.mv_tok[:, n, h, :], start=True, stop=True)
            last.then_inc(self.num.s, 1)

    @property
    def qs(self):
        return self.k.qs_view

    def dve(self, dve):
        k, ps, p = self.k, self.k.ps, self.k.proj
        for j in range(2):
            dve.tensor_tensor(k.qs_view[:, j, :], p[:, E_MQ + j, 0:SEQ], k.cs[:, j, 0:SEQ], ALU.mult)
        for n in range(NBLK):
            c = slice(n * P, n * P + P)
            dve.wait_ge(self.weights.s, n + 1)
            k.dve_link(dve.tensor_tensor(self.kw[:, :, :], k.mk_tok[:, n, :].rearrange("p (h d) -> p h d", h=4),
                                         k.w_ml[:, :, n * P + P - 1:n * P + P].to_broadcast([P, 4, 64]), ALU.mult))
            dve.wait_ge(self.st.s, n + 1)
            for t in range(2):
                ins = dve.tensor_tensor(self.a[:, t::2, :], blocks(ps[:, 4 * t, 0:2 * P]), k.w_ml[:, t::2, c], ALU.mult)
            ins.then_inc(self.a_ready.s, 1)
            dve.wait_ge(self.num.s, n + 1)
            for t in range(2):
                ins = dve.scalar_tensor_tensor(self.den[:, t::2, :], blocks(ps[:, 2 + 4 * t, 0:2 * P]), -1.0,
                                               k.em[:, t::2, c], ALU.mult, ALU.max)
            k.dve_link(ins)
            for t in range(2):
                ins = dve.tensor_tensor(self.den[:, t::2, :], self.den[:, t::2, :], blocks(ps[:, 2 + 4 * t, 0:2 * P]),
                                        ALU.max)
            k.dve_link(ins)
            k.dve_link(dve.reciprocal(self.den[:, :, :], self.den[:, :, :]))
            for t in range(2):
                dve.tensor_tensor(p[:, E_MV + t:E_MV + 4:2, c], blocks(ps[:, 1 + 4 * t, 0:2 * P]), self.den[:, t::2, :],
                                  ALU.mult)
            if n == 0:
                ins = dve.tensor_copy(k.ml_state[:, :, :], ps[:, 3, 0:2 * (P + 1)].rearrange("p (j e) -> p j e", j=2))
            else:
                for j in range(2):
                    ins = dve.scalar_tensor_tensor(k.ml_state[:, j, :], k.ml_state[:, j, :],
                                                   k.cs[:, j, n * P + P - 1:n * P + P],
                                                   ps[:, 3, j * (P + 1):(j + 1) * (P + 1)], ALU.mult, ALU.add)
            ins.then_inc(self.state.s, 1)
            dve.wait_ge(self.state.s, n + 1)


class MlstmSample(Stage):

    def __init__(self, k):
        super().__init__(k)
        k.small.reset(k.even_kept2)
        self.c = k.small("mls_c", [P, 8, 2, P])
        self.t = k.small("mls_t", [P, 2, 2, P])
        self.ntok, self.nout = k.small("mls_n_tok", [8, 2 * P]), k.small("mls_n_out", [8, 2 * P])
        self.n, self.kw, self.prod = (k.small(f"mls_{n}", [P, 2, 8]) for n in ("n", "kw", "prod"))
        self.qz = k.small("mls_q", [P, 8, 2, 2])
        self.den = k.small("mls_den", [P, 2, 2, 8])
        (self.here, self.nturn, self.prep, self.vb, self.c_new, self.num) = (
            k.counter(f"mls_{n}") for n in ("here", "n_turned", "prepared", "v_spread", "c_new", "num"))
        self.n_out, self.n_back = k.counter("mls_n_out"), k.counter("mls_n_back")

    def act(self, act):
        k = self.k
        act.dma_start(self.ntok[:, :], k.A["state_mlstm_n"][0].rearrange("b h d -> b (h d)")).then_inc(self.here.s, 16)
        act.dma_start(self.c[:, :, :, :], k.A["state_mlstm_C"][0].rearrange("b (j t) d e -> (t d) b j e", t=2))\
           .then_inc(self.here.s, 16)
        act.wait_ge(self.c_new.s, 8)
        k.store(k.O["s_C"][0].rearrange("b (j t) d e -> (t d) b j e", t=2), self.c[:, :, :, :])
        act.wait_ge(self.n_out.s, 1)
        k.store(k.O["s_n"][0].rearrange("b h d -> b (h d)"), self.nout[:, :])
        k.stores_done()

    def pe(self, pe):
        k, ps = self.k, self.k.ps
        pe.wait_ge(self.here.s, 32)
        for j in range(2):
            last = pe.transpose(ps[:, 0, 8 * j:8 * j + 8], self.ntok[:, j * P:j * P + P], k.c("ident", 8)[:, 0:8])
        last.then_inc(self.nturn.s, 1)
        for b in range(8):
            if b >= 4:
                pe.wait_ge(self.c_new.s, b - 3)
            pe.matmul(ps[:, 4 + b % 4, :], k.onehot(b, 8), k.mv_s[:, :], start=True, stop=True).then_inc(self.vb.s, 1)
        pe.wait_ge(self.prep.s, 1)
        for t in range(2):
            pe.matmul(ps[:, 1, 16 * t:16 * t + 16], k.c("blk64")[:, 64 * t:64 * t + 1].to_broadcast([P, P]),
                      self.prod[:, :, :], start=True, stop=True)
        for j in range(2):
            last = pe.transpose(ps[0:8, 3, j * P:j * P + P], self.n[:, j, :], k.c("ident"))
        last.then_inc(self.n_back.s, 1)
        for b in range(8):
            pe.wait_ge(self.c_new.s, b + 1)
            for j in range(2):
                last = pe.matmul(ps[:, 2, 4 * b + 2 * j:4 * b + 2 * j + 2], self.c[:, b, j, :], self.qz[:, b, j, :],
                                 start=True, stop=True)
        last.then_inc(self.num.s, 1)

    def dve(self, dve):
        k, ps, p = self.k, self.k.ps, self.k.proj
        s = slice(SEQ, TOK)
        k.dve_link(dve.memset(self.qz[:, :, :, :], 0.0))
        for t in range(2):
            rows = slice(64 * t, 64 * t + 64)
            dve.tensor_copy(self.qz[rows, :, :, t], p[rows, E_MQ:E_MQ + 2, s].rearrange("p j b -> p b j"))
        k.dve_link(dve.tensor_tensor(self.kw[:, :, :], p[:, E_MK:E_MK + 2, s], k.ws[:, :, :], ALU.mult))
        dve.wait_ge(self.nturn.s, 1)
        k.dve_link(dve.tensor_tensor(self.n[:, :, :], ps[:, 0, 0:16].rearrange("p (j b) -> p j b", j=2), k.cs[:, :, s], ALU.mult))
        k.dve_link(dve.tensor_tensor(self.n[:, :, :], self.n[:, :, :], self.kw[:, :, :], ALU.add))
        dve.tensor_tensor(self.prod[:, :, :], self.n[:, :, :], p[:, E_MQ:E_MQ + 2, s], ALU.mult).then_inc(self.prep.s, 1)
        dve.wait_ge(self.here.s, 32)
        for b in range(8):
            dve.wait_ge(self.vb.s, b + 1)
            t = self.t[:, b % 2, :, :]
            for half in range(2):
                rows = slice(64 * half, 64 * half + 64)
                v = ps[rows, 4 + b % 4, :].rearrange("p (j t e) -> p t j e", j=2, t=2)[:, half]
                dve.tensor_tensor(t[rows], v, self.kw[rows, :, b:b + 1].to_broadcast([64, 2, P]), ALU.mult)
            k.dve_link(dve.tensor_tensor(self.c[:, b, :, :], self.c[:, b, :, :],
                                         k.cs[:, :, SEQ + b:SEQ + b + 1].to_broadcast([P, 2, P]), ALU.mult))
            dve.tensor_tensor(self.c[:, b, :, :], self.c[:, b, :, :], t, ALU.add).then_inc(self.c_new.s, 1)
        dve.wait_ge(self.n_back.s, 1)
        dve.tensor_copy(self.nout[:, :], ps[0:8, 3, 0:2 * P]).then_inc(self.n_out.s, 1)
        em = k.em[:, :, s].rearrange("p (j t) b -> p t j b", t=2)
        den = ps[:, 1, 0:32].rearrange("p (t j b) -> p t j b", t=2, j=2)
        for t in range(2):
            ins = dve.scalar_tensor_tensor(self.den[:, t], den[:, t], -1.0, em[:, t], ALU.mult, ALU.max)
        k.dve_link(ins)
        for t in range(2):
            ins = dve.tensor_tensor(self.den[:, t], self.den[:, t], den[:, t], ALU.max)
        k.dve_link(ins)
        k.dve_link(dve.reciprocal(self.den[:, :, :, :], self.den[:, :, :, :]))
        dve.wait_ge(self.num.s, 1)
        num = ps[:, 2, 0:32].rearrange("p (b j t) -> p t j b", b=8, j=2)
        hb = p[:, E_MV:E_MV + 4, s].rearrange("p (j t) b -> p t j b", t=2)
        for t in range(2):
            dve.tensor_tensor(hb[:, t], num[:, t], self.den[:, t], ALU.mult)


def mlstm_norm(k):
    k.small.reset()
    def apply(dve, u, rstd):
        x = k.proj[:, E_MV + u, :]
        k.dve_link(dve.scalar_tensor_tensor(x, x, k.col(V_MLN + u), rstd, ALU.mult, ALU.mult))
        k.dve_link(dve.tensor_tensor(x, x, k.proj[:, E_MO + u, :], ALU.mult))
        return split_out(k, dve, k.y_hi[:, 4 + u, :], k.y_lo[:, 4 + u, :], x)
    return HeadNorm(k, "ml_norm", [[k.proj[:, E_MV + u, :]] for u in range(4)], k.c("ones"), P, apply)


def even_layer(k):
    s = [even_projection(k)]
    k.small.reset(k.even_kept)
    qk = [k.proj[:, c, :] for c in range(5)]
    s.append(HeadNorm(k, "qk_norm", [[c] for c in qk], k.c("blk64"), 64, gain_in_place(k, qk, [V_SQ] * 4 + [V_SK])))
    s.append(Rope(k, "even_rope", qk, EVEN, k.even_kept))
    s += [EvenTurn(k), SwaPrompt(k), SwaSample(k), even_spread(k)]
    k.mid.reset(8 * TOK * 4)
    k.qs_view = k.mid("ml_scaled_q", [P, 2, SEQ])
    s += [MlstmPrompt(k), MlstmSample(k), mlstm_norm(k)]
    w = k.A["even_w_out"][0]
    tiles = []
    for m in range(DC):
        t, cols = gemm_tile(w, [(m * P, P)], (k.y_hi, k.y_lo), out_residual(k, m)), slice(m * P, m * P + P)
        t["parts"] = [((64 * v, 64 * v + 64), (0, 4), (0, P),
                       w[256 * v:256 * v + 256, cols].rearrange("(k p) n -> p k n", p=64)) for v in range(2)]
        t["parts"].append(((0, P), (4, 8), (0, P), w[512:1024, cols].rearrange("(k p) n -> p k n", p=P)))
        t["finish"] = m
        tiles.append(t)
    k.small.reset()
    s.append(Gemm(k, tiles, next_norm(k, "even_out", V_XATT, k.xc)))
    return s


class Buffers:
    pass


class MemLoad(Stage):

    def __init__(self, k, m, layer):
        super().__init__(k)
        k.small.reset()
        self.mtok = k.small(f"mem_tok{layer}", [P, 2, D_MODEL])
        self.sq = [k.small(f"mem_sq{layer}{i}", [P, MEM]) for i in range(2)]
        k.big.reset(k.cross_kept)
        m.hm_hi, m.hm_lo = (k.big(f"hm_{n}{layer}", [P, DC, MEM], F32R) for n in ("hi", "lo"))
        self.layer, self.m = layer, m
        self.turned, self.free, self.squared, self.summed = k.mem_signals

    def act(self, act):
        k, l = self.k, self.layer
        act.dma_start(self.mtok[:, :, :], k.A["mem_prompt"].rearrange("b (s p) d -> p (b s) d", p=P))\
           .then_inc(k.mem_here.s, 16)
        if l:
            return
        for c in range(DC):
            act.wait_ge(self.turned.s, c + 1)
            if c >= 2:
                act.wait_ge(self.summed.s, c - 1)
            act.activation(self.sq[c % 2][:, :], k.ps[:, c % 4, 0:MEM], ACT.Square).then_inc(self.squared.s, 1)
        act.wait_ge(self.summed.s, DC)
        k.act_link(act.activation(k.mem_rstd[:, :], k.ps[:, 7, 0:MEM], ACT.Ln, scale=1.0 / D_MODEL, bias=k.c("eps")))
        act.activation(k.mem_rstd[:, :], k.mem_rstd[:, :], ACT.Exp, scale=-0.5)

    def pe(self, pe):
        k, l = self.k, self.layer
        pe.wait_ge(k.mem_here.s, 16 * (l + 1))
        def total(c):
            pe.wait_ge(self.squared.s, c + 1)
            pe.matmul(k.ps[:, 7, 0:MEM], k.c("ones"), self.sq[c % 2][:, :], start=c == 0, stop=c == DC - 1)\
              .then_inc(self.summed.s, 1)
        for c in range(DC):
            if c >= 4:
                pe.wait_ge(self.free.s, DC * l + c - 3)
            for s in range(2):
                last = pe.transpose(k.ps[:, c % 4, s * P:s * P + P], self.mtok[:, s, c * P:c * P + P], k.c("ident"))
            last.then_inc(self.turned.s, 1)
            if c and l == 0:
                total(c - 1)
        if l == 0:
            total(DC - 1)

    def dve(self, dve):
        k, m, l = self.k, self.m, self.layer
        for c in range(DC):
            if l:
                dve.wait_ge(self.turned.s, DC * l + c + 1)
            else:
                dve.wait_ge(self.squared.s, c + 1)
            src, g = k.ps[:, c % 4, 0:MEM], k.col(V_MEM + DC * l + c)
            k.dve_link(dve.tensor_scalar(m.hm_hi[:, c, :], src, g, None, ALU.mult))
            dve.scalar_tensor_tensor(m.hm_lo[:, c, :], src, g, m.hm_hi[:, c, :].bitcast(F32), ALU.mult,
                                     ALU.subtract).then_inc(self.free.s, 1)


class KvTurn(Turn):

    def __init__(self, k, m, layer):
        four = lambda b: b[:, 0:512]
        items = []
        for src, dst in ((m.k_t, m.k_tok), (m.v_t, m.v_tok)):
            for s in range(2):
                items.append(([(src[:, h, s * P:s * P + P], h * P) for h in range(4)], four, dst[:, s, :]))
        super().__init__(k, f"kv_turn{layer}", items)
        self.layer, self.m = layer, m

    def act(self, act):
        k, m = self.k, self.m
        super().act(act)
        act.wait_ge(self.free.s, self.base + len(self.items))
        for name, t in (("mem_k", m.k_tok), ("mem_v", m.v_tok)):
            k.store(k.O[name][self.layer, 0].rearrange("(s p) h d -> p s (h d)", p=P), t[:, :, :])


class CrossPrompt(Stage):

    def __init__(self, k, m, layer):
        super().__init__(k)
        k.small.reset()
        self.s = [k.small(f"xa_s{layer}{i}", [P, 4, MEM]) for i in range(2)]
        self.pt = k.small(f"xa_pt{layer}", [P, 4, 2, P])
        self.mx, self.nm, self.den, self.r = (
            [k.small(f"xa_{n}{layer}{i}", [P, 4]) for i in range(2)] for n in ("mx", "nm", "den", "r"))
        (self.scores, self.max_ready, self.exps, self.probs, self.turned, self.pt_ready, self.pv, self.out) = k.xa_signals
        self.n0 = layer * NBLK
        k.mid.reset()
        m.kc = [k.mid(f"kc{layer}{b}", [P, 2, 512]) for b in range(8)]
        k.big.reset(k.cross_kept)
        m.vc = [k.big(f"vc{layer}{b}", [P, 2, 512]) for b in range(8)]
        self.layer, self.m = layer, m

    def pe_scores(self, pe, n):
        k, m, ps = self.k, self.m, self.k.ps
        if n >= 2:
            pe.wait_ge(self.exps.s, self.n0 + n - 1)
        for h in range(4):
            last = pe.matmul(ps[:, 2 * (n % 2) + h // 2, MEM * (h % 2):MEM * (h % 2) + MEM],
                             m.q[:, h, n * P:n * P + P], m.k_t[:, h, :], start=True, stop=True)
        last.then_inc(self.scores.s, 1)

    def pe(self, pe):
        k, m, ps = self.k, self.m, self.k.ps
        self.pe_scores(pe, 0)
        self.pe_scores(pe, 1)
        for n in range(NBLK):
            pe.wait_ge(self.probs.s, self.n0 + n + 1)
            for h in range(4):
                for s in range(2):
                    last = pe.transpose(ps[:, 4 + h // 2, 256 * (h % 2) + s * P:256 * (h % 2) + s * P + P],
                                        self.s[n % 2][:, h, s * P:s * P + P], k.c("ident"))
            last.then_inc(self.turned.s, 1)
            if n + 2 < NBLK:
                self.pe_scores(pe, n + 2)
            pe.wait_ge(self.pt_ready.s, self.n0 + n + 1)
            if n >= 2:
                pe.wait_ge(self.out.s, self.n0 + n - 1)
            for h in range(4):
                for s in range(2):
                    last = pe.matmul(ps[:, 6 + n % 2, h * P:h * P + P], m.v_tok[:, s, h * P:h * P + P],
                                     self.pt[:, h, s, :], start=s == 0, stop=s == 1)
            last.then_inc(self.pv.s, 1)

    def dve_max(self, dve, n):
        k, m, ps = self.k, self.m, self.k.ps
        dve.wait_ge(self.scores.s, self.n0 + n + 1)
        src = ps[:, 2 * (n % 2):2 * (n % 2) + 2, :].rearrange("p a (b m) -> p (a b) m", b=2)
        k.dve_link(dve.tensor_reduce(self.mx[n % 2][:, :], src, AX.X, ALU.max))
        dve.tensor_scalar(self.nm[n % 2][:, :], self.mx[n % 2][:, :], -(P ** -0.5), None, ALU.mult)\
           .then_inc(self.max_ready.s, 1)

    def dve_probs(self, dve, n):
        k, r, s = self.k, self.r[n % 2], self.s[n % 2]
        dve.wait_ge(self.exps.s, self.n0 + n + 1)
        k.dve_link(dve.reciprocal(r[:, :], self.den[n % 2][:, :]))
        dve.tensor_tensor(s[:, :, :], s[:, :, :], r[:, :].unsqueeze(2).to_broadcast([P, 4, MEM]), ALU.mult)\
           .then_inc(self.probs.s, 1)

    def dve(self, dve):
        k, m, ps = self.k, self.m, self.k.ps
        self.dve_max(dve, 0)
        self.dve_max(dve, 1)
        self.dve_probs(dve, 0)
        for n in range(NBLK):
            if n + 1 < NBLK:
                self.dve_probs(dve, n + 1)
            if n + 2 < NBLK:
                self.dve_max(dve, n + 2)
            dve.wait_ge(self.pv.s, self.n0 + n + 1)
            cols = slice(n * P, n * P + P)
            split_out(k, dve, k.xa_hi[:, 0:4, cols], k.xa_lo[:, 0:4, cols], blocks(ps[:, 6 + n % 2, :]))\
                .then_inc(self.out.s, 1)

    def act_exps(self, act, n):
        k, m, ps = self.k, self.m, self.k.ps
        act.wait_ge(self.max_ready.s, self.n0 + n + 1)
        if n >= 2:
            act.wait_ge(self.turned.s, self.n0 + n - 1)
        for h in range(4):
            ins = act.activation(self.s[n % 2][:, h, :], ps[:, 2 * (n % 2) + h // 2, MEM * (h % 2):MEM * (h % 2) + MEM],
                                 ACT.Exp, scale=P ** -0.5, bias=self.nm[n % 2][:, h:h + 1],
                                 accum_out=self.den[n % 2][:, h:h + 1])
        ins.then_inc(self.exps.s, 1)

    def act(self, act):
        k, m, ps = self.k, self.m, self.k.ps
        for cache, tiles in (("cache_mem_k", m.kc), ("cache_mem_v", m.vc)):
            for b in range(8):
                act.dma_start(tiles[b][:, :, :], k.A[cache][self.layer, b].rearrange("(s p) h d -> p s (h d)", p=P))\
                   .then_inc(k.cache_here.s, 16)
        self.act_exps(act, 0)
        self.act_exps(act, 1)
        for n in range(NBLK):
            act.wait_ge(self.turned.s, self.n0 + n + 1)
            for a in range(2):
                ins = act.activation(self.pt[:, 2 * a:2 * a + 2, :, :],
                                     ps[:, 4 + a, :].rearrange("p (h s q) -> p h s q", h=2, s=2), ACT.Copy)
            ins.then_inc(self.pt_ready.s, 1)
            if n + 2 < NBLK:
                self.act_exps(act, n + 2)


class CrossSample(Stage):

    def __init__(self, k, m, layer):
        super().__init__(k)
        k.small.reset()
        self.kt = [k.small(f"xs_kt{layer}{i}", [P, 4, 2, P]) for i in range(2)]
        self.qz = k.small(f"xs_q{layer}", [P, 32 * 32])
        self.pz = k.small(f"xs_p{layer}", [P, 2, 8, 60])
        self.s = k.small(f"xs_s{layer}", [32, MEM])
        self.t = k.small(f"xs_t{layer}", [32, 4, P])
        self.o = k.small(f"xs_o{layer}", [32, P])
        self.mx, self.nm, self.den, self.r = (k.small(f"xs_{n}{layer}", [32, 1]) for n in ("mx", "nm", "den", "r"))
        (self.kturn, self.kt_ready, self.q_ready, self.scored, self.scores, self.max_ready, self.exps, self.probs,
         self.pturn, self.pt_ready, self.pv, self.o_ready, self.oturn) = k.xs_signals
        self.layer, self.m = layer, m

    def pe(self, pe):
        k, m, ps, l = self.k, self.m, self.k.ps, self.layer
        pe.wait_ge(k.cache_here.s, 256 * (l + 1))
        def turn(b):
            if b >= 2:
                pe.wait_ge(self.kt_ready.s, 8 * l + b - 1)
            for h in range(4):
                for s in range(2):
                    last = pe.transpose(ps[:, 2 * (b % 2) + h // 2, 256 * (h % 2) + s * P:256 * (h % 2) + s * P + P],
                                        m.kc[b][:, s, h * P:h * P + P], k.c("ident"))
            last.then_inc(self.kturn.s, 1)
        turn(0)
        pe.wait_ge(self.q_ready.s, l + 1)
        for b in range(8):
            if b < 7:
                turn(b + 1)
            pe.wait_ge(self.kt_ready.s, 8 * l + b + 1)
            for h in range(4):
                r = 4 * b + h
                last = pe.matmul(ps[0:32, 4, 0:MEM], self.qz[:, 32 * r:32 * r + 32], self.kt[b % 2][:, h, :, :],
                                 start=r == 0, stop=r == 31)
            last.then_inc(self.scored.s, 1)
        last = None
        pe.wait_ge(self.probs.s, l + 1)
        for s in range(2):
            last = pe.transpose(ps[:, 5, 32 * s:32 * s + 32], self.s[:, s * P:s * P + P], k.c("ident", 32)[:, 0:32])
        last.then_inc(self.pturn.s, 1)
        pe.wait_ge(self.pt_ready.s, l + 1)
        for b in range(8):
            for s in range(2):
                last = pe.matmul(ps[0:32, 6, :], self.pz[:, s, b, 28 - 4 * b:60 - 4 * b], m.vc[b][:, s, :],
                                 start=b + s == 0, stop=b == 7 and s == 1)
        last.then_inc(self.pv.s, 1)
        pe.wait_ge(self.o_ready.s, l + 1)
        pe.transpose(ps[:, 7, 0:32], self.o[:, :], k.c("ident", 32)[:, 0:32]).then_inc(self.oturn.s, 1)

    def act(self, act):
        k, m, ps, l = self.k, self.m, self.k.ps, self.layer
        for b in range(8):
            act.wait_ge(self.kturn.s, 8 * l + b + 1)
            if b >= 2:
                act.wait_ge(self.scored.s, 8 * l + b - 1)
            for a in range(2):
                ins = act.activation(self.kt[b % 2][:, 2 * a:2 * a + 2, :, :],
                                     ps[:, 2 * (b % 2) + a, :].rearrange("p (h s q) -> p h s q", h=2, s=2), ACT.Copy)
            ins.then_inc(self.kt_ready.s, 1)
        act.wait_ge(self.max_ready.s, l + 1)
        act.activation(self.s[:, :], ps[0:32, 4, 0:MEM], ACT.Exp, scale=P ** -0.5, bias=self.nm[:, :],
                       accum_out=self.den[:, :]).then_inc(self.exps.s, 1)

    def dve(self, dve):
        k, m, ps, l = self.k, self.m, self.k.ps, self.layer
        dve.memset(self.pz[:, :, :, :], 0.0)
        k.dve_link(dve.memset(self.qz[:, :], 0.0))
        dve.tensor_copy(self.qz[:, 0:1024:33].rearrange("p (b h) -> p b h", b=8),
                        m.q[:, :, SEQ:TOK].rearrange("p h b -> p b h")).then_inc(self.q_ready.s, 1)
        dve.wait_ge(self.scored.s, 8 * (l + 1))
        k.dve_link(dve.tensor_reduce(self.mx[:, :], ps[0:32, 4, 0:MEM], AX.X, ALU.max))
        dve.tensor_scalar(self.nm[:, :], self.mx[:, :], -(P ** -0.5), None, ALU.mult).then_inc(self.max_ready.s, 1)
        dve.wait_ge(self.exps.s, l + 1)
        k.dve_link(dve.reciprocal(self.r[:, :], self.den[:, :]))
        dve.tensor_scalar(self.s[:, :], self.s[:, :], self.r[:, :], None, ALU.mult).then_inc(self.probs.s, 1)
        dve.wait_ge(self.pturn.s, l + 1)
        for s in range(2):
            ins = dve.tensor_copy(self.pz[:, s, :, 28:32], ps[:, 5, 32 * s:32 * s + 32].rearrange("p (b h) -> p b h", b=8))
        ins.then_inc(self.pt_ready.s, 1)
        dve.wait_ge(self.pv.s, l + 1)
        k.dve_link(dve.tensor_tensor(self.t[:, :, :], blocks(ps[0:32, 6, :]),
                                     k.c("own_head", 32).unsqueeze(2).to_broadcast([32, 4, P]), ALU.mult))
        dve.tensor_reduce(self.o[:, :], self.t[:, :, :].rearrange("p h d -> p d h"), AX.X, ALU.add)\
           .then_inc(self.o_ready.s, 1)
        dve.wait_ge(self.oturn.s, l + 1)
        split_out(k, dve, k.xa_hi[:, 0:4, SEQ:TOK], k.xa_lo[:, 0:4, SEQ:TOK],
                  ps[:, 7, 0:32].rearrange("p (b h) -> p h b", b=8))


def cross_layer(k, l):
    m = Buffers()
    k.big.reset()
    m.k_t, m.v_t = (k.big(f"mem_{n}_t{l}", [P, 4, MEM]) for n in "kv")
    m.k_tok, m.v_tok = (k.big(f"mem_{n}_tok{l}", [P, 2, 512]) for n in "kv")
    m.q = k.big(f"xq{l}", [P, 4, TOK])
    k.cross_kept = k.big.at
    s = [MemLoad(k, m, l)]
    tiles = []
    for w, dst in (("mem_wk", m.k_t), ("mem_wv", m.v_t)):
        tiles += [gemm_tile(k.A[w][l], [(h * P, P)], (m.hm_hi, m.hm_lo), out_copy(k, dst[:, h, :]), halves=[(0, MEM)])
                  for h in range(4)]
    tiles += [gemm_tile(k.A["mem_wq"][l], [(h * P, P)], k.xc, out_copy(k, m.q[:, h, :])) for h in range(4)]
    s.append(Gemm(k, tiles))
    k.small.reset()
    kt = [m.k_t[:, h, :] for h in range(4)]
    s.append(HeadNorm(k, f"mk_norm{l}", [[c] for c in kt], k.c("ones"), P, gain_in_place(k, kt, [V_KN + l] * 4), MEM))
    k.small.reset()
    q = [m.q[:, h, :] for h in range(4)]
    s.append(HeadNorm(k, f"q_norm{l}", [[c] for c in q], k.c("ones"), P, gain_in_place(k, q, [V_QN + l] * 4)))
    s += [KvTurn(k, m, l), CrossPrompt(k, m, l), CrossSample(k, m, l)]
    w = k.A["mem_wo"][l]
    k.small.reset()
    s.append(Gemm(k, [gemm_tile(w, [(c * P, P)], (k.xa_hi, k.xa_lo), out_residual(k, c), nk=4, finish=c)
                      for c in range(DC)], next_norm(k, f"cross_out{l}", V_FFN + DC * l, k.xn)))
    return s




def odd_projection(k):
    w, xn = k.A["odd_w_in"][0], k.xn
    tiles = [gemm_tile(w, [(20 * P, 16)], xn, out_copy(k, k.proj[0:16, O_DT, :]))]
    order = [*range(O_X, O_X + 12), *range(O_Z, O_Z + 8), *range(O_RG, O_RG + 4), *range(O_RQ, O_RG)]
    for c in order:
        scale = P ** -0.5 if O_RK <= c < O_RV else None
        at = c * P if c < 20 else 20 * P + 16 + (c - O_RQ) * P
        tiles.append(gemm_tile(w, [(at, P)], xn, out_copy(k, k.proj[:, c, :], scale)))
    gates, conv = OddGates(k), Conv(k)
    follow(tiles, 0, gates.dve_input, gates.act_exp)
    follow(tiles, 1, gates.dve_one_plus, gates.act_log)
    follow(tiles, 2, gates.dve_sums, gates.act_ecum)
    follow(tiles, 3, gates.dve_block_decay)
    follow(tiles, 3, conv.dve_history)
    for c in range(12):
        i = 4 + c
        follow(tiles, i, None, lambda act, n, c=c: conv.act_start(act, c))
        follow(tiles, i + 1, lambda dve, n, c=c: conv.dve_taps(dve, c))
        follow(tiles, i + 2, None, lambda act, n, c=c: conv.act_silu(act, c))
    for i, c in enumerate(order):
        if not O_X <= c < O_X + 12 and (c < O_X or c >= O_RG):
            def silu(act, n, c=c):
                act.wait_ge(k.tile_out.s, n + 1)
                act.activation(k.proj[:, c, :], k.proj[:, c, :], ACT.Silu)
            follow(tiles, i + 1, None, silu)
    follow(tiles, len(tiles) - 1, None,
           lambda act, n: k.nc.scalar.preload_act_table_set("natural_log_exp_and_others"))
    return Gemm(k, tiles)


class OddLoads(Stage):

    def __init__(self, k):
        super().__init__(k)
        k.mid.reset(2 * DC * TOK * 4)
        k.conv_old = k.mid("conv_old", [24, 1536])

    def act(self, act):
        k = self.k
        act.dma_start(k.lconst[:, 0:NODD], k.C[:, NCOMMON + NEVEN:NCOMMON + NEVEN + NODD]).then_inc(k.odd_here.s, 16)
        act.dma_start(k.conv_old[:, :], k.A["state_ssd_conv"][0].rearrange("b j c -> (b j) c")).then_inc(k.odd_here.s, 16)


class ConvHistory(Turn):

    def __init__(self, k):
        k.small.reset((k.small.size - 12 * (24 + 11) * 4 - 64) // 32 * 32)
        k.conv_free = k.small.at
        k.hist, k.tail = k.small("conv_hist", [P, 12, 24]), k.small("conv_tail", [P, 12, 11])
        super().__init__(k, "conv_history",
                         [([(k.conv_old[:, c * P:c * P + P], 24 * c) for c in range(12)],
                           lambda b: b[:, 0:288].rearrange("p (c r) -> p c r", c=12), k.hist[:, :, :])])

    def pe(self, pe):
        pe.wait_ge(self.k.odd_here.s, 32)
        super().pe(pe)


class ConvTurn(Turn):

    def __init__(self, k):
        super().__init__(k, "conv_turn",
                         [([(k.tail[:, 4 * g + i, :], i * P) for i in range(4)], lambda b: b[0:11, 0:512],
                           k.conv_new[:, 512 * g:512 * g + 512]) for g in range(3)])

    def act(self, act):
        k = self.k
        super().act(act)
        act.wait_ge(self.free.s, self.base + len(self.items))
        k.store(k.O["p_conv"][0, 0], k.conv_new[0:3, :])
        k.store(k.O["s_conv"][0][:, 2, :], k.conv_new[3:11, :])
        k.store(k.O["s_conv"][0][:, 0:2, :], k.A["state_ssd_conv"][0][:, 1:3, :])
        k.stores_done()


class Conv:

    def __init__(self, k):
        self.k = k
        self.acc = [k.small(f"conv_acc{i}", [P, TOK]) for i in range(3)]
        self.prod = k.small("conv_prod", [P, 3, 12, 8])
        assert k.small.at <= k.conv_free
        self.started, self.acc_ready, self.silu = (k.counter(f"conv_{n}") for n in ("last_tap", "taps", "silu"))

    def act_start(self, act, c):
        k = self.k
        if c >= 3:
            act.wait_ge(self.silu.s, c - 2)
        act.activation(self.acc[c % 3][:, :], k.proj[:, O_X + c, :], ACT.Copy, scale=k.col(V_CW + 36 + c))\
           .then_inc(self.started.s, 1)

    def act_silu(self, act, c):
        k = self.k
        act.wait_ge(self.acc_ready.s, c + 1)
        act.activation(k.proj[:, O_X + c, :], self.acc[c % 3][:, :], ACT.Silu, bias=k.col(V_CB + c))\
           .then_inc(self.silu.s, 1)

    def dve_history(self, dve, n):
        k = self.k
        for j in range(3):
            w = k.vcol[:, V_CW + 12 * j:V_CW + 12 * j + 12].unsqueeze(2).to_broadcast([P, 12, 8])
            ins = dve.tensor_tensor(self.prod[:, j], k.hist[:, :, j::3], w, ALU.mult)
        k.dve_link(ins)
        k.dve_link(dve.tensor_tensor(self.prod[:, 0], self.prod[:, 0], self.prod[:, 1], ALU.add))
        k.dve_link(dve.tensor_tensor(self.prod[:, 0], self.prod[:, 0], self.prod[:, 2], ALU.add))

    def dve_taps(self, dve, c):
        k, acc, x = self.k, self.acc[c % 3], self.k.proj[:, O_X + c, :]
        dve.tensor_copy(k.tail[:, c, :], x[:, SEQ - 3:TOK])
        dve.wait_ge(self.started.s, c + 1)
        dve.tensor_tensor(acc[:, SEQ:TOK], acc[:, SEQ:TOK], self.prod[:, 0, c, :], ALU.add)
        for j in range(3):
            back = 3 - j
            ins = dve.scalar_tensor_tensor(acc[:, back:SEQ], x[:, 0:SEQ - back], k.col(V_CW + 12 * j + c),
                                           acc[:, back:SEQ], ALU.mult, ALU.add)
            if j < 2:
                k.dve_link(ins)
        ins.then_inc(self.acc_ready.s, 1)


class OddGates:

    def __init__(self, k):
        self.k = k
        k.small.reset()
        k.cum = k.small("ssd_cum", [16, TOK])
        k.dt_col, k.dec, k.ncum_col = (k.small(n, [P, NBLK, 16]) for n in ("dt_col", "ssd_dec", "ncum_col"))
        k.dt_pair, k.d_pair = k.small("dt_pair", [P, 8, 8]), k.small("d_pair", [P, 8])
        k.odd_kept = k.small.at
        k.conv_new = k.small("conv_new", [11, 1536])
        k.dt, k.ecum = k.small("ssd_dt", [16, TOK]), k.small("ssd_ecum", [16, TOK])
        k.dg, self.a = k.small("ssd_dg", [16, NBLK, 16]), k.small("ssd_a", [16, 1])
        k.mid.reset(2 * DC * TOK * 4)
        self.x, self.e, self.u, self.l, self.w = (k.mid(f"dt_{n}", [16, TOK]) for n in "xeulw")
        self.log1p = Log1pExp(k, "odd", self.x[:, :], self.e[:, :], self.u[:, :], self.l[:, :], self.w[:, :])
        self.cum_ready, self.a_ready = (k.counter(f"ssd_{n}_ready") for n in ("cum", "a"))
        self.e_ready = k.counter("ssd_ecum_ready")

    def dve_input(self, dve, n):
        k = self.k
        k.dve_link(dve.tensor_scalar(self.x[:, :], k.proj[0:16, O_DT, :], k.dt_bias[:, :], None, ALU.add))
        self.log1p.dve_input(dve)

    def act_exp(self, act, n):
        act.activation(self.a[:, :], self.k.a_log[:, :], ACT.Exp).then_inc(self.a_ready.s, 1)
        self.log1p.act_exp(act)

    def dve_one_plus(self, dve, n):
        self.log1p.dve_one_plus(dve)

    def act_log(self, act, n):
        self.log1p.act_log(act)

    def dve_sums(self, dve, n):
        k, x, w = self.k, self.x[:, :], self.w[:, :]
        self.log1p.dve_result(dve)
        k.dve_link(dve.scalar_tensor_tensor(k.dt[:, :], x, 0.0, self.l[:, :], ALU.max, ALU.add))
        k.dve_link(dve.memset(w, 0.0))
        dve.wait_ge(self.a_ready.s, 1)
        k.dve_link(dve.tensor_scalar(x, k.dt[:, :], self.a[:, :], -1.0, ALU.mult, ALU.mult))
        for b in range(NBLK):
            c = slice(b * P, b * P + P)
            dve.tensor_tensor_scan(k.cum[:, c], x[:, c], w[:, c], 0.0, ALU.add, ALU.add)
        dve.tensor_copy(k.cum[:, SEQ:TOK], x[:, SEQ:TOK]).then_inc(self.cum_ready.s, 1)

    def act_ecum(self, act, n):
        act.wait_ge(self.cum_ready.s, 1)
        act.activation(self.k.ecum[:, :], self.k.cum[:, :], ACT.Exp).then_inc(self.e_ready.s, 1)

    def dve_block_decay(self, dve, n):
        k = self.k
        dve.wait_ge(self.e_ready.s, 1)
        for b in range(NBLK):
            dve.tensor_scalar(k.dg[:, b, :], k.c("ident", 16)[:, 0:16], k.ecum[:, b * P + P - 1:b * P + P], None, ALU.mult)


def odd_spread(k):
    k.mid.reset()
    k.ec = k.mid("ecum_pair", [P, 8, TOK])
    columns = lambda rows: [((16 * n, 16 * n + 16), rows[:, n * P:n * P + P], k.c("ident", 16)[:, 0:16], 0)
                            for n in range(NBLK)]
    items = [(columns(k.dt), lambda dve, b: dve.tensor_copy(k.dt_col[:, :, :],
                                                            b[:, 0:64].rearrange("p (n h) -> p n h", n=NBLK))),
             (columns(k.cum), lambda dve, b: dve.tensor_scalar(k.ncum_col[:, :, :], b[:, 0:64]
                                                               .rearrange("p (n h) -> p n h", n=NBLK), -1.0, None,
                                                               ALU.mult)),
             ([((0, 64), k.c("ones", 16), k.dg[:, :, :], 0)],
              lambda dve, b: dve.tensor_copy(k.dec[:, :, :], b[:, 0:64].rearrange("p (n h) -> p n h", n=NBLK)))]
    eight = lambda src: sum((k.pair(j, 16, (8 * j, 8 * j + 8), src) for j in range(8)), [])
    take = lambda dst: lambda dve, b: dve.tensor_copy(dst, b[:, 0:64].rearrange("p (j b) -> p j b", j=8))
    items.append((eight(k.dt[:, SEQ:TOK]), take(k.dt_pair[:, :, :])))
    items.append((eight(k.ecum[:, SEQ:TOK]), take(k.ec[:, :, SEQ:TOK])))
    items.append((sum((k.pair(j, 16, (j, j + 1), k.d_skip[:, :]) for j in range(8)), []),
                  lambda dve, b: dve.tensor_copy(k.d_pair[:, :], b[:, 0:8])))
    for j in range(8):
        items.append((k.pair(j, 16, (0, SEQ), k.ecum[:, 0:SEQ]),
                      lambda dve, b, j=j: dve.tensor_copy(k.ec[:, j, 0:SEQ], b[:, :])))
    return Spread(k, "odd_spread", items)


def ret_turn(k):
    p = k.proj
    k.small.reset(k.odd_kept)
    k.rk_tok, k.rv_tok = k.small("rk_tok", [P, NBLK, 512]), None
    k.rv_s = k.small("rv_s", [8, 512])
    k.ret_kept = k.small.at
    k.mid.reset(12 * TOK * 4)
    k.rv_tok = k.mid("rv_tok", [P, NBLK, 512])
    items = []
    for base, dst in ((O_RK, k.rk_tok), (O_RV, k.rv_tok)):
        for h in range(4):
            items.append(([(p[:, base + h, n * P:n * P + P], n * P) for n in range(NBLK)],
                          lambda b: blocks(b[:, 0:512]), dst[:, :, h * P:h * P + P]))
    items.append(([(p[:, O_RV + h, SEQ:TOK], h * P) for h in range(4)], lambda b: b[0:8, 0:512], k.rv_s[:, :]))
    return Turn(k, "ret_turn", items)


class RetPrompt(Stage):

    def __init__(self, k):
        super().__init__(k)
        k.small.reset(k.ret_kept)
        self.a, self.qs = ([k.small(f"ret_{n}{i}", [P, 4, P]) for i in range(2)] for n in ("a", "qs"))
        self.ks = [k.mid(f"ret_ks{i}", [P, 4, P]) for i in range(2)]
        self.r = k.mid("ret_state", [P, 4, P])
        self.scores, self.a_ready, self.o, self.state = (k.counter(f"ret_{n}") for n in ("scores", "a", "o", "state"))

    def pe_scores(self, pe, n):
        k, ps, p, c = self.k, self.k.ps, self.k.proj, slice(n * P, n * P + P)
        if n >= 2:
            pe.wait_ge(self.a_ready.s, n - 1)
        for h in range(4):
            last = pe.matmul(ps[:, n % 2, h * P:h * P + P], p[:, O_RK + h, c], p[:, O_RQ + h, c], start=True, stop=True)
        last.then_inc(self.scores.s, 1)

    def pe(self, pe):
        k, ps = self.k, self.k.ps
        self.pe_scores(pe, 0)
        for n in range(NBLK):
            if n + 1 < NBLK:
                self.pe_scores(pe, n + 1)
            pe.wait_ge(self.a_ready.s, n + 1)
            if n:
                pe.wait_ge(self.state.s, n)
            for h in range(4):
                out = ps[:, 2, h * P:h * P + P]
                pe.matmul(out, k.rv_tok[:, n, h * P:h * P + P], self.a[n % 2][:, h, :], start=True, stop=n == 0)
                if n:
                    pe.matmul(out, self.r[:, h, :], self.qs[n % 2][:, h, :], start=False, stop=True)
            for h in range(4):
                last = pe.matmul(ps[:, 3, h * P:h * P + P], self.ks[n % 2][:, h, :], k.rv_tok[:, n, h * P:h * P + P],
                                 start=True, stop=True)
            last.then_inc(self.o.s, 1)

    def dve(self, dve):
        k, ps, p = self.k, self.k.ps, self.k.proj
        def prepare(n):
            c = slice(n * P, n * P + P)
            dve.tensor_tensor(self.ks[n % 2][:, :, :], blocks(k.rk_tok[:, n, :]),
                              k.lc(ODD, "kscale").unsqueeze(2).to_broadcast([P, 4, P]), ALU.mult)
            dve.tensor_tensor(self.qs[n % 2][:, :, :], p[:, O_RQ:O_RQ + 4, c], blocks(k.lc(ODD, "qscale")), ALU.mult)
            dve.wait_ge(self.scores.s, n + 1)
            dve.tensor_tensor(self.a[n % 2][:, :, :], blocks(ps[:, n % 2, :]), blocks(k.lc(ODD, "decay")), ALU.mult)\
               .then_inc(self.a_ready.s, 1)
        prepare(0)
        for n in range(NBLK):
            if n + 1 < NBLK:
                prepare(n + 1)
            c = slice(n * P, n * P + P)
            dve.wait_ge(self.o.s, n + 1)
            dve.tensor_copy(p[:, O_RQ:O_RQ + 4, c], blocks(ps[:, 2, :]))
            if n == 0:
                ins = dve.tensor_copy(self.r[:, :, :], blocks(ps[:, 3, :]))
            else:
                for h in range(4):
                    ins = dve.scalar_tensor_tensor(self.r[:, h, :], self.r[:, h, :], RET_CHUNK_DECAY[h],
                                                   ps[:, 3, h * P:h * P + P], ALU.mult, ALU.add)
            ins.then_inc(self.state.s, 1)
            dve.wait_ge(self.state.s, n + 1)

    def act(self, act):
        k = self.k
        act.wait_ge(self.state.s, NBLK)
        k.store(k.O["p_ret"][0, 0].rearrange("h d e -> d h e"), self.r[:, :, :])
        k.stores_done()


class RetSample(Stage):

    def __init__(self, k):
        super().__init__(k)
        k.small.reset(k.ret_kept)
        self.t = [k.small(f"rets_t{i}", [P, 4, P]) for i in range(2)]
        k.mid.reset(12 * TOK * 4)
        self.r = k.mid("rets_r", [P, 8, 4, P])
        self.here, self.vb, self.r_new, self.o = (k.counter(f"rets_{n}") for n in ("here", "v_spread", "r_new", "o"))

    def act(self, act):
        k = self.k
        act.dma_start(self.r[:, :, :, :], k.A["state_ret"][0].rearrange("b h d e -> d b h e")).then_inc(self.here.s, 16)
        act.wait_ge(self.r_new.s, 8)
        k.store(k.O["s_ret"][0].rearrange("b h d e -> d b h e"), self.r[:, :, :, :])
        k.stores_done()

    def pe(self, pe):
        k, ps, p = self.k, self.k.ps, self.k.proj
        for b in range(8):
            if b >= 4:
                pe.wait_ge(self.r_new.s, b - 3)
            pe.matmul(ps[:, 4 + b % 4, :], k.onehot(b, 8), k.rv_s[:, :], start=True, stop=True).then_inc(self.vb.s, 1)
        for b in range(8):
            pe.wait_ge(self.r_new.s, b + 1)
            for h in range(4):
                last = pe.matmul(ps[:, 0, 8 * h + b:8 * h + b + 1], self.r[:, b, h, :], p[:, O_RQ + h, SEQ + b:SEQ + b + 1],
                                 start=True, stop=True)
        last.then_inc(self.o.s, 1)

    def dve(self, dve):
        k, ps, p = self.k, self.k.ps, self.k.proj
        dve.wait_ge(self.here.s, 16)
        for b in range(8):
            dve.wait_ge(self.vb.s, b + 1)
            t = self.t[b % 2]
            k.dve_link(dve.tensor_tensor(t[:, :, :], blocks(ps[:, 4 + b % 4, :]),
                                         p[:, O_RK:O_RK + 4, SEQ + b:SEQ + b + 1].to_broadcast([P, 4, P]), ALU.mult))
            for h in range(4):
                ins = dve.scalar_tensor_tensor(self.r[:, b, h, :], self.r[:, b, h, :], RET_DECAY[h], t[:, h, :],
                                               ALU.mult, ALU.add)
            ins.then_inc(self.r_new.s, 1)
        dve.wait_ge(self.o.s, 1)
        dve.tensor_copy(p[:, O_RQ:O_RQ + 4, SEQ:TOK], ps[:, 0, 0:32].rearrange("p (h b) -> p h b", h=4))


class Center(Stage):

    def __init__(self, k, name, chunks):
        super().__init__(k)
        self.chunks = chunks
        self.mean, self.free = k.counter(f"{name}_mean"), k.counter(f"{name}_free")

    def pe(self, pe):
        for i, x in enumerate(self.chunks):
            for b, (c0, c1) in enumerate(HALVES):
                last = pe.matmul(self.k.ps[:, 2 * i + b, 0:HALF], self.k.c("ones"), x[:, c0:c1], start=True, stop=True)
            last.then_inc(self.mean.s, 1)

    def dve(self, dve):
        for i, x in enumerate(self.chunks):
            dve.wait_ge(self.mean.s, i + 1)
            dve.scalar_tensor_tensor(two(x), self.k.ps[:, 2 * i:2 * i + 2, 0:HALF], -1.0 / P, two(x), ALU.mult, ALU.add)


def ret_norm(k):
    k.small.reset(k.odd_kept)
    def apply(dve, u, rstd):
        x = k.proj[:, O_RQ + u, :]
        k.dve_link(dve.scalar_tensor_tensor(x, x, k.col(V_RETN + u), rstd, ALU.mult, ALU.mult))
        k.dve_link(dve.tensor_tensor(x, x, k.proj[:, O_RG + u, :], ALU.mult))
        return split_out(k, dve, k.y_hi[:, 8 + u, :], k.y_lo[:, 8 + u, :], x)
    return HeadNorm(k, "ret_norm", [[k.proj[:, O_RQ + u, :]] for u in range(4)], k.c("ones"), P, apply)


class SsdPrompt(Stage):

    def __init__(self, k):
        super().__init__(k)
        k.small.reset(k.odd_kept)
        k.mid.reset(12 * TOK * 4)
        self.l = [k.small(f"ssd_l{i}", [P, 16, P]) for i in range(2)]
        self.t = k.small("ssd_t", [P, 8, P])
        self.bt = [k.small(f"ssd_bt{i}", [P, 2 * P]) for i in range(2)]
        self.xdt = [k.mid(f"ssd_xdt{i}", [P, 16, 64]) for i in range(2)]
        self.xw = k.mid("ssd_xw", [P, 16, 64])
        k.ssd_state = k.mid("ssd_state", [P, 16, 64])
        (self.xturn, self.xdt_ready, self.b_c, self.bt_ready, self.seg, self.masked, self.l_ready, self.w_ready,
         self.y, self.y_later, self.y_read, self.added, self.state) = (k.counter(f"ssd_{n}") for n in (
             "x_turned", "xdt", "b_c", "bt", "seg", "masked", "l", "w", "y", "y_later", "y_read", "added", "state"))
        k.big.reset(O_RQ * TOK * 4)
        k.ssd_s = [k.big(f"ssd_s{b}", [P, 8, P]) for b in range(8)]

    def pe_exponents(self, pe, n, q):
        k, c = self.k, slice(n * P, n * P + P)
        if 4 * n + q >= 2:
            pe.wait_ge(self.masked.s, 4 * n + q - 1)
        for i in range(4):
            last = pe.matmul(k.ps[:, q % 2, i * P:i * P + P], k.onehot(4 * q + i, 16), k.cum[:, c], start=True, stop=True)
        last.then_inc(self.seg.s, 1)

    def pe_front(self, pe, n):
        k, ps, p, c = self.k, self.k.ps, self.k.proj, slice(n * P, n * P + P)
        self.pe_exponents(pe, n, 0)
        self.pe_exponents(pe, n, 1)
        if n >= 2:
            pe.wait_ge(self.state.s, n - 1)
        for j in range(8):
            last = pe.transpose(ps[:, 5 + j // 4, (j % 4) * P:(j % 4) * P + P], p[:, O_X + j, c], k.c("ident"))
        last.then_inc(self.xturn.s, 1)
        self.pe_exponents(pe, n, 2)
        self.pe_exponents(pe, n, 3)
        if n:
            pe.wait_ge(self.w_ready.s, n)
        for g in range(2):
            pe.transpose(ps[:, 7, g * P:g * P + P], p[:, O_B + g, c], k.c("ident"))
        for g in range(2):
            last = pe.matmul(ps[:, 7, (2 + g) * P:(3 + g) * P], p[:, O_B + g, c], p[:, O_C + g, c], start=True, stop=True)
        last.then_inc(self.b_c.s, 1)

    def pe_state(self, pe, n, a):
        k = self.k
        for j in range(4 * a, 4 * a + 4):
            last = pe.matmul(k.ps[:, 3, (j % 4) * P:(j % 4) * P + P], k.ssd_state[:, 2 * j:2 * j + 2, :],
                             k.proj[:, O_C + a, n * P:n * P + P], start=True, stop=True)
        return last

    def pe(self, pe):
        k, ps = self.k, self.k.ps
        self.pe_front(pe, 0)
        for n in range(NBLK):
            if n + 1 < NBLK:
                self.pe_front(pe, n + 1)
            pe.wait_ge(self.w_ready.s, n + 1)
            pe.wait_ge(self.bt_ready.s, n + 1)
            if n:
                pe.wait_ge(self.state.s, n)
            for h in range(16):
                j = h // 2
                last = pe.matmul(ps[64 * (h % 2):64 * (h % 2) + 64, 2 + 2 * (j // 4), (j % 4) * P:(j % 4) * P + P],
                                 self.xdt[n % 2][:, h, :], self.l[n % 2][:, h, :], start=True, stop=True)
            if n:
                last = self.pe_state(pe, n, 0)
            last.then_inc(self.y.s, 1)
            if n + 1 < NBLK:
                pe.wait_ge(self.xdt_ready.s, n + 2)
            for g in range(2):
                last = pe.matmul(ps[:, 5 + g, :], self.bt[n % 2][:, g * P:g * P + P], self.xw[:, 8 * g:8 * g + 8, :],
                                 start=True, stop=True)
            last.then_inc(self.added.s, 1)
            if n:
                pe.wait_ge(self.y_read.s, n)
                self.pe_state(pe, n, 1).then_inc(self.y_later.s, 1)

    def act(self, act):
        k, ps = self.k, self.k.ps
        for b in range(8):
            act.dma_start(k.ssd_s[b][:, :, :], k.A["state_ssd"][0, b].rearrange("(j t) p n -> (t p) j n", t=2))\
               .then_inc(k.ssd_here.s, 16)
        for n in range(NBLK):
            l = self.l[n % 2]
            act.wait_ge(self.b_c.s, n + 1)
            if n >= 2:
                act.wait_ge(self.added.s, n - 1)
            act.activation(self.bt[n % 2][:, :], ps[:, 7, 0:2 * P], ACT.Copy).then_inc(self.bt_ready.s, 1)
            for q in range(4):
                act.wait_ge(self.masked.s, 4 * n + q + 1)
                for h in range(4 * q, 4 * q + 4):
                    ins = act.activation(l[:, h, :], l[:, h, :], ACT.Exp, bias=k.ncum_col[:, n, h:h + 1])
                ins.then_inc(self.l_ready.s, 1)

    def dve_mask(self, dve, n, q):
        k = self.k
        dve.wait_ge(self.seg.s, 4 * n + q + 1)
        dve.tensor_tensor(self.l[n % 2][:, 4 * q:4 * q + 4, :], blocks(k.ps[:, q % 2, :]),
                          k.c("causal").unsqueeze(1).to_broadcast([P, 4, P]), ALU.add).then_inc(self.masked.s, 1)

    def dve_front(self, dve, n):
        k, ps = self.k, self.k.ps
        self.dve_mask(dve, n, 0)
        self.dve_mask(dve, n, 1)
        dve.wait_ge(self.xturn.s, n + 1)
        for g in range(2):
            ins = dve.tensor_tensor(self.xdt[n % 2][:, 8 * g:8 * g + 8, :],
                                    ps[:, 5 + g, :].rearrange("p (h d) -> p h d", h=8),
                                    k.dt_col[:, n, 8 * g:8 * g + 8].unsqueeze(2).to_broadcast([P, 8, 64]), ALU.mult)
        ins.then_inc(self.xdt_ready.s, 1)
        self.dve_mask(dve, n, 2)
        self.dve_mask(dve, n, 3)

    def dve_weights(self, dve, n):
        k, l, xdt = self.k, self.l[n % 2], self.xdt[n % 2]
        dve.wait_ge(self.l_ready.s, 4 * n + 4)
        dve.wait_ge(self.xdt_ready.s, n + 1)
        k.dve_link(dve.tensor_tensor(self.xw[:, :, :], xdt[:, :, :], l[:, :, P - 1:P].to_broadcast([P, 16, 64]),
                                     ALU.mult))
        for g in range(2):
            ins = dve.tensor_tensor(l[:, 8 * g:8 * g + 8, :], l[:, 8 * g:8 * g + 8, :],
                                    k.ps[:, 7, (2 + g) * P:(3 + g) * P].unsqueeze(1).to_broadcast([P, 8, P]), ALU.mult)
        ins.then_inc(self.w_ready.s, 1)

    def dve(self, dve):
        k, ps, p = self.k, self.k.ps, self.k.proj
        self.dve_front(dve, 0)
        for n in range(NBLK):
            c = slice(n * P, n * P + P)
            self.dve_weights(dve, n)
            if n + 1 < NBLK:
                self.dve_front(dve, n + 1)
            dve.wait_ge(self.y.s, n + 1)
            for a in range(2):
                t = self.t[:, 4 * a:4 * a + 4, :]
                if n:
                    if a:
                        dve.wait_ge(self.y_later.s, n)
                    ins = dve.tensor_tensor(t, blocks(ps[:, 3, :]), k.ec[:, 4 * a:4 * a + 4, c], ALU.mult)
                    if a == 0:
                        ins.then_inc(self.y_read.s, 1)
                        dve.wait_ge(self.y_read.s, n)
                    else:
                        k.dve_link(ins)
                    k.dve_link(dve.tensor_tensor(t, t, blocks(ps[:, 2 + 2 * a, :]), ALU.add))
                else:
                    k.dve_link(dve.tensor_copy(t, blocks(ps[:, 2 + 2 * a, :])))
                for j in range(4 * a, 4 * a + 4):
                    x = p[:, O_X + j, c]
                    dve.scalar_tensor_tensor(x, x, k.d_pair[:, j:j + 1], self.t[:, j, :], ALU.mult, ALU.add)
            if n:
                k.dve_link(dve.tensor_tensor(k.ssd_state[:, :, :], k.ssd_state[:, :, :],
                                             k.dec[:, n, :].unsqueeze(2).to_broadcast([P, 16, 64]), ALU.mult))
            dve.wait_ge(self.added.s, n + 1)
            for g in range(2):
                s, q = k.ssd_state[:, 8 * g:8 * g + 8, :], ps[:, 5 + g, :].rearrange("p (h d) -> p h d", h=8)
                ins = dve.tensor_tensor(s, s, q, ALU.add) if n else dve.tensor_copy(s, q)
            ins.then_inc(self.state.s, 1)
            dve.wait_ge(self.state.s, n + 1)


class SsdTurn(Turn):

    def __init__(self, k):
        k.small.reset(k.odd_kept)
        self.out = k.small("ssd_out", [P, 8, P])
        k.bc_s = k.small("ssd_bc_s", [8, 512])
        k.ssd_kept = k.small.at
        items = [([(k.ssd_state[:, 2 * j:2 * j + 2, :].rearrange("p a b -> p (a b)"), (j - 4 * a) * P)
                   for j in range(4 * a, 4 * a + 4)], lambda b: blocks(b[:, 0:512]), self.out[:, 4 * a:4 * a + 4, :])
                 for a in range(2)]
        items.append(([(k.proj[:, O_B + i, SEQ:TOK], i * P) for i in range(4)], lambda b: b[0:8, 0:512], k.bc_s[:, :]))
        super().__init__(k, "ssd_turn", items)

    def act(self, act):
        k = self.k
        super().act(act)
        act.wait_ge(self.free.s, self.base + len(self.items))
        k.store(k.O["p_ssd"][0, 0].rearrange("(j t) p n -> (t p) j n", t=2), self.out[:, :, :])


class SsdSample(Stage):

    def __init__(self, k):
        super().__init__(k)
        k.small.reset(k.ssd_kept)
        self.xdt, self.y = k.small("ssds_xdt", [P, 8, 8]), k.small("ssds_y", [P, 8, 8])
        k.mid.reset(12 * TOK * 4)
        self.t = [k.mid(f"ssds_t{i}", [P, 8, P]) for i in range(2)]
        self.u = [k.mid(f"ssds_u{i}", [P, 8, P]) for i in range(2)]
        self.bc, self.scaled, self.s_new, self.free = (k.counter(f"ssds_{n}") for n in ("bc", "scaled", "s_new", "bc_free"))

    def act(self, act):
        k = self.k
        act.wait_ge(k.ssd_here.s, 128)
        for b in range(8):
            for j in range(8):
                ins = act.activation(k.ssd_s[b][:, j, :], k.ssd_s[b][:, j, :], ACT.Copy,
                                     scale=k.ec[:, j, SEQ + b:SEQ + b + 1])
            ins.then_inc(self.scaled.s, 1)
        for b in range(8):
            act.wait_ge(self.s_new.s, b + 1)
            k.store(k.O["s_ssd"][0, b].rearrange("(j t) p n -> (t p) j n", t=2), k.ssd_s[b][:, :, :])

    def pe(self, pe):
        k, ps = self.k, self.k.ps
        for b in range(8):
            if b >= 4:
                pe.wait_ge(self.free.s, b - 3)
            pe.matmul(ps[:, b % 4, :], k.onehot(b, 8), k.bc_s[:, :], start=True, stop=True).then_inc(self.bc.s, 1)

    def dve(self, dve):
        k, ps, p = self.k, self.k.ps, self.k.proj
        s = slice(SEQ, TOK)
        x = p[:, O_X:O_X + 8, s]
        k.dve_link(dve.tensor_tensor(self.xdt[:, :, :], x, k.dt_pair[:, :, :], ALU.mult))
        four = lambda t: t.rearrange("p (g j) n -> p g j n", g=2)
        for b in range(8):
            row = lambda i: ps[:, b % 4, 256 * i:256 * i + 256].rearrange("p (g n) -> p g n", g=2).unsqueeze(2)\
                .to_broadcast([P, 2, 4, P])
            t, u, st = self.t[b % 2][:, :, :], self.u[b % 2][:, :, :], k.ssd_s[b][:, :, :]
            dve.wait_ge(self.bc.s, b + 1)
            k.dve_link(dve.tensor_tensor(four(t), row(0),
                                         four(self.xdt[:, :, b:b + 1].to_broadcast([P, 8, P])), ALU.mult))
            dve.wait_ge(self.scaled.s, b + 1)
            dve.tensor_tensor(st, st, t, ALU.add).then_inc(self.s_new.s, 1)
            dve.wait_ge(self.s_new.s, b + 1)
            dve.tensor_tensor(four(u), four(st), row(1), ALU.mult).then_inc(self.free.s, 1)
            dve.wait_ge(self.free.s, b + 1)
            ins = dve.tensor_reduce(self.y[:, :, b:b + 1], u, AX.X, ALU.add)
        k.dve_link(ins)
        k.dve_link(dve.tensor_tensor(self.xdt[:, :, :], x, k.d_pair[:, :].unsqueeze(2).to_broadcast([P, 8, 8]), ALU.mult))
        dve.tensor_tensor(x, self.xdt[:, :, :], self.y[:, :, :], ALU.add)


class SsdGate(Stage):

    def dve(self, dve):
        p = self.k.proj
        dve.tensor_tensor(p[:, O_X:O_X + 8, :], p[:, O_X:O_X + 8, :], p[:, O_Z:O_Z + 8, :], ALU.mult)


def ssd_norm(k):
    k.small.reset(k.ssd_kept)
    def apply(dve, u, rstd):
        for j in range(4 * u, 4 * u + 4):
            x = k.proj[:, O_X + j, :]
            k.dve_link(dve.scalar_tensor_tensor(x, x, k.col(V_SSDN + j), rstd, ALU.mult, ALU.mult))
            last = split_out(k, dve, k.y_hi[:, j, :], k.y_lo[:, j, :], x)
        return last
    return HeadNorm(k, "ssd_norm", [[k.proj[:, O_X + 4 * u + j, :] for j in range(4)] for u in range(2)], k.c("ones"),
                    512, apply)


class OddStored(Stage):

    def act(self, act):
        self.k.stores_done()


def odd_layer(k):
    s = [ConvHistory(k), odd_projection(k), ConvTurn(k), odd_spread(k)]
    k.small.reset(k.odd_kept)
    kept = k.odd_kept
    rope = Rope(k, "odd_rope", [k.proj[:, c, :] for c in range(O_RQ, O_RV)], ODD, kept)
    s += [rope, ret_turn(k), RetPrompt(k), RetSample(k), Center(k, "ret", [k.proj[:, O_RQ + h, :] for h in range(4)]),
          ret_norm(k), SsdPrompt(k), SsdTurn(k), SsdSample(k), SsdGate(k), ssd_norm(k), OddStored(k)]
    w = k.A["odd_w_out"][0]
    k.small.reset()
    s.append(Gemm(k, [gemm_tile(w, [(m * P, P)], (k.y_hi, k.y_lo), out_residual(k, m), nk=6, k0=6 * i,
                                **({"finish": m} if i else {})) for i in range(2) for m in range(DC)],
                  next_norm(k, "odd_out", V_XATT + DC, k.xc)))
    return s


def plan(k):
    stages = [Load(k)]
    for layer, mixer in enumerate((even_layer, odd_layer)):
        stages += mixer(k) + cross_layer(k, layer)
        if layer == 0:
            stages.append(OddLoads(k))
        stages.append(Ffn(k, layer))
    return stages + [Emit(k)]


class Emit(Stage):

    def __init__(self, k):
        super().__init__(k)
        k.big.reset()
        self.y = k.big("y_tok", [P, NBLK, D_MODEL])
        self.ys = k.big("ys_tok", [NSAMPLE, D_MODEL])
        items = []
        for n in range(NBLK):
            for g in range(2):
                items.append(([(k.x[:, 4 * g + c, n * P:n * P + P], c * P) for c in range(4)],
                              lambda b: b[:, 0:512], self.y[:, n, 512 * g:512 * g + 512]))
        for g in range(2):
            items.append(([(k.x[:, 4 * g + c, SEQ:TOK], c * P) for c in range(4)],
                          lambda b: b[0:8, 0:512], self.ys[:, 512 * g:512 * g + 512]))
        self.turn = Turn(k, "emit", items)

    def pe(self, pe): self.turn.pe(pe)
    def dve(self, dve): self.turn.dve(dve)

    def act(self, act):
        k = self.k
        self.turn.act(act)
        act.wait_ge(self.turn.free.s, self.turn.base + len(self.turn.items))
        k.store(k.O["y_prompt"].rearrange("b (n p) d -> p (b n) d", p=P), self.y[:, :, :])
        k.store(k.O["y_sample"].rearrange("b t d -> (b t) d"), self.ys[:, :])


def program(nc, A, C, O):
    with ExitStack() as ctx:
        k = Core(nc, ctx, A, C, O)
        k.gate_i, k.gate_f = k.params("gate_i", [4, 1]), k.params("gate_f", [4, 1])
        k.dt_bias, k.a_log, k.d_skip = (k.params(n, [16, 1]) for n in ("dt_bias", "a_log", "d_skip"))
        k.sink_row, k.sink_col = k.params("sink_row", [P, 8]), k.params("sink_col", [64, 1])
        k.norm_signals = [k.counter(n) for n in ("squares_ready", "squares_summed", "rstd_ready", "rstd_used")]
        k.norm_count = (0, 0)
        k.turn_signals, k.turn_count = (k.counter("turned"), k.counter("turn_copied")), 0
        k.spread_signals, k.spread_count = (k.counter("spread"), k.counter("spread_free")), 0
        k.ssd_here, k.odd_here = k.counter("ssd_states_here"), k.counter("odd_constants_here")
        k.mem_here, k.cache_here = k.counter("memory_here"), k.counter("memory_cache_here")
        k.mem_signals = [k.counter(f"mem_{n}") for n in ("turned", "split", "squared", "summed")]
        k.xa_signals = [k.counter(f"xa_{n}") for n in ("scores", "max", "exps", "probs", "turned", "pt", "pv", "out")]
        k.xs_signals = [k.counter(f"xs_{n}") for n in ("k_turned", "kt", "q", "scored", "scores", "max", "exps", "probs",
                                                      "p_turned", "pt", "pv", "o", "o_turned")]
        k.ffn_signals = [k.counter(n) for n in ("relu_ready", "squared", "hidden_ready")]
        stages = plan(k)
        count = [0] * RING
        k.arrivals = []
        for n, t in enumerate(k.tiles):
            count[n % RING] += len(t["parts"])
            k.arrivals.append(count[n % RING])
        block = ctx.enter_context(nc.Block())

        @block.sync
        def _(sp):
            stream_weights(k, sp)

        @block.gpsimd
        def _(pool):
            split_low(k, pool)

        @block.tensor
        def _(pe):
            for s in stages:
                s.pe(pe)
                k.fence(pe, "pe")

        @block.vector
        def _(dve):
            for s in stages:
                s.dve(dve)
                k.fence(dve, "dve")

        @block.scalar
        def _(act):
            for s in stages:
                s.act(act)
                k.fence(act, "act")
            k.stores_done()


OUTPUTS = [
    ("y_prompt", (1, SEQ, D_MODEL)), ("y_sample", (8, 1, D_MODEL)),
    ("mem_k", (2, 1, MEM, 4, P)), ("mem_v", (2, 1, MEM, 4, P)),
    ("p_swa_k", (1, 1, P, 2, 64)), ("p_swa_v", (1, 1, P, 2, 64)),
    ("p_C", (1, 1, 4, 64, P)), ("p_n", (1, 1, 4, 64)), ("p_m", (1, 1, 4)),
    ("p_conv", (1, 1, 3, 1536)), ("p_ssd", (1, 1, 16, 64, P)), ("p_ret", (1, 1, 4, P, P)),
    ("s_swa_k", (1, 8, P, 2, 64)), ("s_swa_v", (1, 8, P, 2, 64)),
    ("s_C", (1, 8, 4, 64, P)), ("s_n", (1, 8, 4, 64)), ("s_m", (1, 8, 4)),
    ("s_conv", (1, 8, 3, 1536)), ("s_ssd", (1, 8, 16, 64, P)), ("s_ret", (1, 8, 4, P, P)),
]


def kernel(**inputs):
    import concourse.bacc as bacc
    from concourse.bass_utils import run_bass_kernel_spmd

    nc = bacc.Bacc("TRN2", target_bir_lowering=False, num_devices=1)
    arrays, A, O = {}, {}, {}
    for name, a in inputs.items():
        a = np.ascontiguousarray(a)
        arrays[f"in_{name}"] = a
        A[name] = nc.dram_tensor(f"in_{name}", a.shape, mybir.dt.from_np(a.dtype), kind="ExternalInput").ap()
    arrays["shape_constants"] = shape_constants()
    C = nc.dram_tensor("shape_constants", arrays["shape_constants"].shape, F32, kind="ExternalInput").ap()
    for name, shape in OUTPUTS:
        O[name] = nc.dram_tensor(f"out_{name}", shape, F32, kind="ExternalOutput").ap()
    program(nc, A, C, O)
    r = run_bass_kernel_spmd(nc, [arrays], core_ids=[0])
    return tuple(r.results[0][f"out_{name}"] for name, _ in OUTPUTS)
```

```python
import math
from contextlib import ExitStack

import numpy as np

import concourse.bass as bass
from concourse import mybir

F32 = mybir.dt.float32
F32R = mybir.dt.float32r
ALU = mybir.AluOpType
ACT = mybir.ActivationFunctionType
AX = mybir.AxisListType

P = 128
D_MODEL, SEQ, NSAMPLE, PAST = 1024, 512, 8, 1024
TOK = SEQ + NSAMPLE
HALF = TOK // 2
DC = D_MODEL // P
NBLK = SEQ // P
MEM = 256
FFN = 4 * D_MODEL
EPS = 1e-6
NEG = -1e30
RING = 2

E_SQ, E_SK, E_SV, E_MQ, E_MK, E_MV, E_MO, E_GI, E_GF = 0, 4, 5, 6, 8, 10, 14, 18, 19
O_Z, O_X, O_B, O_C, O_DT, O_RQ, O_RK, O_RV, O_RG = 0, 8, 16, 18, 20, 21, 25, 29, 33
NPROJ = 37

V_MIX, V_XATT, V_MEM, V_FFN, V_MLN, V_SSDN, V_RETN, V_CB = 0, 16, 32, 48, 64, 68, 76, 80
V_CW, V_QN, V_KN, V_SQ, V_SK = 92, 140, 142, 144, 145


def layout(parts):
    at, out = 0, {}
    for name, n in parts:
        out[name] = (at, n)
        at += n
    return out, at


COMMON, NCOMMON = layout([("ident", P), ("ones", P), ("blk64", P), ("causal", P), ("own_head", 4), ("eps", 1)])
EVEN, NEVEN = layout([("rot", P), ("mask_first", 2 * P), ("mask_later", 2 * P), ("cos", TOK), ("sin", TOK)])
ODD, NODD = layout([("rot", P), ("cos", TOK), ("sin", TOK), ("decay", 4 * P), ("qscale", 4 * P), ("kscale", 4)])
NLAYER = max(NEVEN, NODD)


def shape_constants():
    p = np.arange(P)
    pos = np.concatenate([np.arange(SEQ), PAST + np.zeros(NSAMPLE)]).astype(np.float32)

    def rope(rot_dim, head, theta):
        half = rot_dim // 2
        inv = np.power(np.float32(theta), -np.arange(half, dtype=np.float32) * np.float32(2.0 / rot_dim))
        ang = (pos[None, :] * inv[:, None]).astype(np.float32)
        cos, sin, rot = np.ones((P, TOK)), np.zeros((P, TOK)), np.zeros((P, P))
        for at in range(0, P, head):
            for part in range(2):
                rows = at + part * half + np.arange(half)
                cos[rows], sin[rows] = np.cos(ang), np.sin(ang)
            for i in range(half):
                rot[at + i + half, at + i] = -1.0
                rot[at + i, at + i + half] = 1.0
        return cos, sin, rot

    c = {"ident": np.eye(P), "ones": np.ones((P, P)), "blk64": np.kron(np.eye(2), np.ones((64, 64))),
         "causal": np.where(p[:, None] <= p[None, :], 0.0, NEG),
         "own_head": np.tile(np.eye(4), (P // 4, 1)), "eps": np.full((P, 1), EPS)}
    e, o = {}, {}
    e["cos"], e["sin"], e["rot"] = rope(16, 64, 500000.0)
    k = np.arange(2 * P)
    e["mask_first"] = np.where(p[:, None] >= k[None, :], 0.0, NEG)
    diff = P + p[:, None] - k[None, :]
    e["mask_later"] = np.where((diff >= 0) & (diff <= P), 0.0, NEG)
    o["cos"], o["sin"], o["rot"] = rope(128, 128, 10000.0)
    lg = np.log(1.0 - np.exp2(-5.0 - np.arange(4)))
    d = p[None, :] - p[:, None]
    o["decay"] = np.concatenate([np.where(d >= 0, np.exp(np.maximum(d, 0) * g), 0.0) for g in lg], axis=1)
    o["qscale"] = np.concatenate([np.tile(np.exp((p + 1.0) * g), (P, 1)) for g in lg], axis=1)
    o["kscale"] = np.exp((P - 1.0 - p)[:, None] * lg[None, :])
    out = np.zeros((P, NCOMMON + NEVEN + NODD), np.float32)
    for table, at, vals in ((COMMON, 0, c), (EVEN, NCOMMON, e), (ODD, NCOMMON + NEVEN, o)):
        for name, (a, n) in table.items():
            out[:, at + a:at + a + n] = vals[name]
    return out


RET_DECAY = [float(1.0 - 2.0 ** (-5.0 - h)) for h in range(4)]
RET_CHUNK_DECAY = [float(np.exp(P * np.log(1.0 - 2.0 ** (-5.0 - h)))) for h in range(4)]


class Signal:

    def __init__(self, s):
        self.s, self.seen = s, {}

    def next(self, reader, n=1):
        self.seen[reader] = self.seen.get(reader, 0) + n
        return self.seen[reader]


class Region:

    def __init__(self, nc, base, size):
        self.nc, self.base, self.size, self.at = nc, base, size, 0

    def reset(self, at=0):
        self.at = at

    def __call__(self, name, shape, dt=F32):
        n = 4 * int(np.prod(shape[1:]))
        n = -(-n // 32) * 32
        assert self.at + n <= self.size, (name, self.at, n, self.size)
        t = self.nc.alloc_sbuf_tensor_at(name, shape, dt, offset=self.base + self.at)
        self.at += n
        return t


class Core:

    def __init__(self, nc, ctx, A, C, O):
        self.nc, self.ctx, self.A, self.C, self.O = nc, ctx, A, C, O
        self.n_semaphores = 0
        size = 212800
        arena = ctx.enter_context(nc.sbuf_tensor("arena", [P, size // 4], F32))
        base = size_of_base(nc, arena, size)
        whole = Region(nc, base, size)
        self.x = whole("x", [P, DC, TOK])
        self.w_raw = [whole(f"w_raw{i}", [P, DC, P]) for i in range(RING)]
        self.w_hi = [whole(f"w_hi{i}", [P, DC, P], F32R) for i in range(RING)]
        self.w_lo = [whole(f"w_lo{i}", [P, DC, P], F32R) for i in range(RING)]
        self.const = whole("const", [P, NCOMMON])
        self.lconst = whole("lconst", [P, NLAYER])
        self.vcol = whole("vcol", [P, V_SK + 1])
        self.params = Region(nc, base + whole.at, 256 + 64)
        whole.at += 320
        self.rstd = whole("rstd", [P, TOK])
        self.mem_rstd = whole("mem_rstd", [P, MEM])
        at = whole.at
        self.big = Region(nc, base + at, NPROJ * TOK * 4)
        whole.at += NPROJ * TOK * 4
        at = whole.at
        self.mid = Region(nc, base + at, 24 * TOK * 4)
        whole.at += 24 * TOK * 4
        self.small = Region(nc, base + whole.at, size - whole.at)
        self.proj = self.big("proj", [P, NPROJ, TOK])
        self.big.reset()
        self.hid_hi = [self.big(f"hid_hi{i}", [P, DC, TOK], F32R) for i in range(2)]
        self.hid_lo = [self.big(f"hid_lo{i}", [P, DC, TOK], F32R) for i in range(2)]
        self.big.reset(self.big.size - 2 * DC * TOK * 4)
        self.xn = tuple(self.mid(f"xn_{n}", [P, DC, TOK], F32R) for n in ("hi", "lo"))
        self.xc = tuple(self.big(f"xc_{n}", [P, DC, TOK], F32R) for n in ("hi", "lo"))
        self.xa_hi, self.xa_lo = (self.mid(f"xa_{n}", [P, 4, TOK], F32R) for n in ("hi", "lo"))
        self.mid.reset()
        self.y_hi = self.mid("y_hi", [P, 12, TOK], F32R)
        self.y_lo = self.mid("y_lo", [P, 12, TOK], F32R)
        self.ps = ctx.enter_context(nc.psum_tensor("banks", [P, 8, 512], F32))
        self.w_here = [self.counter(f"weight_arrived{i}") for i in range(RING)]
        self.w_hi_ready = self.counter("weight_high_ready")
        self.w_lo_ready = self.counter("weight_low_ready")
        self.tile_done = self.counter("gemm_tile_done")
        self.tile_out = self.counter("gemm_bank_free")
        self.square_ready, self.square_summed = self.counter("square_ready"), self.counter("square_summed")
        self.rstd_done, self.n_squares = self.counter("rstd_done"), 0
        self.end = {e: self.counter(f"stage_end_{e}") for e in ("pe", "dve", "act")}
        self.dve_step, self.act_step = self.counter("dve_step"), self.counter("act_step")
        self.stored = self.counter("stored")
        self.n_stored = 0
        self.state_stored, self.n_state_stored = self.counter("state_stored"), 0
        self.n_tiles = 0
        self.tiles = []

    def counter(self, name):
        self.n_semaphores += 1
        return Signal(self.ctx.enter_context(self.nc.semaphore(name)))

    def c(self, name, rows=P):
        a, n = COMMON[name]
        return self.const[0:rows, a:a + n]

    def lc(self, table, name):
        a, n = table[name]
        return self.lconst[:, a:a + n]

    def col(self, v):
        return self.vcol[:, v:v + 1]

    def pair(self, j, rows, cols, rhs):
        return [(cols, self.const[0:rows, 2 * j + t:2 * j + t + 1].to_broadcast([rows, 64]), rhs, 64 * t)
                for t in range(2)]

    def spread_split(self, pe, out, h, rows, parts):
        sel = self.ident_r[0:rows, h:h + 1].to_broadcast([rows, P])
        pe.matmul(out, sel, parts[0], start=True, stop=False)
        return pe.matmul(out, sel, parts[1], start=False, stop=True)

    def onehot(self, h, rows):
        return self.const[0:rows, h:h + 1].to_broadcast([rows, P])

    def dve_link(self, ins):
        ins.then_inc(self.dve_step.s, 1)
        self.nc.vector.wait_ge(self.dve_step.s, self.dve_step.next("dve"))

    def act_link(self, ins):
        ins.then_inc(self.act_step.s, 1)
        self.nc.scalar.wait_ge(self.act_step.s, self.act_step.next("act"))

    def fence(self, eng, me):
        eng.drain().then_inc(self.end[me].s, 1)
        for other in ("pe", "dve", "act"):
            eng.wait_ge(self.end[other].s, self.end[other].next(me))

    def store(self, out, in_, few=False):
        self.nc.scalar.dma_start(out, in_, allow_slow_non_contiguous=few).then_inc(self.stored.s, 16)
        self.n_stored += 1

    def store_state(self, out, in_):
        self.nc.scalar.dma_start(out, in_).then_inc(self.state_stored.s, 16)
        self.n_state_stored += 1

    def state_stores_done(self):
        self.nc.scalar.wait_ge(self.state_stored.s, 16 * self.n_state_stored)

    def stores_done(self):
        self.nc.scalar.wait_ge(self.stored.s, 16 * self.n_stored)


def size_of_base(nc, arena, size):
    lo = nc.sbuf_usable_end - nc.sbuf_base
    base = -(-(nc.sbuf_base - size) // 32) * 32
    assert base >= 0 and lo >= 0
    return base


class Stage:
    def __init__(self, k):
        self.k = k

    def pe(self, pe): pass
    def dve(self, dve): pass
    def act(self, act): pass


class NextNorm:

    def __init__(self, k, gain, dst, sq):
        self.k, self.gain, self.dst, self.sq = k, gain, dst, sq
        self.first = k.n_squares
        k.n_squares += DC

    def dve(self, dve, c):
        k, x, g = self.k, self.k.x[:, c, :], self.k.col(self.gain + c)
        hi, lo = self.dst[0][:, c, :], self.dst[1][:, c, :]
        k.dve_link(dve.tensor_scalar(hi, x, g, None, ALU.mult))
        dve.scalar_tensor_tensor(lo, x, g, hi.bitcast(F32), ALU.mult, ALU.subtract)

    def act(self, act, c):
        k = self.k
        if c >= 2:
            act.wait_ge(k.square_summed.s, self.first + c - 1)
        act.activation(self.sq[c % 2][:, :], k.x[:, c, :], ACT.Square).then_inc(k.square_ready.s, 1)

    def pe(self, pe, c):
        k = self.k
        pe.wait_ge(k.square_ready.s, self.first + c + 1)
        for b, (c0, c1) in enumerate(HALVES):
            last = pe.matmul(k.ps[:, 6 + b, 0:HALF], k.c("ones"), self.sq[c % 2][:, c0:c1],
                             start=c == 0, stop=c == DC - 1)
        last.then_inc(k.square_summed.s, 1)

    def act_rstd(self, act):
        k = self.k
        act.wait_ge(k.square_summed.s, self.first + DC)
        k.act_link(act.activation(two(k.rstd[:, :]), k.ps[:, 6:8, 0:HALF], ACT.Ln, scale=1.0 / D_MODEL,
                                  bias=k.c("eps")))
        act.activation(k.rstd[:, :], k.rstd[:, :], ACT.Exp, scale=-0.5)


def next_norm(k, name, gain, dst):
    return NextNorm(k, gain, dst, [k.small(f"{name}_sq{i}", [P, TOK]) for i in range(2)])


class Gemm(Stage):

    def __init__(self, k, tiles, norm=None):
        super().__init__(k)
        self.norm = norm
        self.base = len(k.tiles)
        self.mine = tiles
        k.tiles += tiles

    def pe(self, pe):
        k, ps = self.k, self.k.ps
        for i, t in enumerate(self.mine):
            n = self.base + i
            if "pe_before" in t:
                t["pe_before"](pe)
            pe.wait_ge(k.w_hi_ready.s, n + 1)
            pe.wait_ge(k.w_lo_ready.s, n + 1)
            if n >= 3:
                pe.wait_ge(k.tile_out.s, n - 2)
            if "rhs_ready" in t:
                sig, count = t["rhs_ready"]
                pe.wait_ge(sig.s, count)
            hi, lo = k.w_hi[n % RING], k.w_lo[n % RING]
            rh, rl = t["rhs"]
            m, nk = t["m"], t["nk"]
            last = None
            for kk in range(nk):
                for b, (c0, c1) in enumerate(t["halves"]):
                    out = ps[0:m, 2 * (n % 3) + b, 0:c1 - c0]
                    r, q = rh[:, t["k0"] + kk, c0:c1], rl[:, t["k0"] + kk, c0:c1]
                    pe.matmul(out, hi[:, kk, 0:m], r, start=kk == 0, stop=False)
                    pe.matmul(out, hi[:, kk, 0:m], q, start=False, stop=False)
                    last = pe.matmul(out, lo[:, kk, 0:m], r, start=False, stop=kk == nk - 1)
            last.then_inc(k.tile_done.s, 1)
            if i and "finish" in self.mine[i - 1]:
                self.norm.pe(pe, self.mine[i - 1]["finish"])
        if "finish" in t:
            self.norm.pe(pe, t["finish"])

    def dve(self, dve):
        k, ps = self.k, self.k.ps
        for i, t in enumerate(self.mine):
            n = self.base + i
            dve.wait_ge(k.tile_done.s, n + 1)
            w = t["halves"][0][1] - t["halves"][0][0]
            nb = len(t["halves"])
            src = ps[0:t["m"], 2 * (n % 3):2 * (n % 3) + nb, 0:w]
            t["out"](dve, src, nb)
            dve.wait_ge(k.tile_out.s, n + 1)
            for step in t.get("dve_after", ()):
                step(dve, n)
            if "finish" in t:
                self.norm.dve(dve, t["finish"])

    def act(self, act):
        k = self.k
        for i, t in enumerate(self.mine):
            n = self.base + i
            if n + RING < len(k.tiles):
                act.wait_ge(k.tile_done.s, n + 1)
                split_high(k, act, n + RING)
            if "finish" in t:
                act.wait_ge(k.tile_out.s, n + 1)
                self.norm.act(act, t["finish"])
            for step in t.get("act_after", ()):
                step(act, n)
        if "finish" in t:
            self.norm.act_rstd(act)


def split_high(k, act, n):
    t = k.tiles[n]
    act.wait_ge(k.w_here[n % RING].s, 16 * k.arrivals[n])
    act.activation(k.w_hi[n % RING][:, 0:t["nk"], 0:t["m"]], k.w_raw[n % RING][:, 0:t["nk"], 0:t["m"]],
                   ACT.Copy).then_inc(k.w_hi_ready.s, 1)


def split_low(k, pool):
    for n, t in enumerate(k.tiles):
        pool.wait_ge(k.w_hi_ready.s, n + 1)
        if n >= RING:
            pool.wait_ge(k.tile_done.s, n - RING + 1)
        view = slice(0, t["nk"]), slice(0, t["m"])
        pool.tensor_tensor(k.w_lo[n % RING][:, view[0], view[1]], k.w_raw[n % RING][:, view[0], view[1]],
                           k.w_hi[n % RING][:, view[0], view[1]].bitcast(F32),
                           ALU.subtract).then_inc(k.w_lo_ready.s, 1)


def stream_weights(k, sp, load):
    for n, t in enumerate(k.tiles):
        if n == RING:
            load.sp(sp)
        if n >= RING:
            sp.wait_ge(k.w_lo_ready.s, n - RING + 1)
        for (p0, p1), (k0, k1), (c0, c1), src in t["parts"]:
            sp.dma_start(k.w_raw[n % RING][p0:p1, k0:k1, c0:c1], src).then_inc(k.w_here[n % RING].s, 16)


def weight_parts(w, k0, nk, pieces):
    v = w.rearrange("(k p) n -> p k n", p=P)
    out, at = [], 0
    for c, n in pieces:
        out.append(((0, P), (0, nk), (at, at + n), v[:, k0:k0 + nk, c:c + n]))
        at += n
    return out, at


HALVES = [(0, HALF), (HALF, TOK)]


def two(ap):
    return ap.rearrange("p (a b) -> p a b", a=2)


def gemm_tile(w, pieces, rhs, out, k0=0, nk=DC, halves=HALVES, row0=None, **more):
    parts, m = weight_parts(w, k0 if row0 is None else row0, nk, pieces)
    return dict(parts=parts, m=m, nk=nk, k0=k0, rhs=rhs, halves=halves, out=out, **more)


def out_copy(k, dst, scale=None):
    def emit(dve, src, nb):
        d = two(dst) if nb == 2 else dst.unsqueeze(1)
        m = dst.shape[0]
        r = two(k.rstd[0:m, :]) if nb == 2 else k.mem_rstd[0:m, :].unsqueeze(1)
        if scale is None:
            dve.tensor_tensor(d, src, r, ALU.mult).then_inc(k.tile_out.s, 1)
        else:
            dve.scalar_tensor_tensor(d, src, scale, r, ALU.mult, ALU.mult).then_inc(k.tile_out.s, 1)
    return emit


def out_residual(k, m):
    def emit(dve, src, nb):
        d = two(k.x[:, m, :])
        dve.tensor_tensor(d, src, d, ALU.add).then_inc(k.tile_out.s, 1)
    return emit


def follow(tiles, i, dve=None, act=None):
    for key, step in (("dve_after", dve), ("act_after", act)):
        if step:
            tiles[i].setdefault(key, []).append(step)


class HeadNorm(Stage):

    def __init__(self, k, name, units, mask, features, apply, width=TOK, region=None):
        super().__init__(k)
        self.units, self.mask, self.features, self.apply, self.width = units, mask, features, apply, width
        region = region or k.small
        self.sq = [region(f"{name}_sq{i}", [P, width]) for i in range(2)]
        self.rstd = [region(f"{name}_rstd{i}", [P, width]) for i in range(2)]
        s = k.norm_signals
        self.sq_ready, self.summed, self.rstd_ready, self.rstd_used = s
        self.halves = HALVES if width == TOK else [(0, width)]
        self.first, self.first_unit = k.norm_count
        k.norm_count = (self.first + sum(len(c) for c in units), self.first_unit + len(units))

    def banks(self, u, rows=P):
        w = self.halves[0][1]
        return self.k.ps[:, 2 * (u % 2):2 * (u % 2) + len(self.halves), 0:w]

    def pe(self, pe):
        n = 0
        for u, chunks in enumerate(self.units):
            if u >= 2:
                pe.wait_ge(self.rstd_used.s, self.first_unit + u - 1)
            for i, _ in enumerate(chunks):
                pe.wait_ge(self.sq_ready.s, self.first + n + 1)
                for b, (c0, c1) in enumerate(self.halves):
                    last = pe.matmul(self.k.ps[:, 2 * (u % 2) + b, 0:c1 - c0], self.mask,
                                     self.sq[n % 2][:, c0:c1],
                                     start=i == 0, stop=i == len(chunks) - 1)
                last.then_inc(self.summed.s, 1)
                n += 1

    def squares(self, act, u):
        for src in self.units[u]:
            n = self.sent
            if n >= 2:
                act.wait_ge(self.summed.s, self.first + n - 1)
            act.activation(self.sq[n % 2][:, 0:self.width], src, ACT.Square).then_inc(self.sq_ready.s, 1)
            self.sent += 1

    def act(self, act):
        k = self.k
        self.sent = 0
        nb, w = len(self.halves), self.halves[0][1]
        self.squares(act, 0)
        for u, chunks in enumerate(self.units):
            if u + 1 < len(self.units):
                self.squares(act, u + 1)
            act.wait_ge(self.summed.s, self.first + sum(len(c) for c in self.units[:u + 1]))
            if u >= 2:
                act.wait_ge(self.rstd_used.s, self.first_unit + u - 1)
            rstd = self.rstd[u % 2][:, 0:self.width]
            ln = rstd.rearrange("p (a b) -> p a b", a=nb)
            k.act_link(act.activation(ln, self.banks(u), ACT.Ln, scale=1.0 / self.features, bias=k.c("eps")))
            act.activation(rstd, rstd, ACT.Exp, scale=-0.5).then_inc(self.rstd_ready.s, 1)

    def dve(self, dve):
        for u in range(len(self.units)):
            dve.wait_ge(self.rstd_ready.s, self.first_unit + u + 1)
            last = self.apply(dve, u, self.rstd[u % 2][:, 0:self.width])
            last.then_inc(self.rstd_used.s, 1)


class Load(Stage):

    def __init__(self, k):
        super().__init__(k)
        r = k.big
        r.reset()
        self.xtok = r("xtok", [P, NBLK, D_MODEL])
        self.xs = r("xs", [NSAMPLE, D_MODEL])
        self.rows = [r("param_rows0", [P, P]), r("param_rows1", [P, P])]
        k.small.reset()
        self.norm = next_norm(k, "load", V_MIX, k.xn)
        self.here, self.done, self.out = k.counter("inputs_here"), k.counter("in_transposed"), k.counter("in_free")
        self.late_here, self.vectors = k.counter("late_inputs_here"), k.counter("vectors_turned")
        A = k.A
        self.first = [(k.const[:, :], k.C[:, 0:NCOMMON]),
                      (self.xtok[:, :, :], A["x_prompt"].rearrange("b (n p) d -> p (b n) d", p=P)),
                      (self.xs[:, :], A["x_sample"].rearrange("b t d -> (b t) d")),
                      (self.rows[0][0:16, :], A["norm_mix"].rearrange("l (c p) -> (l c) p", p=P))]
        self.loads = [(k.lconst[:, 0:NEVEN], k.C[:, NCOMMON:NCOMMON + NEVEN])]
        at = 16
        for name, n in (("norm_xattn", 16), ("norm_mem", 16), ("norm_ffn", 16),
                        ("mlstm_out_norm", 4), ("ssd_norm", 8), ("ret_norm", 4), ("ssd_conv_b", 12)):
            self.loads.append((self.rows[0][at:at + n, :], A[name].rearrange("l (c p) -> (l c) p", p=P)))
            at += n
        self.n0 = at
        self.loads.append((self.rows[1][0:48, :], A["ssd_conv_w"].rearrange("l j (c p) -> (l j c) p", p=P)))
        self.loads.append((self.rows[1][48:50, :], A["mem_q_norm"]))
        self.loads.append((self.rows[1][50:52, :], A["mem_k_norm"]))
        for i, name in ((52, "swa_q_norm"), (53, "swa_k_norm")):
            for half in range(2):
                self.loads.append((self.rows[1][i:i + 1, 64 * half:64 * half + 64], A[name]))
        colv = lambda ap, n: ap.rearrange("l (h a) -> (l h) a", a=1)[0:n]
        gb = A["mlstm_gate_bias"]
        self.loads += [(k.gate_i[:, :], gb[:, 0:4].rearrange("l (h a) -> (l h) a", a=1)),
                       (k.gate_f[:, :], gb[:, 4:8].rearrange("l (h a) -> (l h) a", a=1)),
                       (k.dt_bias[:, :], A["ssd_dt_bias"].rearrange("l (h a) -> (l h) a", a=1)),
                       (k.a_log[:, :], A["ssd_a_log"].rearrange("l (h a) -> (l h) a", a=1)),
                       (k.d_skip[:, :], A["ssd_d"].rearrange("l (h a) -> (l h) a", a=1)),
                       (k.sink_row[:, :], A["swa_sinks"].to_broadcast([P, 8]))]
        for b in range(NSAMPLE):
            self.loads.append((k.sink_col[8 * b:8 * b + 8, :], A["swa_sinks"].rearrange("l (h a) -> (l h) a", a=1)))

    def pe(self, pe):
        k, ps = self.k, self.k.ps
        pe.wait_ge(self.here.s, 16 * len(self.first))
        ident = k.c("ident")
        pe.transpose(ps[:, 4, 0:16], self.rows[0][0:16, :], k.c("ident", 16)[:, 0:16]).then_inc(self.done.s, 1)
        for c in range(DC):
            if c >= 2:
                pe.wait_ge(self.out.s, c - 1)
            b = 2 * (c % 2)
            for n in range(NBLK):
                pe.transpose(ps[:, b, n * P:n * P + P], self.xtok[:, n, c * P:c * P + P], ident)
            pe.transpose(ps[:, b + 1, 0:8], self.xs[:, c * P:c * P + P], k.c("ident", 8)[:, 0:8])\
              .then_inc(self.done.s, 1)
            if c:
                self.norm.pe(pe, c - 1)
        self.norm.pe(pe, DC - 1)
        pe.wait_ge(self.late_here.s, 16 * len(self.loads))
        pe.transpose(ps[:, 5, 0:self.n0], self.rows[0][0:self.n0, :], k.c("ident", self.n0)[:, 0:self.n0])
        pe.transpose(ps[:, 5, 128:182], self.rows[1][0:54, :], k.c("ident", 54)[:, 0:54]).then_inc(self.vectors.s, 1)

    def dve(self, dve):
        k, ps = self.k, self.k.ps
        dve.wait_ge(self.done.s, 1)
        k.dve_link(dve.tensor_copy(k.vcol[:, 0:16], ps[:, 4, 0:16]))
        for c in range(DC):
            dve.wait_ge(self.done.s, c + 2)
            b = 2 * (c % 2)
            dve.tensor_copy(k.x[:, c, 0:SEQ], ps[:, b, :])
            dve.tensor_copy(k.x[:, c, SEQ:TOK], ps[:, b + 1, 0:8]).then_inc(self.out.s, 1)
            dve.wait_ge(self.out.s, c + 1)
            self.norm.dve(dve, c)
        dve.wait_ge(self.vectors.s, 1)
        dve.tensor_copy(k.ident_r[:, :], k.c("ident", 16)[:, 0:16])
        dve.tensor_copy(k.vcol[:, 16:self.n0], ps[:, 5, 16:self.n0])
        dve.tensor_copy(k.vcol[:, self.n0:self.n0 + 54], ps[:, 5, 128:182])

    def sp(self, sp):
        for out, src in self.loads:
            sp.dma_start(out, src).then_inc(self.late_here.s, 16)

    def act(self, act):
        for out, src in self.first:
            act.dma_start(out, src).then_inc(self.here.s, 16)
        self.k.nc.scalar.preload_act_table_set("natural_log_exp_and_others")
        for n in range(RING):
            split_high(self.k, act, n)
        for c in range(DC):
            act.wait_ge(self.out.s, c + 1)
            self.norm.act(act, c)
        self.norm.act_rstd(act)


class Rope:

    def __init__(self, k, name, chunks, table, t):
        self.k, self.chunks, self.table, self.t = k, chunks, table, t
        self.rot, self.free = k.counter(f"{name}_rotated"), k.counter(f"{name}_free")

    def pe_rotate(self, pe, i, sig, count):
        pe.wait_ge(sig.s, count)
        if i:
            pe.wait_ge(self.free.s, i)
        for b, (c0, c1) in enumerate(HALVES):
            last = pe.matmul(self.k.ps[:, 6 + b, 0:HALF], self.k.lc(self.table, "rot"), self.chunks[i][:, c0:c1],
                             start=True, stop=True)
        last.then_inc(self.rot.s, 1)

    def dve_apply(self, dve, i):
        k, x, t = self.k, self.chunks[i], self.t[i % 2][:, :]
        dve.wait_ge(self.rot.s, i + 1)
        dve.tensor_tensor(two(t), k.ps[:, 6:8, 0:HALF], two(k.lc(self.table, "sin")), ALU.mult)\
           .then_inc(self.free.s, 1)
        k.dve_link(dve.tensor_tensor(x, x, k.lc(self.table, "cos"), ALU.mult))
        dve.tensor_tensor(x, x, t, ALU.add)


class Turn(Stage):

    def __init__(self, k, name, items):
        super().__init__(k)
        self.items = items
        self.done, self.free = k.turn_signals
        self.base = k.turn_count
        k.turn_count += len(items)

    def pe(self, pe):
        k = self.k
        for i, (pieces, _, _) in enumerate(self.items):
            if i >= 4:
                pe.wait_ge(self.free.s, self.base + i - 3)
            for src, c0 in pieces:
                rows, n = src.shape
                last = pe.transpose(k.ps[0:n, 4 + i % 4, c0:c0 + rows], src, self.ident(src, rows))
            last.then_inc(self.done.s, 1)

    def ident(self, src, rows):
        at = src.base_partition() if callable(src.base_partition) else src.base_partition
        return self.k.const[at:at + rows, at:at + rows]

    def copy(self, eng, me):
        k = self.k
        for i, (_, view, dst) in enumerate(self.items):
            if (i % 2 == 0) == (me == "dve"):
                eng.wait_ge(self.done.s, self.base + i + 1)
                src = view(k.ps[:, 4 + i % 4, :])
                if i:
                    eng.wait_ge(self.free.s, self.base + i)
                if me == "dve":
                    eng.tensor_copy(dst, src).then_inc(self.free.s, 1)
                else:
                    eng.activation(dst, src, ACT.Copy).then_inc(self.free.s, 1)

    def dve(self, dve):
        self.copy(dve, "dve")

    def act(self, act):
        self.copy(act, "act")


def split_out(k, dve, dst_hi, dst_lo, src):
    k.dve_link(dve.tensor_copy(dst_hi, src))
    return dve.tensor_tensor(dst_lo, src, dst_hi.bitcast(F32), ALU.subtract)


class Ffn(Gemm):

    def __init__(self, k, layer):
        w1, w2 = k.A["ffn_w1"][layer], k.A["ffn_w2"][layer]
        k.small.reset()
        self.relu = [k.small(f"relu{layer}_{i}", [P, TOK]) for i in range(2)]
        self.sqr = [k.small(f"sqr{layer}_{i}", [P, TOK]) for i in range(2)]
        self.relu_ready, self.sq_ready, self.hid_ready = k.ffn_signals
        self.hid0 = layer * FFN // P
        tiles = []
        for what, q in (("up", 0), ("up", 1), ("down", 0), ("up", 2), ("down", 1), ("up", 3), ("down", 2), ("down", 3)):
            for m in range(DC):
                if what == "up":
                    h = q * DC + m
                    tiles.append(gemm_tile(w1, [(h * P, P)], k.xn, None, hidden=h))
                else:
                    tiles.append(gemm_tile(w2, [(m * P, P)], (k.hid_hi[q % 2], k.hid_lo[q % 2]),
                                           out_residual(k, m), row0=q * DC,
                                           **({"finish": m} if q == 3 and layer == 0 else {}),
                                           rhs_ready=(self.hid_ready, self.hid0 + (q + 1) * DC)))
        super().__init__(k, tiles, next_norm(k, f"ffn{layer}", V_MIX + DC, k.xn) if layer == 0 else None)

    def low(self, dve, h):
        k = self.k
        dve.wait_ge(self.sq_ready.s, self.hid0 + h + 1)
        hi, lo = k.hid_hi[h // DC % 2][:, h % DC, :], k.hid_lo[h // DC % 2][:, h % DC, :]
        dve.tensor_tensor(lo, self.sqr[h % 2][:, :], hi.bitcast(F32), ALU.subtract).then_inc(self.hid_ready.s, 1)

    def dve(self, dve):
        k, ps = self.k, self.k.ps
        pending = None
        for i, t in enumerate(self.mine):
            n = self.base + i
            dve.wait_ge(k.tile_done.s, n + 1)
            src = ps[:, 2 * (n % 3):2 * (n % 3) + 2, 0:HALF]
            if "hidden" in t:
                h = t["hidden"]
                dve.scalar_tensor_tensor(two(self.relu[h % 2][:, :]), src, 0.0, two(k.rstd[:, :]), ALU.max,
                                         ALU.mult).then_inc(k.tile_out.s, 1)
            else:
                t["out"](dve, src, 2)
            dve.wait_ge(k.tile_out.s, n + 1)
            if "finish" in t:
                self.norm.dve(dve, t["finish"])
            if pending is not None:
                self.low(dve, pending)
            pending = t.get("hidden")

    def act(self, act):
        k = self.k
        for i, t in enumerate(self.mine):
            n = self.base + i
            if n + RING < len(k.tiles):
                act.wait_ge(k.tile_done.s, n + 1)
                split_high(k, act, n + RING)
            if "hidden" in t:
                h = t["hidden"]
                act.wait_ge(k.tile_out.s, n + 1)
                hi = k.hid_hi[h // DC % 2][:, h % DC, :]
                act.activation(self.sqr[h % 2][:, :], self.relu[h % 2][:, :], ACT.Square)
                act.activation(hi, self.relu[h % 2][:, :], ACT.Square).then_inc(self.sq_ready.s, 1)
            if "finish" in t:
                act.wait_ge(k.tile_out.s, n + 1)
                self.norm.act(act, t["finish"])
        if self.norm:
            self.norm.act_rstd(act)


class Spread(Stage):

    def __init__(self, k, name, items):
        super().__init__(k)
        self.items = items
        self.full, self.free = k.spread_signals
        self.base = k.spread_count
        k.spread_count += len(items)

    def pe(self, pe):
        for i, (products, _) in enumerate(self.items):
            if i >= 8:
                pe.wait_ge(self.free.s, self.base + i - 7)
            for (c0, c1), lhsT, rhs, row in products:
                last = pe.matmul(self.k.ps[row:row + lhsT.shape[1], i % 8, c0:c1], lhsT, rhs, start=True, stop=True)
            last.then_inc(self.full.s, 1)

    def dve(self, dve):
        for i, (_, take) in enumerate(self.items):
            dve.wait_ge(self.full.s, self.base + i + 1)
            take(dve, self.k.ps[:, i % 8, :]).then_inc(self.free.s, 1)


class Beside:

    def __init__(self, k, name, items, banks):
        self.k, self.items, self.banks = k, items, banks
        self.full, self.free = k.counter(f"{name}_full"), k.counter(f"{name}_free")

    def pe(self, pe, i):
        if i >= len(self.banks):
            pe.wait_ge(self.free.s, i - len(self.banks) + 1)
        bank = self.k.ps[:, self.banks[i % len(self.banks)], :]
        for (c0, c1), lhsT, rhs, row in self.items[i][0]:
            last = pe.matmul(bank[row:row + lhsT.shape[1], c0:c1], lhsT, rhs, start=True, stop=True)
        last.then_inc(self.full.s, 1)

    def take(self, eng, i):
        eng.wait_ge(self.full.s, i + 1)
        self.items[i][1](eng, self.k.ps[:, self.banks[i % len(self.banks)], :]).then_inc(self.free.s, 1)


def blocks(ap):
    return ap.rearrange("p (n t) -> p n t", t=P)


def even_small(k):
    k.small.reset()
    (k.g_m, k.g_a, k.g_c, k.g_em, k.g_cs) = (k.small(f"gate_{n}", [4, TOK]) for n in ("m", "a", "c", "em", "cs"))
    k.g_m0, k.g_ws = k.small("gate_m0", [4, 8]), k.small("gate_ws", [4, 8])
    k.kout = k.small("k_last_block", [P, P])
    k.kv_s = k.small("kv_sample", [NSAMPLE, 2, P])
    k.mv_s = k.small("mv_sample", [NSAMPLE, 512])
    k.even_kept = k.small.at


class QueryKeyNorm:

    def __init__(self, k, tiles, first):
        self.k = k
        k.small.reset(k.even_kept)
        self.sq, self.rstd = k.small("qk_sq", [P, TOK]), k.small("qk_rstd", [P, TOK])
        t = [k.small(f"qk_rope_t{i}", [P, TOK]) for i in range(2)]
        self.chunks = [k.proj[:, c, :] for c in range(5)]
        self.rope = Rope(k, "even_rope", self.chunks, EVEN, t)
        self.squared, self.summed, self.rstd_ready, self.normed = k.row_norm_signals
        k.n_row_norms += 5
        for c in range(5):
            i = first + 2 * c
            follow(tiles, i, None, lambda act, n, c=c: self.act_square(act, c))
            tiles[i + 2]["pe_before"] = lambda pe, c=c: self.pe_sum(pe, c)
            follow(tiles, i + 1, None, lambda act, n, c=c: self.act_rstd(act, c))
            follow(tiles, i + 2, lambda dve, n, c=c: self.dve_norm(dve, c))
            tiles[i + 5]["pe_before"] = lambda pe, c=c: self.pe_rotate(pe, c)
            follow(tiles, i + 4, lambda dve, n, c=c: self.rope.dve_apply(dve, c))

    def act_square(self, act, c):
        act.wait_ge(self.k.tile_out.s, self.tile0 + c + 1)
        if c:
            act.wait_ge(self.summed.s, c)
        act.activation(self.sq[:, :], self.chunks[c], ACT.Square).then_inc(self.squared.s, 1)

    def pe_sum(self, pe, c):
        k = self.k
        pe.wait_ge(self.squared.s, c + 1)
        if c >= 2:
            pe.wait_ge(self.rope.free.s, c - 1)
        for b, (c0, c1) in enumerate(HALVES):
            last = pe.matmul(k.ps[:, 6 + b, 0:HALF], k.c("blk64"), self.sq[:, c0:c1], start=True, stop=True)
        last.then_inc(self.summed.s, 1)

    def pe_rotate(self, pe, c):
        pe.wait_ge(self.rstd_ready.s, min(c + 2, 5))
        self.rope.pe_rotate(pe, c, self.normed, c + 1)

    def act_rstd(self, act, c):
        k = self.k
        act.wait_ge(self.summed.s, c + 1)
        if c:
            act.wait_ge(self.normed.s, c)
        k.act_link(act.activation(two(self.rstd[:, :]), k.ps[:, 6:8, 0:HALF], ACT.Ln, scale=1.0 / 64, bias=k.c("eps")))
        act.activation(self.rstd[:, :], self.rstd[:, :], ACT.Exp, scale=-0.5).then_inc(self.rstd_ready.s, 1)

    def dve_norm(self, dve, c):
        k, x = self.k, self.chunks[c]
        dve.wait_ge(self.rstd_ready.s, c + 1)
        dve.scalar_tensor_tensor(x, x, k.col(V_SQ if c < 4 else V_SK), self.rstd[:, :], ALU.mult, ALU.mult)\
           .then_inc(self.normed.s, 1)


def even_projection(k):
    w, xn = k.A["even_w_in"][0], k.xn
    tiles = []
    def gates_out(dve, src, nb):
        for rows, c in ((slice(0, 4), E_GI), (slice(32, 36), E_GF)):
            ins = dve.tensor_tensor(two(k.proj[0:4, c, :]), src[rows], two(k.rstd[rows, :]), ALU.mult)
        ins.then_inc(k.tile_out.s, 1)
    tiles.append(gemm_tile(w, [(18 * P, 4), (0, 28), (18 * P + 4, 4)], xn, gates_out))
    for g in range(4):
        tiles.append(gemm_tile(w, [(64 * g, 64), (256 + 64 * g, 64)], xn, out_copy(k, k.proj[:, g, :])))
    for c in range(4, 18):
        scale = 64 ** -0.5 if E_MK <= c < E_MV else None
        tiles.append(gemm_tile(w, [(c * P, P)], xn, out_copy(k, k.proj[:, c, :], scale)))
    gates = EvenGates(k)
    follow(tiles, 0, None, gates.act_load)
    follow(tiles, 0, gates.dve_input, gates.act_exp)
    follow(tiles, 1, gates.dve_one_plus, gates.act_log)
    follow(tiles, 2, gates.dve_running)
    follow(tiles, 3, gates.dve_exponents, gates.act_exponents)
    qk = QueryKeyNorm(k, tiles, 5)
    qk.tile0 = len(k.tiles) + 1
    for c in range(E_MO, E_MO + 4):
        def sigmoid(act, n, c=c):
            act.wait_ge(k.tile_out.s, n + 1)
            act.activation(k.proj[:, c, :], k.proj[:, c, :], ACT.Sigmoid)
        follow(tiles, c + 1, None, sigmoid)
    follow(tiles, len(tiles) - 1, None,
           lambda act, n: k.nc.scalar.preload_act_table_set("natural_log_exp_and_others"))
    return Gemm(k, tiles)


class EvenTurn(Turn):

    def __init__(self, k):
        p = k.proj
        k.big.reset(20 * TOK * 4)
        k.sv_tok = k.big("sv_tok", [P, NBLK, P])
        k.mk_tok = k.big("mk_tok", [P, NBLK, 2 * P])
        k.mv_tok = k.big("mv_tok", [P, NBLK, 4, P + 1])
        four = lambda b: blocks(b[:, 0:512])
        turn4 = lambda c: [(p[:, c, n * P:n * P + P], n * P) for n in range(NBLK)]
        items = [(turn4(E_SV), four, k.sv_tok[:, :, :])]
        items += [(turn4(E_MK + j), four, k.mk_tok[:, :, j * P:j * P + P]) for j in range(2)]
        items += [(turn4(E_MV + h), four, k.mv_tok[:, :, h, 0:P]) for h in range(4)]
        items.append(([(p[:, E_SK, 3 * P:SEQ], 0)], lambda b: b[:, 0:P], k.kout[:, :]))
        items.append(([(p[:, E_SK + i, SEQ:TOK], i * P) for i in range(2)],
                      lambda b: b[0:8, 0:2 * P].rearrange("p (i f) -> p i f", i=2), k.kv_s[:, :, :]))
        items.append(([(p[:, E_MV + h, SEQ:TOK], h * P) for h in range(4)], lambda b: b[0:8, 0:512], k.mv_s[:, :]))
        super().__init__(k, "even_turn", items)

    def dve(self, dve):
        dve.memset(self.k.mv_tok[:, :, :, P:P + 1], 1.0)
        super().dve(dve)

    def act(self, act):
        k = self.k
        super().act(act)
        act.wait_ge(self.free.s, self.base + len(self.items))
        k.store(k.O["p_swa_k"].rearrange("l b p h d -> (l b p) (h d)"), k.kout[:, :])
        k.store(k.O["p_swa_v"].rearrange("l b p h d -> (l b p) (h d)"), k.sv_tok[:, 3, :])
        for i, name in enumerate(("k", "v")):
            new = k.O[f"s_swa_{name}"][0].rearrange("b s h d -> b s (h d)")
            old = k.A[f"cache_swa_{name}"][0].rearrange("b s h d -> b s (h d)")
            k.store(new[:, 0:P - 1, :], old[:, 1:P, :])
            k.store(new[:, P - 1, :], k.kv_s[:, i, :])


class SwaPrompt(Stage):

    def __init__(self, k):
        super().__init__(k)
        k.small.reset(k.even_kept)
        kept = k.big.at
        self.s = [k.big(f"swa_s{i}", [P, 8, 2 * P]) for i in range(2)]
        k.big.reset(kept)
        self.pt = k.small("swa_pt", [P, 4, 4, P])
        self.mx, self.m, self.nm, self.d, self.den, self.es, self.r = (
            [k.small(f"swa_{n}{i}", [P, 8]) for i in range(2)] for n in ("mx", "m", "nm", "d", "den", "es", "r"))
        (self.scores, self.masked, self.max_ready, self.exps, self.probs, self.turned, self.pt_ready, self.pv,
         self.pv_free) = (k.counter(f"swa_{n}") for n in ("scores", "masked", "max", "exps", "probs", "turned", "pt",
                                                         "pv", "pv_free"))

    def pe_scores(self, pe, n):
        k, ps, p = self.k, self.k.ps, self.k.proj
        kb = max(n - 1, 0)
        if n:
            pe.wait_ge(self.masked.s, n)
        for g in range(4):
            for v in range(2):
                rows, at = slice(64 * v, 64 * v + 64), 256 * (g % 2)
                last = pe.matmul(ps[:, 2 * v + g // 2, at:at + 256], p[rows, g, n * P:n * P + P],
                                 p[rows, E_SK, kb * P:kb * P + 2 * P], start=True, stop=True)
        last.then_inc(self.scores.s, 1)

    def pe(self, pe):
        k, ps, p = self.k, self.k.ps, self.k.proj
        self.pe_scores(pe, 0)
        self.pe_scores(pe, 1)
        self.pe_scores(pe, 2)
        for n in range(NBLK):
            kb = max(n - 1, 0)
            pe.wait_ge(self.probs.s, n + 1)
            if n:
                pe.wait_ge(self.pv_free.s, n)
            for g in range(4):
                for v in range(2):
                    for s in range(2):
                        at = (2 * v + s) * P
                        last = pe.transpose(ps[:, 4 + g, at:at + P], self.s[n % 2][:, 4 * v + g, s * P:s * P + P],
                                            k.c("ident"))
            last.then_inc(self.turned.s, 1)
            pe.wait_ge(self.pt_ready.s, n + 1)
            for g in range(4):
                for v in range(2):
                    for s in range(2):
                        last = pe.matmul(ps[64 * v:64 * v + 64, 4, g * P:g * P + P],
                                         k.sv_tok[:, kb + s, 64 * v:64 * v + 64], self.pt[:, g, 2 * v + s, :],
                                         start=s == 0, stop=s == 1)
            last.then_inc(self.pv.s, 1)
            if n + 3 < NBLK:
                self.pe_scores(pe, n + 3)

    def dve_max(self, dve, n):
        k, ps, i, sink = self.k, self.k.ps, n % 2, self.k.sink_row[:, :]
        mask = k.lc(EVEN, "mask_later" if n else "mask_first").unsqueeze(1).to_broadcast([P, 2, 2 * P])
        dve.wait_ge(self.scores.s, n + 1)
        if n >= 2:
            dve.wait_ge(self.turned.s, n - 1)
        for g in range(4):
            ins = dve.tensor_tensor(self.s[i][:, 2 * g:2 * g + 2, :],
                                    ps[:, g, :].rearrange("p (v s) -> p v s", v=2), mask, ALU.add)
        ins.then_inc(self.masked.s, 1)
        dve.wait_ge(self.masked.s, n + 1)
        k.dve_link(dve.tensor_reduce(self.mx[i][:, :], self.s[i][:, :, :], AX.X, ALU.max))
        k.dve_link(dve.scalar_tensor_tensor(self.m[i][:, :], self.mx[i][:, :], 0.125, sink, ALU.mult, ALU.max))
        dve.tensor_tensor(self.d[i][:, :], sink, self.m[i][:, :], ALU.subtract)
        dve.tensor_scalar(self.nm[i][:, :], self.m[i][:, :], -1.0, None, ALU.mult).then_inc(self.max_ready.s, 1)

    def dve_probs(self, dve, n):
        k, s, r = self.k, self.s[n % 2][:, :, :], self.r[n % 2][:, :]
        dve.wait_ge(self.exps.s, n + 1)
        k.dve_link(dve.tensor_tensor(r, self.den[n % 2][:, :], self.es[n % 2][:, :], ALU.add))
        k.dve_link(dve.reciprocal(r, r))
        dve.tensor_tensor(s, s, r.unsqueeze(2).to_broadcast([P, 8, 2 * P]), ALU.mult).then_inc(self.probs.s, 1)

    def dve(self, dve):
        k, ps = self.k, self.k.ps
        self.dve_max(dve, 0)
        self.dve_max(dve, 1)
        self.dve_probs(dve, 0)
        for n in range(NBLK):
            if n + 1 < NBLK:
                self.dve_probs(dve, n + 1)
            if n + 2 < NBLK:
                self.dve_max(dve, n + 2)
            dve.wait_ge(self.pv.s, n + 1)
            cols = slice(n * P, n * P + P)
            split_out(k, dve, k.y_hi[:, 0:4, cols], k.y_lo[:, 0:4, cols], blocks(ps[:, 4, :]))\
                .then_inc(self.pv_free.s, 1)

    def act_exps(self, act, n):
        i = n % 2
        act.wait_ge(self.max_ready.s, n + 1)
        for h in range(8):
            act.activation(self.s[i][:, h, :], self.s[i][:, h, :], ACT.Exp, scale=0.125, bias=self.nm[i][:, h:h + 1],
                           accum_out=self.den[i][:, h:h + 1])
        act.activation(self.es[i][:, :], self.d[i][:, :], ACT.Exp).then_inc(self.exps.s, 1)

    def act(self, act):
        k, ps = self.k, self.k.ps
        self.act_exps(act, 0)
        self.act_exps(act, 1)
        for n in range(NBLK):
            act.wait_ge(self.turned.s, n + 1)
            for g in range(4):
                ins = act.activation(self.pt[:, g, :, :], blocks(ps[:, 4 + g, :]), ACT.Copy)
            ins.then_inc(self.pt_ready.s, 1)
            if n + 2 < NBLK:
                self.act_exps(act, n + 2)


class SwaSample(Stage):

    def __init__(self, k):
        super().__init__(k)
        k.w_ml = k.big("ml_weight", [P, 4, SEQ])
        k.em = k.big("ml_em", [P, 4, TOK])
        k.cs = k.big("ml_cs", [P, 2, TOK])
        def mask(h):
            return lambda dve, bank: dve.tensor_tensor(blocks(k.w_ml[:, h, :]), blocks(bank[:, 0:512]),
                                                       k.c("causal").unsqueeze(1).to_broadcast([P, NBLK, P]), ALU.add)
        copy = lambda dst: lambda act, bank: act.activation(dst, bank[:, 0:SEQ], ACT.Copy)
        self.weights = Beside(k, "ml_weights", [([((0, SEQ), k.onehot(h, 4), k.g_a[:, 0:SEQ], 0)], mask(h))
                                                for h in range(4)], range(4, 8))
        self.scales = Beside(k, "ml_scales", [([((0, SEQ), k.onehot(h, 4), k.g_em[:, 0:SEQ], 0)],
                                               copy(k.em[:, h, 0:SEQ])) for h in range(4)]
                             + [(k.pair(j, 4, (0, SEQ), k.g_cs[:, 0:SEQ]), copy(k.cs[:, j, 0:SEQ])) for j in range(2)],
                             range(4, 8))
        k.small.reset(k.even_kept)
        self.kc, self.vc, self.kt = (k.small(f"swas_{n}", [P, 8, P]) for n in ("kc", "vc", "kt"))
        self.qz = k.small("swas_q", [P, 8, 2, 4])
        self.prod, self.st, self.pt, self.o, self.t = (
            k.small(f"swas_{n}", [P, 64]) for n in ("prod", "st", "pt", "o", "t"))
        self.s = k.small("swas_s", [64, P])
        self.own, self.mx, self.m, self.nm, self.d, self.den, self.eo, self.es, self.r = (
            k.small(f"swas_{n}", [64, 1]) for n in ("own", "mx", "m", "nm", "d", "den", "eo", "es", "r"))
        (self.here, self.kturn, self.kt_ready, self.q_ready, self.scores, self.st_ready, self.rows, self.max_ready,
         self.exps, self.probs, self.pturn, self.pt_ready, self.pv) = (
            k.counter(f"swas_{n}") for n in ("here", "kturn", "kt", "q", "scores", "st", "rows", "max", "exps",
                                            "probs", "pturn", "pt", "pv"))

    def act(self, act):
        k, ps = self.k, self.k.ps
        for t, name in ((self.kc, "k"), (self.vc, "v")):
            act.dma_start(t[:, :, :], k.A[f"cache_swa_{name}"][0].rearrange("b s h d -> s b (h d)"))\
               .then_inc(self.here.s, 16)
        act.wait_ge(self.kturn.s, 1)
        for i in range(2):
            ins = act.activation(self.kt[:, 4 * i:4 * i + 4, :], blocks(ps[:, i, :]), ACT.Copy)
        ins.then_inc(self.kt_ready.s, 1)
        act.wait_ge(self.max_ready.s, 1)
        act.activation(self.s[:, :], self.s[:, :], ACT.Exp, scale=0.125, bias=self.nm[:, :], accum_out=self.den[:, :])
        act.activation(self.eo[:, :], self.own[:, :], ACT.Exp, scale=0.125, bias=self.nm[:, :])
        act.activation(self.es[:, :], self.d[:, :], ACT.Exp).then_inc(self.exps.s, 1)
        for i in range(6):
            self.scales.take(act, i)

    def pe(self, pe):
        k, ps = self.k, self.k.ps
        for i in range(4):
            self.weights.pe(pe, i)
        pe.wait_ge(self.here.s, 32)
        for b in range(8):
            last = pe.transpose(ps[:, b // 4, (b % 4) * P:(b % 4) * P + P], self.kc[:, b, :], k.c("ident"))
        last.then_inc(self.kturn.s, 1)
        pe.wait_ge(self.kt_ready.s, 1)
        pe.wait_ge(self.q_ready.s, 1)
        for b in range(8):
            pe.matmul(ps[:, 2, 8 * b:8 * b + 8], self.kt[:, b, :], self.qz[:, b, :, :], start=True, stop=True)
        pe.matmul(ps[0:64, 3, 0:1], self.prod[:, :], k.c("ones")[:, 0:1], start=True, stop=True)\
          .then_inc(self.scores.s, 1)
        pe.wait_ge(self.st_ready.s, 1)
        pe.transpose(ps[0:64, 0, 0:P], self.st[:, :], k.c("ident")).then_inc(self.rows.s, 1)
        pe.wait_ge(self.weights.free.s, 4)
        for i in range(4):
            self.scales.pe(pe, i)
        pe.wait_ge(self.probs.s, 1)
        pe.transpose(ps[:, 1, 0:64], self.s[:, :], k.c("ident", 64)[:, 0:64])
        pe.matmul(ps[:, 3, 0:64], self.eo[:, :].to_broadcast([64, P]), k.c("ident", 64)[:, 0:64], start=True, stop=True)\
          .then_inc(self.pturn.s, 1)
        pe.wait_ge(self.pt_ready.s, 1)
        for b in range(8):
            last = pe.matmul(ps[:, 2, 8 * b:8 * b + 8], self.vc[:, b, :], self.pt[:, 8 * b:8 * b + 8], start=True, stop=True)
        last.then_inc(self.pv.s, 1)
        for i in range(4, 6):
            self.scales.pe(pe, i)

    def dve(self, dve):
        k, ps, p = self.k, self.k.ps, self.k.proj
        k.dve_link(dve.memset(self.qz[:, :, :, :], 0.0))
        for v in range(2):
            rows = slice(64 * v, 64 * v + 64)
            ins = dve.tensor_copy(self.qz[rows, :, v, :], p[rows, 0:4, SEQ:TOK].rearrange("p g b -> p b g"))
        k.dve_link(ins)
        spread = lambda t: t[:, :].rearrange("p (b h) -> p b h", b=8)
        new = lambda c: p[:, c, SEQ:TOK].unsqueeze(2).to_broadcast([P, 8, 8])
        dve.tensor_tensor(spread(self.prod), self.qz[:, :, :, :].rearrange("p b v g -> p b (v g)"), new(E_SK), ALU.mult)\
           .then_inc(self.q_ready.s, 1)
        for i in range(4):
            self.weights.take(dve, i)
        dve.wait_ge(self.scores.s, 1)
        dve.tensor_copy(self.own[:, :], ps[0:64, 3, 0:1])
        dve.tensor_copy(self.st[:, :], ps[:, 2, 0:64]).then_inc(self.st_ready.s, 1)
        dve.wait_ge(self.rows.s, 1)
        k.dve_link(dve.tensor_copy(self.s[:, :], ps[0:64, 0, 0:P]))
        k.dve_link(dve.tensor_reduce(self.mx[:, :], self.s[:, :], AX.X, ALU.max))
        k.dve_link(dve.tensor_tensor(self.mx[:, :], self.mx[:, :], self.own[:, :], ALU.max))
        k.dve_link(dve.scalar_tensor_tensor(self.m[:, :], self.mx[:, :], 0.125, k.sink_col[:, :], ALU.mult, ALU.max))
        dve.tensor_tensor(self.d[:, :], k.sink_col[:, :], self.m[:, :], ALU.subtract)
        dve.tensor_scalar(self.nm[:, :], self.m[:, :], -1.0, None, ALU.mult).then_inc(self.max_ready.s, 1)
        dve.wait_ge(self.exps.s, 1)
        k.dve_link(dve.tensor_tensor(self.r[:, :], self.den[:, :], self.es[:, :], ALU.add))
        k.dve_link(dve.tensor_tensor(self.r[:, :], self.r[:, :], self.eo[:, :], ALU.add))
        k.dve_link(dve.reciprocal(self.r[:, :], self.r[:, :]))
        dve.tensor_tensor(self.eo[:, :], self.eo[:, :], self.r[:, :], ALU.mult)
        dve.tensor_scalar(self.s[:, :], self.s[:, :], self.r[:, :], None, ALU.mult).then_inc(self.probs.s, 1)
        dve.wait_ge(self.pturn.s, 1)
        dve.tensor_copy(self.pt[:, :], ps[:, 1, 0:64]).then_inc(self.pt_ready.s, 1)
        k.dve_link(dve.tensor_tensor(spread(self.t), ps[:, 3, 0:64].rearrange("p (b h) -> p b h", b=8), new(E_SV), ALU.mult))
        dve.wait_ge(self.pv.s, 1)
        k.dve_link(dve.tensor_tensor(self.o[:, :], self.t[:, :], ps[:, 2, 0:64], ALU.add))
        for v in range(2):
            rows = slice(64 * v, 64 * v + 64)
            src = self.o[rows, :].rearrange("p (b v g) -> p v g b", b=8, v=2)[:, v]
            split_out(k, dve, k.y_hi[rows, 0:4, SEQ:TOK], k.y_lo[rows, 0:4, SEQ:TOK], src)


class Log1pExp:

    def __init__(self, k, x, e, u, l, w):
        self.k, self.x, self.e, self.u, self.l, self.w = k, x, e, u, l, w
        self.input, self.exp, self.one_plus, self.log = k.log_signals
        k.n_logs += 1
        self.nth = k.n_logs

    def dve_input(self, dve):
        dve.scalar_tensor_tensor(self.e, self.x, -1.0, self.x, ALU.mult, ALU.min).then_inc(self.input.s, 1)

    def act_exp(self, act):
        act.wait_ge(self.input.s, self.nth)
        act.activation(self.e, self.e, ACT.Exp).then_inc(self.exp.s, 1)

    def dve_one_plus(self, dve):
        dve.wait_ge(self.exp.s, self.nth)
        dve.tensor_scalar(self.u, self.e, 1.0, None, ALU.add).then_inc(self.one_plus.s, 1)

    def act_log(self, act):
        act.wait_ge(self.one_plus.s, self.nth)
        act.activation(self.l, self.u, ACT.Ln).then_inc(self.log.s, 1)

    def dve_result(self, dve):
        k, e, u, l, w = self.k, self.e, self.u, self.l, self.w
        dve.wait_ge(self.log.s, self.nth)
        k.dve_link(dve.tensor_scalar(w, u, -1.0, None, ALU.add))
        k.dve_link(dve.tensor_tensor(w, e, w, ALU.subtract))
        k.dve_link(dve.reciprocal(u, u))
        k.dve_link(dve.tensor_tensor(w, w, u, ALU.mult))
        k.dve_link(dve.tensor_tensor(l, l, w, ALU.add))


class EvenGates:

    def __init__(self, k):
        self.k = k
        even_small(k)
        k.big.reset(20 * TOK * 4)
        (k.g_i, k.g_f, self.x, self.e, self.u, self.l, self.w, k.g_cum) = (
            k.big(f"gate_{n}", [4, TOK]) for n in ("i_", "f_", "x", "e", "u", "l", "w", "cum"))
        self.log1p = Log1pExp(k, self.x[:, :], self.e[:, :], self.u[:, :], self.l[:, :], self.w[:, :])
        self.here, self.exponents, self.ready = (k.counter(f"gates_{n}") for n in ("m0_here", "exponents", "ready"))

    def act_load(self, act, n):
        act.dma_start(self.k.g_m0[:, :], self.k.A["state_mlstm_m"][0].rearrange("b h -> h b"),
                      allow_slow_non_contiguous=True).then_inc(self.here.s, 16)

    def dve_input(self, dve, n):
        k, p = self.k, self.k.proj
        dve.tensor_scalar(k.g_i[:, :], p[0:4, E_GI, :], k.gate_i[:, :], None, ALU.add)
        k.dve_link(dve.tensor_scalar(self.x[:, :], p[0:4, E_GF, :], k.gate_f[:, :], None, ALU.add))
        self.log1p.dve_input(dve)

    def act_exp(self, act, n):
        self.log1p.act_exp(act)

    def dve_one_plus(self, dve, n):
        self.log1p.dve_one_plus(dve)

    def act_log(self, act, n):
        self.log1p.act_log(act)

    def dve_running(self, dve, n):
        k = self.k
        self.log1p.dve_result(dve)
        k.dve_link(dve.scalar_tensor_tensor(k.g_f[:, :], self.x[:, :], 0.0, self.l[:, :], ALU.min, ALU.subtract))
        k.dve_link(dve.memset(self.w[:, :], 0.0))
        for b in range(NBLK):
            c = slice(b * P, b * P + P)
            dve.tensor_tensor_scan(k.g_cum[:, c], k.g_f[:, c], self.w[:, c], 0.0, ALU.add, ALU.add)
        dve.tensor_tensor_scan(k.g_m[:, 0:SEQ], k.g_f[:, 0:SEQ], k.g_i[:, 0:SEQ], 0.0, ALU.add, ALU.max)

    def dve_exponents(self, dve, n):
        k = self.k
        dve.wait_ge(self.here.s, 16)
        k.dve_link(dve.tensor_tensor(k.g_cs[:, SEQ:TOK], k.g_f[:, SEQ:TOK], k.g_m0[:, :], ALU.add))
        k.dve_link(dve.tensor_tensor(k.g_m[:, SEQ:TOK], k.g_cs[:, SEQ:TOK], k.g_i[:, SEQ:TOK], ALU.max))
        dve.tensor_tensor(k.g_cs[:, SEQ:TOK], k.g_cs[:, SEQ:TOK], k.g_m[:, SEQ:TOK], ALU.subtract)
        dve.tensor_tensor(k.g_ws[:, :], k.g_i[:, SEQ:TOK], k.g_m[:, SEQ:TOK], ALU.subtract)
        dve.tensor_tensor(k.g_c[:, 0:SEQ], k.g_i[:, 0:SEQ], k.g_cum[:, 0:SEQ], ALU.subtract)
        k.dve_link(dve.tensor_tensor(k.g_a[:, 0:SEQ], k.g_cum[:, 0:SEQ], k.g_m[:, 0:SEQ], ALU.subtract))
        ins = dve.tensor_copy(k.g_cs[:, 0:P], k.g_a[:, 0:P])
        for b in range(1, NBLK):
            c = slice(b * P, b * P + P)
            ins = dve.tensor_scalar(k.g_cs[:, c], k.g_a[:, c], k.g_m[:, b * P - 1:b * P], None, ALU.add)
        ins.then_inc(self.exponents.s, 1)

    def act_exponents(self, act, n):
        k = self.k
        act.wait_ge(self.exponents.s, 1)
        act.activation(k.g_em[:, :], k.g_m[:, :], ACT.Exp, scale=-1.0)
        act.activation(k.g_cs[:, :], k.g_cs[:, :], ACT.Exp)
        act.activation(k.g_ws[:, :], k.g_ws[:, :], ACT.Exp)


def even_spread(k):
    k.small.reset(k.even_kept)
    k.c_col = k.small("ml_c_col", [P, NBLK, 4])
    k.ws = k.small("ml_ws", [P, 2, 8])
    k.even_kept2 = k.small.at
    items = []
    items.append(([((8 * h, 8 * h + 8), k.onehot(h, 4), k.g_em[:, SEQ:TOK], 0) for h in range(4)],
                  lambda dve, bank: dve.tensor_copy(k.em[:, :, SEQ:TOK], bank[:, 0:32].rearrange("p (h b) -> p h b", h=4))))
    pairs = lambda src: k.pair(0, 4, (0, 8), src) + k.pair(1, 4, (8, 16), src)
    take = lambda dst: lambda dve, bank: dve.tensor_copy(dst, bank[:, 0:16].rearrange("p (j b) -> p j b", j=2))
    items.append((pairs(k.g_cs[:, SEQ:TOK]), take(k.cs[:, :, SEQ:TOK])))
    items.append((pairs(k.g_ws[:, :]), take(k.ws[:, :, :])))
    items.append(([((4 * n, 4 * n + 4), k.g_c[:, n * P:n * P + P], k.c("ident", 4)[:, 0:4], 0) for n in range(NBLK)],
                  lambda dve, bank: dve.tensor_copy(k.c_col[:, :, :], bank[:, 0:16].rearrange("p (n h) -> p n h", n=4))))
    return Spread(k, "even_spread", items)


class MlstmPrompt(Stage):

    def __init__(self, k):
        super().__init__(k)
        k.small.reset(k.even_kept2)
        k.ml_state = k.small("ml_state", [P, 2, P + 1])
        k.ml_kept = k.small.at
        self.a = [k.small(f"ml_a{i}", [P, 4, P]) for i in range(2)]
        self.kw = [k.small(f"ml_kw{i}", [P, 4, 64]) for i in range(2)]
        self.den = k.small("ml_den", [P, 4, P])
        self.weights, self.st, self.a_ready, self.num, self.state, self.read = (
            k.counter(f"ml_{n}") for n in ("weights", "scores", "weighted", "num", "state", "num_read"))

    def act(self, act):
        k = self.k
        act.dma_start(k.ml_n[:, :], k.A["state_mlstm_n"][0].rearrange("b h d -> b (h d)")).then_inc(k.ml_here.s, 16)
        act.dma_start(k.ml_c[:, :, :, :], k.A["state_mlstm_C"][0].rearrange("b (j t) d e -> (t d) b j e", t=2))\
           .then_inc(k.ml_here.s, 16)
        for n in range(NBLK):
            c = slice(n * P, n * P + P)
            for h in range(4):
                ins = act.activation(k.w_ml[:, h, c], k.w_ml[:, h, c], ACT.Exp, bias=k.c_col[:, n, h:h + 1])
            ins.then_inc(self.weights.s, 1)
        act.wait_ge(self.state.s, NBLK)
        k.store(k.O["p_C"][0, 0].rearrange("(j t) d e -> (t d) j e", t=2), k.ml_state[:, :, 0:P])
        k.store(k.O["p_n"][0, 0].rearrange("(j t) d -> (t d) j", t=2), k.ml_state[:, :, P], few=True)
        k.store(k.O["p_m"].rearrange("l b h -> h (l b)"), k.g_m[:, SEQ - 1:SEQ])
        k.store(k.O["s_m"][0].rearrange("b h -> h b"), k.g_m[:, SEQ:TOK], few=True)

    def pe_scores(self, pe, n):
        k, p, c = self.k, self.k.proj, slice(n * P, n * P + P)
        if n:
            pe.wait_ge(self.a_ready.s, n)
        for h in range(4):
            rows, at = slice(64 * (h % 2), 64 * (h % 2) + 64), (h // 2) * P
            last = pe.matmul(k.ps[:, h % 2, at:at + P], p[rows, E_MK + h // 2, c], p[rows, E_MQ + h // 2, c],
                             start=True, stop=True)
        last.then_inc(self.st.s, 1)

    def pe(self, pe):
        k, ps, p = self.k, self.k.ps, self.k.proj
        self.pe_scores(pe, 0)
        for n in range(NBLK):
            c = slice(n * P, n * P + P)
            if n + 1 < NBLK:
                self.pe_scores(pe, n + 1)
            pe.wait_ge(self.a_ready.s, n + 1)
            if n:
                pe.wait_ge(self.state.s, n)
            if n >= 2:
                pe.wait_ge(self.read.s, n - 1)
            a, kw = self.a[n % 2], self.kw[n % 2]
            for h in range(4):
                rows, j = slice(64 * (h % 2), 64 * (h % 2) + 64), h // 2
                bank = 2 + 2 * (n % 2) + h % 2
                out = ps[:, bank, j * P:j * P + P]
                pe.matmul(out, k.mv_tok[:, n, h, 0:P], a[:, h, :], start=True, stop=n == 0)
                if n:
                    pe.matmul(out, k.ml_state[rows, j, 0:P], k.qs_view[rows, j, c], start=False, stop=True)
                out = ps[:, bank, (2 + j) * P:(3 + j) * P]
                pe.matmul(out, k.c("ones"), a[:, h, :], start=True, stop=n == 0)
                if n:
                    pe.matmul(out, k.ml_state[rows, j, P:P + 1].to_broadcast([64, P]), k.qs_view[rows, j, c],
                              start=False, stop=True)
            for h in range(4):
                last = pe.matmul(ps[64 * (h % 2):64 * (h % 2) + 64, 6, (h // 2) * (P + 1):(h // 2 + 1) * (P + 1)],
                                 kw[:, h, :], k.mv_tok[:, n, h, :], start=True, stop=True)
            last.then_inc(self.num.s, 1)

    def dve_weigh(self, dve, n):
        k, ps, c = self.k, self.k.ps, slice(n * P, n * P + P)
        dve.wait_ge(self.weights.s, n + 1)
        dve.tensor_tensor(self.kw[n % 2][:, :, :], k.mk_tok[:, n, :].rearrange("p (h d) -> p h d", h=4),
                          k.w_ml[:, :, n * P + P - 1:n * P + P].to_broadcast([P, 4, 64]), ALU.mult)
        dve.wait_ge(self.st.s, n + 1)
        for t in range(2):
            ins = dve.tensor_tensor(self.a[n % 2][:, t::2, :], blocks(ps[:, t, 0:2 * P]), k.w_ml[:, t::2, c], ALU.mult)
        ins.then_inc(self.a_ready.s, 1)

    def dve(self, dve):
        k, ps, p = self.k, self.k.ps, self.k.proj
        for j in range(2):
            dve.tensor_tensor(k.qs_view[:, j, :], p[:, E_MQ + j, 0:SEQ], k.cs[:, j, 0:SEQ], ALU.mult)
        k.dve_link(dve.tensor_copy(k.mv_split[0], k.mv_s[:, :]))
        dve.tensor_tensor(k.mv_split[1], k.mv_s[:, :], k.mv_split[0].bitcast(F32), ALU.subtract)
        self.dve_weigh(dve, 0)
        for n in range(NBLK):
            c = slice(n * P, n * P + P)
            if n + 1 < NBLK:
                self.dve_weigh(dve, n + 1)
            dve.wait_ge(self.num.s, n + 1)
            if n == 0:
                ins = dve.tensor_copy(k.ml_state[:, :, :], ps[:, 6, 0:2 * (P + 1)].rearrange("p (j e) -> p j e", j=2))
            else:
                for j in range(2):
                    ins = dve.scalar_tensor_tensor(k.ml_state[:, j, :], k.ml_state[:, j, :],
                                                   k.cs[:, j, n * P + P - 1:n * P + P],
                                                   ps[:, 6, j * (P + 1):(j + 1) * (P + 1)], ALU.mult, ALU.add)
            ins.then_inc(self.state.s, 1)
            num = [blocks(ps[:, 2 + 2 * (n % 2) + t, 0:2 * P]) for t in range(2)]
            den = [blocks(ps[:, 2 + 2 * (n % 2) + t, 2 * P:4 * P]) for t in range(2)]
            for t in range(2):
                ins = dve.scalar_tensor_tensor(self.den[:, t::2, :], den[t], -1.0, k.em[:, t::2, c], ALU.mult, ALU.max)
            k.dve_link(ins)
            for t in range(2):
                ins = dve.tensor_tensor(self.den[:, t::2, :], self.den[:, t::2, :], den[t], ALU.max)
            k.dve_link(ins)
            k.dve_link(dve.reciprocal(self.den[:, :, :], self.den[:, :, :]))
            for t in range(2):
                ins = dve.tensor_tensor(p[:, E_MV + t:E_MV + 4:2, c], num[t], self.den[:, t::2, :], ALU.mult)
            ins.then_inc(self.read.s, 1)
            dve.wait_ge(self.state.s, n + 1)
            dve.wait_ge(self.read.s, n + 1)


class MlstmSample(Stage):

    def __init__(self, k):
        super().__init__(k)
        k.small.reset(k.ml_kept)
        self.c, self.ntok, self.here = k.ml_c, k.ml_n, k.ml_here
        self.t = k.small("mls_t", [P, 2, 2, P])
        self.nout = k.small("mls_n_out", [8, 2 * P])
        self.n, self.kw, self.prod = (k.small(f"mls_{n}", [P, 2, 8]) for n in ("n", "kw", "prod"))
        self.qz = k.small("mls_q", [P, 8, 2, 2])
        self.den = k.small("mls_den", [P, 2, 2, 8])
        (self.nturn, self.prep, self.vb, self.c_new, self.num) = (
            k.counter(f"mls_{n}") for n in ("n_turned", "prepared", "v_spread", "c_new", "num"))
        self.n_out, self.n_back = k.counter("mls_n_out"), k.counter("mls_n_back")

    def act(self, act):
        k = self.k
        act.wait_ge(self.c_new.s, 8)
        k.store_state(k.O["s_C"][0].rearrange("b (j t) d e -> (t d) b j e", t=2), self.c[:, :, :, :])
        act.wait_ge(self.n_out.s, 1)
        k.store(k.O["s_n"][0].rearrange("b h d -> b (h d)"), self.nout[:, :])
        k.stores_done()

    def pe(self, pe):
        k, ps = self.k, self.k.ps
        pe.wait_ge(self.here.s, 32)
        for j in range(2):
            last = pe.transpose(ps[:, 0, 8 * j:8 * j + 8], self.ntok[:, j * P:j * P + P], k.c("ident", 8)[:, 0:8])
        last.then_inc(self.nturn.s, 1)
        for b in range(8):
            if b >= 4:
                pe.wait_ge(self.c_new.s, b - 3)
            k.spread_split(pe, ps[:, 4 + b % 4, :], b, 8, k.mv_split).then_inc(self.vb.s, 1)
        pe.wait_ge(self.prep.s, 1)
        for t in range(2):
            pe.matmul(ps[:, 1, 16 * t:16 * t + 16], k.c("blk64")[:, 64 * t:64 * t + 1].to_broadcast([P, P]),
                      self.prod[:, :, :], start=True, stop=True)
        for j in range(2):
            last = pe.transpose(ps[0:8, 3, j * P:j * P + P], self.n[:, j, :], k.c("ident"))
        last.then_inc(self.n_back.s, 1)
        for b in range(8):
            pe.wait_ge(self.c_new.s, b + 1)
            for j in range(2):
                last = pe.matmul(ps[:, 2, 4 * b + 2 * j:4 * b + 2 * j + 2], self.c[:, b, j, :], self.qz[:, b, j, :],
                                 start=True, stop=True)
        last.then_inc(self.num.s, 1)

    def dve(self, dve):
        k, ps, p = self.k, self.k.ps, self.k.proj
        s = slice(SEQ, TOK)
        k.dve_link(dve.memset(self.qz[:, :, :, :], 0.0))
        for t in range(2):
            rows = slice(64 * t, 64 * t + 64)
            dve.tensor_copy(self.qz[rows, :, :, t], p[rows, E_MQ:E_MQ + 2, s].rearrange("p j b -> p b j"))
        k.dve_link(dve.tensor_tensor(self.kw[:, :, :], p[:, E_MK:E_MK + 2, s], k.ws[:, :, :], ALU.mult))
        dve.wait_ge(self.nturn.s, 1)
        k.dve_link(dve.tensor_tensor(self.n[:, :, :], ps[:, 0, 0:16].rearrange("p (j b) -> p j b", j=2), k.cs[:, :, s], ALU.mult))
        k.dve_link(dve.tensor_tensor(self.n[:, :, :], self.n[:, :, :], self.kw[:, :, :], ALU.add))
        dve.tensor_tensor(self.prod[:, :, :], self.n[:, :, :], p[:, E_MQ:E_MQ + 2, s], ALU.mult).then_inc(self.prep.s, 1)
        dve.wait_ge(self.here.s, 32)
        for b in range(8):
            dve.wait_ge(self.vb.s, b + 1)
            t = self.t[:, b % 2, :, :]
            for half in range(2):
                rows = slice(64 * half, 64 * half + 64)
                v = ps[rows, 4 + b % 4, :].rearrange("p (j t e) -> p t j e", j=2, t=2)[:, half]
                dve.tensor_tensor(t[rows], v, self.kw[rows, :, b:b + 1].to_broadcast([64, 2, P]), ALU.mult)
            k.dve_link(dve.tensor_tensor(self.c[:, b, :, :], self.c[:, b, :, :],
                                         k.cs[:, :, SEQ + b:SEQ + b + 1].to_broadcast([P, 2, P]), ALU.mult))
            dve.tensor_tensor(self.c[:, b, :, :], self.c[:, b, :, :], t, ALU.add).then_inc(self.c_new.s, 1)
        dve.wait_ge(self.n_back.s, 1)
        dve.tensor_copy(self.nout[:, :], ps[0:8, 3, 0:2 * P]).then_inc(self.n_out.s, 1)
        em = k.em[:, :, s].rearrange("p (j t) b -> p t j b", t=2)
        den = ps[:, 1, 0:32].rearrange("p (t j b) -> p t j b", t=2, j=2)
        for t in range(2):
            ins = dve.scalar_tensor_tensor(self.den[:, t], den[:, t], -1.0, em[:, t], ALU.mult, ALU.max)
        k.dve_link(ins)
        for t in range(2):
            ins = dve.tensor_tensor(self.den[:, t], self.den[:, t], den[:, t], ALU.max)
        k.dve_link(ins)
        k.dve_link(dve.reciprocal(self.den[:, :, :, :], self.den[:, :, :, :]))
        dve.wait_ge(self.num.s, 1)
        num = ps[:, 2, 0:32].rearrange("p (b j t) -> p t j b", b=8, j=2)
        hb = p[:, E_MV:E_MV + 4, s].rearrange("p (j t) b -> p t j b", t=2)
        for t in range(2):
            dve.tensor_tensor(hb[:, t], num[:, t], self.den[:, t], ALU.mult)


def mlstm_norm(k):
    k.small.reset()
    def apply(dve, u, rstd):
        x = k.proj[:, E_MV + u, :]
        k.dve_link(dve.scalar_tensor_tensor(x, x, k.col(V_MLN + u), rstd, ALU.mult, ALU.mult))
        k.dve_link(dve.tensor_tensor(x, x, k.proj[:, E_MO + u, :], ALU.mult))
        return split_out(k, dve, k.y_hi[:, 4 + u, :], k.y_lo[:, 4 + u, :], x)
    return HeadNorm(k, "ml_norm", [[k.proj[:, E_MV + u, :]] for u in range(4)], k.c("ones"), P, apply)


def even_layer(k):
    s = [even_projection(k)]
    s += [EvenTurn(k), SwaPrompt(k), SwaSample(k), even_spread(k)]
    k.mid.reset(8 * TOK * 4)
    k.qs_view = k.mid("ml_scaled_q", [P, 2, SEQ])
    k.ml_n = k.mid("ml_n", [8, 2 * P])
    k.mid.reset(20 * TOK * 4)
    k.ml_c = k.mid("ml_c", [P, 8, 2, P])
    k.ml_here = k.counter("ml_states_here")
    kept = k.big.at
    k.mv_split = []
    for c in (E_GI, E_GF):
        k.big.reset(c * TOK * 4)
        k.mv_split.append(k.big(f"mv_split{c}", [8, 512], F32R)[:, :])
    k.big.reset(kept)
    s += [MlstmPrompt(k), MlstmSample(k), mlstm_norm(k)]
    w = k.A["even_w_out"][0]
    tiles = []
    for m in range(DC):
        t, cols = gemm_tile(w, [(m * P, P)], (k.y_hi, k.y_lo), out_residual(k, m)), slice(m * P, m * P + P)
        t["parts"] = [((64 * v, 64 * v + 64), (0, 4), (0, P),
                       w[256 * v:256 * v + 256, cols].rearrange("(k p) n -> p k n", p=64)) for v in range(2)]
        t["parts"].append(((0, P), (4, 8), (0, P), w[512:1024, cols].rearrange("(k p) n -> p k n", p=P)))
        t["finish"] = m
        tiles.append(t)
    k.small.reset()
    s.append(Gemm(k, tiles, next_norm(k, "even_out", V_XATT, k.xc)))
    prefetch_memory(k, tiles, 0)
    return s


class Buffers:
    pass


def prefetch_memory(k, tiles, layer):
    k.mtok = k.small(f"mem_tok{layer}", [P, 2, D_MODEL])
    k.mtok_end = k.small.at
    dst = k.mtok[:, :, :]
    follow(tiles, 0, None, lambda act, n: act.dma_start(dst, k.A["mem_prompt"].rearrange("b (s p) d -> p (b s) d", p=P))
           .then_inc(k.mem_here.s, 16))


class MemLoad(Stage):

    def __init__(self, k, m, layer):
        super().__init__(k)
        k.small.reset(k.mtok_end)
        self.mtok = k.mtok
        if layer == 0:
            self.sq = [k.small(f"mem_sq{i}", [P, MEM]) for i in range(2)]
        k.big.reset(k.cross_kept)
        m.hm_hi, m.hm_lo = (k.big(f"hm_{n}{layer}", [P, DC, MEM], F32R) for n in ("hi", "lo"))
        self.layer, self.m = layer, m
        self.turned, self.free, self.squared, self.summed = k.mem_signals

    def act(self, act):
        k, l = self.k, self.layer
        k.state_stores_done()
        if l:
            return
        for c in range(DC):
            act.wait_ge(self.turned.s, c + 1)
            if c >= 2:
                act.wait_ge(self.summed.s, c - 1)
            act.activation(self.sq[c % 2][:, :], k.ps[:, c % 4, 0:MEM], ACT.Square).then_inc(self.squared.s, 1)
        act.wait_ge(self.summed.s, DC)
        k.act_link(act.activation(k.mem_rstd[:, :], k.ps[:, 7, 0:MEM], ACT.Ln, scale=1.0 / D_MODEL, bias=k.c("eps")))
        act.activation(k.mem_rstd[:, :], k.mem_rstd[:, :], ACT.Exp, scale=-0.5)

    def pe(self, pe):
        k, l = self.k, self.layer
        pe.wait_ge(k.mem_here.s, 16 * (l + 1))
        def total(c):
            pe.wait_ge(self.squared.s, c + 1)
            pe.matmul(k.ps[:, 7, 0:MEM], k.c("ones"), self.sq[c % 2][:, :], start=c == 0, stop=c == DC - 1)\
              .then_inc(self.summed.s, 1)
        for c in range(DC):
            if c >= 4:
                pe.wait_ge(self.free.s, DC * l + c - 3)
            for s in range(2):
                last = pe.transpose(k.ps[:, c % 4, s * P:s * P + P], self.mtok[:, s, c * P:c * P + P], k.c("ident"))
            last.then_inc(self.turned.s, 1)
            if c and l == 0:
                total(c - 1)
        if l == 0:
            total(DC - 1)

    def dve(self, dve):
        k, m, l = self.k, self.m, self.layer
        for c in range(DC):
            if l:
                dve.wait_ge(self.turned.s, DC * l + c + 1)
            else:
                dve.wait_ge(self.squared.s, c + 1)
            src, g = k.ps[:, c % 4, 0:MEM], k.col(V_MEM + DC * l + c)
            k.dve_link(dve.tensor_scalar(m.hm_hi[:, c, :], src, g, None, ALU.mult))
            dve.scalar_tensor_tensor(m.hm_lo[:, c, :], src, g, m.hm_hi[:, c, :].bitcast(F32), ALU.mult,
                                     ALU.subtract).then_inc(self.free.s, 1)


class KvTurn(Turn):

    def __init__(self, k, m, layer):
        four = lambda b: b[:, 0:512]
        items = []
        for src, dst in ((m.k_t, m.k_tok), (m.v_t, m.v_tok)):
            for s in range(2):
                items.append(([(src[:, h, s * P:s * P + P], h * P) for h in range(4)], four, dst[:, s, :]))
        super().__init__(k, f"kv_turn{layer}", items)
        self.layer, self.m = layer, m

    def act(self, act):
        k, m = self.k, self.m
        super().act(act)
        act.wait_ge(self.free.s, self.base + len(self.items))
        for name, t in (("mem_k", m.k_tok), ("mem_v", m.v_tok)):
            k.store(k.O[name][self.layer, 0].rearrange("(s p) h d -> p s (h d)", p=P), t[:, :, :])


class CrossPrompt(Stage):

    def __init__(self, k, m, layer):
        super().__init__(k)
        k.small.reset()
        self.s = [k.small(f"xa_s{layer}{i}", [P, 4, MEM]) for i in range(2)]
        self.pt = k.small(f"xa_pt{layer}", [P, 4, 2, P])
        self.mx, self.nm, self.den, self.r = (
            [k.small(f"xa_{n}{layer}{i}", [P, 4]) for i in range(2)] for n in ("mx", "nm", "den", "r"))
        (self.scores, self.max_ready, self.exps, self.probs, self.turned, self.pt_ready, self.pv, self.out) = k.xa_signals
        self.n0 = layer * NBLK
        k.mid.reset()
        m.kc = [k.mid(f"kc{layer}{b}", [P, 2, 512]) for b in range(8)]
        k.big.reset(k.cross_kept)
        m.vc = [k.big(f"vc{layer}{b}", [P, 2, 512]) for b in range(8)]
        self.layer, self.m = layer, m

    def pe_scores(self, pe, n):
        k, m, ps = self.k, self.m, self.k.ps
        if n >= 2:
            pe.wait_ge(self.exps.s, self.n0 + n - 1)
        for h in range(4):
            last = pe.matmul(ps[:, 2 * (n % 2) + h // 2, MEM * (h % 2):MEM * (h % 2) + MEM],
                             m.q[:, h, n * P:n * P + P], m.k_t[:, h, :], start=True, stop=True)
        last.then_inc(self.scores.s, 1)

    def pe(self, pe):
        k, m, ps = self.k, self.m, self.k.ps
        self.pe_scores(pe, 0)
        self.pe_scores(pe, 1)
        for n in range(NBLK):
            pe.wait_ge(self.probs.s, self.n0 + n + 1)
            for h in range(4):
                for s in range(2):
                    last = pe.transpose(ps[:, 4 + h // 2, 256 * (h % 2) + s * P:256 * (h % 2) + s * P + P],
                                        self.s[n % 2][:, h, s * P:s * P + P], k.c("ident"))
            last.then_inc(self.turned.s, 1)
            if n + 2 < NBLK:
                self.pe_scores(pe, n + 2)
            pe.wait_ge(self.pt_ready.s, self.n0 + n + 1)
            if n >= 2:
                pe.wait_ge(self.out.s, self.n0 + n - 1)
            for h in range(4):
                for s in range(2):
                    last = pe.matmul(ps[:, 6 + n % 2, h * P:h * P + P], m.v_tok[:, s, h * P:h * P + P],
                                     self.pt[:, h, s, :], start=s == 0, stop=s == 1)
            last.then_inc(self.pv.s, 1)

    def dve_max(self, dve, n):
        k, m, ps = self.k, self.m, self.k.ps
        dve.wait_ge(self.scores.s, self.n0 + n + 1)
        src = ps[:, 2 * (n % 2):2 * (n % 2) + 2, :].rearrange("p a (b m) -> p (a b) m", b=2)
        k.dve_link(dve.tensor_reduce(self.mx[n % 2][:, :], src, AX.X, ALU.max))
        dve.tensor_scalar(self.nm[n % 2][:, :], self.mx[n % 2][:, :], -(P ** -0.5), None, ALU.mult)\
           .then_inc(self.max_ready.s, 1)

    def dve_probs(self, dve, n):
        k, r, s = self.k, self.r[n % 2], self.s[n % 2]
        dve.wait_ge(self.exps.s, self.n0 + n + 1)
        k.dve_link(dve.reciprocal(r[:, :], self.den[n % 2][:, :]))
        dve.tensor_tensor(s[:, :, :], s[:, :, :], r[:, :].unsqueeze(2).to_broadcast([P, 4, MEM]), ALU.mult)\
           .then_inc(self.probs.s, 1)

    def dve(self, dve):
        k, m, ps = self.k, self.m, self.k.ps
        self.dve_max(dve, 0)
        self.dve_max(dve, 1)
        self.dve_probs(dve, 0)
        for n in range(NBLK):
            if n + 1 < NBLK:
                self.dve_probs(dve, n + 1)
            if n + 2 < NBLK:
                self.dve_max(dve, n + 2)
            dve.wait_ge(self.pv.s, self.n0 + n + 1)
            cols = slice(n * P, n * P + P)
            split_out(k, dve, k.xa_hi[:, 0:4, cols], k.xa_lo[:, 0:4, cols], blocks(ps[:, 6 + n % 2, :]))\
                .then_inc(self.out.s, 1)

    def act_exps(self, act, n):
        k, m, ps = self.k, self.m, self.k.ps
        act.wait_ge(self.max_ready.s, self.n0 + n + 1)
        if n >= 2:
            act.wait_ge(self.turned.s, self.n0 + n - 1)
        for h in range(4):
            ins = act.activation(self.s[n % 2][:, h, :], ps[:, 2 * (n % 2) + h // 2, MEM * (h % 2):MEM * (h % 2) + MEM],
                                 ACT.Exp, scale=P ** -0.5, bias=self.nm[n % 2][:, h:h + 1],
                                 accum_out=self.den[n % 2][:, h:h + 1])
        ins.then_inc(self.exps.s, 1)

    def act(self, act):
        k, m, ps = self.k, self.m, self.k.ps
        for cache, tiles in (("cache_mem_k", m.kc), ("cache_mem_v", m.vc)):
            for b in range(8):
                act.dma_start(tiles[b][:, :, :], k.A[cache][self.layer, b].rearrange("(s p) h d -> p s (h d)", p=P))\
                   .then_inc(k.cache_here.s, 16)
        self.act_exps(act, 0)
        self.act_exps(act, 1)
        for n in range(NBLK):
            act.wait_ge(self.turned.s, self.n0 + n + 1)
            for a in range(2):
                ins = act.activation(self.pt[:, 2 * a:2 * a + 2, :, :],
                                     ps[:, 4 + a, :].rearrange("p (h s q) -> p h s q", h=2, s=2), ACT.Copy)
            ins.then_inc(self.pt_ready.s, 1)
            if n + 2 < NBLK:
                self.act_exps(act, n + 2)


class CrossSample(Stage):

    def __init__(self, k, m, layer):
        super().__init__(k)
        k.small.reset()
        self.kt = [k.small(f"xs_kt{layer}{i}", [P, 4, 2, P]) for i in range(2)]
        self.qz = k.small(f"xs_q{layer}", [P, 32 * 32])
        self.pz = k.small(f"xs_p{layer}", [P, 2, 8, 60])
        self.s = k.small(f"xs_s{layer}", [32, MEM])
        self.t = k.small(f"xs_t{layer}", [32, 4, P])
        self.o = k.small(f"xs_o{layer}", [32, P])
        self.mx, self.nm, self.den, self.r = (k.small(f"xs_{n}{layer}", [32, 1]) for n in ("mx", "nm", "den", "r"))
        (self.kturn, self.kt_ready, self.q_ready, self.scored, self.scores, self.max_ready, self.exps, self.probs,
         self.pturn, self.pt_ready, self.pv, self.o_ready, self.oturn) = k.xs_signals
        self.layer, self.m = layer, m

    def pe(self, pe):
        k, m, ps, l = self.k, self.m, self.k.ps, self.layer
        pe.wait_ge(k.cache_here.s, 256 * (l + 1))
        def turn(b):
            if b >= 2:
                pe.wait_ge(self.kt_ready.s, 8 * l + b - 1)
            for h in range(4):
                for s in range(2):
                    last = pe.transpose(ps[:, 2 * (b % 2) + h // 2, 256 * (h % 2) + s * P:256 * (h % 2) + s * P + P],
                                        m.kc[b][:, s, h * P:h * P + P], k.c("ident"))
            last.then_inc(self.kturn.s, 1)
        turn(0)
        pe.wait_ge(self.q_ready.s, l + 1)
        for b in range(8):
            if b < 7:
                turn(b + 1)
            pe.wait_ge(self.kt_ready.s, 8 * l + b + 1)
            for h in range(4):
                r = 4 * b + h
                last = pe.matmul(ps[0:32, 4, 0:MEM], self.qz[:, 32 * r:32 * r + 32], self.kt[b % 2][:, h, :, :],
                                 start=r == 0, stop=r == 31)
            last.then_inc(self.scored.s, 1)
        last = None
        pe.wait_ge(self.probs.s, l + 1)
        for s in range(2):
            last = pe.transpose(ps[:, 5, 32 * s:32 * s + 32], self.s[:, s * P:s * P + P], k.c("ident", 32)[:, 0:32])
        last.then_inc(self.pturn.s, 1)
        pe.wait_ge(self.pt_ready.s, l + 1)
        for b in range(8):
            for s in range(2):
                last = pe.matmul(ps[0:32, 6, :], self.pz[:, s, b, 28 - 4 * b:60 - 4 * b], m.vc[b][:, s, :],
                                 start=b + s == 0, stop=b == 7 and s == 1)
        last.then_inc(self.pv.s, 1)
        pe.wait_ge(self.o_ready.s, l + 1)
        pe.transpose(ps[:, 7, 0:32], self.o[:, :], k.c("ident", 32)[:, 0:32]).then_inc(self.oturn.s, 1)

    def act(self, act):
        k, m, ps, l = self.k, self.m, self.k.ps, self.layer
        for b in range(8):
            act.wait_ge(self.kturn.s, 8 * l + b + 1)
            if b >= 2:
                act.wait_ge(self.scored.s, 8 * l + b - 1)
            for a in range(2):
                ins = act.activation(self.kt[b % 2][:, 2 * a:2 * a + 2, :, :],
                                     ps[:, 2 * (b % 2) + a, :].rearrange("p (h s q) -> p h s q", h=2, s=2), ACT.Copy)
            ins.then_inc(self.kt_ready.s, 1)
        act.wait_ge(self.max_ready.s, l + 1)
        act.activation(self.s[:, :], ps[0:32, 4, 0:MEM], ACT.Exp, scale=P ** -0.5, bias=self.nm[:, :],
                       accum_out=self.den[:, :]).then_inc(self.exps.s, 1)

    def dve(self, dve):
        k, m, ps, l = self.k, self.m, self.k.ps, self.layer
        dve.memset(self.pz[:, :, :, :], 0.0)
        k.dve_link(dve.memset(self.qz[:, :], 0.0))
        dve.tensor_copy(self.qz[:, 0:1024:33].rearrange("p (b h) -> p b h", b=8),
                        m.q[:, :, SEQ:TOK].rearrange("p h b -> p b h")).then_inc(self.q_ready.s, 1)
        dve.wait_ge(self.scored.s, 8 * (l + 1))
        k.dve_link(dve.tensor_reduce(self.mx[:, :], ps[0:32, 4, 0:MEM], AX.X, ALU.max))
        dve.tensor_scalar(self.nm[:, :], self.mx[:, :], -(P ** -0.5), None, ALU.mult).then_inc(self.max_ready.s, 1)
        dve.wait_ge(self.exps.s, l + 1)
        k.dve_link(dve.reciprocal(self.r[:, :], self.den[:, :]))
        dve.tensor_scalar(self.s[:, :], self.s[:, :], self.r[:, :], None, ALU.mult).then_inc(self.probs.s, 1)
        dve.wait_ge(self.pturn.s, l + 1)
        for s in range(2):
            ins = dve.tensor_copy(self.pz[:, s, :, 28:32], ps[:, 5, 32 * s:32 * s + 32].rearrange("p (b h) -> p b h", b=8))
        ins.then_inc(self.pt_ready.s, 1)
        dve.wait_ge(self.pv.s, l + 1)
        k.dve_link(dve.tensor_tensor(self.t[:, :, :], blocks(ps[0:32, 6, :]),
                                     k.c("own_head", 32).unsqueeze(2).to_broadcast([32, 4, P]), ALU.mult))
        dve.tensor_reduce(self.o[:, :], self.t[:, :, :].rearrange("p h d -> p d h"), AX.X, ALU.add)\
           .then_inc(self.o_ready.s, 1)
        dve.wait_ge(self.oturn.s, l + 1)
        split_out(k, dve, k.xa_hi[:, 0:4, SEQ:TOK], k.xa_lo[:, 0:4, SEQ:TOK],
                  ps[:, 7, 0:32].rearrange("p (b h) -> p h b", b=8))


class CrossNorm:

    def __init__(self, k, tiles, chunks, layer):
        self.k, self.chunks, self.tile0, self.base = k, chunks, len(k.tiles), k.n_row_norms
        k.n_row_norms += len(chunks)
        k.small.reset()
        self.sq = k.small(f"qk_sq{layer}", [P, TOK])
        self.rstd = [k.small(f"qk_rstd{layer}{i}", [P, TOK]) for i in range(2)]
        self.squared, self.summed, self.rstd_ready, self.normed = k.row_norm_signals
        for j in range(len(chunks)):
            if j:
                follow(tiles, j, None, lambda act, n, j=j: self.act_rstd(act, j - 1))
            follow(tiles, j, None, lambda act, n, j=j: self.act_square(act, j))
            tiles[j + 2]["pe_before"] = lambda pe, j=j: self.pe_sum(pe, j)
            follow(tiles, j + 2, lambda dve, n, j=j: self.dve_norm(dve, j))
        follow(tiles, len(chunks), None, lambda act, n: self.act_rstd(act, len(chunks) - 1))

    def banks(self, width):
        return self.k.ps[:, 6:8, 0:HALF] if width == TOK else self.k.ps[:, 6:7, 0:width]

    def act_square(self, act, j):
        x = self.chunks[j][0]
        act.wait_ge(self.k.tile_out.s, self.tile0 + j + 1)
        if j:
            act.wait_ge(self.summed.s, self.base + j)
        act.activation(self.sq[:, 0:x.shape[1]], x, ACT.Square).then_inc(self.squared.s, 1)

    def pe_sum(self, pe, j):
        k, width = self.k, self.chunks[j][0].shape[1]
        pe.wait_ge(self.squared.s, self.base + j + 1)
        if j:
            pe.wait_ge(self.rstd_ready.s, self.base + j)
        for b, (c0, c1) in enumerate(HALVES if width == TOK else [(0, width)]):
            last = pe.matmul(k.ps[:, 6 + b, 0:c1 - c0], k.c("ones"), self.sq[:, c0:c1], start=True, stop=True)
        last.then_inc(self.summed.s, 1)

    def act_rstd(self, act, j):
        k, width = self.k, self.chunks[j][0].shape[1]
        act.wait_ge(self.summed.s, self.base + j + 1)
        if j >= 2:
            act.wait_ge(self.normed.s, self.base + j - 1)
        rstd, src = self.rstd[j % 2][:, 0:width], self.banks(width)
        k.act_link(act.activation(rstd.rearrange("p (a b) -> p a b", b=src.shape[2]), src, ACT.Ln, scale=1.0 / P,
                                  bias=k.c("eps")))
        act.activation(rstd, rstd, ACT.Exp, scale=-0.5).then_inc(self.rstd_ready.s, 1)

    def dve_norm(self, dve, j):
        x, gain = self.chunks[j]
        dve.wait_ge(self.rstd_ready.s, self.base + j + 1)
        dve.scalar_tensor_tensor(x, x, self.k.col(gain), self.rstd[j % 2][:, 0:x.shape[1]], ALU.mult, ALU.mult)\
           .then_inc(self.normed.s, 1)


def cross_layer(k, l):
    m = Buffers()
    k.big.reset()
    m.k_t, m.v_t = (k.big(f"mem_{n}_t{l}", [P, 4, MEM]) for n in "kv")
    m.k_tok, m.v_tok = (k.big(f"mem_{n}_tok{l}", [P, 2, 512]) for n in "kv")
    m.q = k.big(f"xq{l}", [P, 4, TOK])
    k.cross_kept = k.big.at
    s = [MemLoad(k, m, l)]
    tiles = [gemm_tile(k.A["mem_wq"][l], [(h * P, P)], k.xc, out_copy(k, m.q[:, h, :])) for h in range(4)]
    for w, dst in (("mem_wk", m.k_t), ("mem_wv", m.v_t)):
        tiles += [gemm_tile(k.A[w][l], [(h * P, P)], (m.hm_hi, m.hm_lo), out_copy(k, dst[:, h, :]), halves=[(0, MEM)])
                  for h in range(4)]
    CrossNorm(k, tiles, [(m.q[:, h, :], V_QN + l) for h in range(4)] + [(m.k_t[:, h, :], V_KN + l) for h in range(4)], l)
    s.append(Gemm(k, tiles))
    s += [KvTurn(k, m, l), CrossPrompt(k, m, l), CrossSample(k, m, l)]
    w = k.A["mem_wo"][l]
    k.small.reset()
    s.append(Gemm(k, [gemm_tile(w, [(c * P, P)], (k.xa_hi, k.xa_lo), out_residual(k, c), nk=4, finish=c)
                      for c in range(DC)], next_norm(k, f"cross_out{l}", V_FFN + DC * l, k.xn)))
    return s




def odd_projection(k):
    w, xn = k.A["odd_w_in"][0], k.xn
    tiles = [gemm_tile(w, [(20 * P, 16)], xn, out_copy(k, k.proj[0:16, O_DT, :]))]
    order = [*range(O_X, O_X + 12), *range(O_Z, O_Z + 8), *range(O_RQ, O_RV), *range(O_RG, O_RG + 4),
             *range(O_RV, O_RV + 4)]
    for c in order:
        scale = P ** -0.5 if O_RK <= c < O_RV else None
        at = c * P if c < 20 else 20 * P + 16 + (c - O_RQ) * P
        tiles.append(gemm_tile(w, [(at, P)], xn, out_copy(k, k.proj[:, c, :], scale)))
    gates, conv = OddGates(k), Conv(k)
    follow(tiles, 0, gates.dve_input, gates.act_exp)
    follow(tiles, 1, gates.dve_one_plus, gates.act_log)
    follow(tiles, 2, gates.dve_sums, gates.act_ecum)
    follow(tiles, 3, gates.dve_block_decay)
    follow(tiles, 3, conv.dve_history)
    for c in range(12):
        i = 4 + c
        follow(tiles, i, None, lambda act, n, c=c: conv.act_start(act, c))
        follow(tiles, i + 1, lambda dve, n, c=c: conv.dve_taps(dve, c))
        follow(tiles, i + 2, None, lambda act, n, c=c: conv.act_silu(act, c))
    for i, c in enumerate(order):
        if not O_X <= c < O_X + 12 and (c < O_X or c >= O_RG):
            def silu(act, n, c=c):
                act.wait_ge(k.tile_out.s, n + 1)
                act.activation(k.proj[:, c, :], k.proj[:, c, :], ACT.Silu)
            follow(tiles, i + 1, None, silu)
    rope = Rope(k, "odd_rope", [k.proj[:, c, :] for c in range(O_RQ, O_RV)], ODD, gates.rope_t)
    for j in range(8):
        i = 1 + order.index(O_RQ + j)
        tiles[i + 2]["pe_before"] = lambda pe, j=j, n=len(k.tiles) + i: rope.pe_rotate(pe, j, k.tile_out, n + 1)
        follow(tiles, i + 1, lambda dve, n, j=j: rope.dve_apply(dve, j))
    follow(tiles, len(tiles) - 1, None,
           lambda act, n: k.nc.scalar.preload_act_table_set("natural_log_exp_and_others"))
    return Gemm(k, tiles)


class OddLoads(Stage):

    def __init__(self, k):
        super().__init__(k)
        k.mid.reset(2 * DC * TOK * 4)
        k.conv_old = k.mid("conv_old", [24, 1536])

    def act(self, act):
        k = self.k
        act.dma_start(k.lconst[:, 0:NODD], k.C[:, NCOMMON + NEVEN:NCOMMON + NEVEN + NODD]).then_inc(k.odd_here.s, 16)
        act.dma_start(k.conv_old[:, :], k.A["state_ssd_conv"][0].rearrange("b j c -> (b j) c")).then_inc(k.odd_here.s, 16)


class ConvHistory(Turn):

    def __init__(self, k):
        k.small.reset((k.small.size - 12 * (24 + 11) * 4 - 64) // 32 * 32)
        k.conv_free = k.small.at
        k.hist, k.tail = k.small("conv_hist", [P, 12, 24]), k.small("conv_tail", [P, 12, 11])
        super().__init__(k, "conv_history",
                         [([(k.conv_old[:, c * P:c * P + P], 24 * c) for c in range(12)],
                           lambda b: b[:, 0:288].rearrange("p (c r) -> p c r", c=12), k.hist[:, :, :])])

    def pe(self, pe):
        pe.wait_ge(self.k.odd_here.s, 32)
        super().pe(pe)


class ConvTurn(Turn):

    def __init__(self, k):
        super().__init__(k, "conv_turn",
                         [([(k.tail[:, 4 * g + i, :], i * P) for i in range(4)], lambda b: b[0:11, 0:512],
                           k.conv_new[:, 512 * g:512 * g + 512]) for g in range(3)])

    def act(self, act):
        k = self.k
        super().act(act)
        act.wait_ge(self.free.s, self.base + len(self.items))
        k.store(k.O["p_conv"][0, 0], k.conv_new[0:3, :])
        k.store(k.O["s_conv"][0][:, 2, :], k.conv_new[3:11, :])
        k.store(k.O["s_conv"][0][:, 0:2, :], k.A["state_ssd_conv"][0][:, 1:3, :])
        k.stores_done()


class Conv:

    def __init__(self, k):
        self.k = k
        self.acc = [k.small(f"conv_acc{i}", [P, TOK]) for i in range(3)]
        self.prod = k.small("conv_prod", [P, 3, 12, 8])
        assert k.small.at <= k.conv_free
        self.started, self.acc_ready, self.silu = (k.counter(f"conv_{n}") for n in ("last_tap", "taps", "silu"))

    def act_start(self, act, c):
        k = self.k
        if c >= 3:
            act.wait_ge(self.silu.s, c - 2)
        act.activation(self.acc[c % 3][:, :], k.proj[:, O_X + c, :], ACT.Copy, scale=k.col(V_CW + 36 + c))\
           .then_inc(self.started.s, 1)

    def act_silu(self, act, c):
        k = self.k
        act.wait_ge(self.acc_ready.s, c + 1)
        act.activation(k.proj[:, O_X + c, :], self.acc[c % 3][:, :], ACT.Silu, bias=k.col(V_CB + c))\
           .then_inc(self.silu.s, 1)

    def dve_history(self, dve, n):
        k = self.k
        for j in range(3):
            w = k.vcol[:, V_CW + 12 * j:V_CW + 12 * j + 12].unsqueeze(2).to_broadcast([P, 12, 8])
            ins = dve.tensor_tensor(self.prod[:, j], k.hist[:, :, j::3], w, ALU.mult)
        k.dve_link(ins)
        k.dve_link(dve.tensor_tensor(self.prod[:, 0], self.prod[:, 0], self.prod[:, 1], ALU.add))
        k.dve_link(dve.tensor_tensor(self.prod[:, 0], self.prod[:, 0], self.prod[:, 2], ALU.add))

    def dve_taps(self, dve, c):
        k, acc, x = self.k, self.acc[c % 3], self.k.proj[:, O_X + c, :]
        dve.tensor_copy(k.tail[:, c, :], x[:, SEQ - 3:TOK])
        dve.wait_ge(self.started.s, c + 1)
        dve.tensor_tensor(acc[:, SEQ:TOK], acc[:, SEQ:TOK], self.prod[:, 0, c, :], ALU.add)
        for j in range(3):
            back = 3 - j
            ins = dve.scalar_tensor_tensor(acc[:, back:SEQ], x[:, 0:SEQ - back], k.col(V_CW + 12 * j + c),
                                           acc[:, back:SEQ], ALU.mult, ALU.add)
            if j < 2:
                k.dve_link(ins)
        ins.then_inc(self.acc_ready.s, 1)


class OddGates:

    def __init__(self, k):
        self.k = k
        k.small.reset()
        k.cum = k.small("ssd_cum", [16, TOK])
        k.ecum = k.small("ssd_ecum", [16, TOK])
        k.dt_col, k.dec, k.ncum_col = (k.small(n, [P, NBLK, 16]) for n in ("dt_col", "ssd_dec", "ncum_col"))
        k.dt_pair, k.d_pair = k.small("dt_pair", [P, 8, 8]), k.small("d_pair", [P, 8])
        k.odd_kept = k.small.at
        k.conv_new = k.small("conv_new", [11, 1536])
        k.dt = k.small("ssd_dt", [16, TOK])
        k.dg, self.a = k.small("ssd_dg", [16, NBLK, 16]), k.small("ssd_a", [16, 1])
        k.dt_placed, k.ec_placed = k.small("dt_placed", [16, 8, 8]), k.small("ec_placed", [16, 8, 8])
        self.of_pair, k.d_placed, k.parity = (k.small(n, [16, w]) for n, w in (
            ("of_pair", 8), ("d_placed", 8), ("parity", 2)))
        k.mid.reset(2 * DC * TOK * 4)
        self.x, self.e, self.u, self.l, self.w = (k.mid(f"dt_{n}", [16, TOK]) for n in "xeulw")
        self.rope_t = [k.mid(f"odd_rope_t{i}", [P, TOK]) for i in range(2)]
        self.log1p = Log1pExp(k, self.x[:, :], self.e[:, :], self.u[:, :], self.l[:, :], self.w[:, :])
        self.cum_ready, self.a_ready = (k.counter(f"ssd_{n}_ready") for n in ("cum", "a"))
        self.e_ready = k.counter("ssd_ecum_ready")

    def dve_input(self, dve, n):
        k = self.k
        k.dve_link(dve.tensor_scalar(self.x[:, :], k.proj[0:16, O_DT, :], k.dt_bias[:, :], None, ALU.add))
        self.log1p.dve_input(dve)

    def act_exp(self, act, n):
        act.activation(self.a[:, :], self.k.a_log[:, :], ACT.Exp).then_inc(self.a_ready.s, 1)
        self.log1p.act_exp(act)

    def dve_one_plus(self, dve, n):
        self.log1p.dve_one_plus(dve)

    def act_log(self, act, n):
        self.log1p.act_log(act)

    def dve_sums(self, dve, n):
        k, x, w = self.k, self.x[:, :], self.w[:, :]
        self.log1p.dve_result(dve)
        k.dve_link(dve.scalar_tensor_tensor(k.dt[:, :], x, 0.0, self.l[:, :], ALU.max, ALU.add))
        k.dve_link(dve.memset(w, 0.0))
        dve.wait_ge(self.a_ready.s, 1)
        k.dve_link(dve.tensor_scalar(x, k.dt[:, :], self.a[:, :], -1.0, ALU.mult, ALU.mult))
        for b in range(NBLK):
            c = slice(b * P, b * P + P)
            dve.tensor_tensor_scan(k.cum[:, c], x[:, c], w[:, c], 0.0, ALU.add, ALU.add)
        dve.tensor_copy(k.cum[:, SEQ:TOK], x[:, SEQ:TOK]).then_inc(self.cum_ready.s, 1)

    def act_ecum(self, act, n):
        act.wait_ge(self.cum_ready.s, 1)
        act.activation(self.k.ecum[:, :], self.k.cum[:, :], ACT.Exp).then_inc(self.e_ready.s, 1)

    def dve_block_decay(self, dve, n):
        k = self.k
        dve.wait_ge(self.e_ready.s, 1)
        for b in range(NBLK):
            dve.tensor_scalar(k.dg[:, b, :], k.c("ident", 16)[:, 0:16], k.ecum[:, b * P + P - 1:b * P + P], None, ALU.mult)
        pairs = k.c("ident", 16)[:, 0:16].rearrange("p (j t) -> p t j", t=2)
        for t in range(2):
            dve.tensor_reduce(k.parity[:, t:t + 1], pairs[:, t], AX.X, ALU.add)
        k.dve_link(dve.tensor_tensor(self.of_pair[:, :], pairs[:, 0], pairs[:, 1], ALU.add))
        place = self.of_pair[:, :].unsqueeze(2).to_broadcast([16, 8, 8])
        for out, row in ((k.dt_placed, k.dt), (k.ec_placed, k.ecum)):
            dve.tensor_tensor(out[:, :, :], row[:, SEQ:TOK].unsqueeze(1).to_broadcast([16, 8, 8]), place, ALU.mult)
        dve.tensor_scalar(k.d_placed[:, :], self.of_pair[:, :], k.d_skip[:, :], None, ALU.mult)


def odd_spread(k):
    k.mid.reset()
    k.ec = k.mid("ecum_pair", [P, 8, TOK])
    columns = lambda rows: [((16 * n, 16 * n + 16), rows[:, n * P:n * P + P], k.c("ident", 16)[:, 0:16], 0)
                            for n in range(NBLK)]
    items = [(columns(k.dt), lambda dve, b: dve.tensor_copy(k.dt_col[:, :, :],
                                                            b[:, 0:64].rearrange("p (n h) -> p n h", n=NBLK))),
             (columns(k.cum), lambda dve, b: dve.tensor_scalar(k.ncum_col[:, :, :], b[:, 0:64]
                                                               .rearrange("p (n h) -> p n h", n=NBLK), -1.0, None,
                                                               ALU.mult)),
             ([((0, 64), k.c("ones", 16), k.dg[:, :, :], 0)],
              lambda dve, b: dve.tensor_copy(k.dec[:, :, :], b[:, 0:64].rearrange("p (n h) -> p n h", n=NBLK)))]
    halves = lambda placed, n: [((0, n), k.parity[:, t:t + 1].to_broadcast([16, 64]), placed, 64 * t) for t in range(2)]
    take = lambda dst: lambda dve, b: dve.tensor_copy(dst, b[:, 0:64].rearrange("p (j b) -> p j b", j=8))
    items.append((halves(k.dt_placed[:, :, :], 64), take(k.dt_pair[:, :, :])))
    items.append((halves(k.ec_placed[:, :, :], 64), take(k.ec[:, :, SEQ:TOK])))
    items.append((halves(k.d_placed[:, :], 8), lambda dve, b: dve.tensor_copy(k.d_pair[:, :], b[:, 0:8])))
    return Spread(k, "odd_spread", items)


def ret_turn(k):
    p = k.proj
    k.small.reset(k.odd_kept)
    k.rk_tok, k.rv_tok = k.small("rk_tok", [P, NBLK, 512]), None
    k.rv_s = k.small("rv_s", [8, 512])
    k.rv_split = [k.small(f"rv_split{i}", [8, 512], F32R)[:, :] for i in range(2)]
    k.ret_kept = k.small.at
    k.mid.reset(12 * TOK * 4)
    k.rv_tok = k.mid("rv_tok", [P, NBLK, 512])
    items = []
    for base, dst in ((O_RK, k.rk_tok), (O_RV, k.rv_tok)):
        for h in range(4):
            items.append(([(p[:, base + h, n * P:n * P + P], n * P) for n in range(NBLK)],
                          lambda b: blocks(b[:, 0:512]), dst[:, :, h * P:h * P + P]))
    items.append(([(p[:, O_RV + h, SEQ:TOK], h * P) for h in range(4)], lambda b: b[0:8, 0:512], k.rv_s[:, :]))
    return Turn(k, "ret_turn", items)


def spread_decays(k, pairs, banks):
    return Beside(k, f"ssd_decays{pairs[0]}", [(k.pair(j, 16, (0, SEQ), k.ecum[:, 0:SEQ]), lambda act, bank, j=j:
                                                act.activation(k.ec[:, j, 0:SEQ], bank[:, :], ACT.Copy))
                                               for j in pairs], banks)


class RetPrompt(Stage):

    def __init__(self, k):
        super().__init__(k)
        self.decays = spread_decays(k, range(0, 4), range(4, 8))
        kept = k.mid.at
        k.ret_s = []
        for i, at in enumerate((8, 20)):
            k.mid.reset(at * TOK * 4)
            k.ret_s.append(k.mid(f"ret_s{i}", [P, 4, 4, P]))
        k.mid.reset(kept)
        k.ret_here = k.counter("ret_states_here")
        k.small.reset(k.ret_kept)
        self.a, self.qs = ([k.small(f"ret_{n}{i}", [P, 4, P]) for i in range(2)] for n in ("a", "qs"))
        self.ks = [k.mid(f"ret_ks{i}", [P, 4, P]) for i in range(2)]
        self.r = k.mid("ret_state", [P, 4, P])
        self.scores, self.a_ready, self.o, self.state = (k.counter(f"ret_{n}") for n in ("scores", "a", "o", "state"))

    def pe_scores(self, pe, n):
        k, ps, p, c = self.k, self.k.ps, self.k.proj, slice(n * P, n * P + P)
        if n >= 2:
            pe.wait_ge(self.a_ready.s, n - 1)
        for h in range(4):
            last = pe.matmul(ps[:, n % 2, h * P:h * P + P], p[:, O_RK + h, c], p[:, O_RQ + h, c], start=True, stop=True)
        last.then_inc(self.scores.s, 1)

    def pe(self, pe):
        k, ps = self.k, self.k.ps
        self.pe_scores(pe, 0)
        for n in range(NBLK):
            if n + 1 < NBLK:
                self.pe_scores(pe, n + 1)
            self.decays.pe(pe, n)
            pe.wait_ge(self.a_ready.s, n + 1)
            if n:
                pe.wait_ge(self.state.s, n)
            for h in range(4):
                out = ps[:, 2, h * P:h * P + P]
                pe.matmul(out, k.rv_tok[:, n, h * P:h * P + P], self.a[n % 2][:, h, :], start=True, stop=n == 0)
                if n:
                    pe.matmul(out, self.r[:, h, :], self.qs[n % 2][:, h, :], start=False, stop=True)
            for h in range(4):
                last = pe.matmul(ps[:, 3, h * P:h * P + P], self.ks[n % 2][:, h, :], k.rv_tok[:, n, h * P:h * P + P],
                                 start=True, stop=True)
            last.then_inc(self.o.s, 1)

    def dve(self, dve):
        k, ps, p = self.k, self.k.ps, self.k.proj
        def prepare(n):
            c = slice(n * P, n * P + P)
            dve.tensor_tensor(self.ks[n % 2][:, :, :], blocks(k.rk_tok[:, n, :]),
                              k.lc(ODD, "kscale").unsqueeze(2).to_broadcast([P, 4, P]), ALU.mult)
            dve.tensor_tensor(self.qs[n % 2][:, :, :], p[:, O_RQ:O_RQ + 4, c], blocks(k.lc(ODD, "qscale")), ALU.mult)
            dve.wait_ge(self.scores.s, n + 1)
            dve.tensor_tensor(self.a[n % 2][:, :, :], blocks(ps[:, n % 2, :]), blocks(k.lc(ODD, "decay")), ALU.mult)\
               .then_inc(self.a_ready.s, 1)
        k.dve_link(dve.tensor_copy(k.rv_split[0], k.rv_s[:, :]))
        dve.tensor_tensor(k.rv_split[1], k.rv_s[:, :], k.rv_split[0].bitcast(F32), ALU.subtract)
        prepare(0)
        for n in range(NBLK):
            if n + 1 < NBLK:
                prepare(n + 1)
            c = slice(n * P, n * P + P)
            dve.wait_ge(self.o.s, n + 1)
            dve.tensor_copy(p[:, O_RQ:O_RQ + 4, c], blocks(ps[:, 2, :]))
            if n == 0:
                ins = dve.tensor_copy(self.r[:, :, :], blocks(ps[:, 3, :]))
            else:
                for h in range(4):
                    ins = dve.scalar_tensor_tensor(self.r[:, h, :], self.r[:, h, :], RET_CHUNK_DECAY[h],
                                                   ps[:, 3, h * P:h * P + P], ALU.mult, ALU.add)
            ins.then_inc(self.state.s, 1)
            dve.wait_ge(self.state.s, n + 1)

    def act(self, act):
        k = self.k
        for i in range(2):
            act.dma_start(k.ret_s[i][:, :, :, :], k.A["state_ret"][0, 4 * i:4 * i + 4].rearrange("b h d e -> d b h e"))\
               .then_inc(k.ret_here.s, 16)
        for i in range(4):
            self.decays.take(act, i)
        act.wait_ge(self.state.s, NBLK)
        k.store(k.O["p_ret"][0, 0].rearrange("h d e -> d h e"), self.r[:, :, :])
        k.stores_done()


class RetSample(Stage):

    def __init__(self, k):
        super().__init__(k)
        self.decays = spread_decays(k, range(4, 8), range(1, 4))
        k.small.reset(k.ret_kept)
        self.t = [k.small(f"rets_t{i}", [P, 4, P]) for i in range(2)]
        self.vb, self.r_new, self.o = (k.counter(f"rets_{n}") for n in ("v_spread", "r_new", "o"))

    def act(self, act):
        k = self.k
        for i in range(4):
            self.decays.take(act, i)
        for i in range(2):
            act.wait_ge(self.r_new.s, 4 * i + 4)
            k.store_state(k.O["s_ret"][0, 4 * i:4 * i + 4].rearrange("b h d e -> d b h e"), k.ret_s[i][:, :, :, :])

    def pe(self, pe):
        k, ps, p = self.k, self.k.ps, self.k.proj
        for b in range(8):
            if b >= 4:
                pe.wait_ge(self.r_new.s, b - 3)
            k.spread_split(pe, ps[:, 4 + b % 4, :], b, 8, k.rv_split).then_inc(self.vb.s, 1)
            if b < 4:
                self.decays.pe(pe, b)
            if b >= 3:
                self.pe_out(pe, b - 3)
        for b in range(5, 8):
            last = self.pe_out(pe, b)
        last.then_inc(self.o.s, 1)

    def pe_out(self, pe, b):
        k = self.k
        pe.wait_ge(self.r_new.s, b + 1)
        for h in range(4):
            last = pe.matmul(k.ps[:, 0, 8 * h + b:8 * h + b + 1], k.ret_s[b // 4][:, b % 4, h, :],
                             k.proj[:, O_RQ + h, SEQ + b:SEQ + b + 1], start=True, stop=True)
        return last

    def dve(self, dve):
        k, ps, p = self.k, self.k.ps, self.k.proj
        dve.wait_ge(k.ret_here.s, 32)
        for b in range(8):
            dve.wait_ge(self.vb.s, b + 1)
            t = self.t[b % 2]
            k.dve_link(dve.tensor_tensor(t[:, :, :], blocks(ps[:, 4 + b % 4, :]),
                                         p[:, O_RK:O_RK + 4, SEQ + b:SEQ + b + 1].to_broadcast([P, 4, P]), ALU.mult))
            for h in range(4):
                ins = dve.scalar_tensor_tensor(k.ret_s[b // 4][:, b % 4, h, :], k.ret_s[b // 4][:, b % 4, h, :], RET_DECAY[h], t[:, h, :],
                                               ALU.mult, ALU.add)
            ins.then_inc(self.r_new.s, 1)
        dve.wait_ge(self.o.s, 1)
        dve.tensor_copy(p[:, O_RQ:O_RQ + 4, SEQ:TOK], ps[:, 0, 0:32].rearrange("p (h b) -> p h b", h=4))


class Center(Stage):

    def __init__(self, k, name, chunks):
        super().__init__(k)
        self.chunks = chunks
        self.mean, self.free = k.counter(f"{name}_mean"), k.counter(f"{name}_free")

    def act(self, act):
        self.k.state_stores_done()

    def pe(self, pe):
        for i, x in enumerate(self.chunks):
            for b, (c0, c1) in enumerate(HALVES):
                last = pe.matmul(self.k.ps[:, 2 * i + b, 0:HALF], self.k.c("ones"), x[:, c0:c1], start=True, stop=True)
            last.then_inc(self.mean.s, 1)

    def dve(self, dve):
        for i, x in enumerate(self.chunks):
            dve.wait_ge(self.mean.s, i + 1)
            dve.scalar_tensor_tensor(two(x), self.k.ps[:, 2 * i:2 * i + 2, 0:HALF], -1.0 / P, two(x), ALU.mult, ALU.add)


def ret_norm(k):
    k.small.reset(k.odd_kept)
    def apply(dve, u, rstd):
        x = k.proj[:, O_RQ + u, :]
        k.dve_link(dve.scalar_tensor_tensor(x, x, k.col(V_RETN + u), rstd, ALU.mult, ALU.mult))
        k.dve_link(dve.tensor_tensor(x, x, k.proj[:, O_RG + u, :], ALU.mult))
        return split_out(k, dve, k.y_hi[:, 8 + u, :], k.y_lo[:, 8 + u, :], x)
    return HeadNorm(k, "ret_norm", [[k.proj[:, O_RQ + u, :]] for u in range(4)], k.c("ones"), P, apply)


class SsdPrompt(Stage):

    def __init__(self, k):
        super().__init__(k)
        k.small.reset(k.odd_kept)
        k.mid.reset(12 * TOK * 4)
        self.l = [k.small(f"ssd_l{i}", [P, 16, P]) for i in range(2)]
        self.t = k.small("ssd_t", [P, 8, P])
        self.bt = [k.small(f"ssd_bt{i}", [P, 2 * P]) for i in range(2)]
        self.xdt = [k.mid(f"ssd_xdt{i}", [P, 16, 64]) for i in range(2)]
        self.xw = k.mid("ssd_xw", [P, 16, 64])
        k.ssd_state = k.mid("ssd_state", [P, 16, 64])
        (self.xturn, self.xdt_ready, self.b_c, self.bt_ready, self.seg, self.masked, self.l_ready, self.w_ready,
         self.y, self.y_later, self.y_read, self.added, self.state) = (k.counter(f"ssd_{n}") for n in (
             "x_turned", "xdt", "b_c", "bt", "seg", "masked", "l", "w", "y", "y_later", "y_read", "added", "state"))
        k.big.reset(O_RQ * TOK * 4)
        k.ssd_s = [k.big(f"ssd_s{b}", [P, 8, P]) for b in range(8)]

    def pe_exponents(self, pe, n, q):
        k, c = self.k, slice(n * P, n * P + P)
        if 4 * n + q >= 2:
            pe.wait_ge(self.masked.s, 4 * n + q - 1)
        for i in range(4):
            last = pe.matmul(k.ps[:, q % 2, i * P:i * P + P], k.onehot(4 * q + i, 16), k.cum[:, c], start=True, stop=True)
        last.then_inc(self.seg.s, 1)

    def pe_front(self, pe, n):
        k, ps, p, c = self.k, self.k.ps, self.k.proj, slice(n * P, n * P + P)
        self.pe_exponents(pe, n, 0)
        self.pe_exponents(pe, n, 1)
        if n >= 2:
            pe.wait_ge(self.state.s, n - 1)
        for j in range(8):
            last = pe.transpose(ps[:, 5 + j // 4, (j % 4) * P:(j % 4) * P + P], p[:, O_X + j, c], k.c("ident"))
        last.then_inc(self.xturn.s, 1)
        self.pe_exponents(pe, n, 2)
        self.pe_exponents(pe, n, 3)
        if n:
            pe.wait_ge(self.w_ready.s, n)
        for g in range(2):
            pe.transpose(ps[:, 7, g * P:g * P + P], p[:, O_B + g, c], k.c("ident"))
        for g in range(2):
            last = pe.matmul(ps[:, 7, (2 + g) * P:(3 + g) * P], p[:, O_B + g, c], p[:, O_C + g, c], start=True, stop=True)
        last.then_inc(self.b_c.s, 1)

    def pe_state(self, pe, n, a):
        k = self.k
        for j in range(4 * a, 4 * a + 4):
            last = pe.matmul(k.ps[:, 3, (j % 4) * P:(j % 4) * P + P], k.ssd_state[:, 2 * j:2 * j + 2, :],
                             k.proj[:, O_C + a, n * P:n * P + P], start=True, stop=True)
        return last

    def pe(self, pe):
        k, ps = self.k, self.k.ps
        self.pe_front(pe, 0)
        for n in range(NBLK):
            if n + 1 < NBLK:
                self.pe_front(pe, n + 1)
            pe.wait_ge(self.w_ready.s, n + 1)
            pe.wait_ge(self.bt_ready.s, n + 1)
            if n:
                pe.wait_ge(self.state.s, n)
            for h in range(16):
                j = h // 2
                last = pe.matmul(ps[64 * (h % 2):64 * (h % 2) + 64, 2 + 2 * (j // 4), (j % 4) * P:(j % 4) * P + P],
                                 self.xdt[n % 2][:, h, :], self.l[n % 2][:, h, :], start=True, stop=True)
            if n:
                last = self.pe_state(pe, n, 0)
            last.then_inc(self.y.s, 1)
            if n + 1 < NBLK:
                pe.wait_ge(self.xdt_ready.s, n + 2)
            for g in range(2):
                last = pe.matmul(ps[:, 5 + g, :], self.bt[n % 2][:, g * P:g * P + P], self.xw[:, 8 * g:8 * g + 8, :],
                                 start=True, stop=True)
            last.then_inc(self.added.s, 1)
            if n:
                pe.wait_ge(self.y_read.s, n)
                self.pe_state(pe, n, 1).then_inc(self.y_later.s, 1)

    def act(self, act):
        k, ps = self.k, self.k.ps
        for b in range(8):
            act.dma_start(k.ssd_s[b][:, :, :], k.A["state_ssd"][0, b].rearrange("(j t) p n -> (t p) j n", t=2))\
               .then_inc(k.ssd_here.s, 16)
        for n in range(NBLK):
            l = self.l[n % 2]
            for q in range(4):
                act.wait_ge(self.masked.s, 4 * n + q + 1)
                for h in range(4 * q, 4 * q + 4):
                    ins = act.activation(l[:, h, :], l[:, h, :], ACT.Exp, bias=k.ncum_col[:, n, h:h + 1])
                ins.then_inc(self.l_ready.s, 1)
            act.wait_ge(self.b_c.s, n + 1)
            if n >= 2:
                act.wait_ge(self.added.s, n - 1)
            act.activation(self.bt[n % 2][:, :], ps[:, 7, 0:2 * P], ACT.Copy).then_inc(self.bt_ready.s, 1)

    def dve_mask(self, dve, n, q):
        k = self.k
        dve.wait_ge(self.seg.s, 4 * n + q + 1)
        dve.tensor_tensor(self.l[n % 2][:, 4 * q:4 * q + 4, :], blocks(k.ps[:, q % 2, :]),
                          k.c("causal").unsqueeze(1).to_broadcast([P, 4, P]), ALU.add).then_inc(self.masked.s, 1)

    def dve_front(self, dve, n):
        k, ps = self.k, self.k.ps
        self.dve_mask(dve, n, 0)
        self.dve_mask(dve, n, 1)
        dve.wait_ge(self.xturn.s, n + 1)
        for g in range(2):
            ins = dve.tensor_tensor(self.xdt[n % 2][:, 8 * g:8 * g + 8, :],
                                    ps[:, 5 + g, :].rearrange("p (h d) -> p h d", h=8),
                                    k.dt_col[:, n, 8 * g:8 * g + 8].unsqueeze(2).to_broadcast([P, 8, 64]), ALU.mult)
        ins.then_inc(self.xdt_ready.s, 1)

    def dve_weights(self, dve, n):
        k, l, xdt = self.k, self.l[n % 2], self.xdt[n % 2]
        dve.wait_ge(self.l_ready.s, 4 * n + 4)
        dve.wait_ge(self.xdt_ready.s, n + 1)
        k.dve_link(dve.tensor_tensor(self.xw[:, :, :], xdt[:, :, :], l[:, :, P - 1:P].to_broadcast([P, 16, 64]),
                                     ALU.mult))
        dve.wait_ge(self.bt_ready.s, n + 1)
        for g in range(2):
            ins = dve.tensor_tensor(l[:, 8 * g:8 * g + 8, :], l[:, 8 * g:8 * g + 8, :],
                                    k.ps[:, 7, (2 + g) * P:(3 + g) * P].unsqueeze(1).to_broadcast([P, 8, P]), ALU.mult)
        ins.then_inc(self.w_ready.s, 1)

    def dve(self, dve):
        k, ps, p = self.k, self.k.ps, self.k.proj
        self.dve_front(dve, 0)
        self.dve_mask(dve, 0, 2)
        self.dve_mask(dve, 0, 3)
        for n in range(NBLK):
            c = slice(n * P, n * P + P)
            if n + 1 < NBLK:
                self.dve_front(dve, n + 1)
            self.dve_weights(dve, n)
            if n + 1 < NBLK:
                self.dve_mask(dve, n + 1, 2)
                self.dve_mask(dve, n + 1, 3)
            dve.wait_ge(self.y.s, n + 1)
            for a in range(2):
                t = self.t[:, 4 * a:4 * a + 4, :]
                if n:
                    if a:
                        dve.wait_ge(self.y_later.s, n)
                    ins = dve.tensor_tensor(t, blocks(ps[:, 3, :]), k.ec[:, 4 * a:4 * a + 4, c], ALU.mult)
                    if a == 0:
                        ins.then_inc(self.y_read.s, 1)
                        dve.wait_ge(self.y_read.s, n)
                    else:
                        k.dve_link(ins)
                    k.dve_link(dve.tensor_tensor(t, t, blocks(ps[:, 2 + 2 * a, :]), ALU.add))
                else:
                    k.dve_link(dve.tensor_copy(t, blocks(ps[:, 2 + 2 * a, :])))
                for j in range(4 * a, 4 * a + 4):
                    x = p[:, O_X + j, c]
                    dve.scalar_tensor_tensor(x, x, k.d_pair[:, j:j + 1], self.t[:, j, :], ALU.mult, ALU.add)
            if n:
                k.dve_link(dve.tensor_tensor(k.ssd_state[:, :, :], k.ssd_state[:, :, :],
                                             k.dec[:, n, :].unsqueeze(2).to_broadcast([P, 16, 64]), ALU.mult))
            dve.wait_ge(self.added.s, n + 1)
            for g in range(2):
                s, q = k.ssd_state[:, 8 * g:8 * g + 8, :], ps[:, 5 + g, :].rearrange("p (h d) -> p h d", h=8)
                ins = dve.tensor_tensor(s, s, q, ALU.add) if n else dve.tensor_copy(s, q)
            ins.then_inc(self.state.s, 1)
            dve.wait_ge(self.state.s, n + 1)


class SsdTurn(Turn):

    def __init__(self, k):
        k.small.reset(k.odd_kept)
        self.out = k.small("ssd_out", [P, 8, P])
        k.bc_s = k.small("ssd_bc_s", [8, 512])
        k.ssd_kept = k.small.at
        items = [([(k.ssd_state[:, 2 * j:2 * j + 2, :].rearrange("p a b -> p (a b)"), (j - 4 * a) * P)
                   for j in range(4 * a, 4 * a + 4)], lambda b: blocks(b[:, 0:512]), self.out[:, 4 * a:4 * a + 4, :])
                 for a in range(2)]
        items.append(([(k.proj[:, O_B + i, SEQ:TOK], i * P) for i in range(4)], lambda b: b[0:8, 0:512], k.bc_s[:, :]))
        super().__init__(k, "ssd_turn", items)

    def act(self, act):
        k = self.k
        super().act(act)
        act.wait_ge(self.free.s, self.base + len(self.items))
        k.store(k.O["p_ssd"][0, 0].rearrange("(j t) p n -> (t p) j n", t=2), self.out[:, :, :])


class SsdSample(Gemm):

    def __init__(self, k):
        k.small.reset(k.ssd_kept)
        self.xdt, self.y = k.small("ssds_xdt", [P, 8, 8]), k.small("ssds_y", [P, 8, 8])
        k.mid.reset(12 * TOK * 4)
        self.t = [k.mid(f"ssds_t{i}", [P, 8, P]) for i in range(2)]
        self.u = [k.mid(f"ssds_u{i}", [P, 8, P]) for i in range(2)]
        self.bc, self.scaled, self.s_new, self.free = (k.counter(f"ssds_{n}") for n in ("bc", "scaled", "s_new", "bc_free"))
        w = k.A["odd_w_out"][0]
        tiles = [gemm_tile(w, [(m * P, P)], (k.y_hi, k.y_lo), out_residual(k, m), k0=8, nk=4) for m in range(DC)]
        for b in range(NSAMPLE):
            tiles[b]["pe_before"] = lambda pe, b=b: self.pe_spread(pe, b)
            follow(tiles, b, lambda dve, n, b=b: self.dve_step(dve, b), lambda act, n, b=b: self.act_step(act, b))
        super().__init__(k, tiles)

    def act_store(self, act, b):
        k = self.k
        act.wait_ge(self.s_new.s, b + 1)
        k.store(k.O["s_ssd"][0, b].rearrange("(j t) p n -> (t p) j n", t=2), k.ssd_s[b][:, :, :])

    def act_step(self, act, b):
        k = self.k
        if b == 0:
            act.wait_ge(k.ssd_here.s, 128)
        for j in range(8):
            ins = act.activation(k.ssd_s[b][:, j, :], k.ssd_s[b][:, j, :], ACT.Copy,
                                 scale=k.ec[:, j, SEQ + b:SEQ + b + 1])
        ins.then_inc(self.scaled.s, 1)
        if b >= 2:
            self.act_store(act, b - 2)

    def act(self, act):
        super().act(act)
        for b in range(NSAMPLE - 2, NSAMPLE):
            self.act_store(act, b)

    def pe_spread(self, pe, b):
        k = self.k
        if b >= 2:
            pe.wait_ge(self.free.s, b - 1)
        pe.matmul(k.ps[:, 6 + b % 2, :], k.onehot(b, 8), k.bc_s[:, :], start=True, stop=True).then_inc(self.bc.s, 1)

    def dve_step(self, dve, b):
        k = self.k
        four = lambda t: t.rearrange("p (g j) n -> p g j n", g=2)
        row = lambda i: k.ps[:, 6 + b % 2, 256 * i:256 * i + 256].rearrange("p (g n) -> p g n", g=2).unsqueeze(2)\
            .to_broadcast([P, 2, 4, P])
        t, u, st = self.t[b % 2][:, :, :], self.u[b % 2][:, :, :], k.ssd_s[b][:, :, :]
        dve.wait_ge(self.bc.s, b + 1)
        k.dve_link(dve.tensor_tensor(four(t), row(0), four(self.xdt[:, :, b:b + 1].to_broadcast([P, 8, P])), ALU.mult))
        dve.wait_ge(self.scaled.s, b + 1)
        dve.tensor_tensor(st, st, t, ALU.add).then_inc(self.s_new.s, 1)
        dve.wait_ge(self.s_new.s, b + 1)
        dve.tensor_tensor(four(u), four(st), row(1), ALU.mult).then_inc(self.free.s, 1)
        dve.wait_ge(self.free.s, b + 1)
        self.last = dve.tensor_reduce(self.y[:, :, b:b + 1], u, AX.X, ALU.add)

    def dve(self, dve):
        k = self.k
        x = k.proj[:, O_X:O_X + 8, SEQ:TOK]
        k.dve_link(dve.tensor_tensor(self.xdt[:, :, :], x, k.dt_pair[:, :, :], ALU.mult))
        super().dve(dve)
        k.dve_link(self.last)
        k.dve_link(dve.tensor_tensor(self.xdt[:, :, :], x, k.d_pair[:, :].unsqueeze(2).to_broadcast([P, 8, 8]), ALU.mult))
        dve.tensor_tensor(x, self.xdt[:, :, :], self.y[:, :, :], ALU.add)


class SsdNorm(Stage):

    def __init__(self, k):
        super().__init__(k)
        k.small.reset(k.ssd_kept)
        self.sq = [k.small(f"ssd_sq{i}", [P, TOK]) for i in range(2)]
        k.ssd_rstd_at = k.small.at
        k.ssd_rstd = [k.small(f"ssd_rstd{i}", [P, TOK]) for i in range(2)]
        k.ssd_rstd_end = k.small.at
        self.gated, self.squared, self.high, self.summed = (
            k.counter(f"ssd_{n}") for n in ("gated", "squared", "high", "summed"))

    def dve(self, dve):
        k, p = self.k, self.k.proj
        for c in range(8):
            dve.tensor_tensor(p[:, O_X + c, :], p[:, O_X + c, :], p[:, O_Z + c, :], ALU.mult).then_inc(self.gated.s, 1)
        for c in range(8):
            dve.wait_ge(self.gated.s, c + 1)
            dve.wait_ge(self.high.s, c + 1)
            dve.scalar_tensor_tensor(k.y_lo[:, c, :], p[:, O_X + c, :], k.col(V_SSDN + c), k.y_hi[:, c, :].bitcast(F32),
                                     ALU.mult, ALU.subtract)

    def act(self, act):
        k, p = self.k, self.k.proj
        for c in range(8):
            act.wait_ge(self.gated.s, c + 1)
            act.activation(k.y_hi[:, c, :], p[:, O_X + c, :], ACT.Copy, scale=k.col(V_SSDN + c)).then_inc(self.high.s, 1)
            if c >= 2:
                act.wait_ge(self.summed.s, c - 1)
            act.activation(self.sq[c % 2][:, :], p[:, O_X + c, :], ACT.Square).then_inc(self.squared.s, 1)
        for u in range(2):
            act.wait_ge(self.summed.s, 4 * u + 4)
            rstd = k.ssd_rstd[u][:, :]
            k.act_link(act.activation(two(rstd), k.ps[:, 2 * u:2 * u + 2, 0:HALF], ACT.Ln, scale=1.0 / 512,
                                      bias=k.c("eps")))
            act.activation(rstd, rstd, ACT.Exp, scale=-0.5)

    def pe(self, pe):
        k = self.k
        for c in range(8):
            pe.wait_ge(self.squared.s, c + 1)
            for b, (c0, c1) in enumerate(HALVES):
                last = pe.matmul(k.ps[:, 2 * (c // 4) + b, 0:HALF], k.c("ones"), self.sq[c % 2][:, c0:c1],
                                 start=c % 4 == 0, stop=c % 4 == 3)
            last.then_inc(self.summed.s, 1)


def out_ssd(k, m, u, t):
    def emit(dve, src, nb):
        k.dve_link(dve.tensor_tensor(two(t[:, :]), src, two(k.ssd_rstd[u][:, :]), ALU.mult))
        dve.tensor_tensor(k.x[:, m, :], k.x[:, m, :], t[:, :], ALU.add).then_inc(k.tile_out.s, 1)
    return emit


class OddStored(Stage):

    def act(self, act):
        self.k.stores_done()


def odd_layer(k):
    s = [ConvHistory(k), odd_projection(k), ConvTurn(k), odd_spread(k)]
    s += [ret_turn(k), RetPrompt(k), RetSample(k), Center(k, "ret", [k.proj[:, O_RQ + h, :] for h in range(4)]),
          ret_norm(k), SsdPrompt(k), SsdTurn(k), SsdSample(k), SsdNorm(k), OddStored(k)]
    w = k.A["odd_w_out"][0]
    k.small.reset()
    norm = next_norm(k, "odd_out", V_XATT + DC, k.xc)
    t = k.small("odd_out_t", [P, TOK])
    assert k.small.at <= k.ssd_rstd_at
    s.append(Gemm(k, [gemm_tile(w, [(m * P, P)], (k.y_hi, k.y_lo), out_ssd(k, m, u, t), k0=4 * u, nk=4,
                                **({"finish": m} if u else {})) for m in range(DC) for u in range(2)], norm))
    k.small.reset(k.ssd_rstd_end)
    prefetch_memory(k, s[-1].mine, 1)
    return s


def plan(k):
    stages = [Load(k)]
    for layer, mixer in enumerate((even_layer, odd_layer)):
        stages += mixer(k) + cross_layer(k, layer)
        if layer == 0:
            stages.append(OddLoads(k))
        stages.append(Ffn(k, layer))
    return stages + [Emit(k)]


class Emit(Stage):

    def __init__(self, k):
        super().__init__(k)
        k.big.reset()
        self.y = k.big("y_tok", [P, NBLK, D_MODEL])
        self.ys = k.big("ys_tok", [NSAMPLE, D_MODEL])
        items = []
        for n in range(NBLK):
            for g in range(2):
                items.append(([(k.x[:, 4 * g + c, n * P:n * P + P], c * P) for c in range(4)],
                              lambda b: b[:, 0:512], self.y[:, n, 512 * g:512 * g + 512]))
        for g in range(2):
            items.append(([(k.x[:, 4 * g + c, SEQ:TOK], c * P) for c in range(4)],
                          lambda b: b[0:8, 0:512], self.ys[:, 512 * g:512 * g + 512]))
        self.turn = Turn(k, "emit", items)

    def pe(self, pe): self.turn.pe(pe)
    def dve(self, dve): self.turn.dve(dve)

    def act(self, act):
        k = self.k
        self.turn.act(act)
        act.wait_ge(self.turn.free.s, self.turn.base + len(self.turn.items))
        k.store(k.O["y_prompt"].rearrange("b (n p) d -> p (b n) d", p=P), self.y[:, :, :])
        k.store(k.O["y_sample"].rearrange("b t d -> (b t) d"), self.ys[:, :])


def program(nc, A, C, O):
    with ExitStack() as ctx:
        k = Core(nc, ctx, A, C, O)
        k.gate_i, k.gate_f = k.params("gate_i", [4, 1]), k.params("gate_f", [4, 1])
        k.dt_bias, k.a_log, k.d_skip = (k.params(n, [16, 1]) for n in ("dt_bias", "a_log", "d_skip"))
        k.sink_row, k.sink_col = k.params("sink_row", [P, 8]), k.params("sink_col", [64, 1])
        k.norm_signals = [k.counter(n) for n in ("squares_ready", "squares_summed", "rstd_ready", "rstd_used")]
        k.norm_count = (0, 0)
        k.ident_r = k.params("ident_r", [16, 16], F32R)
        k.n_row_norms, k.n_logs = 0, 0
        k.row_norm_signals = [k.counter(f"row_norm_{n}") for n in ("squared", "summed", "rstd", "normed")]
        k.log_signals = [k.counter(n) for n in ("minus_abs", "exp_ready", "one_plus_exp", "log_ready")]
        k.turn_signals, k.turn_count = (k.counter("turned"), k.counter("turn_copied")), 0
        k.spread_signals, k.spread_count = (k.counter("spread"), k.counter("spread_free")), 0
        k.ssd_here, k.odd_here = k.counter("ssd_states_here"), k.counter("odd_constants_here")
        k.mem_here, k.cache_here = k.counter("memory_here"), k.counter("memory_cache_here")
        k.mem_signals = [k.counter(f"mem_{n}") for n in ("turned", "split", "squared", "summed")]
        k.xa_signals = [k.counter(f"xa_{n}") for n in ("scores", "max", "exps", "probs", "turned", "pt", "pv", "out")]
        k.xs_signals = [k.counter(f"xs_{n}") for n in ("k_turned", "kt", "q", "scored", "scores", "max", "exps", "probs",
                                                      "p_turned", "pt", "pv", "o", "o_turned")]
        k.ffn_signals = [k.counter(n) for n in ("relu_ready", "squared", "hidden_ready")]
        stages = plan(k)
        count = [0] * RING
        k.arrivals = []
        for n, t in enumerate(k.tiles):
            count[n % RING] += len(t["parts"])
            k.arrivals.append(count[n % RING])
        block = ctx.enter_context(nc.Block())

        @block.sync
        def _(sp):
            stream_weights(k, sp, stages[0])

        @block.gpsimd
        def _(pool):
            split_low(k, pool)

        @block.tensor
        def _(pe):
            for s in stages:
                s.pe(pe)
                k.fence(pe, "pe")

        @block.vector
        def _(dve):
            for s in stages:
                s.dve(dve)
                k.fence(dve, "dve")

        @block.scalar
        def _(act):
            for s in stages:
                s.act(act)
                k.fence(act, "act")
            k.stores_done()
            k.state_stores_done()


OUTPUTS = [
    ("y_prompt", (1, SEQ, D_MODEL)), ("y_sample", (8, 1, D_MODEL)),
    ("mem_k", (2, 1, MEM, 4, P)), ("mem_v", (2, 1, MEM, 4, P)),
    ("p_swa_k", (1, 1, P, 2, 64)), ("p_swa_v", (1, 1, P, 2, 64)),
    ("p_C", (1, 1, 4, 64, P)), ("p_n", (1, 1, 4, 64)), ("p_m", (1, 1, 4)),
    ("p_conv", (1, 1, 3, 1536)), ("p_ssd", (1, 1, 16, 64, P)), ("p_ret", (1, 1, 4, P, P)),
    ("s_swa_k", (1, 8, P, 2, 64)), ("s_swa_v", (1, 8, P, 2, 64)),
    ("s_C", (1, 8, 4, 64, P)), ("s_n", (1, 8, 4, 64)), ("s_m", (1, 8, 4)),
    ("s_conv", (1, 8, 3, 1536)), ("s_ssd", (1, 8, 16, 64, P)), ("s_ret", (1, 8, 4, P, P)),
]


def kernel(**inputs):
    import concourse.bacc as bacc
    from concourse.bass_utils import run_bass_kernel_spmd

    nc = bacc.Bacc("TRN2", target_bir_lowering=False, num_devices=1)
    arrays, A, O = {}, {}, {}
    for name, a in inputs.items():
        a = np.ascontiguousarray(a)
        arrays[f"in_{name}"] = a
        A[name] = nc.dram_tensor(f"in_{name}", a.shape, mybir.dt.from_np(a.dtype), kind="ExternalInput").ap()
    arrays["shape_constants"] = shape_constants()
    C = nc.dram_tensor("shape_constants", arrays["shape_constants"].shape, F32, kind="ExternalInput").ap()
    for name, shape in OUTPUTS:
        O[name] = nc.dram_tensor(f"out_{name}", shape, F32, kind="ExternalOutput").ap()
    program(nc, A, C, O)
    r = run_bass_kernel_spmd(nc, [arrays], core_ids=[0])
    return tuple(r.results[0][f"out_{name}"] for name, _ in OUTPUTS)
```
